# Optimizing a Trainium2 kernel written in Bass

```python
import math
import numpy as np
import jax
import jax.numpy as jnp
from jax import lax

D_MODEL = 1024
BATCH = 1
SEQ = 1024
DEPTH = 2

HEAD_DIM = 64
Q_BLOCK = 128
SB_HEADS = 8
SB_WIDTH = SB_HEADS * HEAD_DIM
NSA_HEADS = 8
NSA_KV_GROUPS = 2
NSA_REP = NSA_HEADS // NSA_KV_GROUPS
NSA_WIDTH = NSA_HEADS * HEAD_DIM
NSA_KV_WIDTH = NSA_KV_GROUPS * HEAD_DIM
NSA_N_BRANCH = 3
CMP_LEN = 32
CMP_STRIDE = 16
CMP_HIDDEN = 256
SLC_LEN = 64
SLC_TOPN = 8
SLC_LOCAL = 2
SLC_FORCE_BONUS = 1e4
WINDOW = 512
ROPE_THETA = 500000.0
ROPE_DIM = HEAD_DIM // 4
SSM_GROUP = 16
SSM_GROUPS = D_MODEL // SSM_GROUP
SSM_STATE = 64
DT_MIN = 1e-3
DT_MAX = 1e-1
N_EXPERTS = 64
N_EXPERT_GROUPS = 8
TOPK_GROUPS = 4
TOP_K = 6
EXPERT_HIDDEN = 256
SHARED_HIDDEN = 256
ROUTED_SCALE = 2.5
MOE_BLOCK = 128
DN_ALPHA = (2 * DEPTH) ** 0.25
DN_BETA = (8 * DEPTH) ** -0.25
LN_EPS = 1e-5
NEG_INF = -1e30

kernel_name = "hybrid_sb_nsa_s5_moe_deepnorm"

def _mix0_layout():
    sizes = [SB_WIDTH] * 3 + [NSA_WIDTH] + [NSA_KV_WIDTH] * 6 + [NSA_HEADS * NSA_N_BRANCH]
    value_cols = (2, 5, 7, 9)
    scales = [DN_BETA if i in value_cols else 1.0 for i in range(len(sizes))]
    return sizes, scales

def layer_norm(x, g, b):
    xf = x.astype(jnp.float32)
    mu = jnp.mean(xf, axis=-1, keepdims=True)
    var = jnp.mean(jnp.square(xf - mu), axis=-1, keepdims=True)
    y = (xf - mu) * lax.rsqrt(var + LN_EPS)
    return (y * g.astype(jnp.float32) + b.astype(jnp.float32)).astype(x.dtype)

def masked_softmax(s, mask):
    s = jnp.where(mask, s.astype(jnp.float32), NEG_INF)
    p = jax.nn.softmax(s, axis=-1)
    return jnp.where(mask, p, 0.0)

def rope_tables(S):
    inv = jnp.power(ROPE_THETA, -jnp.arange(0, ROPE_DIM, 2, dtype=jnp.float32) / ROPE_DIM)
    ang = jnp.arange(S, dtype=jnp.float32)[:, None] * inv[None, :]
    return jnp.cos(ang), jnp.sin(ang)

def rope_partial(x, cos, sin):
    half = ROPE_DIM // 2
    c = cos.astype(x.dtype)
    s = sin.astype(x.dtype)
    x1 = x[..., :half]
    x2 = x[..., half:ROPE_DIM]
    return jnp.concatenate([x1 * c - x2 * s, x2 * c + x1 * s, x[..., ROPE_DIM:]], axis=-1)

def hybrid_attention_mixer(x, w_in, cmp_pos_k, cmp_pos_v, cmp_k_w1, cmp_k_w2,
                           cmp_v_w1, cmp_v_w2, w_out):
    B, S, _ = x.shape
    dt = x.dtype
    G, R, d = NSA_KV_GROUPS, NSA_REP, HEAD_DIM
    nq = S // Q_BLOCK
    scale = HEAD_DIM ** -0.5
    sizes, _ = _mix0_layout()
    splits = np.cumsum(sizes)[:-1].tolist()
    proj = x @ w_in
    (q_a, k_a, v_a, q_b, kc, vc, ks, vs, kw, vw, g_raw) = jnp.split(proj, splits, axis=-1)

    def heads(t, n):
        return t.reshape(B, S, n, d).transpose(0, 2, 1, 3)

    q_a, k_a, v_a = heads(q_a, SB_HEADS), heads(k_a, SB_HEADS), heads(v_a, SB_HEADS)
    qa_blocks = q_a.reshape(B, SB_HEADS, nq, Q_BLOCK, d).transpose(2, 0, 1, 3, 4)
    key_idx = jnp.arange(S)

    def sb_block(args):
        q_blk, i = args
        t = i * Q_BLOCK + jnp.arange(Q_BLOCK)
        z = jnp.einsum('bhqd,bhkd->bhqk', q_blk, k_a).astype(jnp.float32) * scale
        causal = key_idx[None, :] < t[:, None]
        log_1m = jnp.where(causal, -jax.nn.softplus(z), 0.0)
        suffix = lax.cumsum(log_1m, axis=z.ndim - 1, reverse=True) - log_1m
        w = jnp.where(causal, jnp.exp(jax.nn.log_sigmoid(z) + suffix), 0.0)
        return jnp.einsum('bhqk,bhkd->bhqd', w.astype(dt), v_a)

    o_a = lax.map(sb_block, (qa_blocks, jnp.arange(nq)))
    o_a = o_a.transpose(1, 0, 3, 2, 4).reshape(B, S, SB_WIDTH)

    cos, sin = rope_tables(S)
    qn = rope_partial(heads(q_b, NSA_HEADS), cos, sin).reshape(B, G, R, S, d)
    qn_blocks = qn.reshape(B, G, R, nq, Q_BLOCK, d).transpose(3, 0, 1, 2, 4, 5)
    gates = jax.nn.sigmoid(g_raw).reshape(B, S, NSA_HEADS, NSA_N_BRANCH).transpose(0, 2, 1, 3)
    gate_blocks = gates.reshape(B, G, R, nq, Q_BLOCK, NSA_N_BRANCH).transpose(3, 0, 1, 2, 4, 5)

    n_cmp = (S - CMP_LEN) // CMP_STRIDE + 1
    n_slc = S // SLC_LEN
    cmp_start = np.arange(n_cmp) * CMP_STRIDE
    cmp_stop = cmp_start + CMP_LEN - 1
    slc_start = np.arange(n_slc) * SLC_LEN
    slc_stop = slc_start + SLC_LEN - 1
    cmp_idx = cmp_start[:, None] + np.arange(CMP_LEN)[None, :]
    overlap = jnp.asarray(((cmp_start[:, None] <= slc_stop[None, :]) &
                           (cmp_stop[:, None] >= slc_start[None, :])).astype(np.float32))
    cmp_end = jnp.asarray(cmp_stop)
    kc_tok = rope_partial(heads(kc, G), cos, sin)
    vc_tok = heads(vc, G)
    kc_blk = (kc_tok[:, :, cmp_idx] + cmp_pos_k).reshape(B, G, n_cmp, CMP_LEN * d)
    vc_blk = (vc_tok[:, :, cmp_idx] + cmp_pos_v).reshape(B, G, n_cmp, CMP_LEN * d)
    k_cmp = jax.nn.gelu(kc_blk @ cmp_k_w1) @ cmp_k_w2
    v_cmp = jax.nn.gelu(vc_blk @ cmp_v_w1) @ cmp_v_w2

    k_slc = rope_partial(heads(ks, G), cos, sin).reshape(B, G, n_slc, SLC_LEN, d)
    v_slc = heads(vs, G).reshape(B, G, n_slc, SLC_LEN, d)
    n_top = min(SLC_TOPN, n_slc)
    blk_ids = jnp.arange(n_slc)
    bi = jnp.arange(B)[:, None, None, None]
    gi = jnp.arange(G)[None, :, None, None]

    pad = ((0, 0), (0, 0), (WINDOW, 0), (0, 0))
    k_win_pad = jnp.pad(rope_partial(heads(kw, G), cos, sin), pad)
    v_win_pad = jnp.pad(heads(vw, G), pad)

    def nsa_block(args):
        q_blk, g_blk, i = args
        t = i * Q_BLOCK + jnp.arange(Q_BLOCK)
        s_c = jnp.einsum('bgrqd,bgnd->bgrqn', q_blk, k_cmp) * scale
        p_c = masked_softmax(s_c, cmp_end[None, :] <= t[:, None])
        o_c = jnp.einsum('bgrqn,bgnd->bgrqd', p_c.astype(dt), v_cmp)
        imp = jnp.einsum('bgrqn,nm->bgqm', p_c, overlap)
        cur = t // SLC_LEN
        valid = blk_ids[None, :] <= cur[:, None]
        forced = (blk_ids[None, :] == 0) | (valid & (blk_ids[None, :] > cur[:, None] - SLC_LOCAL))
        imp = jnp.where(forced, imp + SLC_FORCE_BONUS, jnp.where(valid, imp, NEG_INF))
        _, sel = lax.top_k(imp, n_top)
        k_sel = k_slc[bi, gi, sel]
        v_sel = v_slc[bi, gi, sel]
        s_s = jnp.einsum('bgrqd,bgqnld->bgrqnl', q_blk, k_sel) * scale
        key_pos = sel[..., None] * SLC_LEN + jnp.arange(SLC_LEN)
        m_s = (key_pos <= t[None, None, :, None, None]).reshape(B, G, 1, Q_BLOCK, n_top * SLC_LEN)
        p_s = masked_softmax(s_s.reshape(B, G, R, Q_BLOCK, n_top * SLC_LEN), m_s)
        p_s = p_s.reshape(B, G, R, Q_BLOCK, n_top, SLC_LEN).astype(dt)
        o_s = jnp.einsum('bgrqnl,bgqnld->bgrqd', p_s, v_sel)
        k_w = lax.dynamic_slice_in_dim(k_win_pad, i * Q_BLOCK, Q_BLOCK + WINDOW, axis=2)
        v_w = lax.dynamic_slice_in_dim(v_win_pad, i * Q_BLOCK, Q_BLOCK + WINDOW, axis=2)
        kp = i * Q_BLOCK - WINDOW + jnp.arange(Q_BLOCK + WINDOW)
        m_w = (kp[None, :] <= t[:, None]) & (kp[None, :] > t[:, None] - WINDOW) & (kp[None, :] >= 0)
        s_w = jnp.einsum('bgrqd,bgkd->bgrqk', q_blk, k_w) * scale
        p_w = masked_softmax(s_w, m_w)
        o_w = jnp.einsum('bgrqk,bgkd->bgrqd', p_w.astype(dt), v_w)
        return g_blk[..., 0:1] * o_c + g_blk[..., 1:2] * o_s + g_blk[..., 2:3] * o_w

    o_b = lax.map(nsa_block, (qn_blocks, gate_blocks, jnp.arange(nq)))
    o_b = o_b.transpose(1, 0, 4, 2, 3, 5).reshape(B, S, NSA_WIDTH)

    return jnp.concatenate([o_a, o_b], axis=-1) @ w_out

def s5_mixer(x, w_in, lambda_re, lambda_im, b_re, b_im, c_re, c_im, d_skip, log_dt,
             w_glu, w_out):
    B, S, _ = x.shape
    f32 = jnp.float32
    u = (x @ w_in).astype(f32).reshape(B, S, SSM_GROUPS, SSM_GROUP)
    lre = lambda_re.astype(f32)
    lim = lambda_im.astype(f32)
    step = jnp.exp(log_dt.astype(f32))[:, None]
    mag = jnp.exp(lre * step)
    abar_re = mag * jnp.cos(lim * step)
    abar_im = mag * jnp.sin(lim * step)
    den = lre * lre + lim * lim
    zoh_re = ((abar_re - 1.0) * lre + abar_im * lim) / den
    zoh_im = (abar_im * lre - (abar_re - 1.0) * lim) / den
    bre, bim = b_re.astype(f32), b_im.astype(f32)
    bbar_re = zoh_re[..., None] * bre - zoh_im[..., None] * bim
    bbar_im = zoh_re[..., None] * bim + zoh_im[..., None] * bre
    cre, cim = c_re.astype(f32), c_im.astype(f32)
    dsk = d_skip.astype(f32)

    def combine(e1, e2):
        a1r, a1i, b1r, b1i = e1
        a2r, a2i, b2r, b2i = e2
        return (a2r * a1r - a2i * a1i, a2r * a1i + a2i * a1r,
                a2r * b1r - a2i * b1i + b2r, a2r * b1i + a2i * b1r + b2i)

    def scan_one(u_b):
        bu_re = jnp.einsum('sgh,gph->sgp', u_b, bbar_re)
        bu_im = jnp.einsum('sgh,gph->sgp', u_b, bbar_im)
        a_re = jnp.broadcast_to(abar_re, bu_re.shape)
        a_im = jnp.broadcast_to(abar_im, bu_im.shape)
        _, _, h_re, h_im = lax.associative_scan(combine, (a_re, a_im, bu_re, bu_im), axis=0)
        return (jnp.einsum('ghp,sgp->sgh', cre, h_re) - jnp.einsum('ghp,sgp->sgh', cim, h_im)
                + dsk * u_b)

    y = lax.map(scan_one, u).reshape(B, S, D_MODEL)
    y = jax.nn.gelu(y).astype(x.dtype)
    y = y * jax.nn.sigmoid(y @ w_glu)
    return y @ w_out

def moe_ffn(x, router, router_bias, w_gate, w_up, w_down, sh_gate, sh_up, sh_down):
    B, S, D = x.shape
    T = B * S
    xf = x.reshape(T, D)
    scores = jax.nn.sigmoid((xf @ router).astype(jnp.float32))
    biased = scores + router_bias.astype(jnp.float32)
    per_grp = N_EXPERTS // N_EXPERT_GROUPS
    grp_score = lax.top_k(biased.reshape(T, N_EXPERT_GROUPS, per_grp), 2)[0].sum(-1)
    _, top_grp = lax.top_k(grp_score, TOPK_GROUPS)
    grp_keep = jnp.any(top_grp[:, :, None] == jnp.arange(N_EXPERT_GROUPS)[None, None, :], axis=1)
    expert_keep = jnp.repeat(grp_keep, per_grp, axis=1)
    _, eidx = lax.top_k(jnp.where(expert_keep, biased, -jnp.inf), TOP_K)
    gate = jnp.take_along_axis(scores, eidx, axis=1)
    gate = gate / jnp.sum(gate, axis=-1, keepdims=True) * ROUTED_SCALE

    n_assign = T * TOP_K
    flat_e = eidx.reshape(-1)
    flat_tok = jnp.repeat(jnp.arange(T, dtype=jnp.int32), TOP_K)
    flat_g = gate.reshape(-1)
    order = jnp.argsort(flat_e)
    se, stok, sg = flat_e[order], flat_tok[order], flat_g[order]
    counts = jnp.bincount(flat_e, length=N_EXPERTS)
    padded = (counts + MOE_BLOCK - 1) // MOE_BLOCK * MOE_BLOCK
    pad_end = jnp.cumsum(padded)
    pad_start = pad_end - padded
    start = jnp.cumsum(counts) - counts
    dest = pad_start[se] + jnp.arange(n_assign) - start[se]
    n_blocks = n_assign // MOE_BLOCK + N_EXPERTS
    n_rows = n_blocks * MOE_BLOCK
    buf_tok = jnp.zeros((n_rows,), jnp.int32).at[dest].set(stok)
    buf_g = jnp.zeros((n_rows,), jnp.float32).at[dest].set(sg)
    blk_e = jnp.minimum(jnp.searchsorted(pad_end, jnp.arange(n_blocks) * MOE_BLOCK, side='right'),
                        N_EXPERTS - 1)

    def expert_block(args):
        tok, g, e = args
        h = xf[tok]
        a = jax.nn.silu(h @ w_gate[e]) * (h @ w_up[e])
        return (a @ w_down[e]) * g[:, None].astype(x.dtype)

    y_blk = lax.map(expert_block, (buf_tok.reshape(n_blocks, MOE_BLOCK),
                                   buf_g.reshape(n_blocks, MOE_BLOCK), blk_e))
    routed = jnp.zeros_like(xf).at[buf_tok].add(y_blk.reshape(n_rows, D))
    shared = (jax.nn.silu(xf @ sh_gate) * (xf @ sh_up)) @ sh_down
    return (routed + shared).reshape(B, S, D)

def setup_inputs(seed: int = 0) -> dict:
    key = jax.random.key(seed)
    keys = iter(jax.random.split(key, 64))

    def nrm(shape, scale):
        return jax.random.normal(next(keys), shape, jnp.float32) * scale

    def add_ln(p, name):
        p[name + "_g"] = 1.0 + nrm((D_MODEL,), 0.01)
        p[name + "_b"] = nrm((D_MODEL,), 0.01)

    def add_moe(p, pre):
        p[pre + "_router"] = nrm((D_MODEL, N_EXPERTS), D_MODEL ** -0.5)
        p[pre + "_router_bias"] = nrm((N_EXPERTS,), 0.01)
        p[pre + "_w_gate"] = nrm((N_EXPERTS, D_MODEL, EXPERT_HIDDEN), D_MODEL ** -0.5)
        p[pre + "_w_up"] = nrm((N_EXPERTS, D_MODEL, EXPERT_HIDDEN), D_MODEL ** -0.5)
        p[pre + "_w_down"] = nrm((N_EXPERTS, EXPERT_HIDDEN, D_MODEL), EXPERT_HIDDEN ** -0.5 * DN_BETA)
        p[pre + "_sh_gate"] = nrm((D_MODEL, SHARED_HIDDEN), D_MODEL ** -0.5)
        p[pre + "_sh_up"] = nrm((D_MODEL, SHARED_HIDDEN), D_MODEL ** -0.5)
        p[pre + "_sh_down"] = nrm((SHARED_HIDDEN, D_MODEL), SHARED_HIDDEN ** -0.5 * DN_BETA)

    p = {}
    p["x"] = nrm((BATCH, SEQ, D_MODEL), 1.0)
    sizes, scales = _mix0_layout()
    col_scale = jnp.concatenate([jnp.full((n,), s, jnp.float32) for n, s in zip(sizes, scales)])
    p["l0_w_in"] = nrm((D_MODEL, sum(sizes)), D_MODEL ** -0.5) * col_scale
    p["l0_cmp_pos_k"] = nrm((CMP_LEN, HEAD_DIM), 0.1)
    p["l0_cmp_pos_v"] = nrm((CMP_LEN, HEAD_DIM), 0.1)
    p["l0_cmp_k_w1"] = nrm((CMP_LEN * HEAD_DIM, CMP_HIDDEN), (CMP_LEN * HEAD_DIM) ** -0.5)
    p["l0_cmp_k_w2"] = nrm((CMP_HIDDEN, HEAD_DIM), CMP_HIDDEN ** -0.5)
    p["l0_cmp_v_w1"] = nrm((CMP_LEN * HEAD_DIM, CMP_HIDDEN), (CMP_LEN * HEAD_DIM) ** -0.5)
    p["l0_cmp_v_w2"] = nrm((CMP_HIDDEN, HEAD_DIM), CMP_HIDDEN ** -0.5)
    p["l0_w_out"] = nrm((SB_WIDTH + NSA_WIDTH, D_MODEL), (SB_WIDTH + NSA_WIDTH) ** -0.5 * DN_BETA)
    add_ln(p, "l0_ln1")
    add_moe(p, "l0")
    add_ln(p, "l0_ln2")
    p["l1_w_in"] = nrm((D_MODEL, D_MODEL), D_MODEL ** -0.5)
    p["l1_lambda_re"] = -0.5 + nrm((SSM_GROUPS, SSM_STATE), 0.02)
    p["l1_lambda_im"] = math.pi * jnp.arange(SSM_STATE, dtype=jnp.float32)[None, :] + nrm((SSM_GROUPS, SSM_STATE), 0.02)
    p["l1_b_re"] = nrm((SSM_GROUPS, SSM_STATE, SSM_GROUP), (2 * SSM_GROUP) ** -0.5)
    p["l1_b_im"] = nrm((SSM_GROUPS, SSM_STATE, SSM_GROUP), (2 * SSM_GROUP) ** -0.5)
    p["l1_c_re"] = nrm((SSM_GROUPS, SSM_GROUP, SSM_STATE), (2 * SSM_STATE) ** -0.5)
    p["l1_c_im"] = nrm((SSM_GROUPS, SSM_GROUP, SSM_STATE), (2 * SSM_STATE) ** -0.5)
    p["l1_d"] = nrm((SSM_GROUPS, SSM_GROUP), 1.0)
    p["l1_log_dt"] = jax.random.uniform(next(keys), (SSM_GROUPS,), jnp.float32,
                                        math.log(DT_MIN), math.log(DT_MAX))
    p["l1_w_glu"] = nrm((D_MODEL, D_MODEL), D_MODEL ** -0.5)
    p["l1_w_out"] = nrm((D_MODEL, D_MODEL), D_MODEL ** -0.5 * DN_BETA)
    add_ln(p, "l1_ln1")
    add_moe(p, "l1")
    add_ln(p, "l1_ln2")
    return p

def reference(x, l0_w_in, l0_cmp_pos_k, l0_cmp_pos_v, l0_cmp_k_w1, l0_cmp_k_w2, l0_cmp_v_w1,
              l0_cmp_v_w2, l0_w_out, l0_ln1_g, l0_ln1_b, l0_router, l0_router_bias, l0_w_gate,
              l0_w_up, l0_w_down, l0_sh_gate, l0_sh_up, l0_sh_down, l0_ln2_g, l0_ln2_b,
              l1_w_in, l1_lambda_re, l1_lambda_im, l1_b_re, l1_b_im, l1_c_re, l1_c_im, l1_d,
              l1_log_dt, l1_w_glu, l1_w_out, l1_ln1_g, l1_ln1_b, l1_router, l1_router_bias,
              l1_w_gate, l1_w_up, l1_w_down, l1_sh_gate, l1_sh_up, l1_sh_down, l1_ln2_g,
              l1_ln2_b):
    mixer_params = [
        (l0_w_in, l0_cmp_pos_k, l0_cmp_pos_v, l0_cmp_k_w1, l0_cmp_k_w2, l0_cmp_v_w1,
         l0_cmp_v_w2, l0_w_out),
        (l1_w_in, l1_lambda_re, l1_lambda_im, l1_b_re, l1_b_im, l1_c_re, l1_c_im, l1_d,
         l1_log_dt, l1_w_glu, l1_w_out),
    ]
    norm1 = [(l0_ln1_g, l0_ln1_b), (l1_ln1_g, l1_ln1_b)]
    moe_params = [
        (l0_router, l0_router_bias, l0_w_gate, l0_w_up, l0_w_down, l0_sh_gate, l0_sh_up, l0_sh_down),
        (l1_router, l1_router_bias, l1_w_gate, l1_w_up, l1_w_down, l1_sh_gate, l1_sh_up, l1_sh_down),
    ]
    norm2 = [(l0_ln2_g, l0_ln2_b), (l1_ln2_g, l1_ln2_b)]
    h = x
    for layer in range(DEPTH):
        if layer % 2 == 0:
            mixed = hybrid_attention_mixer(h, *mixer_params[layer])
        else:
            mixed = s5_mixer(h, *mixer_params[layer])
        h = layer_norm(DN_ALPHA * h + mixed, *norm1[layer])
        h = layer_norm(DN_ALPHA * h + moe_ffn(h, *moe_params[layer]), *norm2[layer])
    return h


_drawn_inputs = setup_inputs


def setup_inputs(seed=0):
    import zlib

    import numpy as np

    out = dict(_drawn_inputs(seed))
    spreads = {}
    factors = {'l0_cmp_pos_k': 6.641,
     'l1_lambda_re': 8.0,
     'l1_b_re': 3.105,
     'l1_b_im': 3.069,
     'l1_c_re': 3.052,
     'l1_c_im': 3.117,
     'l1_ln2_g': 5.543,
     'l1_ln2_b': 5.661}
    for name, (base, spread) in spreads.items():
        noise = np.random.default_rng([zlib.crc32(name.encode()), seed]).standard_normal(out[name].shape)
        drawn = base * np.exp(spread * noise) if base else spread * noise
        out[name] = jnp.asarray(drawn.astype(out[name].dtype))
    for name, factor in factors.items():
        out[name] = (out[name] * factor).astype(out[name].dtype)
    return out
```

```python
import math
from contextlib import ExitStack

import numpy as np

import concourse.bass as bass
from concourse import mybir

F32 = mybir.dt.float32
I32 = mybir.dt.int32
U32 = mybir.dt.uint32
ALU = mybir.AluOpType
ACT = mybir.ActivationFunctionType
AX = mybir.AxisListType.X

P = 128
D = 1024
S = 1024
NT = S // P
KC = D // P
HD = 64
N_IN = 2840
NCMP = 63
NSEL = 16
FAR = -3.0e38
L = 8
NC = S // L
NG = 64
NQ = NG // 2
GC = 16
NE = 64
TOPK = 6
CAP = P
NSPILL = S * TOPK // CAP
SPILL0 = NE * CAP
NBLK = NE + NSPILL
FH = 256
ALPHA = 4 ** 0.25
LN_EPS = 1e-5
NEG = -1e30


def const_arrays():
    c = {}
    c["c_ident"] = np.eye(P, dtype=np.float32)
    inv = np.power(np.float32(500000.0), -np.arange(0, 16, 2, dtype=np.float32) / np.float32(16))
    ang = np.arange(S, dtype=np.float32)[:, None] * inv[None, :].astype(np.float32)
    rotated = np.array([1] * 10 + [0, 0] + [1, 1] + [0, 0] + [1, 1] + [0, 0], np.float32)[None, :, None]
    cos, sin = np.cos(ang)[:, None, :], np.sin(ang)[:, None, :]
    c["c_cos"] = (cos * rotated + (1 - rotated)).astype(np.float32)
    c["c_sin"] = (sin * rotated).astype(np.float32)
    k, q = np.arange(P)[:, None], np.arange(P)[None, :]
    c["c_stick"] = np.stack([np.where(k > q, -1.0, 0.0), np.where(k <= q, -1.0, 0.0),
                             np.where(k < q, 1.0, 0.0), np.where(k < q, 0.0, NEG)], 1).astype(np.float32)
    t = np.arange(S)
    seen = (np.arange(NCMP) * 16 + 31)[None, :] <= t[:, None]
    both = np.stack([np.where(seen, 0.0, NEG), np.where(seen, 1.0, 0.0)], 1)
    c["c_cmp"] = np.ascontiguousarray(both.reshape(NT, P, 2, NCMP).transpose(1, 0, 2, 3)).astype(np.float32)
    blk, cur = np.arange(NSEL)[None, :], (t // 64)[:, None]
    valid = blk <= cur
    forced = (blk == 0) | (valid & (blk > cur - 2))
    imp = np.stack([np.where(valid | forced, 1.0, 0.0), np.where(forced, 1e4, np.where(valid, 0.0, NEG))], 1)
    c["c_imp"] = np.ascontiguousarray(imp.reshape(NT, P, 2, NSEL).transpose(1, 0, 2, 3)).astype(np.float32)
    qq, kk = np.arange(P)[:, None], np.arange(P)[None, :]
    win = np.zeros((P, 5 * P))
    win[:, 0:P] = np.where(kk > qq, 0.0, NEG)
    win[:, 4 * P:] = np.where(kk <= qq, 0.0, NEG)
    c["c_win"] = win.astype(np.float32)
    causal = np.zeros((P, S))
    causal[:, S - P:] = np.where(kk <= qq, 0.0, NEG)
    c["c_causal"] = causal.astype(np.float32)
    c["c_tri8"] = np.ascontiguousarray(np.broadcast_to(np.tril(np.ones((8, 8), np.float32), -1)[None], (P, 8, 8)))
    e = np.arange(NE)
    c["c_exp"] = np.ascontiguousarray(np.broadcast_to(np.stack([e, e * CAP, SPILL0 - CAP - e * CAP])[None], (P, 3, NE))).astype(np.float32)
    c["c_before"] = np.stack([np.where(k < q, 1.0, 0.0), np.ones((P, P))], 1).astype(np.float32)
    c["c_spill"] = np.arange(NSPILL, dtype=np.float32)[None]
    c["c_tok"] = (np.arange(NT)[None, :] * P + np.arange(P)[:, None]).astype(np.float32)
    c["c_zero"] = np.zeros((NBLK, CAP), np.float32)
    c["c_diag16"] = np.tile(np.eye(16, dtype=np.float32), (2, 1))
    return c


class Stage:

    def __init__(self, nc, ctx, stage):
        self.nc, self.ctx, self.stage, self.sems = nc, ctx, stage, []
        ctx.callback(self.end)

    def end(self):
        if self.sems:
            self.nc.clear_and_free_semaphores(self.sems)
            self.nc.all_engine_barrier()

    def sb(self, name, shape, dt=F32):
        return self.ctx.enter_context(self.nc.sbuf_tensor(f"{self.stage}_{name}", shape, dt))

    def ps(self, name, shape, dt=F32):
        return self.ctx.enter_context(self.nc.psum_tensor(f"{self.stage}_{name}", shape, dt))

    def sem(self, name):
        self.sems.append(self.nc.alloc_semaphore(f"{self.stage}_{name}"))
        return self.sems[-1]


class Norm:

    def __init__(self, m, name):
        self.g = m.sb(f"{name}_g", [P, D])
        self.b = m.sb(f"{name}_b", [P, D])
        self.stats = m.sb(f"{name}_stats", [P, 2, 6])
        self.mv = m.sb(f"{name}_mv", [P, 2])
        self.inv = m.sb(f"{name}_inv", [P, 1])
        self.rstd = m.sb(f"{name}_rstd", [P, 1])
        self.gb_in = m.sem(f"{name}_gb_in")
        self.var_ready = m.sem(f"{name}_var_ready")
        self.rstd_ready = m.sem(f"{name}_rstd_ready")

    def load(self, eng, g, b):
        eng.dma_start(self.g[:, :], g.partition_broadcast(P)).then_inc(self.gb_in, 16)
        eng.dma_start(self.b[:, :], b.partition_broadcast(P)).then_inc(self.gb_in, 16)

    def on_act(self, act, n):
        act.wait_ge(self.var_ready, n + 1)
        act.activation(self.rstd[:, :], self.inv[:, :], ACT.Sqrt).then_inc(self.rstd_ready, 1)

    def on_dve(self, dve, then, y, n):
        if n == 0:
            dve.wait_ge(self.gb_in, 32)
        dve.bn_stats(self.stats[:, 0, :], y[:, 0:512])
        then(dve.bn_stats(self.stats[:, 1, :], y[:, 512:1024]))
        then(dve.bn_aggr(self.mv[:, :], self.stats[:, :, :].rearrange("p a b -> p (a b)")))
        then(dve.tensor_scalar(self.inv[:, :], self.mv[:, 1:2], LN_EPS, None, ALU.add))
        dve.reciprocal(self.inv[:, :], self.inv[:, :]).then_inc(self.var_ready, 1)
        dve.wait_ge(self.rstd_ready, n + 1)
        then(dve.tensor_scalar(y, y, self.mv[:, 0:1], self.rstd[:, 0:1], ALU.subtract, ALU.mult))
        then(dve.tensor_tensor(y, y, self.g[:, :], ALU.mult))
        return dve.tensor_tensor(y, y, self.b[:, :], ALU.add)


def stage_project(nc, x, w_in, cos, sin, ident, keep):
    with ExitStack() as ctx:
        m = Stage(nc, ctx, "proj")
        x_tile = m.sb("x_tile", [P, 2, D])
        xT = m.sb("xT", [P, KC, S])
        w = m.sb("w", [P, 2, KC, 512])
        tok = m.sb("tok", [P, 2, 512])
        dup = m.sb("dup", [P, 2, 6, 2, HD])
        cs = m.sb("cs", [P, 2, 2, 8, 8])
        r1 = m.sb("r1", [P, 4, 64])
        ps_mm = m.ps("ps_mm", [P, 4, 512])
        ps_t = m.ps("ps_t", [P, 2, 1024])
        const_in = m.sem("const_in")
        x_in = [m.sem(f"x_in{i}") for i in range(2)]
        w_inx = [m.sem(f"w_in{i}") for i in range(2)]
        cs_in = [m.sem(f"cs_in{i}") for i in range(2)]
        x_transposed = m.sem("x_transposed")
        xT_by_act = m.sem("xT_by_act")
        xT_by_dve = m.sem("xT_by_dve")
        mm_done = m.sem("mm_done")
        evicted = m.sem("evicted")
        roped = m.sem("roped")
        dup_done = m.sem("dup_done")
        transposed = m.sem("transposed")
        t_copied = m.sem("t_copied")
        dve_step = m.sem("dve_step")

        w_cols = [(0, 512), (512, 512), (1024, 512), (1536, 512), (2048, 512), (2560, 280)]
        w_view = w_in.rearrange("(c p) n -> p c n", p=P)
        units = [(g, tt) for g in range(6) for tt in range(8)]
        FIRST_ROPE = 24

        def n_rope(g):
            return {3: (0, 8), 4: (8, 8), 5: (16, 4)}[g]

        block = ctx.enter_context(nc.Block())

        @block.sync
        def _(sp):
            sp.dma_start(keep["ident"][:, :], ident).then_inc(const_in, 16)
            for g in range(2):
                c0, n = w_cols[g]
                if g == 0:
                    for tt in range(2):
                        sp.dma_start(x_tile[:, tt, :], x[tt * P:(tt + 1) * P, :]).then_inc(x_in[tt], 16)
                sp.dma_start(w[:, g, :, 0:n], w_view[:, :, c0:c0 + n]).then_inc(w_inx[g], 16)
            for tt in range(2, 8):
                sp.wait_ge(x_transposed, tt - 1)
                sp.dma_start(x_tile[:, tt % 2, :], x[tt * P:(tt + 1) * P, :]).then_inc(x_in[tt % 2], 16)
            for g in range(2, 6):
                c0, n = w_cols[g]
                sp.wait_ge(mm_done, 8 * (g - 1))
                sp.dma_start(w[:, g % 2, :, 0:n], w_view[:, :, c0:c0 + n]).then_inc(w_inx[g % 2], 16)

        @block.gpsimd
        def _(pool):
            for u, (g, tt) in enumerate(units):
                if g < 3:
                    continue
                v = u - FIRST_ROPE
                if v >= 2:
                    pool.wait_ge(roped, v - 1)
                h0, nh = n_rope(g)
                pool.dma_start(cs[:, v % 2, 0, 0:nh, :], cos[tt * P:(tt + 1) * P, h0:h0 + nh, :]).then_inc(cs_in[v % 2], 16)
                pool.dma_start(cs[:, v % 2, 1, 0:nh, :], sin[tt * P:(tt + 1) * P, h0:h0 + nh, :]).then_inc(cs_in[v % 2], 16)

        @block.tensor
        def _(pe):
            pe.wait_ge(const_in, 16)
            for tt in range(8):
                pe.wait_ge(x_in[tt % 2], 16 * (tt // 2 + 1))
                if tt >= 2:
                    pe.wait_ge(xT_by_act, tt - 1)
                    pe.wait_ge(xT_by_dve, tt - 1)
                for c in range(KC):
                    t = pe.transpose(ps_t[:, tt % 2, c * P:(c + 1) * P], x_tile[:, tt % 2, c * P:(c + 1) * P],
                                     keep["ident"][:, :])
                t.then_inc(x_transposed, 1)
            pe.wait_ge(xT_by_act, 8)
            pe.wait_ge(xT_by_dve, 8)

            def transposes(u):
                g, tt = units[u]
                v = u - FIRST_ROPE
                pe.wait_ge(roped, v + 1)
                if g > 3:
                    pe.wait_ge(dup_done, v - 8 + 1)
                if v >= 2:
                    pe.wait_ge(t_copied, v - 1)
                n = {3: 4, 4: 6, 5: 2}[g]
                for k in range(n):
                    src = tok[:, v % 2, k * P:(k + 1) * P] if g == 3 else dup[:, v % 2, k, :, :].rearrange("p a d -> p (a d)")
                    t = pe.transpose(ps_t[:, v % 2, k * P:(k + 1) * P], src, keep["ident"][:, :])
                t.then_inc(transposed, 1)

            for u, (g, tt) in enumerate(units):
                pe.wait_ge(w_inx[g % 2], 16 * (g // 2 + 1))
                if u >= 4:
                    pe.wait_ge(evicted, u - 3)
                n = w_cols[g][1]
                for c in range(KC):
                    if g < 2:
                        fc, half = tt // 2, tt % 2
                        t = pe.matmul(ps_mm[:, u % 4, :], w[:, g % 2, c, fc * P:(fc + 1) * P],
                                      xT[:, c, half * 512:(half + 1) * 512], start=(c == 0), stop=(c == KC - 1))
                    else:
                        t = pe.matmul(ps_mm[:, u % 4, 0:n], xT[:, c, tt * P:(tt + 1) * P],
                                      w[:, g % 2, c, 0:n], start=(c == 0), stop=(c == KC - 1))
                t.then_inc(mm_done, 1)
                if u > FIRST_ROPE:
                    transposes(u - 1)
            transposes(len(units) - 1)

        @block.scalar
        def _(act):
            for tt in range(8):
                act.wait_ge(x_transposed, tt + 1)
                act.activation(xT[:, 0:4, tt * P:(tt + 1) * P],
                               ps_t[:, tt % 2, 0:512].rearrange("p (c t) -> p c t", c=4), ACT.Copy).then_inc(xT_by_act, 1)
            for u, (g, tt) in enumerate(units):
                act.wait_ge(mm_done, u + 1)
                v = u - FIRST_ROPE
                n = w_cols[g][1]
                src = ps_mm[:, u % 4, 0:n]
                if g == 0:
                    act.activation(keep["qaT"][:, tt // 2, (tt % 2) * 512:(tt % 2 + 1) * 512], src, ACT.Copy, scale=0.125).then_inc(evicted, 1)
                elif g == 1:
                    act.activation(keep["kaT"][:, tt // 2, (tt % 2) * 512:(tt % 2 + 1) * 512], src, ACT.Copy).then_inc(evicted, 1)
                elif g == 2:
                    act.activation(keep["va"][:, tt, :], src, ACT.Copy).then_inc(evicted, 1)
                else:
                    if v >= 2:
                        act.wait_ge(transposed, v - 1)
                    act.activation(tok[:, v % 2, 0:n], src, ACT.Copy, scale=0.125 if g == 3 else 1.0).then_inc(evicted, 1)
                    if g > 3:
                        act.wait_ge(roped, v + 1)
                        if g == 4:
                            act.activation(dup[:, v % 2, :, :, :],
                                           tok[:, v % 2, 0:384].rearrange("p (h d) -> p h d", h=6).unsqueeze(2).to_broadcast([P, 6, 2, HD]),
                                           ACT.Copy)
                            act.activation(keep["vs"][:, tt, :], tok[:, v % 2, 384:512], ACT.Copy).then_inc(dup_done, 1)
                        else:
                            act.activation(dup[:, v % 2, 0:2, :, :],
                                           tok[:, v % 2, 0:128].rearrange("p (h d) -> p h d", h=2).unsqueeze(2).to_broadcast([P, 2, 2, HD]),
                                           ACT.Copy)
                            act.activation(keep["gate"][:, tt, :], tok[:, v % 2, 256:280], ACT.Copy)
                            act.activation(keep["vw"][:, tt, :], tok[:, v % 2, 128:256], ACT.Copy).then_inc(dup_done, 1)

        def copy_out(dve, v):
            g, tt = units[v + FIRST_ROPE]
            dve.wait_ge(transposed, v + 1)
            cols = slice(tt * P, (tt + 1) * P)
            if g == 3:
                dve.tensor_copy(keep["qbT"][:, :, cols], ps_t[:, v % 2, 0:512].rearrange("p (c t) -> p c t", c=4)).then_inc(t_copied, 1)
            elif g == 4:
                dve.tensor_copy(keep["kcT"][:, :, cols], ps_t[:, v % 2, 0:256].rearrange("p (c t) -> p c t", c=2))
                dve.tensor_copy(keep["vcT"][:, :, cols], ps_t[:, v % 2, 256:512].rearrange("p (c t) -> p c t", c=2))
                dve.tensor_copy(keep["ksT"][:, :, cols], ps_t[:, v % 2, 512:768].rearrange("p (c t) -> p c t", c=2)).then_inc(t_copied, 1)
            else:
                dve.tensor_copy(keep["kwT"][:, :, cols], ps_t[:, v % 2, 0:256].rearrange("p (c t) -> p c t", c=2)).then_inc(t_copied, 1)

        @block.vector
        def _(dve):
            steps = [0]

            def done(ins):
                steps[0] += 1
                ins.then_inc(dve_step, 1)

            for tt in range(8):
                dve.wait_ge(x_transposed, tt + 1)
                dve.tensor_copy(xT[:, 4:8, tt * P:(tt + 1) * P],
                                ps_t[:, tt % 2, 512:1024].rearrange("p (c t) -> p c t", c=4)).then_inc(xT_by_dve, 1)
            for u, (g, tt) in enumerate(units):
                if g < 3:
                    continue
                v = u - FIRST_ROPE
                h0, nh = n_rope(g)
                dve.wait_ge(evicted, u + 1)
                dve.wait_ge(cs_in[v % 2], 32 * (v // 2 + 1))
                heads = tok[:, v % 2, 0:nh * HD].rearrange("p (h d) -> p h d", h=nh)
                x1, x2 = heads[:, :, 0:8], heads[:, :, 8:16]
                c_, s_ = cs[:, v % 2, 0, 0:nh, :], cs[:, v % 2, 1, 0:nh, :]
                t = [r1[:, i, 0:nh * 8].rearrange("p (h d) -> p h d", h=nh) for i in range(4)]
                if v:
                    dve.wait_ge(dve_step, steps[0])
                done(dve.tensor_tensor(t[0], x1, c_, ALU.mult))
                done(dve.tensor_tensor(t[1], x2, s_, ALU.mult))
                done(dve.tensor_tensor(t[2], x2, c_, ALU.mult))
                done(dve.tensor_tensor(t[3], x1, s_, ALU.mult))
                dve.wait_ge(dve_step, steps[0])
                done(dve.tensor_tensor(x1, t[0], t[1], ALU.subtract))
                dve.wait_ge(dve_step, steps[0])
                steps[0] += 1
                dve.tensor_tensor(x2, t[2], t[3], ALU.add).then_inc(dve_step, 1)
                dve.wait_ge(dve_step, steps[0])
                dve.engine_nop().then_inc(roped, 1)
                if v >= 1:
                    copy_out(dve, v - 1)
            copy_out(dve, len(units) - 1 - FIRST_ROPE)


def keep_attention(nc, ctx):
    m = Stage(nc, ctx, "keep")
    k = {"ident": m.sb("ident", [P, P])}
    for n, shape in (("qaT", [P, 4, S]), ("kaT", [P, 4, S]), ("va", [P, NT, 512]), ("qbT", [P, 4, S]),
                     ("kcT", [P, 2, S]), ("vcT", [P, 2, S]), ("ksT", [P, 2, S]), ("kwT", [P, 2, S]),
                     ("vs", [P, NT, P]), ("vw", [P, NT, P]), ("gate", [P, NT, 24]),
                     ("sel", [P, 2, NT, NSEL]), ("o_tok", [P, NT, 512])):
        k[n] = m.sb(n, shape)
    return k


def stage_stick(nc, stick, expert_rows, keep):
    with ExitStack() as ctx:
        m = Stage(nc, ctx, "sb")
        masks = m.sb("masks", [P, 4, P])
        tri_after, tri_rest, before, not_before = (masks[:, i, :] for i in range(4))
        q_st = m.sb("q_st", [P, S])
        k_st = m.sb("k_st", [P, S])
        v_st = m.sb("v_st", [P, NT, P])
        mag = m.sb("mag", [P, 2, 512])
        ln1 = m.sb("ln1", [P, 2, 512])
        sp_ = m.sb("sp", [P, 3, 512])
        zsp = m.sb("zsp", [P, 3, 512])
        t_ = m.sb("t", [P, 2, 512])
        w_ = m.sb("w", [P, 2, 512])
        zeros = m.sb("zeros", [P, D])
        zeros_ready, cleared = m.sem("zeros_ready"), m.sem("cleared")
        ps_z = m.ps("ps_z", [P, 2, 512])
        ps_s = m.ps("ps_s", [P, 2, S])
        ps_o = m.ps("ps_o", [P, S])
        const_in, qk_staged, v_staged, z_done, ln_done, sp_done, tri_done, t_done, w_done, conv_done, pv_done, o_evicted, act_step, dve_step = (
            m.sem(n) for n in "const_in qk_staged v_staged z_done ln_done sp_done tri_done t_done w_done conv_done pv_done o_evicted act_step dve_step".split())

        units = []
        for kt in range(NT - 1, -1, -1):
            pieces = [(kt * P, S)] if kt >= 4 else [(kt * P, 512), (512, S)]
            for a, b in pieces:
                for hh in range(2):
                    units.append((hh, kt, a, b - a))
        N = len(units)
        PAIRS = 4
        DVE_STEPS = sum(1 + 2 * (a == kt * P) for _, kt, a, _ in units)
        block = ctx.enter_context(nc.Block())

        @block.sync
        def _(sp):
            sp.dma_start(masks[:, :, :], stick).then_inc(const_in, 16)
            sp.wait_ge(zeros_ready, 1)
            with sp.Fori(0, NSPILL) as b:
                sp.dma_start(expert_rows[bass.ds(SPILL0 + b * CAP, CAP), :], zeros[:, :]).then_inc(cleared, 16)
            sp.wait_ge(cleared, 16 * NSPILL)

        @block.gpsimd
        def _(pool):
            pool.memset(zeros[:, :], 0.0).then_inc(zeros_ready, 1)
            with pool.Fori(0, PAIRS) as i:
                pool.wait_ge(pv_done, i * N)
                pool.tensor_copy(v_st[:, :, :], keep["va"][:, :, bass.ds(i * P, P)]).then_inc(v_staged, 1)

        @block.tensor
        def _(pe):
            pe.wait_ge(const_in, 16)

            def scores(i, n):
                hh, kt, a, w = units[n]
                h = slice(hh * HD, (hh + 1) * HD)
                if n < 2:
                    pe.wait_ge(sp_done, i * N)
                else:
                    pe.wait_ge(sp_done, i * N + n - 1)
                pe.matmul(ps_z[:, n % 2, 0:w], k_st[h, kt * P:(kt + 1) * P], q_st[h, a:a + w],
                          start=True, stop=True).then_inc(z_done, 1)

            def suffix(i, n):
                hh, kt, a, w = units[n]
                pe.wait_ge(sp_done, i * N + n + 1)
                first = (kt == NT - 1) or (kt == 3 and a < 512)
                pe.matmul(ps_s[:, hh, a:a + w], tri_after, sp_[:, n % 3, 0:w], start=first, stop=True,
                          skip_group_check=True).then_inc(tri_done, 1)

            def to_whole(i, n):
                hh, kt, a, w = units[n]
                pe.wait_ge(t_done, i * N + n + 1)
                pe.matmul(ps_s[:, hh, a:a + w], tri_rest, sp_[:, n % 3, 0:w], start=False, stop=True,
                          skip_group_check=True).then_inc(conv_done, 1)

            def values(i, n):
                hh, kt, a, w = units[n]
                pe.wait_ge(w_done, i * N + n + 1)
                if n == 0:
                    pe.wait_ge(v_staged, i + 1)
                    pe.wait_ge(o_evicted, i)
                first = (kt == NT - 1) or (kt == 3 and a < 512)
                pe.matmul(ps_o[hh * HD:(hh + 1) * HD, a:a + w], v_st[:, kt, hh * HD:(hh + 1) * HD],
                          w_[:, n % 2, 0:w], start=first, stop=True, skip_group_check=True).then_inc(pv_done, 1)

            with pe.Fori(0, PAIRS) as i:
                pe.wait_ge(qk_staged, i + 1)
                scores(i, 0)
                scores(i, 1)
                for n in range(N):
                    if n + 2 < N:
                        scores(i, n + 2)
                    if n:
                        to_whole(i, n - 1)
                    suffix(i, n)
                    if n:
                        values(i, n - 1)
                to_whole(i, N - 1)
                values(i, N - 1)

        @block.scalar
        def _(act):
            act.preload_act_table_set("natural_log_exp_and_others")

            def softplus_part(i, n):
                w = units[n][3]
                z = ps_z[:, n % 2, 0:w]
                act.wait_ge(z_done, i * N + n + 1)
                act.activation(mag[:, n % 2, 0:w], z, ACT.Abs).then_inc(act_step, 1)
                act.wait_ge(act_step, i * 2 * N + 2 * n + 1)
                act.activation(mag[:, n % 2, 0:w], mag[:, n % 2, 0:w], ACT.Exp, scale=-1.0).then_inc(act_step, 1)
                act.wait_ge(act_step, i * 2 * N + 2 * n + 2)
                if n < 2:
                    act.wait_ge(sp_done, i * N)
                else:
                    act.wait_ge(sp_done, i * N + n - 1)
                act.activation(ln1[:, n % 2, 0:w], mag[:, n % 2, 0:w], ACT.Ln, bias=1.0).then_inc(ln_done, 1)

            def weights(i, n):
                w = units[n][3]
                act.wait_ge(t_done, i * N + n + 1)
                if n < 2:
                    act.wait_ge(pv_done, i * N)
                else:
                    act.wait_ge(pv_done, i * N + n - 1)
                act.activation(w_[:, n % 2, 0:w], t_[:, n % 2, 0:w], ACT.Exp).then_inc(w_done, 1)

            with act.Fori(0, PAIRS) as i:
                softplus_part(i, 0)
                for n in range(N):
                    if n + 1 < N:
                        softplus_part(i, n + 1)
                    weights(i, n)

        @block.vector
        def _(dve):
            step = [0]

            def then(i, ins):
                step[0] += 1
                ins.then_inc(dve_step, 1)
                dve.wait_ge(dve_step, i * DVE_STEPS + step[0])

            def softplus(i, n):
                hh, kt, a, w = units[n]
                diagonal = a == kt * P
                z = ps_z[:, n % 2, 0:w]
                s = n % 3
                dve.wait_ge(ln_done, i * N + n + 1)
                if n < 3:
                    dve.wait_ge(conv_done, i * N)
                else:
                    dve.wait_ge(conv_done, i * N + n - 2)
                then(i, dve.scalar_tensor_tensor(out=sp_[:, s, 0:w], in0=z, scalar=0.0, in1=ln1[:, n % 2, 0:w],
                                                 op0=ALU.max, op1=ALU.add))
                last = dve.tensor_tensor(zsp[:, s, 0:w], z, sp_[:, s, 0:w], ALU.subtract)
                if diagonal:
                    then(i, last)
                    then(i, dve.tensor_tensor(sp_[:, s, 0:P], sp_[:, s, 0:P], before, ALU.mult))
                    last = dve.tensor_tensor(zsp[:, s, 0:P], zsp[:, s, 0:P], not_before, ALU.add)
                last.then_inc(sp_done, 1)

            def exponent(i, n):
                hh, kt, a, w = units[n]
                dve.wait_ge(tri_done, i * N + n + 1)
                if n < 2:
                    dve.wait_ge(w_done, i * N)
                else:
                    dve.wait_ge(w_done, i * N + n - 1)
                dve.wait_ge(sp_done, i * N + n + 1)
                dve.tensor_tensor(t_[:, n % 2, 0:w], zsp[:, n % 3, 0:w], ps_s[:, hh, a:a + w], ALU.add).then_inc(t_done, 1)

            dve.wait_ge(const_in, 16)
            with dve.Fori(0, PAIRS) as i:
                step[0] = 0
                dve.wait_ge(z_done, i * N)
                dve.tensor_scalar(q_st[:, :], keep["qaT"][:, i, :], 1.0, None, ALU.mult)
                dve.tensor_scalar(k_st[:, :], keep["kaT"][:, i, :], 1.0, None, ALU.mult).then_inc(qk_staged, 1)
                softplus(i, 0)
                for n in range(N):
                    if n + 1 < N:
                        softplus(i, n + 1)
                    exponent(i, n)
                assert step[0] == DVE_STEPS
                dve.wait_ge(pv_done, i * N + N)
                dve.tensor_scalar(keep["qaT"][:, i, :], ps_o[:, :], 1.0, None, ALU.mult).then_inc(o_evicted, 1)


def stage_compress(nc, pos_k, pos_v, k_w1, k_w2, v_w1, v_w2, c_cmp, c_imp, keep):
    with ExitStack() as ctx:
        m = Stage(nc, ctx, "cmp")
        w1 = m.sb("w1", [P, 2, 16, 256])
        w2k = m.sb("w2k", [P, 2, 2, HD])
        w2v = m.sb("w2v", [P, 2, HD])
        pos = m.sb("pos", [P, 2, 16])
        mcmp = m.sb("mcmp", [P, NT, 2, NCMP])
        mimp = m.sb("mimp", [P, NT, 2, NSEL])
        kpos = m.sb("kpos", [P, 2, 2, 16, NCMP])
        hid = m.sb("hid", [P, 2, 2, 2 * NCMP])
        kcmp = m.sb("kcmp", [P, 2, NCMP])
        vcmp = m.sb("vcmp", [NCMP, 2, HD])
        s_ = m.sb("s", [P, 2, 8, NCMP])
        e_ = m.sb("e", [P, 2, 8, NCMP])
        p_ = m.sb("p", [P, 2, 8, NCMP])
        st = m.sb("st", [P, 3, 8])
        psum4 = m.sb("psum4", [P, 2, NCMP + 2])
        imp = m.sb("imp", [P, 2, NSEL])
        top = m.sb("top", [P, 2, 8])
        rest = m.sb("rest", [P, 2, NSEL])
        pT = m.sb("pT", [NCMP, 2, 8, P])
        ps_c = m.ps("ps_c", [P, 2, 2, 8, 64])
        ps_t = m.ps("ps_t", [P, 8, P])
        ps_o = m.ps("ps_o", [P, 2, 8, HD])
        (w_in, c_in, kpos_k, kpos_v, hid_mm, gelu_done, cmp_mm, cmp_copied, sc_done, e_done, gate_done, p_done,
         t_done, t_copied, o_done, o_copied, dve_step, s_read, shifted) = (m.sem(n) for n in
            "w_in c_in kpos_k kpos_v hid_mm gelu_done cmp_mm cmp_copied sc_done e_done gate_done p_done t_done t_copied o_done o_copied dve_step s_read shifted".split())
        ps_h = ps_t[:, :, :].rearrange("p a b -> p (a b)")
        block = ctx.enter_context(nc.Block())

        @block.sync
        def _(sp):
            for i, (pp, wa) in enumerate(((pos_k, k_w1), (pos_v, v_w1))):
                with nc.allow_non_contiguous_dma(reason="2048 elements"):
                    sp.dma_start(pos[:, i, :], pp.rearrange("(i two) d -> (two d) i", two=2)).then_inc(w_in, 16)
                sp.dma_start(w1[:, i, :, :], wa.rearrange("(i p) f -> p i f", p=P)).then_inc(w_in, 16)
            for a in range(2):
                sp.dma_start(w2k[:, :, a, :], k_w2.rearrange("(c p) d -> p c d", p=P)).then_inc(w_in, 16)
            sp.dma_start(w2v[:, :, :], v_w2.rearrange("(c p) d -> p c d", p=P)).then_inc(w_in, 16)
            sp.dma_start(mcmp[:, :, :, :], c_cmp).then_inc(c_in, 16)
            sp.dma_start(mimp[:, :, :, :], c_imp).then_inc(c_in, 16)

        def add_pos(eng, kind, done):
            src = keep["kcT"] if kind == 0 else keep["vcT"]
            for odd in range(2):
                h = slice(odd * HD, (odd + 1) * HD)
                for g in range(2):
                    v = src[h, g, :].rearrange("p (n r) -> p r n", r=16)[:, odd::2, :]
                    for late in range(2):
                        x = eng.tensor_tensor(kpos[h, kind, g, 8 * late:8 * late + 8, :], v[:, :, late:late + NCMP],
                                              pos[h, kind, 8 * late:8 * late + 8].unsqueeze(2).to_broadcast([HD, 8, NCMP]), ALU.add)
            x.then_inc(done, 1)

        @block.gpsimd
        def _(pool):
            pool.wait_ge(w_in, 16 * 7)
            add_pos(pool, 1, kpos_v)

        @block.tensor
        def _(pe):
            pe.wait_ge(w_in, 16 * 7)
            for kind in range(2):
                pe.wait_ge(kpos_k if kind == 0 else kpos_v, 1)
                for fc in range(2):
                    o = (kind * 2 + fc) * 2 * NCMP
                    for l in range(16):
                        x = pe.matmul(ps_h[:, o:o + 2 * NCMP], w1[:, kind, l, fc * P:(fc + 1) * P], kpos[:, kind, :, l, :],
                                      start=(l == 0), stop=(l == 15), skip_group_check=True)
                    x.then_inc(hid_mm, 1)
            pe.wait_ge(gelu_done, 4)
            for c in range(2):
                x = pe.matmul(ps_c[:, 0, 0, :, :].rearrange("p a b -> p (a b)")[:, 0:2 * NCMP], w2k[:, c, :, :].rearrange("p a d -> p (a d)"),
                              hid[:, 0, c, :], start=(c == 0), stop=(c == 1))
            x.then_inc(cmp_mm, 1)
            for g in range(2):
                for c in range(2):
                    x = pe.matmul(ps_o[0:NCMP, 0, g, :], hid[:, 1, c, g * NCMP:(g + 1) * NCMP], w2v[:, c, :],
                                  start=(c == 0), stop=(c == 1), skip_group_check=True)
            x.then_inc(cmp_mm, 1)
            pe.wait_ge(cmp_copied, 2)

            def scores(i):
                if i >= 2:
                    pe.wait_ge(s_read, i - 1)
                for h in range(8):
                    hp = slice((h % 2) * HD, (h % 2 + 1) * HD)
                    x = pe.matmul(ps_c[:, i % 2, h % 2, h // 2, 0:NCMP], keep["qbT"][hp, h // 2, i * P:(i + 1) * P], kcmp[hp, h // 4, :],
                                  start=True, stop=True, skip_group_check=True)
                x.then_inc(sc_done, 1)

            scores(0)
            for i in range(NT):
                if i + 1 < NT:
                    scores(i + 1)
                pe.wait_ge(p_done, i + 1)
                if i:
                    pe.wait_ge(t_copied, i)
                for h in range(8):
                    x = pe.transpose(ps_t[0:NCMP, h, :], p_[:, i % 2, h, :], keep["ident"][:, :])
                x.then_inc(t_done, 1)
                pe.wait_ge(t_copied, i + 1)
                if i >= 2:
                    pe.wait_ge(o_copied, i - 1)
                for h in range(8):
                    x = pe.matmul(ps_o[:, i % 2, h, :], pT[:, i % 2, h, :], vcmp[:, h // 4, :], start=True, stop=True,
                                  skip_group_check=True)
                x.then_inc(o_done, 1)

        @block.scalar
        def _(act):
            act.activation(keep["gate"][:, :, :], keep["gate"][:, :, :], ACT.Sigmoid).then_inc(gate_done, 1)
            act.wait_ge(hid_mm, 4)
            for k in range(4):
                act.activation(hid[:, k // 2, k % 2, :], ps_h[:, k * 2 * NCMP:(k + 1) * 2 * NCMP], ACT.Gelu_apprx_tanh).then_inc(gelu_done, 1)
            for i in range(NT):
                act.wait_ge(shifted, i + 1)
                act.activation(e_[:, i % 2, :, :], s_[:, i % 2, :, :], ACT.Exp).then_inc(e_done, 1)
                act.wait_ge(t_done, i + 1)
                if i >= 2:
                    act.wait_ge(o_done, i - 1)
                act.activation(pT[:, i % 2, :, :], ps_t[0:NCMP, :, :], ACT.Copy).then_inc(t_copied, 1)

        @block.vector
        def _(dve):
            step = [0]

            def then(ins):
                step[0] += 1
                ins.then_inc(dve_step, 1)
                dve.wait_ge(dve_step, step[0])

            then(dve.memset(psum4[:, :, :], 0.0))
            dve.wait_ge(w_in, 16 * 7)
            add_pos(dve, 0, kpos_k)
            dve.wait_ge(cmp_mm, 2)
            dve.tensor_copy(kcmp[:, :, :], ps_c[:, 0, 0, :, :].rearrange("p a b -> p (a b)")[:, 0:2 * NCMP].rearrange("p (g n) -> p g n", g=2)).then_inc(cmp_copied, 1)
            dve.tensor_copy(vcmp[:, :, :], ps_o[0:NCMP, 0, 0:2, :]).then_inc(cmp_copied, 1)
            dve.wait_ge(c_in, 32)
            dve.wait_ge(gate_done, 1)

            def wide(x):
                return x.unsqueeze(2).to_broadcast([P, 8, NCMP])

            def shift(i):
                s = s_[:, i % 2, :, :]
                dve.wait_ge(sc_done, i + 1)
                if i >= 2:
                    dve.wait_ge(e_done, i - 1)
                dve.tensor_tensor(s.rearrange("p (b a) n -> p b a n", a=2), ps_c[:, i % 2, :, 0:4, 0:NCMP].rearrange("p a b n -> p b a n"),
                                  mcmp[:, i, 0, :].unsqueeze(1).unsqueeze(1).to_broadcast([P, 4, 2, NCMP]), ALU.add).then_inc(s_read, 1)
                dve.wait_ge(s_read, i + 1)
                then(dve.tensor_reduce(st[:, 0, :], s, AX, ALU.max))
                dve.tensor_tensor(s, s, wide(st[:, 0, :]), ALU.subtract).then_inc(shifted, 1)

            shift(0)
            for i in range(NT):
                if i + 1 < NT:
                    shift(i + 1)
                e, p = e_[:, i % 2, :, :], p_[:, i % 2, :, :]
                dve.wait_ge(e_done, i + 1)
                then(dve.tensor_reduce(st[:, 1, :], e, AX, ALU.add))
                then(dve.reciprocal(st[:, 2, :], st[:, 1, :]))
                then(dve.tensor_tensor(e, e, wide(st[:, 2, :]), ALU.mult))
                if i >= 2:
                    dve.wait_ge(t_done, i - 1)
                dve.tensor_tensor(p, e, mcmp[:, i, 1, :].unsqueeze(1).to_broadcast([P, 8, NCMP]), ALU.mult).then_inc(p_done, 1)
                dve.wait_ge(p_done, i + 1)
                then(dve.tensor_reduce(psum4[:, :, 1:NCMP + 1], p.rearrange("p (g r) n -> p g n r", g=2), AX, ALU.add))
                base = psum4[:, :, :]
                taps = bass.AP(base.tensor, base.offset, [list(base.ap[0]), [NCMP + 2, 2], [4, NSEL], [1, 5]])
                then(dve.tensor_reduce(imp[:, :, :], taps, AX, ALU.add))
                then(dve.tensor_tensor(imp[:, :, :], imp[:, :, :], mimp[:, i, 0, :].unsqueeze(1).to_broadcast([P, 2, NSEL]), ALU.mult))
                then(dve.tensor_tensor(imp[:, :, :], imp[:, :, :], mimp[:, i, 1, :].unsqueeze(1).to_broadcast([P, 2, NSEL]), ALU.add))
                for g in range(2):
                    then(dve.max(top[:, g, :], imp[:, g, :]))
                for g in range(2):
                    then(dve.match_replace(rest[:, g, :], top[:, g, :], imp[:, g, :], FAR))
                then(dve.tensor_tensor(imp[:, :, :], rest[:, :, :], imp[:, :, :], ALU.is_equal))
                then(dve.tensor_scalar(keep["sel"][:, :, i, :], imp[:, :, :], NEG, None, ALU.mult))
                dve.wait_ge(o_done, i + 1)
                gate0 = keep["gate"][:, i, :].rearrange("p (h b) -> p h b", b=3)[:, :, 0:1].to_broadcast([P, 8, HD])
                dve.tensor_tensor(keep["o_tok"][:, i, :].rearrange("p (h d) -> p h d", h=8), ps_o[:, i % 2, :, :], gate0, ALU.mult).then_inc(o_copied, 1)


def stage_selected(nc, c_win, c_causal, keep):
    with ExitStack() as ctx:
        m = Stage(nc, ctx, "sel")
        win = m.sb("win", [P, 5 * P])
        causal = m.sb("causal", [P, S])
        nothing = m.sb("nothing", [P, 1])
        q_st = m.sb("q_st", [P, 2, S])
        ks_st = m.sb("ks_st", [P, S])
        kw_st = m.sb("kw_st", [P, S])
        vs_st = m.sb("vs_st", [P, NT, HD])
        vw_st = m.sb("vw_st", [P, NT, HD])
        sel_st = m.sb("sel_st", [P, NT, NSEL])
        gate_st = m.sb("gate_st", [P, NT, 4, 3])
        o_st = m.sb("o_st", [P, NT, 4, HD])
        mask = m.sb("mask", [P, 2, S])
        sc = m.sb("sc", [P, 2, 13 * P])
        pr = m.sb("pr", [P, 2, 13 * P])
        pT = m.sb("pT", [P, 2, 13 * P])
        mx = m.sb("mx", [P, 2, 2])
        nmx = m.sb("nmx", [P, 2, 2])
        sums = m.sb("sums", [P, 2, 2])
        cf = m.sb("cf", [P, 2, 2])
        ps_s = m.ps("ps_s", [P, S])
        ps_w = m.ps("ps_w", [P, S])
        ps_t = m.ps("ps_t", [P, 2, 512])
        ps_o = m.ps("ps_o", [P, 2, 512])
        (c_in, st_act, st_dve, mask_done, sc_done, sc_read, e_done, t_done, tc_act, tc_dve, o_done, o_used, dve_step, out_done) = (
            m.sem(n) for n in "c_in st_act st_dve mask_done sc_done sc_read e_done t_done tc_act tc_dve o_done o_used dve_step out_done".split())
        units = [(i, r) for i in range(NT) for r in range(4)]
        N = len(units)

        def tiles(i):
            return [(0, j) for j in range(i + 1)] + [(1, j) for j in range(max(0, i - 4), i + 1)]

        chunks = [(n, k, tiles(i)[k:k + 4]) for n, (i, r) in enumerate(units) for k in range(0, len(tiles(i)), 4)]
        NCH = len(chunks)
        first_chunk = [next(c for c, (u, _, _) in enumerate(chunks) if u == n) for n in range(N)] + [NCH]
        by_act = lambda c: c % 2 == 0
        n_act = lambda c: (c + 1) // 2
        n_dve = lambda c: c // 2
        NA, ND = n_act(NCH), n_dve(NCH)
        assert NCH % 2 == 0
        DSTEP = 4 * N
        block = ctx.enter_context(nc.Block())

        def cols(r):
            return slice((r % 2) * HD, (r % 2 + 1) * HD)

        @block.sync
        def _(sp):
            sp.dma_start(win[:, :], c_win).then_inc(c_in, 16)
            sp.dma_start(causal[:, :], c_causal).then_inc(c_in, 16)

        @block.gpsimd
        def _(pool):
            pool.wait_ge(c_in, 32)
            with pool.Fori(0, 2) as g:
                for i in range(NT):
                    if i == 0:
                        pool.wait_ge(st_dve, g + 1)
                    pool.wait_ge(sc_read, g * N + 4 * max(0, i - 1))
                    w = (i + 1) * P
                    pool.tensor_tensor(mask[:, i % 2, 0:w].rearrange("p (b l) -> p b l", l=64),
                                       sel_st[:, i, 0:w // 64].unsqueeze(2).to_broadcast([P, w // 64, 64]),
                                       causal[:, S - w:S].rearrange("p (b l) -> p b l", l=64), ALU.add).then_inc(mask_done, 1)

        @block.tensor
        def _(pe):
            def scores(g, n):
                i, r = units[n]
                pe.wait_ge(sc_read, g * N + n)
                q = q_st[cols(r), r // 2, i * P:(i + 1) * P]
                w = (i + 1) * P
                for a in range(0, w, 512):
                    b = min(a + 512, w)
                    pe.matmul(ps_s[:, a:b], q, ks_st[cols(r), a:b], start=True, stop=True)
                k0 = max(0, i - 4) * P
                ww = w - k0
                for a in range(0, ww, 512):
                    b = min(a + 512, ww)
                    x = pe.matmul(ps_w[:, a:b], q, kw_st[cols(r), k0 + a:k0 + b], start=True, stop=True)
                x.then_inc(sc_done, 1)

            def transposes(g, c):
                n, k, ts = chunks[c]
                for j in range(len(ts)):
                    x = pe.transpose(ps_t[:, c % 2, j * P:(j + 1) * P], pr[:, n % 2, (k + j) * P:(k + j + 1) * P], keep["ident"][:, :])
                x.then_inc(t_done, 1)

            def values(g, c):
                n, k, ts = chunks[c]
                i = units[n][0]
                if by_act(c):
                    pe.wait_ge(tc_act, g * NA + n_act(c + 1))
                else:
                    pe.wait_ge(tc_dve, g * ND + n_dve(c + 1))
                for j, (branch, kt) in enumerate(ts):
                    v = (vs_st, vw_st)[branch]
                    x = pe.matmul(ps_o[:, n % 2, branch * HD:(branch + 1) * HD], pT[:, n % 2, (k + j) * P:(k + j + 1) * P], v[:, kt, :],
                                  start=(kt == (0, max(0, i - 4))[branch]), stop=(kt == i), skip_group_check=True)
                if c + 1 == first_chunk[n + 1]:
                    x.then_inc(o_done, 1)

            with pe.Fori(0, 2) as g:
                pe.wait_ge(st_act, g + 1)
                pe.wait_ge(st_dve, g + 1)
                scores(g, 0)
                for n in range(N):
                    if n + 1 < N:
                        scores(g, n + 1)
                    pe.wait_ge(e_done, g * N + n + 1)
                    if n >= 2:
                        pe.wait_ge(o_used, g * N + n - 1)
                    else:
                        pe.wait_ge(o_used, g * N)
                    for c in range(first_chunk[n], first_chunk[n + 1]):
                        transposes(g, c)
                        if c > first_chunk[n]:
                            values(g, c - 1)
                    values(g, first_chunk[n + 1] - 1)

        def copy_chunk(eng, c, done):
            n, k, ts = chunks[c]
            w = len(ts) * P
            out, src = pT[:, n % 2, k * P:k * P + w], ps_t[:, c % 2, 0:w]
            (eng.activation(out, src, ACT.Copy) if by_act(c) else eng.tensor_copy(out, src)).then_inc(done, 1)

        @block.scalar
        def _(act):
            act.preload_act_table_set("exp_and_others")

            def exps(g, n):
                i, r = units[n]
                act.wait_ge(sc_read, g * N + n + 1)
                if n >= 2:
                    act.wait_ge(t_done, g * NCH + first_chunk[n - 1])
                    act.wait_ge(o_used, g * N + n - 1)
                else:
                    act.wait_ge(o_used, g * N)
                w = (i + 1) * P
                ww = w - max(0, i - 4) * P
                act.activation(pr[:, n % 2, 0:w], sc[:, n % 2, 0:w], ACT.Exp, bias=nmx[:, n % 2, 0:1], accum_out=sums[:, n % 2, 0:1])
                act.activation(pr[:, n % 2, w:w + ww], sc[:, n % 2, w:w + ww], ACT.Exp, bias=nmx[:, n % 2, 1:2],
                               accum_out=sums[:, n % 2, 1:2]).then_inc(e_done, 1)

            with act.Fori(0, 2) as g:
                act.wait_ge(out_done, g)
                act.activation(ks_st[:, :], keep["ksT"][:, g, :], ACT.Copy)
                act.activation(kw_st[:, :], keep["kwT"][:, g, :], ACT.Copy).then_inc(st_act, 1)
                exps(g, 0)
                for n in range(N):
                    for c in range(first_chunk[n], first_chunk[n + 1]):
                        if by_act(c):
                            act.wait_ge(t_done, g * NCH + c + 1)
                            copy_chunk(act, c, tc_act)
                    if n + 1 < N:
                        exps(g, n + 1)

        @block.vector
        def _(dve):
            step = [0]

            def then(g, ins):
                step[0] += 1
                ins.then_inc(dve_step, 1)
                dve.wait_ge(dve_step, g * DSTEP + step[0])

            def masked_max(g, n):
                i, r = units[n]
                w = (i + 1) * P
                ww = w - max(0, i - 4) * P
                if r == 0:
                    dve.wait_ge(mask_done, g * NT + i + 1)
                dve.wait_ge(sc_done, g * N + n + 1)
                if n >= 2:
                    dve.wait_ge(e_done, g * N + n - 1)
                else:
                    dve.wait_ge(e_done, g * N)
                dve.memset(nothing[:, :], 0.0)
                dve.tensor_tensor_reduce(sc[:, n % 2, 0:w], ps_s[:, 0:w], mask[:, i % 2, 0:w], 1.0, FAR, ALU.add, ALU.max, mx[:, n % 2, 0:1])
                then(g, dve.tensor_tensor_reduce(sc[:, n % 2, w:w + ww], ps_w[:, 0:ww], win[:, 5 * P - ww:5 * P], 1.0, FAR, ALU.add, ALU.max, mx[:, n % 2, 1:2]))
                dve.tensor_scalar(nmx[:, n % 2, :], mx[:, n % 2, :], -1.0, None, ALU.mult).then_inc(sc_read, 1)

            def combine(g, n):
                i, r = units[n]
                dve.wait_ge(e_done, g * N + n + 1)
                then(g, dve.reciprocal(cf[:, n % 2, :], sums[:, n % 2, :]))
                then(g, dve.tensor_tensor(cf[:, n % 2, :], cf[:, n % 2, :], gate_st[:, i, r, 1:3], ALU.mult))
                dve.wait_ge(o_done, g * N + n + 1)
                o = o_st[:, i, r, :]
                then(g, dve.scalar_tensor_tensor(out=o, in0=ps_o[:, n % 2, 0:HD], scalar=cf[:, n % 2, 0:1], in1=o, op0=ALU.mult, op1=ALU.add))
                dve.scalar_tensor_tensor(out=o, in0=ps_o[:, n % 2, HD:2 * HD], scalar=cf[:, n % 2, 1:2], in1=o, op0=ALU.mult, op1=ALU.add).then_inc(o_used, 1)

            dve.wait_ge(c_in, 32)
            with dve.Fori(0, 2) as g:
                step[0] = 0
                dve.tensor_scalar(q_st[:, :, :], keep["qbT"][:, bass.ds(g * 2, 2), :], 1.0, None, ALU.mult)
                dve.tensor_scalar(vs_st[:, :, :], keep["vs"][:, :, bass.ds(g * HD, HD)], 1.0, None, ALU.mult)
                dve.tensor_scalar(vw_st[:, :, :], keep["vw"][:, :, bass.ds(g * HD, HD)], 1.0, None, ALU.mult)
                dve.tensor_scalar(sel_st[:, :, :], keep["sel"][:, g, :, :], 1.0, None, ALU.mult)
                dve.tensor_scalar(gate_st[:, :, :, :].rearrange("p i r b -> p i (r b)"), keep["gate"][:, :, bass.ds(g * 12, 12)], 1.0, None, ALU.mult)
                dve.tensor_scalar(o_st[:, :, :, :].rearrange("p i r d -> p i (r d)"), keep["o_tok"][:, :, bass.ds(g * 256, 256)], 1.0, None, ALU.mult).then_inc(st_dve, 1)
                dve.wait_ge(st_dve, g + 1)
                masked_max(g, 0)
                for n in range(N):
                    if n + 1 < N:
                        masked_max(g, n + 1)
                    for c in range(first_chunk[n], first_chunk[n + 1]):
                        if not by_act(c):
                            dve.wait_ge(t_done, g * NCH + c + 1)
                            copy_chunk(dve, c, tc_dve)
                    combine(g, n)
                while step[0] < DSTEP:
                    then(g, dve.memset(cf[:, 0, 0:1], 0.0))
                dve.wait_ge(o_used, g * N + N)
                dve.tensor_scalar(keep["o_tok"][:, :, bass.ds(g * 256, 256)], o_st[:, :, :, :].rearrange("p i r d -> p i (r d)"), 1.0, None, ALU.mult).then_inc(out_done, 1)
                dve.wait_ge(out_done, g + 1)


def stage_attention_out(nc, w_out, x, g, b, keep, h_out):
    with ExitStack() as ctx:
        m = Stage(nc, ctx, "ao")
        w = m.sb("w", [P, KC, D])
        oT = m.sb("oT", [P, 2, 4, P])
        y = m.sb("y", [P, 2, D])
        xr = m.sb("xr", [P, 2, D])
        norm = Norm(m, "ln")
        ps_t = m.ps("ps_t", [P, 2, 512])
        ps_y = m.ps("ps_y", [P, 2, D])
        w_in, transposed, t_copied, y_mm, y_ready, dve_step, y_read = (m.sem(n) for n in "w_in transposed t_copied y_mm y_ready dve_step y_read".split())
        x_in = [m.sem(f"x_in{k}") for k in range(2)]
        stored = [m.sem(f"stored{k}") for k in range(2)]
        block = ctx.enter_context(nc.Block())

        @block.sync
        def _(sp):
            sp.dma_start(w[:, :, :], w_out.rearrange("(c p) n -> p c n", p=P)).then_inc(w_in, 16)
            norm.load(sp, g, b)
            for i in range(NT):
                if i >= 2:
                    sp.wait_ge(y_read, i - 1)
                sp.dma_start(xr[:, i % 2, :], x[i * P:(i + 1) * P, :]).then_inc(x_in[i % 2], 16)
                if i:
                    sp.wait_ge(y_ready, i)
                    sp.dma_start(h_out[(i - 1) * P:i * P, :], y[:, (i - 1) % 2, :]).then_inc(stored[(i - 1) % 2], 16)
            sp.wait_ge(y_ready, NT)
            sp.dma_start(h_out[(NT - 1) * P:, :], y[:, (NT - 1) % 2, :]).then_inc(stored[(NT - 1) % 2], 16)
            for k in range(2):
                sp.wait_ge(stored[k], 16 * NT // 2)

        @block.tensor
        def _(pe):
            def transposes(i):
                if i >= 2:
                    pe.wait_ge(t_copied, i - 1)
                for c in range(4):
                    x_ = pe.transpose(ps_t[:, i % 2, c * P:(c + 1) * P], keep["o_tok"][:, i, c * P:(c + 1) * P], keep["ident"][:, :])
                x_.then_inc(transposed, 1)

            transposes(0)
            pe.wait_ge(w_in, 16)
            for i in range(NT):
                if i + 1 < NT:
                    transposes(i + 1)
                if i >= 2:
                    pe.wait_ge(y_read, i - 1)
                pe.wait_ge(t_copied, i + 1)
                for half in range(2):
                    for c in range(KC):
                        lhs = keep["qaT"][:, c, i * P:(i + 1) * P] if c < 4 else oT[:, i % 2, c - 4, :]
                        x_ = pe.matmul(ps_y[:, i % 2, half * 512:(half + 1) * 512], lhs, w[:, c, half * 512:(half + 1) * 512],
                                       start=(c == 0), stop=(c == KC - 1))
                x_.then_inc(y_mm, 1)

        @block.scalar
        def _(act):
            for i in range(NT):
                act.wait_ge(transposed, i + 1)
                if i >= 2:
                    act.wait_ge(y_mm, i - 1)
                act.activation(oT[:, i % 2, :, :], ps_t[:, i % 2, :].rearrange("p (c t) -> p c t", c=4), ACT.Copy).then_inc(t_copied, 1)
                if i:
                    norm.on_act(act, i - 1)
            norm.on_act(act, NT - 1)

        @block.vector
        def _(dve):
            step = [0]

            def then(ins):
                step[0] += 1
                ins.then_inc(dve_step, 1)
                dve.wait_ge(dve_step, step[0])

            for i in range(NT):
                dve.wait_ge(y_mm, i + 1)
                dve.wait_ge(x_in[i % 2], 16 * (i // 2 + 1))
                if i >= 2:
                    dve.wait_ge(stored[i % 2], 16 * (i // 2))
                yy = y[:, i % 2, :]
                dve.scalar_tensor_tensor(out=yy, in0=xr[:, i % 2, :], scalar=ALPHA, in1=ps_y[:, i % 2, :],
                                         op0=ALU.mult, op1=ALU.add).then_inc(y_read, 1)
                dve.wait_ge(y_read, i + 1)
                norm.on_dve(dve, then, yy, i).then_inc(y_ready, 1)


class Moe:

    def __init__(self, nc, ctx, name, y, w_gate, w_up, w_down):
        m = self.m = Stage(nc, ctx, name)
        self.name, self.w_gate, self.w_up, self.w_down = name, w_gate, w_up, w_down
        self.ident = m.sb("ident", [P, P])
        self.acc = m.sb("acc", [P, NT, D])
        self.w = m.sb("w", [P, 4, 3, 2048])
        self.dest = m.sb("dest", [P, NT, TOPK], I32)
        self.gates = m.sb("gates", [P, NT, TOPK])
        self.slot_tok = m.sb("slot_tok", [CAP, NBLK])
        self.spill = m.sb("spill", [1, 1 + NSPILL], I32)
        self.wgu_in = [m.sem(f"wgu_in{s}") for s in range(4)]
        self.wd_in = [m.sem(f"wd_in{s}") for s in range(4)]
        self.tab = nc.dram_tensor(f"{name}_tab", (NBLK * CAP, 1), F32, kind="Internal").ap()
        self.y = y

    def gu(self, s):
        return self.w[:, s, 0:2, :].rearrange("p a b -> p (a b)").rearrange("p (c f) -> p c f", c=KC)

    def down(self, s):
        return self.w[:, s, 2, :].rearrange("p (c n) -> p c n", c=2)

    def load(self, eng, e, s):
        gu = self.gu(s)

        def rows(w):
            v = w[bass.ds(e, 1), :, :]
            return v.rearrange("a (p c) f -> p (a c) f", p=P)

        eng.dma_start(gu[:, :, 0:FH], rows(self.w_gate)).then_inc(self.wgu_in[s], 16)
        eng.dma_start(gu[:, :, FH:2 * FH], rows(self.w_up)).then_inc(self.wgu_in[s], 16)
        eng.dma_start(self.down(s), rows(self.w_down)).then_inc(self.wd_in[s], 16)


def stage_route(nc, M, h, router, bias, sh_gate, sh_up, sh_down, consts):
    with ExitStack() as ctx:
        m = Stage(nc, ctx, M.name + "r")
        spare = M.w[:, 2:4, :, :].rearrange("p s a b -> p (s a b)")
        hT = spare[:, 0:8192].rearrange("p (c t) -> p c t", c=KC)
        hidT = spare[:, 8192:10240].rearrange("p (c t) -> p c t", c=2)
        w_sh = m.sb("w_sh", [P, 2, KC, FH])
        w_shd = m.sb("w_shd", [P, 2, D])
        w_r = m.sb("w_r", [P, KC, NE])
        bias_sb = m.sb("bias", [P, NE])
        tri8 = m.sb("tri8", [P, 8, 8])
        cexp = m.sb("cexp", [P, 3, NE])
        before = m.sb("before", [P, 2, P])
        cspill = m.sb("cspill", [1, NSPILL])
        ctok = m.sb("ctok", [P, NT])
        score = m.sb("score", [P, NT, NE])
        biased = m.sb("biased", [P, NT, NE])
        m8 = m.sb("m8", [P, NT * 8, 8])
        gs = m.sb("gs", [P, 3, NT, 8])
        cmp_ = m.sb("cmp", [P, 2, NT, 8, 8])
        top = m.sb("top", [P, NT, 8])
        tid = m.sb("tid", [P, NT, 8], U32)
        tidf = m.sb("tidf", [P, NT, 8])
        onehot = m.sb("onehot", [P, NT, TOPK, NE])
        prod = m.sb("prod", [P, NT, TOPK, NE])
        mem = m.sb("mem", [P, NT, NE])
        slot = m.sb("slot", [P, NT, NE])
        over = m.sb("over", [P, NT, NE])
        nb = m.sb("nb", [P, 3, NE])
        ones = m.sb("ones", [P, NE])
        gsum = m.sb("gsum", [P, 2, NT])
        destf = m.sb("destf", [P, NT, TOPK])
        sil = m.sb("sil", [P, 2, 512])
        tabT = m.sb("tabT", [NBLK, CAP])
        spillf = m.sb("spillf", [1, 1 + NSPILL])
        ps_t = m.ps("ps_t", [P, 2, 512])
        ps_a = m.ps("ps_a", [P, 4, 512])
        ps_r = m.ps("ps_r", [P, NT, NE])
        ps_p = m.ps("ps_p", [P, NT, NE])
        (h_in, rw_in, sw_in, c_in, tab_zero, transposed, t_act, t_dve, logits_done, score_done, members, pos_done, dest_done,
         hid_mm, sil_done, hid_done, dn_mm, acc_done, dve_step, scattered, tab_in, tab_t, spill_f, cnt_read, cnt_done) = (m.sem(n) for n in
            "h_in rw_in sw_in c_in tab_zero transposed t_act t_dve logits_done score_done members pos_done dest_done hid_mm sil_done hid_done dn_mm acc_done dve_step scattered tab_in tab_t spill_f cnt_read cnt_done".split())
        block = ctx.enter_context(nc.Block())

        @block.sync
        def _(sp):
            sp.dma_start(M.ident[:, :], consts["c_ident"]).then_inc(h_in, 16)
            sp.dma_start(M.acc[:, :, :], h.rearrange("(i p) d -> p i d", p=P)).then_inc(h_in, 16)
            sp.dma_start(w_r[:, :, :], router.rearrange("(p c) e -> p c e", c=KC)).then_inc(rw_in, 16)
            sp.dma_start(M.tab.rearrange("(b s) one -> b (s one)", s=CAP), consts["c_zero"]).then_inc(tab_zero, 16)
            sp.dma_start(bias_sb[:, :], bias.partition_broadcast(P)).then_inc(c_in, 16)
            for dst, n in ((tri8, "c_tri8"), (cexp, "c_exp"), (before, "c_before"), (cspill, "c_spill"), (ctok, "c_tok")):
                sp.dma_start(dst[:], consts[n]).then_inc(c_in, 16)
            for i, w in enumerate((sh_gate, sh_up)):
                sp.dma_start(w_sh[:, i, :, :], w.rearrange("(p c) f -> p c f", c=KC)).then_inc(sw_in, 16)
            sp.dma_start(w_shd[:, :, :], sh_down.rearrange("(p c) n -> p c n", c=2)).then_inc(sw_in, 16)
            for e in range(2):
                M.load(sp, e, e)
            sp.wait_ge(scattered, 16 * NT * TOPK)
            sp.dma_start(tabT[:, :], M.tab.rearrange("(b s) one -> b (s one)", s=CAP)).then_inc(tab_in, 16)

        @block.gpsimd
        def _(pool):
            pool.wait_ge(tab_zero, 16)
            pool.wait_ge(c_in, 96)
            pool.wait_ge(dest_done, 1)
            for i in range(NT):
                for k in range(TOPK):
                    pool.indirect_dma_start(out=M.tab, out_offset=bass.IndirectOffsetOnAxis(ap=M.dest[:, i, k:k + 1], axis=0),
                                            in_=ctok[:, i:i + 1], in_offset=None).then_inc(scattered, 16)

        @block.tensor
        def _(pe):
            pe.wait_ge(h_in, 32)
            for n in range(2 * NT):
                i, c0 = n // 2, 4 * (n % 2)
                if n >= 2:
                    pe.wait_ge((t_act, t_dve)[n % 2], n // 2)
                for c in range(4):
                    x = pe.transpose(ps_t[:, n % 2, c * P:(c + 1) * P],
                                     M.acc[:, i, c0 + c::KC], M.ident[:, :])
                x.then_inc(transposed, 1)
            pe.wait_ge(t_act, NT)
            pe.wait_ge(t_dve, NT)
            pe.wait_ge(rw_in, 16)
            for i in range(NT):
                for c in range(KC):
                    x = pe.matmul(ps_r[:, i, :], hT[:, c, i * P:(i + 1) * P], w_r[:, c, :], start=(c == 0), stop=(c == KC - 1),
                                  skip_group_check=True)
            x.then_inc(logits_done, 1)
            pe.wait_ge(sw_in, 48)
            for u in range(4):
                fc, half = u // 2, u % 2
                if u >= 2:
                    pe.wait_ge(hid_done, u - 1)
                for gu in range(2):
                    for c in range(KC):
                        x = pe.matmul(ps_a[:, 2 * (u % 2) + gu, :], w_sh[:, gu, c, fc::2], hT[:, c, half * 512:(half + 1) * 512],
                                      start=(c == 0), stop=(c == KC - 1))
                x.then_inc(hid_mm, 1)
            pe.wait_ge(c_in, 96)
            pe.wait_ge(members, 1)
            for i in range(NT):
                for j in range(i + 1):
                    x = pe.matmul(ps_p[:, i, :], before[:, 0 if j == i else 1, :], mem[:, j, :], start=(j == 0), stop=(j == i),
                                  skip_group_check=True)
            x.then_inc(pos_done, 1)
            for j in range(NT):
                x = pe.matmul(ps_r[:, 0, :], before[:, 1, :], mem[:, j, :], start=(j == 0), stop=(j == NT - 1), skip_group_check=True)
            x.then_inc(cnt_done, 1)
            for i in range(NT):
                pe.wait_ge(hid_done, 4)
                if i >= 2:
                    pe.wait_ge(acc_done, i - 1)
                for half in range(2):
                    for c in range(2):
                        x = pe.matmul(ps_a[:, 2 * (i % 2) + half, :], hidT[:, c, i * P:(i + 1) * P], w_shd[:, c, half * 512:(half + 1) * 512],
                                      start=(c == 0), stop=(c == 1))
                x.then_inc(dn_mm, 1)
            pe.wait_ge(tab_in, 16)
            pe.transpose(ps_t[0:CAP, 0, 0:NBLK], tabT[:, :], M.ident[0:NBLK, 0:NBLK]).then_inc(tab_t, 1)

        @block.scalar
        def _(act):
            for i in range(NT):
                act.wait_ge(transposed, 2 * i + 1)
                act.activation(hT[:, 0:4, i * P:(i + 1) * P], ps_t[:, 0, :].rearrange("p (c t) -> p c t", c=4), ACT.Copy).then_inc(t_act, 1)
            act.wait_ge(logits_done, 1)
            act.activation(score[:, :, :], ps_r[:, :, :], ACT.Sigmoid).then_inc(score_done, 1)
            for u in range(4):
                act.wait_ge(hid_mm, u + 1)
                if u >= 2:
                    act.wait_ge(hid_done, u - 1)
                act.activation(sil[:, u % 2, :], ps_a[:, 2 * (u % 2), :], ACT.Silu).then_inc(sil_done, 1)

        @block.vector
        def _(dve):
            step = [0]

            def then(ins):
                step[0] += 1
                ins.then_inc(dve_step, 1)
                dve.wait_ge(dve_step, step[0])

            for i in range(NT):
                dve.wait_ge(transposed, 2 * i + 2)
                dve.tensor_copy(hT[:, 4:8, i * P:(i + 1) * P], ps_t[:, 1, :].rearrange("p (c t) -> p c t", c=4)).then_inc(t_dve, 1)

            def hidden(u):
                fc, half = u // 2, u % 2
                dve.wait_ge(sil_done, u + 1)
                dve.tensor_tensor(hidT[:, fc, half * 512:(half + 1) * 512], sil[:, u % 2, :], ps_a[:, 2 * (u % 2) + 1, :], ALU.mult).then_inc(hid_done, 1)

            dve.wait_ge(score_done, 1)
            dve.wait_ge(c_in, 96)
            then(dve.tensor_tensor(biased[:, :, :], score[:, :, :], bias_sb[:, :].unsqueeze(1).to_broadcast([P, NT, NE]), ALU.add))
            bg = biased[:, :, :].rearrange("p i (g e) -> p (i g) e", e=8)
            for n in range(8 * NT):
                x = dve.max(m8[:, n, :], bg[:, n, :])
            then(x)
            pair = m8[:, :, :].rearrange("p (i g) k -> p i g k", g=8)
            then(dve.tensor_tensor(gs[:, 0, :, :], pair[:, :, :, 0], pair[:, :, :, 1], ALU.add))
            other = gs[:, 0, :, :].unsqueeze(2).to_broadcast([P, NT, 8, 8])
            own = gs[:, 0, :, :].unsqueeze(3).to_broadcast([P, NT, 8, 8])
            then(dve.tensor_tensor(cmp_[:, 0, :, :, :], other, own, ALU.is_gt))
            then(dve.tensor_tensor(cmp_[:, 1, :, :, :], other, own, ALU.is_equal))
            then(dve.tensor_tensor(cmp_[:, 1, :, :, :], cmp_[:, 1, :, :, :], tri8[:, :, :].unsqueeze(1).to_broadcast([P, NT, 8, 8]), ALU.mult))
            then(dve.tensor_tensor(cmp_[:, 0, :, :, :], cmp_[:, 0, :, :, :], cmp_[:, 1, :, :, :], ALU.add))
            then(dve.tensor_reduce(gs[:, 1, :, :], cmp_[:, 0, :, :, :], AX, ALU.add))
            then(dve.tensor_scalar(gs[:, 1, :, :], gs[:, 1, :, :], 3.5, None, ALU.is_lt))
            then(dve.tensor_scalar(gs[:, 2, :, :], gs[:, 1, :, :], -NEG, NEG, ALU.mult, ALU.add))
            b4 = biased[:, :, :].rearrange("p i (g e) -> p i g e", e=8)
            then(dve.tensor_tensor(b4, b4, gs[:, 1, :, :].unsqueeze(3).to_broadcast([P, NT, 8, 8]), ALU.mult))
            then(dve.tensor_tensor(b4, b4, gs[:, 2, :, :].unsqueeze(3).to_broadcast([P, NT, 8, 8]), ALU.add))
            for i in range(NT):
                x = dve.max(top[:, i, :], biased[:, i, :])
            then(x)
            for i in range(NT):
                x = dve.max_index(tid[:, i, :], top[:, i, :], biased[:, i, :])
            then(x)
            then(dve.tensor_copy(tidf[:, :, :], tid[:, :, :]))
            then(dve.tensor_tensor(onehot[:, :, :, :], tidf[:, :, 0:TOPK].unsqueeze(3).to_broadcast([P, NT, TOPK, NE]),
                                   cexp[:, 0, :].unsqueeze(1).unsqueeze(1).to_broadcast([P, NT, TOPK, NE]), ALU.is_equal))
            dve.tensor_reduce(mem[:, :, :], onehot[:, :, :, :].rearrange("p i k e -> p i e k"), AX, ALU.add).then_inc(members, 1)
            for u in range(2):
                hidden(u)
            then(dve.tensor_tensor(prod[:, :, :, :], onehot[:, :, :, :], score[:, :, :].unsqueeze(2).to_broadcast([P, NT, TOPK, NE]), ALU.mult))
            then(dve.tensor_reduce(M.gates[:, :, :], prod[:, :, :, :], AX, ALU.add))
            for u in range(2, 4):
                hidden(u)
            then(dve.tensor_reduce(gsum[:, 0, :], M.gates[:, :, :], AX, ALU.add))
            then(dve.reciprocal(gsum[:, 1, :], gsum[:, 0, :]))
            then(dve.tensor_tensor(M.gates[:, :, :], M.gates[:, :, :], gsum[:, 1, :].unsqueeze(2).to_broadcast([P, NT, TOPK]), ALU.mult))
            then(dve.tensor_scalar(M.gates[:, :, :], M.gates[:, :, :], 2.5, None, ALU.mult))
            dve.wait_ge(cnt_done, 1)
            then(dve.memset(ones[:, :], 1.0))
            then(dve.tensor_scalar(nb[:, 0, :], ps_r[:, 0, :], CAP + 0.5, None, ALU.is_gt))
            for k in range(2, S // CAP):
                then(dve.scalar_tensor_tensor(out=nb[:, 0, :], in0=ps_r[:, 0, :], scalar=k * CAP + 0.5, in1=nb[:, 0, :], op0=ALU.is_gt, op1=ALU.add))
            then(dve.tensor_tensor_scan(nb[:, 1, :], ones[:, :], nb[:, 0, :], 0.0, ALU.mult, ALU.add))
            then(dve.tensor_tensor(nb[:, 2, :], nb[:, 1, :], nb[:, 0, :], ALU.subtract))
            then(dve.scalar_tensor_tensor(out=nb[:, 2, :], in0=nb[:, 2, :], scalar=float(CAP), in1=cexp[:, 2, :], op0=ALU.mult, op1=ALU.add))
            dve.wait_ge(pos_done, 1)
            then(dve.tensor_scalar(over[:, :, :], ps_p[:, :, :], CAP - 0.5, None, ALU.is_gt))
            then(dve.tensor_tensor(over[:, :, :], over[:, :, :], nb[:, 2, :].unsqueeze(1).to_broadcast([P, NT, NE]), ALU.mult))
            then(dve.tensor_tensor(slot[:, :, :], ps_p[:, :, :], cexp[:, 1, :].unsqueeze(1).to_broadcast([P, NT, NE]), ALU.add))
            then(dve.tensor_tensor(slot[:, :, :], slot[:, :, :], over[:, :, :], ALU.add))
            then(dve.tensor_tensor(prod[:, :, :, :], onehot[:, :, :, :], slot[:, :, :].unsqueeze(2).to_broadcast([P, NT, TOPK, NE]), ALU.mult))
            then(dve.tensor_reduce(destf[:, :, :], prod[:, :, :, :], AX, ALU.add))
            dve.tensor_copy(M.dest[:, :, :], destf[:, :, :]).then_inc(dest_done, 1)
            sp3 = prod[0:1, :, :, :].rearrange("p i k e -> p (i k) e")
            then(dve.tensor_copy(spillf[:, 0:1], nb[0:1, 1, NE - 1:NE]))
            then(dve.tensor_tensor(sp3, nb[0:1, 1, :].unsqueeze(1).to_broadcast([1, NSPILL, NE]),
                                   cspill[:, :].unsqueeze(2).to_broadcast([1, NSPILL, NE]), ALU.is_le))
            then(dve.tensor_reduce(spillf[:, 1:], sp3, AX, ALU.add))
            then(dve.tensor_scalar(spillf[:, 1:], spillf[:, 1:], float(NE - 1), None, ALU.min))
            then(dve.tensor_copy(M.spill[:, :], spillf[:, :]))
            for i in range(NT):
                dve.wait_ge(dn_mm, i + 1)
                dve.scalar_tensor_tensor(out=M.acc[:, i, :], in0=M.acc[:, i, :], scalar=ALPHA,
                                         in1=ps_a[:, 2 * (i % 2):2 * (i % 2) + 2, :].rearrange("p a b -> p (a b)"),
                                         op0=ALU.mult, op1=ALU.add).then_inc(acc_done, 1)
            dve.wait_ge(tab_t, 1)
            dve.tensor_copy(M.slot_tok[:, :], ps_t[0:CAP, 0, 0:NBLK])


def stage_experts(nc, M, h):
    with ExitStack() as ctx:
        m = Stage(nc, ctx, M.name + "e")
        TURN = 4
        AHEAD = 3
        xg = m.sb("xg", [P, TURN, D])
        xT = m.sb("xT", [P, 2, KC, P])
        idx = m.sb("idx", [P, TURN], I32)
        sil = m.sb("sil", [P, 2, FH])
        a_ = m.sb("a", [P, 2, FH])
        aT = m.sb("aT", [P, 2, 2, P])
        yo = m.sb("yo", [P, 2, D])
        tick = m.sb("tick", [1, 1])
        ps_x = m.ps("ps_x", [P, 2, 512])
        ps_gu = m.ps("ps_gu", [P, 2, 512])
        ps_a = m.ps("ps_a", [P, 512])
        ps_y = m.ps("ps_y", [P, 2, 512])
        (idx_done, xt_mm, x_act, x_dve, gu_done, sil_done, a_done, at_mm, at_done, y_mm, y_act, y_dve) = (m.sem(n) for n in
            "idx_done xt_mm x_act x_dve gu_done sil_done a_done at_mm at_done y_mm y_act y_dve".split())
        ticked = m.sem("ticked")
        gathered = [m.sem(f"gathered{k}") for k in range(TURN)]
        stored = [m.sem(f"stored{k}") for k in range(2)]
        block = ctx.enter_context(nc.Block())

        def turns(eng, steps):
            for s in range(TURN):
                steps(0, s, s)
            with eng.Fori(1, NE // TURN - 1) as t:
                for s in range(TURN):
                    steps(t, s, t * TURN + s)
            for s in range(TURN):
                steps(NE // TURN - 1, s, NE - TURN + s)

        def first(n, count):
            return isinstance(n, int) and n < count

        def last(n, count):
            return isinstance(n, int) and n >= NE - count

        @block.sync
        def _(sp):
            def steps(t, s, n):
                if not first(n, 1):
                    if not last(n, TURN - 1):
                        sp.wait_ge(y_mm, n)
                        M.load(sp, n + (TURN - 1), (s - 1) % TURN)
                    sp.wait_ge(y_act, n)
                    sp.wait_ge(y_dve, n)
                    sp.dma_start(M.y[bass.ds((n - 1) * CAP, CAP), :], yo[:, (s - 1) % 2, :]).then_inc(stored[(s - 1) % 2], 16)

            for s in range(2, TURN):
                M.load(sp, s, s)
            turns(sp, steps)
            sp.wait_ge(y_act, NE)
            sp.wait_ge(y_dve, NE)
            sp.dma_start(M.y[(NE - 1) * CAP:NE * CAP, :], yo[:, (NE - 1) % 2, :]).then_inc(stored[(NE - 1) % 2], 16)
            for k in range(2):
                sp.wait_ge(stored[k], 16 * NE // 2)

        @block.gpsimd
        def _(pool):
            def steps(t, s, n):
                pool.wait_ge(idx_done, n + 1)
                if not first(n, TURN):
                    pool.wait_ge(xt_mm, n - (TURN - 1))
                pool.wait_ge(ticked, n)
                pool.tensor_tensor(tick[:, :], M.slot_tok[0:1, 0:1], M.slot_tok[0:1, 0:1], ALU.add).then_inc(ticked, 1)
                pool.indirect_dma_start(out=xg[:, s, :], out_offset=None, in_=h,
                                        in_offset=bass.IndirectOffsetOnAxis(ap=idx[:, s:s + 1], axis=0)).then_inc(gathered[s], 16)
            turns(pool, steps)

        @block.tensor
        def _(pe):
            def tokens(t, s, n):
                pe.wait_ge(gathered[s], (t + 1) * 16)
                pe.wait_ge(x_act, n)
                pe.wait_ge(x_dve, n)
                for c in range(KC):
                    x = pe.transpose(ps_x[:, c // 4, (c % 4) * P:(c % 4 + 1) * P], xg[:, s, c::KC], M.ident[:, :])
                x.then_inc(xt_mm, 1)

            def gate_up(t, s, n, part):
                if part == 0:
                    pe.wait_ge(M.wgu_in[s], (t + 1) * 32)
                    pe.wait_ge(x_act, n + 1)
                    pe.wait_ge(x_dve, n + 1)
                    if not first(n, 2):
                        pe.wait_ge(a_done, n - 1)
                for c in range(4 * part, 4 * part + 4):
                    x = pe.matmul(ps_gu[:, s % 2, :], xT[:, s % 2, c, :], M.gu(s)[:, c, :], start=(c == 0), stop=(c == KC - 1))
                if part:
                    x.then_inc(gu_done, 1)

            def hidden(s, n):
                pe.wait_ge(a_done, n)
                if not first(n, 2):
                    pe.wait_ge(at_done, n - 1)
                for c in range(2):
                    x = pe.transpose(ps_a[:, c * P:(c + 1) * P], a_[:, (s - 1) % 2, c::2], M.ident[:, :])
                x.then_inc(at_mm, 1)

            def down(wd_count, s, n):
                k = (s - 1) % TURN
                pe.wait_ge(M.wd_in[k], wd_count * 16)
                pe.wait_ge(at_done, n)
                if not first(n, 2):
                    pe.wait_ge(y_act, n - 1)
                    pe.wait_ge(y_dve, n - 1)
                for half in range(2):
                    for c in range(2):
                        x = pe.matmul(ps_y[:, half, :], aT[:, k % 2, c, :], M.down(k)[:, c, half * 512:(half + 1) * 512], start=(c == 0), stop=(c == 1))
                x.then_inc(y_mm, 1)

            def steps(t, s, n):
                if not last(n, 1):
                    tokens(t + (s + 1) // TURN, (s + 1) % TURN, n + 1)
                gate_up(t, s, n, 0)
                if not first(n, 1):
                    hidden(s, n)
                gate_up(t, s, n, 1)
                if not first(n, 1):
                    down(t + 1 if s else t, s, n)

            tokens(0, 0, 0)
            turns(pe, steps)
            hidden(TURN, NE)
            down(NE // TURN, TURN, NE)

        @block.scalar
        def _(act):
            act.preload_act_table(ACT.Silu)

            def tokens(s, n):
                act.wait_ge(xt_mm, n + 1)
                if not first(n, 2):
                    act.wait_ge(gu_done, n - 1)
                act.activation(xT[:, s % 2, 0:4, :], ps_x[:, 0, :].rearrange("p (c t) -> p c t", c=4), ACT.Copy).then_inc(x_act, 1)

            def silu(s, n):
                act.wait_ge(gu_done, n + 1)
                if not first(n, 2):
                    act.wait_ge(a_done, n - 1)
                act.activation(sil[:, s % 2, :], ps_gu[:, s % 2, 0:FH], ACT.Silu).then_inc(sil_done, 1)

            def out(count, s, n):
                act.wait_ge(y_mm, n)
                if not first(n, 3):
                    act.wait_ge(stored[(s - 1) % 2], count * 16)
                act.activation(yo[:, (s - 1) % 2, 0:512], ps_y[:, 0, :], ACT.Copy).then_inc(y_act, 1)

            def steps(t, s, n):
                if not last(n, 1):
                    tokens(s + 1, n + 1)
                silu(s, n)
                if not first(n, 1):
                    out(t * 2 + (s - 1) // 2, s, n)

            tokens(0, 0)
            turns(act, steps)
            out(NE // 2 - 1, TURN, NE)

        @block.vector
        def _(dve):
            def index(t, s, n):
                if not first(n, TURN):
                    dve.wait_ge(gathered[s], t * 16)
                dve.tensor_scalar(idx[:, s:s + 1], M.slot_tok[:, bass.ds(n, 1)], 1.0, None, ALU.mult).then_inc(idx_done, 1)

            def tokens(s, n):
                dve.wait_ge(xt_mm, n + 1)
                if not first(n, 2):
                    dve.wait_ge(gu_done, n - 1)
                dve.tensor_copy(xT[:, s % 2, 4:8, :], ps_x[:, 1, :].rearrange("p (c t) -> p c t", c=4)).then_inc(x_dve, 1)

            def mult(s, n):
                dve.wait_ge(sil_done, n + 1)
                if not first(n, 2):
                    dve.wait_ge(at_mm, n - 1)
                dve.tensor_tensor(a_[:, s % 2, :], sil[:, s % 2, :], ps_gu[:, s % 2, FH:2 * FH], ALU.mult).then_inc(a_done, 1)

            def hidden(s, n):
                dve.wait_ge(at_mm, n)
                if not first(n, 3):
                    dve.wait_ge(y_mm, n - 2)
                dve.tensor_copy(aT[:, (s - 1) % 2, :, :], ps_a[:, 0:2 * P].rearrange("p (c t) -> p c t", c=2)).then_inc(at_done, 1)

            def out(count, s, n):
                dve.wait_ge(y_mm, n)
                if not first(n, 3):
                    dve.wait_ge(stored[(s - 1) % 2], count * 16)
                dve.tensor_copy(yo[:, (s - 1) % 2, 512:1024], ps_y[:, 1, :]).then_inc(y_dve, 1)

            def steps(t, s, n):
                if not last(n, AHEAD):
                    index(t + (s + AHEAD) // TURN, (s + AHEAD) % TURN, n + AHEAD)
                if not last(n, 1):
                    tokens(s + 1, n + 1)
                if not first(n, 1):
                    hidden(s, n)
                mult(s, n)
                if not first(n, 1):
                    out(t * 2 + (s - 1) // 2, s, n)

            for n in range(AHEAD):
                index(0, n, n)
            tokens(0, 0)
            turns(dve, steps)
            hidden(TURN, NE)
            out(NE // 2 - 1, TURN, NE)


def stage_spill(nc, M, h):
    with ExitStack() as ctx:
        m = Stage(nc, ctx, M.name + "s")
        xg = m.sb("xg", [P, D])
        xT = m.sb("xT", [P, KC, P])
        idx = m.sb("idx", [P, 1], I32)
        sil = m.sb("sil", [P, FH])
        a_ = m.sb("a", [P, FH])
        aT = m.sb("aT", [P, 2, P])
        yo = m.sb("yo", [P, D])
        tick = m.sb("tick", [1, 1])
        ps_x = m.ps("ps_x", [P, 2, 512])
        ps_gu = m.ps("ps_gu", [P, 512])
        ps_a = m.ps("ps_a", [P, 512])
        ps_y = m.ps("ps_y", [P, 2, 512])
        (w_in, idx_done, gathered, xt_mm, x_done, gu_done, sil_done, a_done, at_mm, at_done, y_mm, y_done, stored) = (m.sem(n) for n in
            "w_in idx_done gathered xt_mm x_done gu_done sil_done a_done at_mm at_done y_mm y_done stored".split())
        ticked = m.sem("ticked")
        last = m.sb("last", [1, 1])
        gu = M.gu(0)
        block = ctx.enter_context(nc.Block())

        def blocks(eng, body):
            n = eng.value_load(M.spill[0:1, 0:1], min_val=0, max_val=NSPILL)
            with eng.Fori(0, NSPILL) as b:
                with eng.If(b < n):
                    body(b)

        @block.sync
        def _(sp):
            def body(b):
                sp.wait_ge(y_mm, b)
                e = sp.value_load(M.spill[0:1, bass.ds(b + 1, 1)], min_val=0, max_val=NE - 1)
                for dst, w in ((gu[:, :, 0:FH], M.w_gate), (gu[:, :, FH:2 * FH], M.w_up), (M.down(0), M.w_down)):
                    sp.dma_start(dst, w[bass.ds(e, 1), :, :].rearrange("a (p c) f -> p (a c) f", p=P)).then_inc(w_in, 16)
                sp.wait_ge(y_done, b + 1)
                sp.dma_start(M.y[bass.ds(SPILL0 + b * CAP, CAP), :], yo[:, :]).then_inc(stored, 16)
            blocks(sp, body)

        @block.gpsimd
        def _(pool):
            def body(b):
                pool.wait_ge(idx_done, b + 1)
                pool.wait_ge(xt_mm, b)
                pool.wait_ge(ticked, b)
                pool.tensor_tensor(tick[:, :], M.slot_tok[0:1, 0:1], M.slot_tok[0:1, 0:1], ALU.add).then_inc(ticked, 1)
                pool.indirect_dma_start(out=xg[:, :], out_offset=None, in_=h,
                                        in_offset=bass.IndirectOffsetOnAxis(ap=idx[:, 0:1], axis=0)).then_inc(gathered, 16)
            blocks(pool, body)

        @block.tensor
        def _(pe):
            def body(b):
                pe.wait_ge(gathered, (b + 1) * 16)
                for c in range(KC):
                    x = pe.transpose(ps_x[:, c // 4, (c % 4) * P:(c % 4 + 1) * P], xg[:, c::KC], M.ident[:, :])
                x.then_inc(xt_mm, 1)
                pe.wait_ge(x_done, b + 1)
                pe.wait_ge(w_in, (b + 1) * 48)
                for c in range(KC):
                    x = pe.matmul(ps_gu[:, :], xT[:, c, :], gu[:, c, :], start=(c == 0), stop=(c == KC - 1))
                x.then_inc(gu_done, 1)
                pe.wait_ge(a_done, b + 1)
                for c in range(2):
                    x = pe.transpose(ps_a[:, c * P:(c + 1) * P], a_[:, c::2], M.ident[:, :])
                x.then_inc(at_mm, 1)
                pe.wait_ge(at_done, b + 1)
                for half in range(2):
                    for c in range(2):
                        x = pe.matmul(ps_y[:, half, :], aT[:, c, :], M.down(0)[:, c, half * 512:(half + 1) * 512], start=(c == 0), stop=(c == 1))
                x.then_inc(y_mm, 1)
            blocks(pe, body)

        @block.scalar
        def _(act):
            def body(b):
                act.wait_ge(gu_done, b + 1)
                act.activation(sil[:, :], ps_gu[:, 0:FH], ACT.Silu).then_inc(sil_done, 1)
            blocks(act, body)

        @block.vector
        def _(dve):
            def body(b):
                dve.wait_ge(gathered, b * 16)
                dve.tensor_scalar(idx[:, :], M.slot_tok[:, bass.ds(NE + b, 1)], 1.0, None, ALU.mult).then_inc(idx_done, 1)
                dve.wait_ge(xt_mm, b + 1)
                dve.tensor_copy(xT[:, :, :], ps_x[:, :, :].rearrange("p a (c t) -> p (a c) t", c=4)).then_inc(x_done, 1)
                dve.wait_ge(sil_done, b + 1)
                dve.tensor_tensor(a_[:, :], sil[:, :], ps_gu[:, FH:2 * FH], ALU.mult).then_inc(a_done, 1)
                dve.wait_ge(at_mm, b + 1)
                dve.tensor_copy(aT[:, :, :], ps_a[:, 0:2 * P].rearrange("p (c t) -> p c t", c=2)).then_inc(at_done, 1)
                dve.wait_ge(y_mm, b + 1)
                dve.tensor_copy(yo[:, :], ps_y[:, :, :].rearrange("p a b -> p (a b)")).then_inc(y_done, 1)
                dve.wait_ge(stored, (b + 1) * 16)
                dve.memset(last[:, :], 0.0)
            blocks(dve, body)


def stage_combine(nc, M, g, b, h_out):
    with ExitStack() as ctx:
        m = Stage(nc, ctx, M.name + "c")
        rows = m.sb("rows", [P, 2, TOPK, D])
        norm = Norm(m, "ln")
        acc_ready, dve_step, tile_done = (m.sem(n) for n in "acc_ready dve_step tile_done".split())
        rows_in = [m.sem(f"rows_in{k}") for k in range(2)]
        rows_read, stored = m.sem("rows_read"), m.sem("stored")
        block = ctx.enter_context(nc.Block())

        @block.gpsimd
        def _(pool):
            for i in range(NT):
                if i >= 2:
                    pool.wait_ge(rows_read, i - 1)
                for k in range(TOPK):
                    pool.indirect_dma_start(out=rows[:, i % 2, k, :], out_offset=None, in_=M.y,
                                            in_offset=bass.IndirectOffsetOnAxis(ap=M.dest[:, i, k:k + 1], axis=0)).then_inc(rows_in[i % 2], 16)

        @block.sync
        def _(sp):
            norm.load(sp, g, b)
            for i in range(NT):
                sp.wait_ge(tile_done, i + 1)
                sp.dma_start(h_out[i * P:(i + 1) * P, :], M.acc[:, i, :]).then_inc(stored, 16)
            sp.wait_ge(stored, 16 * NT)

        @block.scalar
        def _(act):
            for i in range(NT):
                norm.on_act(act, i)

        @block.vector
        def _(dve):
            step = [0]

            def then(ins):
                step[0] += 1
                ins.then_inc(dve_step, 1)
                dve.wait_ge(dve_step, step[0])

            for i in range(NT):
                y = M.acc[:, i, :]
                dve.wait_ge(rows_in[i % 2], 16 * TOPK * (i // 2 + 1))
                for k in range(TOPK):
                    x = dve.scalar_tensor_tensor(out=y, in0=rows[:, i % 2, k, :], scalar=M.gates[:, i, k:k + 1], in1=y, op0=ALU.mult, op1=ALU.add)
                    if k < TOPK - 1:
                        then(x)
                x.then_inc(rows_read, 1)
                dve.wait_ge(rows_read, i + 1)
                norm.on_dve(dve, then, y, i).then_inc(tile_done, 1)


def moe_layer(nc, name, y, h, weights, ln_g, ln_b, consts, h_out):
    router, bias, w_gate, w_up, w_down, sh_gate, sh_up, sh_down = weights
    with ExitStack() as ctx:
        M = Moe(nc, ctx, name, y, w_gate, w_up, w_down)
        stage_route(nc, M, h, router, bias, sh_gate, sh_up, sh_down, consts)
        stage_experts(nc, M, h)
        stage_spill(nc, M, h)
        stage_combine(nc, M, ln_g, ln_b, h_out)


def stage_ssm_input(nc, h, w_in, c_ident, ident, uT):
    with ExitStack() as ctx:
        m = Stage(nc, ctx, "si")
        ht = m.sb("ht", [P, 2, D])
        hT = m.sb("hT", [P, 2, KC, P])
        w = m.sb("w", [P, KC, D])
        u = m.sb("u", [P, NG, L, GC])
        ps_t = m.ps("ps_t", [P, 2, 512])
        ps_u = m.ps("ps_u", [P, 4, 512])
        (c_in, w_in_, transposed, t_act, t_dve, u_mm, u_done, g_t, g_act, g_dve) = (m.sem(n) for n in
            "c_in w_in transposed t_act t_dve u_mm u_done g_t g_act g_dve".split())
        h_in = [m.sem(f"h_in{k}") for k in range(2)]
        rows = h.rearrange("(c j) d -> j c d", j=L)
        block = ctx.enter_context(nc.Block())

        @block.sync
        def _(sp):
            sp.dma_start(ident[:, :], c_ident).then_inc(c_in, 16)
            for j in range(2):
                sp.dma_start(ht[:, j, :], rows[j]).then_inc(h_in[j], 16)
            sp.dma_start(w[:, :, :], w_in.rearrange("(c p) n -> p c n", p=P)).then_inc(w_in_, 16)
            for j in range(2, L):
                sp.wait_ge(transposed, 2 * (j - 1))
                sp.dma_start(ht[:, j % 2, :], rows[j]).then_inc(h_in[j % 2], 16)

        @block.tensor
        def _(pe):
            def transposes(j):
                pe.wait_ge(h_in[j % 2], 16 * (j // 2 + 1))
                for half in range(2):
                    if j:
                        pe.wait_ge((t_act, t_dve)[half], j)
                    for c in range(4):
                        x = pe.transpose(ps_t[:, half, c * P:(c + 1) * P], ht[:, j % 2, (4 * half + c) * P:(4 * half + c + 1) * P], ident[:, :])
                    x.then_inc(transposed, 1)

            pe.wait_ge(c_in, 16)
            transposes(0)
            pe.wait_ge(w_in_, 16)
            for j in range(L):
                if j + 1 < L:
                    transposes(j + 1)
                pe.wait_ge(t_act, j + 1)
                pe.wait_ge(t_dve, j + 1)
                if j >= 2:
                    pe.wait_ge(u_done, 2 * (j - 1))
                for half in range(2):
                    for c in range(KC):
                        x = pe.matmul(ps_u[:, 2 * (j % 2) + half, :], hT[:, j % 2, c, :], w[:, c, half * 512:(half + 1) * 512],
                                      start=(c == 0), stop=(c == KC - 1))
                    x.then_inc(u_mm, 1)
            pe.wait_ge(u_done, 2 * L)
            for n in range(NG // 4):
                if n >= 2:
                    pe.wait_ge((g_act, g_dve)[n % 2], n // 2)
                else:
                    pe.wait_ge((t_act, t_dve)[n % 2], L)
                for k in range(4):
                    g = 4 * n + k
                    x = pe.transpose(ps_t[:, n % 2, k * P:(k + 1) * P], u[:, g, :, :].rearrange("p j h -> p (j h)"), ident[:, :])
                x.then_inc(g_t, 1)

        @block.scalar
        def _(act):
            for j in range(L):
                act.wait_ge(transposed, 2 * j + 1)
                if j >= 2:
                    act.wait_ge(u_mm, 2 * (j - 1))
                act.activation(hT[:, j % 2, 0:4, :], ps_t[:, 0, :].rearrange("p (c t) -> p c t", c=4), ACT.Copy).then_inc(t_act, 1)
                for half in range(2):
                    act.wait_ge(u_mm, 2 * j + half + 1)
                    act.activation(u[:, half * NQ:(half + 1) * NQ, j, :], ps_u[:, 2 * (j % 2) + half, :].rearrange("p (g h) -> p g h", h=GC), ACT.Copy).then_inc(u_done, 1)
            for n in range(0, NG // 4, 2):
                act.wait_ge(g_t, n + 1)
                act.activation(uT[:, 4 * n:4 * n + 4, :], ps_t[:, 0, :].rearrange("p (c t) -> p c t", c=4), ACT.Copy).then_inc(g_act, 1)

        @block.vector
        def _(dve):
            for j in range(L):
                dve.wait_ge(transposed, 2 * j + 2)
                if j >= 2:
                    dve.wait_ge(u_mm, 2 * (j - 1))
                dve.tensor_copy(hT[:, j % 2, 4:8, :], ps_t[:, 1, :].rearrange("p (c t) -> p c t", c=4)).then_inc(t_dve, 1)
            for n in range(1, NG // 4, 2):
                dve.wait_ge(g_t, n + 1)
                dve.tensor_copy(uT[:, 4 * n:4 * n + 4, :], ps_t[:, 1, :].rearrange("p (c t) -> p c t", c=4)).then_inc(g_dve, 1)


def stage_ssm_poles(nc, lam_re, lam_im, log_dt, b_re, b_im, ident, power, reverse, bbar, into):
    with ExitStack() as ctx:
        m = Stage(nc, ctx, "sp")
        lam = m.sb("lam", [NQ, 3, P])
        ldt = m.sb("ldt", [NQ, 2])
        lp = m.sb("lp", [P, 3, NQ])
        v = m.sb("v", [P, 12, NQ])
        b_ = m.sb("b", [P, 2, NQ, GC])
        tb = m.sb("tb", [P, 4, NQ, GC])
        g_ = m.sb("g", [P, 2, NQ, L, GC])
        tg = m.sb("tg", [P, 2, NQ, L, GC])
        ps_l = m.ps("ps_l", [P, 3, NQ])
        ps_t = m.ps("ps_t", [P, 2, 512])
        (lam_in, ldt_in, b_in, bcast, l_t, l_done, args, acts, g_ready, g_t, g_act, g_dve, dve_step, act_step) = (m.sem(n) for n in
            "lam_in ldt_in b_in bcast l_t l_done args acts g_ready g_t g_act g_dve dve_step act_step".split())
        block = ctx.enter_context(nc.Block())
        TWO_PI, MAGIC, EDGE = 2 * math.pi, 12582912.0, 3.1415925
        C1 = 6.28125
        C2 = float(np.float32(TWO_PI - C1))
        C3 = TWO_PI - C1 - C2

        @block.sync
        def _(sp):
            sp.dma_start(lam[:, 0, :], lam_re.rearrange("(q two) p -> q (two p)", two=2)).then_inc(lam_in, 16)
            sp.dma_start(lam[:, 1, :], lam_im.rearrange("(q two) p -> q (two p)", two=2)).then_inc(lam_in, 16)
            sp.dma_start(ldt[:, :], log_dt.rearrange("(q two) -> q two", two=2)).then_inc(ldt_in, 16)
            for i, b in enumerate((b_re, b_im)):
                sp.dma_start(b_[:, i, :, :], b.rearrange("(q two) p h -> (two p) q h", two=2)).then_inc(b_in, 16)

        @block.tensor
        def _(pe):
            pe.wait_ge(lam_in, 32)
            pe.wait_ge(bcast, 1)
            for k in range(3):
                x = pe.transpose(ps_l[:, k, :], lam[:, k, :], ident[0:NQ, 0:NQ])
            x.then_inc(l_t, 1)
            pe.wait_ge(g_ready, 1)
            for n in range(NQ // 2):
                if n >= 2:
                    pe.wait_ge((g_act, g_dve)[n % 2], n // 2)
                for k in range(4):
                    x = pe.transpose(ps_t[:, n % 2, k * P:(k + 1) * P],
                                     g_[:, k % 2, 2 * n + k // 2, :, :].rearrange("p j h -> p (j h)"), ident[:, :])
                x.then_inc(g_t, 1)

        @block.scalar
        def _(act):
            act.wait_ge(ldt_in, 16)
            act.activation(lam[:, 2, :].rearrange("q (a p) -> q a p", a=2), ldt[:, :].unsqueeze(2).to_broadcast([NQ, 2, 64]), ACT.Copy).then_inc(bcast, 1)
            act.wait_ge(l_done, 1)
            act.activation(v[:, 0, :], lp[:, 2, :], ACT.Exp).then_inc(acts, 1)
            act.wait_ge(args, 1)
            act.activation(v[:, 3, :], v[:, 1, :], ACT.Exp).then_inc(acts, 1)
            act.wait_ge(args, 2)
            act.activation(v[:, 6, :], v[:, 4, :], ACT.Sin).then_inc(acts, 1)
            act.activation(v[:, 7, :], v[:, 5, :], ACT.Sin).then_inc(acts, 1)
            for n in range(0, NQ // 2, 2):
                act.wait_ge(g_t, n + 1)
                act.activation(into[:, 2 * n:2 * n + 2, :, :], ps_t[:, 0, :].rearrange("p (q r s) -> p q r s", q=2, r=2), ACT.Copy).then_inc(g_act, 1)

        @block.vector
        def _(dve):
            step = [0]

            def then(ins):
                step[0] += 1
                ins.then_inc(dve_step, 1)
                dve.wait_ge(dve_step, step[0])

            dve.wait_ge(l_t, 1)
            dve.tensor_copy(lp[:, :, :], ps_l[:, :, :]).then_inc(l_done, 1)
            dve.wait_ge(l_done, 1)
            dve.wait_ge(acts, 1)
            lre, lim, dt = lp[:, 0, :], lp[:, 1, :], v[:, 0, :]
            dve.tensor_tensor(v[:, 1, :], lre, dt, ALU.mult).then_inc(args, 1)
            then(dve.tensor_tensor(v[:, 2, :], lim, dt, ALU.mult))
            for out, turn, shift in ((4, 0.0, 0.0), (5, 0.25, math.pi / 2)):
                k = v[:, 8, :]
                then(dve.tensor_scalar(k, v[:, 2, :], 1 / TWO_PI, turn, ALU.mult, ALU.add))
                then(dve.tensor_scalar(k, k, MAGIC, None, ALU.add))
                then(dve.tensor_scalar(k, k, MAGIC, None, ALU.subtract))
                then(dve.scalar_tensor_tensor(out=v[:, out, :], in0=k, scalar=-C1, in1=v[:, 2, :], op0=ALU.mult, op1=ALU.add))
                then(dve.scalar_tensor_tensor(out=v[:, out, :], in0=k, scalar=-C2, in1=v[:, out, :], op0=ALU.mult, op1=ALU.add))
                then(dve.scalar_tensor_tensor(out=v[:, out, :], in0=k, scalar=-C3, in1=v[:, out, :], op0=ALU.mult, op1=ALU.add))
                then(dve.tensor_scalar(v[:, out, :], v[:, out, :], shift, None, ALU.add))
                then(dve.tensor_scalar(v[:, out, :], v[:, out, :], -EDGE, None, ALU.max))
                x = dve.tensor_scalar(v[:, out, :], v[:, out, :], EDGE, None, ALU.min)
                if out == 4:
                    then(x)
            x.then_inc(args, 1)
            then(dve.memset(power[:, 0, 0, :], 1.0))
            then(dve.memset(power[:, 0, 1, :], 0.0))
            dve.wait_ge(acts, 4)
            ar, ai = power[:, 1, 0, :], power[:, 1, 1, :]
            then(dve.tensor_tensor(ar, v[:, 3, :], v[:, 7, :], ALU.mult))
            then(dve.tensor_tensor(ai, v[:, 3, :], v[:, 6, :], ALU.mult))
            t = [v[:, 4 + i, :] for i in range(4)]
            for n in range(2, L + 1):
                pr, pi = power[:, n - 1, 0, :], power[:, n - 1, 1, :]
                then(dve.tensor_tensor(t[0], pr, ar, ALU.mult))
                then(dve.tensor_tensor(t[1], pi, ai, ALU.mult))
                then(dve.tensor_tensor(t[2], pr, ai, ALU.mult))
                then(dve.tensor_tensor(t[3], pi, ar, ALU.mult))
                then(dve.tensor_tensor(power[:, n, 0, :], t[0], t[1], ALU.subtract))
                then(dve.tensor_tensor(power[:, n, 1, :], t[2], t[3], ALU.add))
            for n in range(L):
                then(dve.tensor_copy(reverse[:, L - 1 - n, :, :], power[:, n, :, :]))
            zr, zi = v[:, 10, :], v[:, 11, :]
            then(dve.tensor_tensor(t[0], lre, lre, ALU.mult))
            then(dve.tensor_tensor(t[1], lim, lim, ALU.mult))
            then(dve.tensor_tensor(t[0], t[0], t[1], ALU.add))
            then(dve.reciprocal(v[:, 8, :], t[0]))
            then(dve.tensor_scalar(v[:, 9, :], ar, -1.0, None, ALU.add))
            then(dve.tensor_tensor(t[0], v[:, 9, :], lre, ALU.mult))
            then(dve.tensor_tensor(t[1], ai, lim, ALU.mult))
            then(dve.tensor_tensor(t[2], ai, lre, ALU.mult))
            then(dve.tensor_tensor(t[3], v[:, 9, :], lim, ALU.mult))
            then(dve.tensor_tensor(zr, t[0], t[1], ALU.add))
            then(dve.tensor_tensor(zi, t[2], t[3], ALU.subtract))
            then(dve.tensor_tensor(zr, zr, v[:, 8, :], ALU.mult))
            then(dve.tensor_tensor(zi, zi, v[:, 8, :], ALU.mult))
            dve.wait_ge(b_in, 32)
            zr_, zi_ = (z.unsqueeze(2).to_broadcast([P, NQ, GC]) for z in (zr, zi))
            then(dve.tensor_tensor(tb[:, 0, :, :], b_[:, 0, :, :], zr_, ALU.mult))
            then(dve.tensor_tensor(tb[:, 1, :, :], b_[:, 1, :, :], zi_, ALU.mult))
            then(dve.tensor_tensor(tb[:, 2, :, :], b_[:, 1, :, :], zr_, ALU.mult))
            then(dve.tensor_tensor(tb[:, 3, :, :], b_[:, 0, :, :], zi_, ALU.mult))
            then(dve.tensor_tensor(bbar[:, 0, :, :], tb[:, 0, :, :], tb[:, 1, :, :], ALU.subtract))
            then(dve.tensor_tensor(bbar[:, 1, :, :], tb[:, 2, :, :], tb[:, 3, :, :], ALU.add))
            wide = [P, NQ, L, GC]
            br, bi = (bbar[:, i, :, :].unsqueeze(2).to_broadcast(wide) for i in range(2))
            rr, ri = (reverse[:, :, i, :].rearrange("p j q -> p q j").unsqueeze(3).to_broadcast(wide) for i in range(2))
            then(dve.tensor_tensor(g_[:, 0, :, :, :], br, rr, ALU.mult))
            then(dve.tensor_tensor(tg[:, 0, :, :, :], bi, ri, ALU.mult))
            then(dve.tensor_tensor(g_[:, 1, :, :, :], br, ri, ALU.mult))
            then(dve.tensor_tensor(tg[:, 1, :, :, :], bi, rr, ALU.mult))
            then(dve.tensor_tensor(g_[:, 0, :, :, :], g_[:, 0, :, :, :], tg[:, 0, :, :, :], ALU.subtract))
            dve.tensor_tensor(g_[:, 1, :, :, :], g_[:, 1, :, :, :], tg[:, 1, :, :, :], ALU.add).then_inc(g_ready, 1)
            for n in range(1, NQ // 2, 2):
                dve.wait_ge(g_t, n + 1)
                dve.tensor_copy(into[:, 2 * n:2 * n + 2, :, :], ps_t[:, 1, :].rearrange("p (q r s) -> p q r s", q=2, r=2)).then_inc(g_dve, 1)


def stage_ssm_kernel(nc, c_re, c_im, d_skip, diag16, ident, power, bbar, out_of, inside, e_y):
    with ExitStack() as ctx:
        m = Stage(nc, ctx, "sk")
        c_ = m.sb("c", [P, 2, 8, P])
        cT = m.sb("cT", [P, 2, NQ, GC])
        tv = inside[:, :, :, :].rearrange("p q a t -> p (q a t)")[:, 0:NQ * (L + 1) * GC].rearrange("p (q t h) -> p q t h", q=NQ, t=L + 1)
        bpad = m.sb("bpad", [P, 2, NQ, 2, GC])
        taps = e_y[0:2 * GC, :].rearrange("p (q t) -> p q t", q=NQ)
        dT = m.sb("dT", [2 * GC, NQ])
        dg = m.sb("dg", [2 * GC, GC])
        dd = m.sb("dd", [2 * GC, NQ, GC])
        ps_c = m.ps("ps_c", [P, 2, S])
        ps_k = m.ps("ps_k", [2 * GC, 2, 512])
        (c_in, d_in, c_t, c_done, v_done, pad_done, pads, k_mm, k_done, taps_done, moved, dve_step) = (m.sem(n) for n in
            "c_in d_in c_t c_done v_done pad_done pads k_mm k_done taps_done moved dve_step".split())
        block = ctx.enter_context(nc.Block())

        @block.sync
        def _(sp):
            for i, c in enumerate((c_re, c_im)):
                for two in range(2):
                    sp.dma_start(c_[:, i, :, two * 64:(two + 1) * 64],
                                 c.rearrange("(n g) h p -> (g h) n p", n=8)).then_inc(c_in, 16)
            with nc.allow_non_contiguous_dma(reason="1024 elements"):
                sp.dma_start(dT[:, :], d_skip.rearrange("(q two) h -> (two h) q", two=2)).then_inc(d_in, 16)
            sp.dma_start(dg[:, :], diag16).then_inc(d_in, 16)
            sp.wait_ge(taps_done, 1)
            for i in range(L):
                for two in range(2):
                    sp.dma_start(inside[i * GC:(i + 1) * GC, :, two, :],
                                 taps[two * GC:(two + 1) * GC, :, (L - i) * GC:(L - i) * GC + P]).then_inc(moved, 16)
            sp.wait_ge(moved, 16 * 2 * L)

        @block.gpsimd
        def _(pool):
            pool.memset(bpad[:, :, :, :, :], 0.0).then_inc(pads, 1)
            pool.memset(taps[:, :, 0:P], 0.0).then_inc(pads, 1)
            pool.wait_ge(pads, 2)
            for two in range(2):
                h = slice(two * 64, two * 64 + 64)
                x = pool.tensor_copy(bpad[h, :, :, two, :], bbar[h, :, :, :])
            x.then_inc(pad_done, 1)

        @block.tensor
        def _(pe):
            pe.wait_ge(c_in, 16 * 4)
            for i in range(2):
                for n in range(8):
                    x = pe.transpose(ps_c[:, i, n * P:(n + 1) * P], c_[:, i, n, :], ident[:, :])
            x.then_inc(c_t, 1)
            pe.wait_ge(v_done, 1)
            pe.wait_ge(pad_done, 1)
            for n in range(NQ // 4):
                if n >= 2:
                    pe.wait_ge(k_done, n - 1)
                for k in range(4):
                    q = 4 * n + k
                    for i in range(2):
                        x = pe.matmul(ps_k[:, n % 2, k * P:(k + 1) * P], bpad[:, i, q, :, :].rearrange("p a h -> p (a h)"),
                                      out_of[:, i, q, 0:L, :].rearrange("p t h -> p (t h)"), start=(i == 0), stop=(i == 1), skip_group_check=True)
                x.then_inc(k_mm, 1)

        @block.scalar
        def _(act):
            act.wait_ge(c_t, 1)
            for i in range(2):
                for two in range(2):
                    half = slice(two * 64, (two + 1) * 64)
                    x = act.activation(cT[half, i, :, :], ps_c[half, i, :].rearrange("p (q a h) -> p q a h", q=NQ, a=2)[:, :, two, :], ACT.Copy)
            x.then_inc(c_done, 1)
            for n in range(NQ // 4):
                act.wait_ge(k_mm, n + 1)
                act.activation(taps[:, 4 * n:4 * n + 4, P:2 * P], ps_k[:, n % 2, :].rearrange("p (q t) -> p q t", q=4), ACT.Copy).then_inc(k_done, 1)

        @block.vector
        def _(dve):
            step = [0]

            def then(ins):
                step[0] += 1
                ins.then_inc(dve_step, 1)
                dve.wait_ge(dve_step, step[0])

            dve.wait_ge(c_done, 1)
            wide = [P, NQ, L + 1, GC]
            cr, ci = (cT[:, i, :, :].unsqueeze(2).to_broadcast(wide) for i in range(2))
            ar, ai = (power[:, :, i, :].rearrange("p t q -> p q t").unsqueeze(3).to_broadcast(wide) for i in range(2))
            then(dve.tensor_tensor(out_of[:, 0, :, :, :], cr, ar, ALU.mult))
            then(dve.tensor_tensor(tv[:, :, :, :], ci, ai, ALU.mult))
            then(dve.tensor_tensor(out_of[:, 0, :, :, :], out_of[:, 0, :, :, :], tv[:, :, :, :], ALU.subtract))
            then(dve.tensor_tensor(out_of[:, 1, :, :, :], cr, ai, ALU.mult))
            then(dve.tensor_tensor(tv[:, :, :, :], ci, ar, ALU.mult))
            then(dve.scalar_tensor_tensor(out=out_of[:, 1, :, :, :].rearrange("p q t h -> p (q t h)"), in0=out_of[:, 1, :, :, :].rearrange("p q t h -> p (q t h)"),
                                          scalar=-1.0, in1=tv[:, :, :, :].rearrange("p q t h -> p (q t h)"), op0=ALU.mult, op1=ALU.subtract))
            dve.engine_nop().then_inc(v_done, 1)
            dve.wait_ge(d_in, 32)
            then(dve.tensor_tensor(dd[:, :, :], dT[:, :].unsqueeze(2).to_broadcast([2 * GC, NQ, GC]), dg[:, :].unsqueeze(1).to_broadcast([2 * GC, NQ, GC]), ALU.mult))
            dve.wait_ge(k_done, NQ // 4)
            dve.wait_ge(pads, 2)
            dve.tensor_tensor(taps[:, :, P:P + GC], taps[:, :, P:P + GC], dd[:, :, :], ALU.add).then_inc(taps_done, 1)


def stage_ssm_scan(nc, uT, power, into, out_of, inside, e_y):
    with ExitStack() as ctx:
        m = Stage(nc, ctx, "sc")
        st = m.sb("st", [P, NC, 2, NQ])
        mul = m.sb("mul", [P, 2, 2, NQ])
        tmp = m.sb("tmp", [P, 2, 2, NQ])
        ps_e = m.ps("ps_e", [P, 4, 512])
        ps_y = m.ps("ps_y", [P, 4, 512])
        (e_mm, e_act, e_dve, swept, y_mm, y_done, dve_step, mul_done) = (m.sem(n) for n in
            "e_mm e_act e_dve swept y_mm y_done dve_step mul_done".split())
        e = e_y[:, :].rearrange("p (c i q) -> p c i q", i=2, q=NQ)
        y = e_y[:, :].rearrange("p (j d) -> p j d", j=L)
        block = ctx.enter_context(nc.Block())

        @block.tensor
        def _(pe):
            for n in range(NQ // 2):
                if n >= 4:
                    pe.wait_ge((e_act, e_dve)[n % 2], (n - 4) // 2 + 1)
                for k in range(4):
                    q, i = 2 * n + k // 2, k % 2
                    for two in range(2):
                        x = pe.matmul(ps_e[two * 64:(two + 1) * 64, n % 4, k * P:(k + 1) * P], into[:, q, i, two * 64:(two + 1) * 64],
                                      uT[:, 2 * q + two, :], start=True, stop=True, skip_group_check=True)
                x.then_inc(e_mm, 1)
            pe.wait_ge(swept, 1)
            for n in range(NG // 4):
                two = n % 2
                half = slice(two * 64, (two + 1) * 64)
                if n >= 4:
                    pe.wait_ge(y_done, n - 3)
                for k in range(4):
                    q = 4 * (n // 2) + k
                    o = ps_y[:, n % 4, k * P:(k + 1) * P]
                    pe.matmul(o, uT[:, 2 * q + two, :], inside[:, q, two, :], start=True, stop=False, skip_group_check=True)
                    for i in range(2):
                        x = pe.matmul(o, st[half, 0:NC, i, q], out_of[half, i, q, 1:L + 1, :].rearrange("p t h -> p (t h)"),
                                      start=False, stop=(i == 1), skip_group_check=True)
                x.then_inc(y_mm, 1)

        def copy_e(eng, n, sem):
            eng.wait_ge(e_mm, n + 1)
            out = e[:, :, :, 2 * n:2 * n + 2].rearrange("p c i q -> p q i c")
            src = ps_e[:, n % 4, :].rearrange("p (q i c) -> p q i c", q=2, i=2)
            (eng.activation(out, src, ACT.Copy) if sem is e_act else eng.tensor_copy(out, src)).then_inc(sem, 1)

        @block.scalar
        def _(act):
            for n in range(0, NQ // 2, 2):
                copy_e(act, n, e_act)
            for n in range(NG // 4):
                act.wait_ge(y_mm, n + 1)
                two = n % 2
                out = y.rearrange("p j (q g) -> p q j g", g=2 * GC)[:, 4 * (n // 2):4 * (n // 2) + 4, :, two * GC:(two + 1) * GC]
                act.activation(out, ps_y[:, n % 4, :].rearrange("p (q j h) -> p q j h", q=4, j=L), ACT.Gelu_apprx_tanh).then_inc(y_done, 1)

        @block.vector
        def _(dve):
            dve.memset(st[:, 0, :, :], 0.0)
            dve.tensor_copy(mul[:, 0, 0, :], power[:, L, 0, :])
            dve.tensor_copy(mul[:, 0, 1, :], power[:, L, 0, :])
            dve.tensor_copy(mul[:, 1, 0, :], power[:, L, 1, :])
            dve.tensor_scalar(mul[:, 1, 1, :], power[:, L, 1, :], -1.0, None, ALU.mult).then_inc(mul_done, 1)
            for n in range(1, NQ // 2, 2):
                copy_e(dve, n, e_dve)
            dve.wait_ge(mul_done, 1)
            dve.wait_ge(e_act, NQ // 4)
            dve.wait_ge(e_dve, NQ // 4)
            state = st[:, :, :, :].rearrange("p c i q -> p c (i q)")
            own = e_y[:, :].rearrange("p (c s) -> p c s", c=NC)
            m0, m1 = (mul[:, k, :, :].rearrange("p i q -> p (i q)") for k in range(2))
            t0, t1 = (tmp[:, k, :, :].rearrange("p i q -> p (i q)") for k in range(2))
            with dve.Fori(0, NC - 1) as c:
                now, new = state[:, bass.ds(c, 1), :].rearrange("p a s -> p (a s)"), state[:, bass.ds(c + 1, 1), :].rearrange("p a s -> p (a s)")
                dve.wait_ge(dve_step, c * 3)
                dve.tensor_tensor(t0, now, m0, ALU.mult)
                dve.tensor_tensor(t1, now, m1, ALU.mult).then_inc(dve_step, 1)
                dve.wait_ge(dve_step, c * 3 + 1)
                dve.tensor_tensor(t0, t0, own[:, bass.ds(c, 1), :].rearrange("p a s -> p (a s)"), ALU.add).then_inc(dve_step, 1)
                dve.wait_ge(dve_step, c * 3 + 2)
                dve.tensor_tensor(new[:, 0:NQ], t0[:, 0:NQ], t1[:, NQ:2 * NQ], ALU.add)
                dve.tensor_tensor(new[:, NQ:2 * NQ], t0[:, NQ:2 * NQ], t1[:, 0:NQ], ALU.add).then_inc(dve_step, 1)
            dve.wait_ge(dve_step, 3 * (NC - 1))
            dve.engine_nop().then_inc(swept, 1)


def stage_ssm_out(nc, h, w_glu, w_out, g, b, ident, e_y, h_out):
    with ExitStack() as ctx:
        m = Stage(nc, ctx, "so")
        y = e_y[:, :].rearrange("p (j d) -> p j d", j=L)
        w = m.sb("w", [P, 2, KC, D])
        yT = m.sb("yT", [P, KC, S])
        sg = m.sb("sg", [P, 2, 512])
        o_ = m.sb("o", [P, 2, D])
        z = m.sb("z", [P, KC, 512])
        hr = m.sb("hr", [P, 2, D])
        norm = Norm(m, "ln")
        ps_t = m.ps("ps_t", [P, 2, 512])
        ps_z = m.ps("ps_z", [P, 2, 512])
        ps_o = m.ps("ps_o", [P, 2, D])
        (wg_in, wo_in, transposed, t_act, t_dve, z_mm, sig_done, z_done, o_mm, o_read, o_ready, dve_step) = (m.sem(n) for n in
            "wg_in wo_in transposed t_act t_dve z_mm sig_done z_done o_mm o_read o_ready dve_step".split())
        h_in = [m.sem(f"h_in{k}") for k in range(2)]
        stored = [m.sem(f"stored{k}") for k in range(2)]
        rows = h.rearrange("(c j) d -> j c d", j=L)
        out_rows = h_out.rearrange("(c j) d -> j c d", j=L)
        block = ctx.enter_context(nc.Block())

        @block.sync
        def _(sp):
            sp.dma_start(w[:, 0, :, :], w_glu.rearrange("(c p) n -> p c n", p=P)).then_inc(wg_in, 16)
            sp.dma_start(w[:, 1, :, :], w_out.rearrange("(c p) n -> p c n", p=P)).then_inc(wo_in, 16)
            norm.load(sp, g, b)
            for j in range(L):
                if j >= 2:
                    sp.wait_ge(o_read, j - 1)
                sp.dma_start(hr[:, j % 2, :], rows[j]).then_inc(h_in[j % 2], 16)
                if j:
                    sp.wait_ge(o_ready, j)
                    sp.dma_start(out_rows[j - 1], o_[:, (j - 1) % 2, :]).then_inc(stored[(j - 1) % 2], 16)
            sp.wait_ge(o_ready, L)
            sp.dma_start(out_rows[L - 1], o_[:, (L - 1) % 2, :]).then_inc(stored[(L - 1) % 2], 16)
            for k in range(2):
                sp.wait_ge(stored[k], 16 * L // 2)

        @block.tensor
        def _(pe):
            for n in range(2 * L):
                j, c0 = n // 2, 4 * (n % 2)
                if n >= 2:
                    pe.wait_ge((t_act, t_dve)[n % 2], n // 2)
                for c in range(4):
                    x = pe.transpose(ps_t[:, n % 2, c * P:(c + 1) * P], y[:, j, (c0 + c) * P:(c0 + c + 1) * P], ident[:, :])
                x.then_inc(transposed, 1)
            pe.wait_ge(wg_in, 16)
            pe.wait_ge(t_act, L)
            pe.wait_ge(t_dve, L)
            for half in range(2):
                for f in range(KC):
                    u = half * KC + f
                    if u >= 2:
                        pe.wait_ge(sig_done, u - 1)
                    for c in range(KC):
                        x = pe.matmul(ps_z[:, u % 2, :], w[:, 0, c, f * P:(f + 1) * P], yT[:, c, half * 512:(half + 1) * 512], start=(c == 0), stop=(c == KC - 1))
                    x.then_inc(z_mm, 1)
                pe.wait_ge(z_done, (half + 1) * KC)
                pe.wait_ge(wo_in, 16)
                for jj in range(4):
                    j = half * 4 + jj
                    if j >= 2:
                        pe.wait_ge(o_read, j - 1)
                    for oh in range(2):
                        for c in range(KC):
                            x = pe.matmul(ps_o[:, j % 2, oh * 512:(oh + 1) * 512], z[:, c, jj * P:(jj + 1) * P], w[:, 1, c, oh * 512:(oh + 1) * 512],
                                          start=(c == 0), stop=(c == KC - 1))
                    x.then_inc(o_mm, 1)

        @block.scalar
        def _(act):
            for j in range(L):
                act.wait_ge(transposed, 2 * j + 1)
                act.activation(yT[:, 0:4, j * P:(j + 1) * P], ps_t[:, 0, :].rearrange("p (c t) -> p c t", c=4), ACT.Copy).then_inc(t_act, 1)
            for half in range(2):
                for f in range(KC):
                    u = half * KC + f
                    act.wait_ge(z_mm, u + 1)
                    if u >= 2:
                        act.wait_ge(z_done, u - 1)
                    act.activation(sg[:, u % 2, :], ps_z[:, u % 2, :], ACT.Sigmoid).then_inc(sig_done, 1)
                for jj in range(4):
                    norm.on_act(act, half * 4 + jj)

        @block.vector
        def _(dve):
            step = [0]

            def then(ins):
                step[0] += 1
                ins.then_inc(dve_step, 1)
                dve.wait_ge(dve_step, step[0])

            for j in range(L):
                dve.wait_ge(transposed, 2 * j + 2)
                dve.tensor_copy(yT[:, 4:8, j * P:(j + 1) * P], ps_t[:, 1, :].rearrange("p (c t) -> p c t", c=4)).then_inc(t_dve, 1)
            dve.wait_ge(t_act, L)
            dve.wait_ge(t_dve, L)
            for half in range(2):
                if half:
                    dve.wait_ge(o_mm, 4)
                for f in range(KC):
                    u = half * KC + f
                    dve.wait_ge(sig_done, u + 1)
                    dve.tensor_tensor(z[:, f, :], sg[:, u % 2, :], yT[:, f, half * 512:(half + 1) * 512], ALU.mult).then_inc(z_done, 1)
                for jj in range(4):
                    j = half * 4 + jj
                    dve.wait_ge(o_mm, j + 1)
                    dve.wait_ge(h_in[j % 2], 16 * (j // 2 + 1))
                    if j >= 2:
                        dve.wait_ge(stored[j % 2], 16 * (j // 2))
                    oo = o_[:, j % 2, :]
                    dve.scalar_tensor_tensor(out=oo, in0=hr[:, j % 2, :], scalar=ALPHA, in1=ps_o[:, j % 2, :], op0=ALU.mult, op1=ALU.add).then_inc(o_read, 1)
                    dve.wait_ge(o_read, j + 1)
                    norm.on_dve(dve, then, oo, j).then_inc(o_ready, 1)


def ssm_layer(nc, h, w, ln_g, ln_b, consts, h_out):
    w_in, lam_re, lam_im, b_re, b_im, c_re, c_im, d_skip, log_dt, w_glu, w_out = w
    with ExitStack() as outer:
        m = Stage(nc, outer, "ss")
        ident = m.sb("ident", [P, P])
        e_y = m.sb("e_y", [P, L * D])
        with ExitStack() as ctx:
            k = Stage(nc, ctx, "sb_")
            uT = k.sb("uT", [P, NG, NC])
            power = k.sb("power", [P, L + 1, 2, NQ])
            bbar = k.sb("bbar", [P, 2, NQ, GC])
            into = k.sb("into", [P, NQ, 2, P])
            stage_ssm_input(nc, h, w_in, consts["c_ident"], ident, uT)
            with ExitStack() as c2:
                reverse = Stage(nc, c2, "sr").sb("reverse", [P, L, 2, NQ])
                stage_ssm_poles(nc, lam_re, lam_im, log_dt, b_re, b_im, ident, power, reverse, bbar, into)
            out_of = k.sb("out_of", [P, 2, NQ, L + 1, GC])
            inside = k.sb("inside", [P, NQ, 2, P])
            stage_ssm_kernel(nc, c_re, c_im, d_skip, consts["c_diag16"], ident, power, bbar, out_of, inside, e_y)
            stage_ssm_scan(nc, uT, power, into, out_of, inside, e_y)
        stage_ssm_out(nc, h, w_glu, w_out, ln_g, ln_b, ident, e_y, h_out)


def trunk(nc, a, consts, out):
    after = [nc.dram_tensor(f"h{n}", (S, D), F32, kind="Internal").ap() for n in range(3)]
    expert_rows = nc.dram_tensor("expert_rows", (NBLK * CAP, D), F32, kind="Internal").ap()
    x = a["x"].rearrange("b s d -> (b s) d")

    def layer(n, names):
        return [a[f"l{n}_{k}"] for k in names.split()]

    moe_names = "router router_bias w_gate w_up w_down sh_gate sh_up sh_down"
    with ExitStack() as ctx:
        keep = keep_attention(nc, ctx)
        stage_project(nc, x, a["l0_w_in"], consts["c_cos"], consts["c_sin"], consts["c_ident"], keep)
        stage_stick(nc, consts["c_stick"], expert_rows, keep)
        stage_compress(nc, *layer(0, "cmp_pos_k cmp_pos_v cmp_k_w1 cmp_k_w2 cmp_v_w1 cmp_v_w2"), consts["c_cmp"], consts["c_imp"], keep)
        stage_selected(nc, consts["c_win"], consts["c_causal"], keep)
        stage_attention_out(nc, a["l0_w_out"], x, a["l0_ln1_g"], a["l0_ln1_b"], keep, after[0])
    moe_layer(nc, "m0", expert_rows, after[0], layer(0, moe_names), a["l0_ln2_g"], a["l0_ln2_b"], consts, after[1])
    ssm_layer(nc, after[1], layer(1, "w_in lambda_re lambda_im b_re b_im c_re c_im d log_dt w_glu w_out"),
              a["l1_ln1_g"], a["l1_ln1_b"], consts, after[2])
    moe_layer(nc, "m1", expert_rows, after[2], layer(1, moe_names), a["l1_ln2_g"], a["l1_ln2_b"], consts, out)


def kernel(**inputs):
    import concourse.bacc as _bacc
    from concourse.bass_utils import run_bass_kernel_spmd as _run

    nc = _bacc.Bacc("TRN2", target_bir_lowering=False, num_devices=1)
    arrays, tensors, consts = {}, {}, {}
    for name, array in inputs.items():
        array = np.ascontiguousarray(array)
        arrays[f"in_{name}"] = array
        tensors[name] = nc.dram_tensor(f"in_{name}", array.shape, mybir.dt.from_np(array.dtype), kind="ExternalInput").ap()
    for name, array in const_arrays().items():
        arrays[name] = array
        consts[name] = nc.dram_tensor(name, array.shape, F32, kind="ExternalInput").ap()
    out = nc.dram_tensor("out_0", (1, S, D), F32, kind="ExternalOutput").ap()
    trunk(nc, tensors, consts, out.rearrange("b s d -> (b s) d"))
    result = _run(nc, [arrays], core_ids=[0])
    return result.results[0]["out_0"]
```

```python
import math
from contextlib import ExitStack

import numpy as np

import concourse.bass as bass
from concourse import mybir

F32 = mybir.dt.float32
I32 = mybir.dt.int32
U32 = mybir.dt.uint32
ALU = mybir.AluOpType
ACT = mybir.ActivationFunctionType
AX = mybir.AxisListType.X

P = 128
D = 1024
S = 1024
NT = S // P
KC = D // P
HD = 64
N_IN = 2840
NCMP = 63
NSEL = 16
FAR = -3.0e38
L = 8
NC = S // L
NG = 64
NQ = NG // 2
GC = 16
NE = 64
TOPK = 6
CAP = P
NSPILL = S * TOPK // CAP
SPILL0 = NE * CAP
NBLK = NE + NSPILL
FH = 256
ALPHA = 4 ** 0.25
LN_EPS = 1e-5
NEG = -1e30


def const_arrays():
    c = {}
    c["c_ident"] = np.eye(P, dtype=np.float32)
    inv = np.power(np.float32(500000.0), -np.arange(0, 16, 2, dtype=np.float32) / np.float32(16))
    ang = np.arange(S, dtype=np.float32)[:, None] * inv[None, :].astype(np.float32)
    rotated = np.array([1] * 10 + [0, 0] + [1, 1] + [0, 0] + [1, 1] + [0, 0], np.float32)[None, :, None]
    cos, sin = np.cos(ang)[:, None, :], np.sin(ang)[:, None, :]
    c["c_cos"] = (cos * rotated + (1 - rotated)).astype(np.float32)
    c["c_sin"] = (sin * rotated).astype(np.float32)
    k, q = np.arange(P)[:, None], np.arange(P)[None, :]
    c["c_stick"] = np.stack([np.where(k > q, -1.0, 0.0), np.where(k <= q, -1.0, 0.0),
                             np.where(k < q, 1.0, 0.0), np.where(k < q, 0.0, NEG)], 1).astype(np.float32)
    t = np.arange(S)
    seen = (np.arange(NCMP) * 16 + 31)[None, :] <= t[:, None]
    both = np.stack([np.where(seen, 0.0, NEG), np.where(seen, 1.0, 0.0)], 1)
    c["c_cmp"] = np.ascontiguousarray(both.reshape(NT, P, 2, NCMP).transpose(1, 0, 2, 3)).astype(np.float32)
    blk, cur = np.arange(NSEL)[None, :], (t // 64)[:, None]
    valid = blk <= cur
    forced = (blk == 0) | (valid & (blk > cur - 2))
    imp = np.stack([np.where(valid | forced, 1.0, 0.0), np.where(forced, 1e4, np.where(valid, 0.0, NEG))], 1)
    c["c_imp"] = np.ascontiguousarray(imp.reshape(NT, P, 2, NSEL).transpose(1, 0, 2, 3)).astype(np.float32)
    qq, kk = np.arange(P)[:, None], np.arange(P)[None, :]
    win = np.zeros((P, 5 * P))
    win[:, 0:P] = np.where(kk > qq, 0.0, NEG)
    win[:, 4 * P:] = np.where(kk <= qq, 0.0, NEG)
    c["c_win"] = win.astype(np.float32)
    c["c_tri8"] = np.ascontiguousarray(np.broadcast_to(np.tril(np.ones((8, 8), np.float32), -1)[None], (P, 8, 8)))
    e = np.arange(NE)
    c["c_exp"] = np.ascontiguousarray(np.broadcast_to(np.stack([e, e * CAP, SPILL0 - CAP - e * CAP])[None], (P, 3, NE))).astype(np.float32)
    c["c_before"] = np.stack([np.where(k < q, 1.0, 0.0), np.ones((P, P))], 1).astype(np.float32)
    c["c_spill"] = np.arange(NSPILL, dtype=np.float32)[None]
    c["c_tok"] = (np.arange(NT)[None, :] * P + np.arange(P)[:, None]).astype(np.float32)
    c["c_zero"] = np.zeros((NBLK, CAP), np.float32)
    c["c_diag16"] = np.tile(np.eye(16, dtype=np.float32), (2, 1))
    return c


class Stage:

    def __init__(self, nc, ctx, stage):
        self.nc, self.ctx, self.stage, self.sems = nc, ctx, stage, []
        ctx.callback(self.end)

    def end(self):
        if self.sems:
            self.nc.clear_and_free_semaphores(self.sems)
            self.nc.all_engine_barrier()

    def sb(self, name, shape, dt=F32):
        return self.ctx.enter_context(self.nc.sbuf_tensor(f"{self.stage}_{name}", shape, dt))

    def ps(self, name, shape, dt=F32):
        return self.ctx.enter_context(self.nc.psum_tensor(f"{self.stage}_{name}", shape, dt))

    def sem(self, name):
        self.sems.append(self.nc.alloc_semaphore(f"{self.stage}_{name}"))
        return self.sems[-1]


class Norm:

    def __init__(self, m, name):
        self.g = m.sb(f"{name}_g", [P, D])
        self.b = m.sb(f"{name}_b", [P, D])
        self.stats = m.sb(f"{name}_stats", [P, 2, 6])
        self.mv = m.sb(f"{name}_mv", [P, 2])
        self.inv = m.sb(f"{name}_inv", [P, 1])
        self.rstd = m.sb(f"{name}_rstd", [P, 1])
        self.gb_in = m.sem(f"{name}_gb_in")
        self.var_ready = m.sem(f"{name}_var_ready")
        self.rstd_ready = m.sem(f"{name}_rstd_ready")

    def load(self, eng, g, b):
        eng.dma_start(self.g[:, :], g.partition_broadcast(P)).then_inc(self.gb_in, 16)
        eng.dma_start(self.b[:, :], b.partition_broadcast(P)).then_inc(self.gb_in, 16)

    def on_act(self, act, n):
        act.wait_ge(self.var_ready, n + 1)
        act.activation(self.rstd[:, :], self.inv[:, :], ACT.Sqrt).then_inc(self.rstd_ready, 1)

    def on_dve(self, dve, then, y, n):
        if n == 0:
            dve.wait_ge(self.gb_in, 32)
        dve.bn_stats(self.stats[:, 0, :], y[:, 0:512])
        then(dve.bn_stats(self.stats[:, 1, :], y[:, 512:1024]))
        then(dve.bn_aggr(self.mv[:, :], self.stats[:, :, :].rearrange("p a b -> p (a b)")))
        then(dve.tensor_scalar(self.inv[:, :], self.mv[:, 1:2], LN_EPS, None, ALU.add))
        dve.reciprocal(self.inv[:, :], self.inv[:, :]).then_inc(self.var_ready, 1)
        dve.wait_ge(self.rstd_ready, n + 1)
        then(dve.tensor_scalar(y, y, self.mv[:, 0:1], self.rstd[:, 0:1], ALU.subtract, ALU.mult))
        then(dve.tensor_tensor(y, y, self.g[:, :], ALU.mult))
        return dve.tensor_tensor(y, y, self.b[:, :], ALU.add)


def stage_project(nc, x, w_in, cos, sin, ident, keep):
    with ExitStack() as ctx:
        m = Stage(nc, ctx, "proj")
        x_tile = m.sb("x_tile", [P, 2, D])
        xT = m.sb("xT", [P, KC, S])
        w = m.sb("w", [P, 2, KC, 512])
        tok = m.sb("tok", [P, 2, 512])
        dup = m.sb("dup", [P, 2, 6, 2, HD])
        cs = m.sb("cs", [P, 2, 2, 8, 8])
        r1 = m.sb("r1", [P, 4, 64])
        ps_mm = m.ps("ps_mm", [P, 4, 512])
        ps_t = m.ps("ps_t", [P, 2, 1024])
        const_in = m.sem("const_in")
        x_in = [m.sem(f"x_in{i}") for i in range(2)]
        w_inx = [m.sem(f"w_in{i}") for i in range(2)]
        cs_in = [m.sem(f"cs_in{i}") for i in range(2)]
        x_transposed = m.sem("x_transposed")
        xT_by_act = m.sem("xT_by_act")
        xT_by_dve = m.sem("xT_by_dve")
        mm_done = m.sem("mm_done")
        evicted = m.sem("evicted")
        roped = m.sem("roped")
        dup_done = m.sem("dup_done")
        transposed = m.sem("transposed")
        t_copied = m.sem("t_copied")
        dve_step = m.sem("dve_step")

        w_cols = [(0, 512), (512, 512), (1024, 512), (1536, 512), (2048, 512), (2560, 280)]
        w_view = w_in.rearrange("(c p) n -> p c n", p=P)
        units = [(g, tt) for g in range(6) for tt in range(8)]
        FIRST_ROPE = 24

        def n_rope(g):
            return {3: (0, 8), 4: (8, 8), 5: (16, 4)}[g]

        block = ctx.enter_context(nc.Block())

        @block.sync
        def _(sp):
            sp.dma_start(keep["ident"][:, :], ident).then_inc(const_in, 16)
            for g in range(2):
                c0, n = w_cols[g]
                if g == 0:
                    for tt in range(2):
                        sp.dma_start(x_tile[:, tt, :], x[tt * P:(tt + 1) * P, :]).then_inc(x_in[tt], 16)
                sp.dma_start(w[:, g, :, 0:n], w_view[:, :, c0:c0 + n]).then_inc(w_inx[g], 16)
            for tt in range(2, 8):
                sp.wait_ge(x_transposed, tt - 1)
                sp.dma_start(x_tile[:, tt % 2, :], x[tt * P:(tt + 1) * P, :]).then_inc(x_in[tt % 2], 16)
            for g in range(2, 6):
                c0, n = w_cols[g]
                sp.wait_ge(mm_done, 8 * (g - 1))
                sp.dma_start(w[:, g % 2, :, 0:n], w_view[:, :, c0:c0 + n]).then_inc(w_inx[g % 2], 16)

        @block.gpsimd
        def _(pool):
            for u, (g, tt) in enumerate(units):
                if g < 3:
                    continue
                v = u - FIRST_ROPE
                if v >= 2:
                    pool.wait_ge(roped, v - 1)
                h0, nh = n_rope(g)
                pool.dma_start(cs[:, v % 2, 0, 0:nh, :], cos[tt * P:(tt + 1) * P, h0:h0 + nh, :]).then_inc(cs_in[v % 2], 16)
                pool.dma_start(cs[:, v % 2, 1, 0:nh, :], sin[tt * P:(tt + 1) * P, h0:h0 + nh, :]).then_inc(cs_in[v % 2], 16)

        @block.tensor
        def _(pe):
            pe.wait_ge(const_in, 16)
            for tt in range(8):
                pe.wait_ge(x_in[tt % 2], 16 * (tt // 2 + 1))
                if tt >= 2:
                    pe.wait_ge(xT_by_act, tt - 1)
                    pe.wait_ge(xT_by_dve, tt - 1)
                for c in range(KC):
                    t = pe.transpose(ps_t[:, tt % 2, c * P:(c + 1) * P], x_tile[:, tt % 2, c * P:(c + 1) * P],
                                     keep["ident"][:, :])
                t.then_inc(x_transposed, 1)
            pe.wait_ge(xT_by_act, 8)
            pe.wait_ge(xT_by_dve, 8)

            def transposes(u):
                g, tt = units[u]
                v = u - FIRST_ROPE
                pe.wait_ge(roped, v + 1)
                if g > 3:
                    pe.wait_ge(dup_done, v - 8 + 1)
                if v >= 2:
                    pe.wait_ge(t_copied, v - 1)
                n = {3: 4, 4: 6, 5: 2}[g]
                for k in range(n):
                    src = tok[:, v % 2, k * P:(k + 1) * P] if g == 3 else dup[:, v % 2, k, :, :].rearrange("p a d -> p (a d)")
                    t = pe.transpose(ps_t[:, v % 2, k * P:(k + 1) * P], src, keep["ident"][:, :])
                t.then_inc(transposed, 1)

            for u, (g, tt) in enumerate(units):
                pe.wait_ge(w_inx[g % 2], 16 * (g // 2 + 1))
                if u >= 4:
                    pe.wait_ge(evicted, u - 3)
                n = w_cols[g][1]
                for c in range(KC):
                    if g < 2:
                        fc, half = tt // 2, tt % 2
                        t = pe.matmul(ps_mm[:, u % 4, :], w[:, g % 2, c, fc * P:(fc + 1) * P],
                                      xT[:, c, half * 512:(half + 1) * 512], start=(c == 0), stop=(c == KC - 1))
                    else:
                        t = pe.matmul(ps_mm[:, u % 4, 0:n], xT[:, c, tt * P:(tt + 1) * P],
                                      w[:, g % 2, c, 0:n], start=(c == 0), stop=(c == KC - 1))
                t.then_inc(mm_done, 1)
                if u > FIRST_ROPE:
                    transposes(u - 1)
            transposes(len(units) - 1)

        @block.scalar
        def _(act):
            for tt in range(8):
                act.wait_ge(x_transposed, tt + 1)
                act.activation(xT[:, 0:4, tt * P:(tt + 1) * P],
                               ps_t[:, tt % 2, 0:512].rearrange("p (c t) -> p c t", c=4), ACT.Copy).then_inc(xT_by_act, 1)
            for u, (g, tt) in enumerate(units):
                act.wait_ge(mm_done, u + 1)
                v = u - FIRST_ROPE
                n = w_cols[g][1]
                src = ps_mm[:, u % 4, 0:n]
                if g == 0:
                    act.activation(keep["qaT"][:, tt // 2, (tt % 2) * 512:(tt % 2 + 1) * 512], src, ACT.Copy, scale=0.125).then_inc(evicted, 1)
                elif g == 1:
                    act.activation(keep["kaT"][:, tt // 2, (tt % 2) * 512:(tt % 2 + 1) * 512], src, ACT.Copy).then_inc(evicted, 1)
                elif g == 2:
                    act.activation(keep["va"][:, tt, :], src, ACT.Copy).then_inc(evicted, 1)
                else:
                    if v >= 2:
                        act.wait_ge(transposed, v - 1)
                    act.activation(tok[:, v % 2, 0:n], src, ACT.Copy, scale=0.125 if g == 3 else 1.0).then_inc(evicted, 1)
                    if g > 3:
                        act.wait_ge(roped, v + 1)
                        if g == 4:
                            act.activation(dup[:, v % 2, :, :, :],
                                           tok[:, v % 2, 0:384].rearrange("p (h d) -> p h d", h=6).unsqueeze(2).to_broadcast([P, 6, 2, HD]),
                                           ACT.Copy)
                            act.activation(keep["vs"][:, tt, :], tok[:, v % 2, 384:512], ACT.Copy).then_inc(dup_done, 1)
                        else:
                            act.activation(dup[:, v % 2, 0:2, :, :],
                                           tok[:, v % 2, 0:128].rearrange("p (h d) -> p h d", h=2).unsqueeze(2).to_broadcast([P, 2, 2, HD]),
                                           ACT.Copy)
                            act.activation(keep["gate"][:, tt, :], tok[:, v % 2, 256:280], ACT.Copy)
                            act.activation(keep["vw"][:, tt, :], tok[:, v % 2, 128:256], ACT.Copy).then_inc(dup_done, 1)

        def copy_out(dve, v):
            g, tt = units[v + FIRST_ROPE]
            dve.wait_ge(transposed, v + 1)
            cols = slice(tt * P, (tt + 1) * P)
            if g == 3:
                dve.tensor_copy(keep["qbT"][:, :, cols], ps_t[:, v % 2, 0:512].rearrange("p (c t) -> p c t", c=4)).then_inc(t_copied, 1)
            elif g == 4:
                dve.tensor_copy(keep["kcT"][:, :, cols], ps_t[:, v % 2, 0:256].rearrange("p (c t) -> p c t", c=2))
                dve.tensor_copy(keep["vcT"][:, :, cols], ps_t[:, v % 2, 256:512].rearrange("p (c t) -> p c t", c=2))
                dve.tensor_copy(keep["ksT"][:, :, cols], ps_t[:, v % 2, 512:768].rearrange("p (c t) -> p c t", c=2)).then_inc(t_copied, 1)
            else:
                dve.tensor_copy(keep["kwT"][:, :, cols], ps_t[:, v % 2, 0:256].rearrange("p (c t) -> p c t", c=2)).then_inc(t_copied, 1)

        @block.vector
        def _(dve):
            steps = [0]

            def done(ins):
                steps[0] += 1
                ins.then_inc(dve_step, 1)

            for tt in range(8):
                dve.wait_ge(x_transposed, tt + 1)
                dve.tensor_copy(xT[:, 4:8, tt * P:(tt + 1) * P],
                                ps_t[:, tt % 2, 512:1024].rearrange("p (c t) -> p c t", c=4)).then_inc(xT_by_dve, 1)
            for u, (g, tt) in enumerate(units):
                if g < 3:
                    continue
                v = u - FIRST_ROPE
                h0, nh = n_rope(g)
                dve.wait_ge(evicted, u + 1)
                dve.wait_ge(cs_in[v % 2], 32 * (v // 2 + 1))
                heads = tok[:, v % 2, 0:nh * HD].rearrange("p (h d) -> p h d", h=nh)
                x1, x2 = heads[:, :, 0:8], heads[:, :, 8:16]
                c_, s_ = cs[:, v % 2, 0, 0:nh, :], cs[:, v % 2, 1, 0:nh, :]
                t = [r1[:, i, 0:nh * 8].rearrange("p (h d) -> p h d", h=nh) for i in range(4)]
                if v:
                    dve.wait_ge(dve_step, steps[0])
                done(dve.tensor_tensor(t[0], x1, c_, ALU.mult))
                done(dve.tensor_tensor(t[1], x2, s_, ALU.mult))
                done(dve.tensor_tensor(t[2], x2, c_, ALU.mult))
                done(dve.tensor_tensor(t[3], x1, s_, ALU.mult))
                dve.wait_ge(dve_step, steps[0])
                done(dve.tensor_tensor(x1, t[0], t[1], ALU.subtract))
                dve.wait_ge(dve_step, steps[0])
                steps[0] += 1
                dve.tensor_tensor(x2, t[2], t[3], ALU.add).then_inc(dve_step, 1)
                dve.wait_ge(dve_step, steps[0])
                dve.engine_nop().then_inc(roped, 1)
                if v >= 1:
                    copy_out(dve, v - 1)
            copy_out(dve, len(units) - 1 - FIRST_ROPE)


def keep_attention(nc, ctx):
    m = Stage(nc, ctx, "keep")
    k = {"ident": m.sb("ident", [P, P])}
    for n, shape in (("qaT", [P, 4, S]), ("kaT", [P, 4, S]), ("va", [P, NT, 512]), ("qbT", [P, 4, S]),
                     ("kcT", [P, 2, S]), ("vcT", [P, 2, S]), ("ksT", [P, 2, S]), ("kwT", [P, 2, S]),
                     ("vs", [P, NT, P]), ("vw", [P, NT, P]), ("gate", [P, NT, 24]),
                     ("sel", [P, 2, NT, NSEL]), ("o_tok", [P, NT, 512])):
        k[n] = m.sb(n, shape)
    return k


def stage_stick(nc, stick, expert_rows, keep):
    with ExitStack() as ctx:
        m = Stage(nc, ctx, "sb")
        masks = m.sb("masks", [P, 4, P])
        tri_after, tri_rest, before, not_before = (masks[:, i, :] for i in range(4))
        q_st = m.sb("q_st", [P, S])
        k_st = m.sb("k_st", [P, 2, S])
        v_st = m.sb("v_st", [P, NT, P])
        mag = m.sb("mag", [P, 2, 512])
        ln1 = m.sb("ln1", [P, 2, 512])
        sp_ = m.sb("sp", [P, 4, 512])
        zsp = m.sb("zsp", [P, 4, 512])
        t_ = m.sb("t", [P, 2, 512])
        w_ = m.sb("w", [P, 4, 512])
        zeros = m.sb("zeros", [P, D])
        zeros_ready, cleared, k_zero = m.sem("zeros_ready"), m.sem("cleared"), m.sem("k_zero")
        ps_z = m.ps("ps_z", [P, 2, 512])
        ps_s = m.ps("ps_s", [P, 2, S])
        ps_o = m.ps("ps_o", [P, S])
        const_in, qk_staged, v_staged, z_done, ln_done, sp_done, tri_done, t_done, w_done, conv_done, pv_done, o_evicted, act_step, dve_step = (
            m.sem(n) for n in "const_in qk_staged v_staged z_done ln_done sp_done tri_done t_done w_done conv_done pv_done o_evicted act_step dve_step".split())

        units = []
        for kt in range(NT - 1, -1, -1):
            pieces = [(kt * P, S)] if kt >= 4 else [(kt * P, 512), (512, S)]
            for a, b in pieces:
                for hh in range(2):
                    units.append((hh, kt, a, b - a))
        N = len(units)
        PAIRS = 4
        DVE_STEPS = sum(1 + 2 * (a == kt * P) for _, kt, a, _ in units)
        block = ctx.enter_context(nc.Block())

        @block.sync
        def _(sp):
            sp.dma_start(masks[:, :, :], stick).then_inc(const_in, 16)
            sp.wait_ge(zeros_ready, 1)
            with sp.Fori(0, NSPILL) as b:
                sp.dma_start(expert_rows[bass.ds(SPILL0 + b * CAP, CAP), :], zeros[:, :]).then_inc(cleared, 16)
            sp.wait_ge(cleared, 16 * NSPILL)

        @block.gpsimd
        def _(pool):
            pool.memset(k_st[HD:P, 0, :], 0.0).then_inc(k_zero, 1)
            pool.wait_ge(k_zero, 1)
            pool.memset(k_st[0:HD, 1, :], 0.0).then_inc(k_zero, 1)
            pool.wait_ge(k_zero, 2)
            pool.memset(zeros[:, :], 0.0).then_inc(zeros_ready, 1)
            with pool.Fori(0, PAIRS) as i:
                pool.wait_ge(pv_done, i * N)
                pool.tensor_copy(v_st[:, :, :], keep["va"][:, :, bass.ds(i * P, P)]).then_inc(v_staged, 1)

        @block.tensor
        def _(pe):
            pe.wait_ge(const_in, 16)
            pe.wait_ge(k_zero, 2)

            def scores(i, n):
                hh, kt, a, w = units[n]
                if n < 2:
                    pe.wait_ge(sp_done, i * N)
                else:
                    pe.wait_ge(sp_done, i * N + n - 1)
                pe.matmul(ps_z[:, n % 2, 0:w], k_st[:, hh, kt * P:(kt + 1) * P], q_st[:, a:a + w],
                          start=True, stop=True).then_inc(z_done, 1)

            def suffix(i, n):
                hh, kt, a, w = units[n]
                pe.wait_ge(sp_done, i * N + n + 1)
                first = (kt == NT - 1) or (kt == 3 and a < 512)
                pe.matmul(ps_s[:, hh, a:a + w], tri_after, sp_[:, n % 4, 0:w], start=first, stop=True,
                          skip_group_check=True).then_inc(tri_done, 1)

            def to_whole(i, n):
                hh, kt, a, w = units[n]
                pe.wait_ge(t_done, i * N + n + 1)
                pe.matmul(ps_s[:, hh, a:a + w], tri_rest, sp_[:, n % 4, 0:w], start=False, stop=True,
                          skip_group_check=True).then_inc(conv_done, 1)

            def values(i, n):
                hh, kt, a, w = units[n]
                pe.wait_ge(w_done, i * N + n + 1)
                if n == 0:
                    pe.wait_ge(v_staged, i + 1)
                    pe.wait_ge(o_evicted, i)
                first = (kt == NT - 1) or (kt == 3 and a < 512)
                pe.matmul(ps_o[hh * HD:(hh + 1) * HD, a:a + w], v_st[:, kt, hh * HD:(hh + 1) * HD],
                          w_[:, n % 4, 0:w], start=first, stop=True, skip_group_check=True).then_inc(pv_done, 1)

            with pe.Fori(0, PAIRS) as i:
                pe.wait_ge(qk_staged, i + 1)
                for n in range(3):
                    scores(i, n)
                for n in range(N):
                    suffix(i, n)
                    if n:
                        to_whole(i, n - 1)
                    if n + 3 < N:
                        scores(i, n + 3)
                    if n and n % 2 == 0:
                        values(i, n - 2)
                        values(i, n - 1)
                to_whole(i, N - 1)
                values(i, N - 2)
                values(i, N - 1)

        @block.scalar
        def _(act):
            act.preload_act_table_set("natural_log_exp_and_others")

            def softplus_part(i, n):
                w = units[n][3]
                z = ps_z[:, n % 2, 0:w]
                act.wait_ge(z_done, i * N + n + 1)
                act.activation(mag[:, n % 2, 0:w], z, ACT.Abs).then_inc(act_step, 1)
                act.wait_ge(act_step, i * 2 * N + 2 * n + 1)
                act.activation(mag[:, n % 2, 0:w], mag[:, n % 2, 0:w], ACT.Exp, scale=-1.0).then_inc(act_step, 1)
                act.wait_ge(act_step, i * 2 * N + 2 * n + 2)
                if n < 2:
                    act.wait_ge(sp_done, i * N)
                else:
                    act.wait_ge(sp_done, i * N + n - 1)
                act.activation(ln1[:, n % 2, 0:w], mag[:, n % 2, 0:w], ACT.Ln, bias=1.0).then_inc(ln_done, 1)

            def weights(i, n):
                w = units[n][3]
                act.wait_ge(t_done, i * N + n + 1)
                if n < 4:
                    act.wait_ge(pv_done, i * N)
                else:
                    act.wait_ge(pv_done, i * N + n - 3)
                act.activation(w_[:, n % 4, 0:w], t_[:, n % 2, 0:w], ACT.Exp).then_inc(w_done, 1)

            with act.Fori(0, PAIRS) as i:
                softplus_part(i, 0)
                softplus_part(i, 1)
                for n in range(N):
                    if n + 2 < N:
                        softplus_part(i, n + 2)
                    weights(i, n)

        @block.vector
        def _(dve):
            step = [0]

            def then(i, ins):
                step[0] += 1
                ins.then_inc(dve_step, 1)
                dve.wait_ge(dve_step, i * DVE_STEPS + step[0])

            def softplus(i, n):
                hh, kt, a, w = units[n]
                diagonal = a == kt * P
                z = ps_z[:, n % 2, 0:w]
                s = n % 4
                dve.wait_ge(ln_done, i * N + n + 1)
                if n < 4:
                    dve.wait_ge(conv_done, i * N)
                else:
                    dve.wait_ge(conv_done, i * N + n - 3)
                then(i, dve.scalar_tensor_tensor(out=sp_[:, s, 0:w], in0=z, scalar=0.0, in1=ln1[:, n % 2, 0:w],
                                                 op0=ALU.max, op1=ALU.add))
                last = dve.tensor_tensor(zsp[:, s, 0:w], z, sp_[:, s, 0:w], ALU.subtract)
                if diagonal:
                    then(i, last)
                    then(i, dve.tensor_tensor(sp_[:, s, 0:P], sp_[:, s, 0:P], before, ALU.mult))
                    last = dve.tensor_tensor(zsp[:, s, 0:P], zsp[:, s, 0:P], not_before, ALU.add)
                last.then_inc(sp_done, 1)

            def exponent(i, n):
                hh, kt, a, w = units[n]
                dve.wait_ge(tri_done, i * N + n + 1)
                if n < 2:
                    dve.wait_ge(w_done, i * N)
                else:
                    dve.wait_ge(w_done, i * N + n - 1)
                dve.wait_ge(sp_done, i * N + n + 1)
                dve.tensor_tensor(t_[:, n % 2, 0:w], zsp[:, n % 4, 0:w], ps_s[:, hh, a:a + w], ALU.add).then_inc(t_done, 1)

            dve.wait_ge(const_in, 16)
            with dve.Fori(0, PAIRS) as i:
                step[0] = 0
                dve.wait_ge(z_done, i * N)
                dve.tensor_scalar(q_st[:, :], keep["qaT"][:, i, :], 1.0, None, ALU.mult)
                for hh in range(2):
                    h = slice(hh * HD, (hh + 1) * HD)
                    x = dve.tensor_scalar(k_st[h, hh, :], keep["kaT"][h, i, :], 1.0, None, ALU.mult)
                x.then_inc(qk_staged, 1)
                softplus(i, 0)
                softplus(i, 1)
                for n in range(N):
                    exponent(i, n)
                    if n + 2 < N:
                        softplus(i, n + 2)
                assert step[0] == DVE_STEPS
                dve.wait_ge(pv_done, i * N + N)
                dve.tensor_scalar(keep["qaT"][:, i, :], ps_o[:, :], 1.0, None, ALU.mult).then_inc(o_evicted, 1)


def stage_compress(nc, pos_k, pos_v, k_w1, k_w2, v_w1, v_w2, c_cmp, c_imp, keep):
    with ExitStack() as ctx:
        m = Stage(nc, ctx, "cmp")
        w1 = m.sb("w1", [P, 2, 16, 256])
        w2k = m.sb("w2k", [P, 2, 2, HD])
        w2v = m.sb("w2v", [P, 2, HD])
        pos = m.sb("pos", [P, 2, 16])
        mcmp = m.sb("mcmp", [P, NT, 2, NCMP])
        mimp = m.sb("mimp", [P, NT, 2, NSEL])
        kpos = m.sb("kpos", [P, 2, 2, 16, NCMP])
        hid = m.sb("hid", [P, 2, 2, 2 * NCMP])
        kcmp = m.sb("kcmp", [P, 2, NCMP])
        vcmp = m.sb("vcmp", [NCMP, 2, HD])
        s_ = m.sb("s", [P, 2, 8, NCMP])
        e_ = m.sb("e", [P, 2, 8, NCMP])
        p_ = m.sb("p", [P, 2, 8, NCMP])
        st = m.sb("st", [P, 3, 8])
        psum4 = m.sb("psum4", [P, 2, NCMP + 2])
        imp = m.sb("imp", [P, 2, NSEL])
        top = m.sb("top", [P, 2, 8])
        rest = m.sb("rest", [P, 2, NSEL])
        pT = m.sb("pT", [NCMP, 2, 8, P])
        ps_c = m.ps("ps_c", [P, 2, 2, 8, 64])
        ps_t = m.ps("ps_t", [P, 8, P])
        ps_o = m.ps("ps_o", [P, 2, 8, HD])
        (w_in, c_in, kpos_k, kpos_v, hid_mm, gelu_done, cmp_mm, cmp_copied, sc_done, e_done, gate_done, p_done,
         t_done, t_copied, o_done, o_copied, dve_step, s_read, shifted) = (m.sem(n) for n in
            "w_in c_in kpos_k kpos_v hid_mm gelu_done cmp_mm cmp_copied sc_done e_done gate_done p_done t_done t_copied o_done o_copied dve_step s_read shifted".split())
        ps_h = ps_t[:, :, :].rearrange("p a b -> p (a b)")
        block = ctx.enter_context(nc.Block())

        @block.sync
        def _(sp):
            for i, (pp, wa) in enumerate(((pos_k, k_w1), (pos_v, v_w1))):
                with nc.allow_non_contiguous_dma(reason="2048 elements"):
                    sp.dma_start(pos[:, i, :], pp.rearrange("(i two) d -> (two d) i", two=2)).then_inc(w_in, 16)
                sp.dma_start(w1[:, i, :, :], wa.rearrange("(i p) f -> p i f", p=P)).then_inc(w_in, 16)
            for a in range(2):
                sp.dma_start(w2k[:, :, a, :], k_w2.rearrange("(c p) d -> p c d", p=P)).then_inc(w_in, 16)
            sp.dma_start(w2v[:, :, :], v_w2.rearrange("(c p) d -> p c d", p=P)).then_inc(w_in, 16)
            sp.dma_start(mcmp[:, :, :, :], c_cmp).then_inc(c_in, 16)
            sp.dma_start(mimp[:, :, :, :], c_imp).then_inc(c_in, 16)

        def add_pos(eng, kind, done):
            src = keep["kcT"] if kind == 0 else keep["vcT"]
            for odd in range(2):
                h = slice(odd * HD, (odd + 1) * HD)
                for g in range(2):
                    v = src[h, g, :].rearrange("p (n r) -> p r n", r=16)[:, odd::2, :]
                    for late in range(2):
                        x = eng.tensor_tensor(kpos[h, kind, g, 8 * late:8 * late + 8, :], v[:, :, late:late + NCMP],
                                              pos[h, kind, 8 * late:8 * late + 8].unsqueeze(2).to_broadcast([HD, 8, NCMP]), ALU.add)
            x.then_inc(done, 1)

        @block.gpsimd
        def _(pool):
            pool.wait_ge(w_in, 16 * 7)
            add_pos(pool, 1, kpos_v)

        @block.tensor
        def _(pe):
            pe.wait_ge(w_in, 16 * 7)
            for kind in range(2):
                pe.wait_ge(kpos_k if kind == 0 else kpos_v, 1)
                for fc in range(2):
                    o = (kind * 2 + fc) * 2 * NCMP
                    for l in range(16):
                        x = pe.matmul(ps_h[:, o:o + 2 * NCMP], w1[:, kind, l, fc * P:(fc + 1) * P], kpos[:, kind, :, l, :],
                                      start=(l == 0), stop=(l == 15), skip_group_check=True)
                    x.then_inc(hid_mm, 1)
            pe.wait_ge(gelu_done, 4)
            for c in range(2):
                x = pe.matmul(ps_c[:, 0, 0, :, :].rearrange("p a b -> p (a b)")[:, 0:2 * NCMP], w2k[:, c, :, :].rearrange("p a d -> p (a d)"),
                              hid[:, 0, c, :], start=(c == 0), stop=(c == 1))
            x.then_inc(cmp_mm, 1)
            for g in range(2):
                for c in range(2):
                    x = pe.matmul(ps_o[0:NCMP, 0, g, :], hid[:, 1, c, g * NCMP:(g + 1) * NCMP], w2v[:, c, :],
                                  start=(c == 0), stop=(c == 1), skip_group_check=True)
            x.then_inc(cmp_mm, 1)
            pe.wait_ge(cmp_copied, 2)

            def scores(i):
                if i >= 2:
                    pe.wait_ge(s_read, i - 1)
                for h in range(8):
                    hp = slice((h % 2) * HD, (h % 2 + 1) * HD)
                    x = pe.matmul(ps_c[:, i % 2, h % 2, h // 2, 0:NCMP], keep["qbT"][hp, h // 2, i * P:(i + 1) * P], kcmp[hp, h // 4, :],
                                  start=True, stop=True, skip_group_check=True)
                x.then_inc(sc_done, 1)

            scores(0)
            for i in range(NT):
                if i + 1 < NT:
                    scores(i + 1)
                pe.wait_ge(p_done, i + 1)
                if i:
                    pe.wait_ge(t_copied, i)
                for h in range(8):
                    x = pe.transpose(ps_t[0:NCMP, h, :], p_[:, i % 2, h, :], keep["ident"][:, :])
                x.then_inc(t_done, 1)
                pe.wait_ge(t_copied, i + 1)
                if i >= 2:
                    pe.wait_ge(o_copied, i - 1)
                for h in range(8):
                    x = pe.matmul(ps_o[:, i % 2, h, :], pT[:, i % 2, h, :], vcmp[:, h // 4, :], start=True, stop=True,
                                  skip_group_check=True)
                x.then_inc(o_done, 1)

        @block.scalar
        def _(act):
            act.activation(keep["gate"][:, :, :], keep["gate"][:, :, :], ACT.Sigmoid).then_inc(gate_done, 1)
            act.wait_ge(hid_mm, 4)
            for k in range(4):
                act.activation(hid[:, k // 2, k % 2, :], ps_h[:, k * 2 * NCMP:(k + 1) * 2 * NCMP], ACT.Gelu_apprx_tanh).then_inc(gelu_done, 1)
            for i in range(NT):
                act.wait_ge(shifted, i + 1)
                act.activation(e_[:, i % 2, :, :], s_[:, i % 2, :, :], ACT.Exp).then_inc(e_done, 1)
                act.wait_ge(t_done, i + 1)
                if i >= 2:
                    act.wait_ge(o_done, i - 1)
                act.activation(pT[:, i % 2, :, :], ps_t[0:NCMP, :, :], ACT.Copy).then_inc(t_copied, 1)

        @block.vector
        def _(dve):
            step = [0]

            def then(ins):
                step[0] += 1
                ins.then_inc(dve_step, 1)
                dve.wait_ge(dve_step, step[0])

            then(dve.memset(psum4[:, :, :], 0.0))
            dve.wait_ge(w_in, 16 * 7)
            add_pos(dve, 0, kpos_k)
            dve.wait_ge(cmp_mm, 2)
            dve.tensor_copy(kcmp[:, :, :], ps_c[:, 0, 0, :, :].rearrange("p a b -> p (a b)")[:, 0:2 * NCMP].rearrange("p (g n) -> p g n", g=2)).then_inc(cmp_copied, 1)
            dve.tensor_copy(vcmp[:, :, :], ps_o[0:NCMP, 0, 0:2, :]).then_inc(cmp_copied, 1)
            dve.wait_ge(c_in, 32)
            dve.wait_ge(gate_done, 1)

            def wide(x):
                return x.unsqueeze(2).to_broadcast([P, 8, NCMP])

            def shift(i):
                s = s_[:, i % 2, :, :]
                dve.wait_ge(sc_done, i + 1)
                if i >= 2:
                    dve.wait_ge(e_done, i - 1)
                dve.tensor_tensor(s.rearrange("p (b a) n -> p b a n", a=2), ps_c[:, i % 2, :, 0:4, 0:NCMP].rearrange("p a b n -> p b a n"),
                                  mcmp[:, i, 0, :].unsqueeze(1).unsqueeze(1).to_broadcast([P, 4, 2, NCMP]), ALU.add).then_inc(s_read, 1)
                dve.wait_ge(s_read, i + 1)
                then(dve.tensor_reduce(st[:, 0, :], s, AX, ALU.max))
                dve.tensor_tensor(s, s, wide(st[:, 0, :]), ALU.subtract).then_inc(shifted, 1)

            shift(0)
            for i in range(NT):
                if i + 1 < NT:
                    shift(i + 1)
                e, p = e_[:, i % 2, :, :], p_[:, i % 2, :, :]
                dve.wait_ge(e_done, i + 1)
                then(dve.tensor_reduce(st[:, 1, :], e, AX, ALU.add))
                then(dve.reciprocal(st[:, 2, :], st[:, 1, :]))
                then(dve.tensor_tensor(e, e, wide(st[:, 2, :]), ALU.mult))
                if i >= 2:
                    dve.wait_ge(t_done, i - 1)
                dve.tensor_tensor(p, e, mcmp[:, i, 1, :].unsqueeze(1).to_broadcast([P, 8, NCMP]), ALU.mult).then_inc(p_done, 1)
                dve.wait_ge(p_done, i + 1)
                then(dve.tensor_reduce(psum4[:, :, 1:NCMP + 1], p.rearrange("p (g r) n -> p g n r", g=2), AX, ALU.add))
                base = psum4[:, :, :]
                taps = bass.AP(base.tensor, base.offset, [list(base.ap[0]), [NCMP + 2, 2], [4, NSEL], [1, 5]])
                then(dve.tensor_reduce(imp[:, :, :], taps, AX, ALU.add))
                then(dve.tensor_tensor(imp[:, :, :], imp[:, :, :], mimp[:, i, 0, :].unsqueeze(1).to_broadcast([P, 2, NSEL]), ALU.mult))
                then(dve.tensor_tensor(imp[:, :, :], imp[:, :, :], mimp[:, i, 1, :].unsqueeze(1).to_broadcast([P, 2, NSEL]), ALU.add))
                for g in range(2):
                    then(dve.max(top[:, g, :], imp[:, g, :]))
                for g in range(2):
                    then(dve.match_replace(rest[:, g, :], top[:, g, :], imp[:, g, :], FAR))
                then(dve.tensor_tensor(imp[:, :, :], rest[:, :, :], imp[:, :, :], ALU.is_equal))
                then(dve.tensor_scalar(keep["sel"][:, :, i, :], imp[:, :, :], NEG, None, ALU.mult))
                dve.wait_ge(o_done, i + 1)
                gate0 = keep["gate"][:, i, :].rearrange("p (h b) -> p h b", b=3)[:, :, 0:1].to_broadcast([P, 8, HD])
                dve.tensor_tensor(keep["o_tok"][:, i, :].rearrange("p (h d) -> p h d", h=8), ps_o[:, i % 2, :, :], gate0, ALU.mult).then_inc(o_copied, 1)


def stage_selected(nc, c_win, keep):
    with ExitStack() as ctx:
        m = Stage(nc, ctx, "sel")
        R = 4
        MOST = 13
        win = m.sb("win", [P, 5 * P])
        q_st = keep["kaT"]
        ks_st, kw_st = keep["kcT"][:, 0, :], keep["kcT"][:, 1, :]
        mask = keep["vcT"]
        spare = keep["va"][:, :, :].rearrange("p a b -> p (a b)")
        pr = spare[:, 0:MOST * P]
        oT = spare[:, MOST * P:MOST * P + 512]
        vs_st = m.sb("vs_st", [P, NT, HD])
        vw_st = m.sb("vw_st", [P, NT, HD])
        sel_st = m.sb("sel_st", [P, NT, NSEL])
        gate_st = m.sb("gate_st", [P, NT, R, 3])
        o_st = m.sb("o_st", [P, NT, R, HD])
        sc = m.sb("sc", [P, MOST * P])
        pT = m.sb("pT", [P, 2 * MOST - 1, R, P])
        scaled = m.sb("scaled", [P, R, 2, HD])
        mx = m.sb("mx", [P, 2, 2])
        nmx = m.sb("nmx", [P, 2, 2])
        nothing = m.sb("nothing", [P, 1])
        sums = m.sb("sums", [P, 3, R, 2])
        cf = m.sb("cf", [P, R, 2])
        ps_s = m.ps("ps_s", [P, S])
        ps_w = m.ps("ps_w", [P, S])
        ps_t = m.ps("ps_t", [P, 2, 512])
        ps_o = m.ps("ps_o", [P, 512])
        ps_b = m.ps("ps_b", [P, R, 2, HD])
        (c_in, st_act, st_dve, zero_done, mask_done, sc_done, sc_read, e_done, t_done, t_copied, o_done, ot_done, back_done,
         o_used, dve_step, out_done) = (m.sem(n) for n in
            "c_in st_act st_dve zero_done mask_done sc_done sc_read e_done t_done t_copied o_done ot_done back_done o_used dve_step out_done".split())
        units = [(i, r) for i in range(NT) for r in range(R)]
        N = len(units)

        def tiles(i):
            return [(0, j) for j in range(i + 1)] + [(1, j) for j in range(max(0, i - 4), i + 1)]

        chunks = [(n, k, len(tiles(i)[k:k + 4])) for n, (i, r) in enumerate(units) for k in range(0, len(tiles(i)), 4)]
        NCH = len(chunks)
        first_chunk = [next(c for c, (u, _, _) in enumerate(chunks) if u == n) for n in range(N)] + [NCH]
        pT_at = lambda i: (i % 2) * (MOST - 1)
        DSTEP = N + 4 * NT
        block = ctx.enter_context(nc.Block())

        @block.sync
        def _(sp):
            sp.dma_start(win[:, :], c_win).then_inc(c_in, 16)

        @block.gpsimd
        def _(pool):
            for r in range(R):
                other = slice((1 - r % 2) * HD, (2 - r % 2) * HD)
                pool.memset(q_st[other, r, :], 0.0).then_inc(zero_done, 1)
                pool.wait_ge(zero_done, r + 1)
            pool.wait_ge(c_in, 16)
            with pool.Fori(0, 2) as g:
                for i in range(NT):
                    if i == 0:
                        pool.wait_ge(st_dve, g + 1)
                    pool.wait_ge(sc_read, g * N + R * max(0, i - 1))
                    w = i * P

                    def blocks(x):
                        return x.rearrange("p (b l) -> p b l", l=64)

                    x = pool.tensor_tensor(blocks(mask[:, i % 2, w:w + P]), sel_st[:, i, w // 64:w // 64 + 2].unsqueeze(2).to_broadcast([P, 2, 64]),
                                           blocks(win[:, 4 * P:5 * P]), ALU.add)
                    if i:
                        x = pool.tensor_copy(blocks(mask[:, i % 2, 0:w]), sel_st[:, i, 0:w // 64].unsqueeze(2).to_broadcast([P, w // 64, 64]))
                    x.then_inc(mask_done, 1)

        @block.tensor
        def _(pe):
            def scores(g, n):
                i, r = units[n]
                pe.wait_ge(sc_read, g * N + n)
                q = q_st[:, r, i * P:(i + 1) * P]
                w = (i + 1) * P
                for a in range(0, w, 512):
                    b = min(a + 512, w)
                    pe.matmul(ps_s[:, a:b], q, ks_st[:, a:b], start=True, stop=True)
                k0 = max(0, i - 4) * P
                ww = w - k0
                for a in range(0, ww, 512):
                    b = min(a + 512, ww)
                    x = pe.matmul(ps_w[:, a:b], q, kw_st[:, k0 + a:k0 + b], start=True, stop=True)
                x.then_inc(sc_done, 1)

            def transposes(g, c):
                n, k, count = chunks[c]
                pe.wait_ge(t_copied, g * NCH + max(0, c - 1))
                for j in range(count):
                    x = pe.transpose(ps_t[:, c % 2, j * P:(j + 1) * P], pr[:, (k + j) * P:(k + j + 1) * P], keep["ident"][:, :])
                x.then_inc(t_done, 1)

            def pairs(i):
                ts = tiles(i)
                s, w = ts[:i + 1], ts[i + 1:]
                return [[(k, s[k])] + ([(i + 1 + k, w[k])] if k < len(w) else []) for k in range(i + 1)]

            def values(g, i, some, last):
                for pair in some:
                    for k, (branch, kt) in pair:
                        v = (vs_st, vw_st)[branch]
                        x = pe.matmul(ps_o[branch * HD:(branch + 1) * HD, :], v[:, kt, :],
                                      pT[:, pT_at(i) + k, :, :].rearrange("p r q -> p (r q)"),
                                      start=(kt == (0, max(0, i - 4))[branch]), stop=(kt == i), skip_group_check=True)
                if last:
                    x.then_inc(o_done, 1)

            def ready(g, i):
                pe.wait_ge(t_copied, g * NCH + first_chunk[R * (i + 1)])
                pe.wait_ge(ot_done, g * NT + i)

            def back(g, i):
                pe.wait_ge(ot_done, g * NT + i + 1)
                pe.wait_ge(o_used, g * NT + i)
                for r in range(R):
                    x = pe.transpose(ps_b[:, r, :, :].rearrange("p a d -> p (a d)"), oT[:, r * P:(r + 1) * P], keep["ident"][:, :])
                x.then_inc(back_done, 1)

            pe.wait_ge(zero_done, R)
            with pe.Fori(0, 2) as g:
                pe.wait_ge(st_act, g + 1)
                pe.wait_ge(st_dve, g + 1)
                scores(g, 0)
                for n in range(N):
                    i, r = units[n]
                    if n + 1 < N:
                        scores(g, n + 1)
                    pe.wait_ge(e_done, g * N + n + 1)
                    todo = pairs(i - 1) if i and r < 3 else []
                    places = 3 * (first_chunk[n + 1] - first_chunk[n])
                    for j, c in enumerate(range(first_chunk[n], first_chunk[n + 1])):
                        transposes(g, c)
                        if todo:
                            if j == 0 and r == 0:
                                ready(g, i - 1)
                            at = r * (places // 3) + j
                            some = todo[len(todo) * at // places:len(todo) * (at + 1) // places]
                            values(g, i - 1, some, at + 1 == places)
                    if i and r == 3:
                        back(g, i - 1)
                ready(g, NT - 1)
                values(g, NT - 1, pairs(NT - 1), True)
                back(g, NT - 1)

        @block.scalar
        def _(act):
            act.preload_act_table_set("exp_and_others")

            def exps(g, n):
                i, r = units[n]
                act.wait_ge(sc_read, g * N + n + 1)
                act.wait_ge(t_done, g * NCH + first_chunk[n])
                act.wait_ge(o_used, g * NT + max(0, i - 2))
                w = (i + 1) * P
                ww = w - max(0, i - 4) * P
                act.activation(pr[:, 0:w], sc[:, 0:w], ACT.Exp, bias=nmx[:, n % 2, 0:1], accum_out=sums[:, i % 3, r, 0:1])
                act.activation(pr[:, w:w + ww], sc[:, w:w + ww], ACT.Exp, bias=nmx[:, n % 2, 1:2],
                               accum_out=sums[:, i % 3, r, 1:2]).then_inc(e_done, 1)

            def copy_out(g, i):
                act.wait_ge(o_done, g * NT + i + 1)
                act.wait_ge(back_done, g * NT + i)
                act.activation(oT[:, :], ps_o[:, :], ACT.Copy).then_inc(ot_done, 1)

            with act.Fori(0, 2) as g:
                act.wait_ge(out_done, g)
                act.activation(ks_st, keep["ksT"][:, g, :], ACT.Copy)
                act.activation(kw_st, keep["kwT"][:, g, :], ACT.Copy)
                act.activation(q_st[HD:P, 1::2, :], keep["qbT"][HD:P, bass.ds(g * 2, 2), :], ACT.Copy).then_inc(st_act, 1)
                exps(g, 0)
                for n in range(N):
                    i, r = units[n]
                    for c in range(first_chunk[n], first_chunk[n + 1]):
                        _, k, count = chunks[c]
                        act.wait_ge(t_done, g * NCH + c + 1)
                        act.wait_ge(o_done, g * NT + max(0, i - 1))
                        act.activation(pT[:, pT_at(i) + k:pT_at(i) + k + count, r, :],
                                       ps_t[:, c % 2, 0:count * P].rearrange("p (k q) -> p k q", q=P), ACT.Copy).then_inc(t_copied, 1)
                        if i and r == 3 and c == first_chunk[n]:
                            copy_out(g, i - 1)
                    if n + 1 < N:
                        exps(g, n + 1)
                copy_out(g, NT - 1)

        @block.vector
        def _(dve):
            step = [0]

            def then(g, ins):
                step[0] += 1
                ins.then_inc(dve_step, 1)
                dve.wait_ge(dve_step, g * DSTEP + step[0])

            def masked_max(g, n):
                i, r = units[n]
                w = (i + 1) * P
                ww = w - max(0, i - 4) * P
                if r == 0:
                    dve.wait_ge(mask_done, g * NT + i + 1)
                dve.wait_ge(sc_done, g * N + n + 1)
                dve.wait_ge(e_done, g * N + n)
                dve.memset(nothing[:, :], 0.0)
                dve.tensor_tensor_reduce(sc[:, 0:w], ps_s[:, 0:w], mask[:, i % 2, 0:w], 1.0, FAR, ALU.add, ALU.max, mx[:, n % 2, 0:1])
                then(g, dve.tensor_tensor_reduce(sc[:, w:w + ww], ps_w[:, 0:ww], win[:, 5 * P - ww:5 * P], 1.0, FAR, ALU.add, ALU.max, mx[:, n % 2, 1:2]))
                dve.tensor_scalar(nmx[:, n % 2, :], mx[:, n % 2, :], -1.0, None, ALU.mult).then_inc(sc_read, 1)

            def combine(g, i):
                dve.wait_ge(e_done, g * N + R * (i + 1))
                then(g, dve.reciprocal(cf[:, :, :], sums[:, i % 3, :, :]))
                then(g, dve.tensor_tensor(cf[:, :, :], cf[:, :, :], gate_st[:, i, :, 1:3], ALU.mult))
                dve.wait_ge(back_done, g * NT + i + 1)
                then(g, dve.tensor_tensor(scaled[:, :, :, :], ps_b[:, :, :, :], cf[:, :, :].unsqueeze(3).to_broadcast([P, R, 2, HD]), ALU.mult))
                o = o_st[:, i, :, :]
                then(g, dve.tensor_tensor(o, o, scaled[:, :, 0, :], ALU.add))
                dve.tensor_tensor(o, o, scaled[:, :, 1, :], ALU.add).then_inc(o_used, 1)

            dve.wait_ge(c_in, 16)
            with dve.Fori(0, 2) as g:
                step[0] = 0
                dve.tensor_scalar(q_st[0:HD, 0::2, :], keep["qbT"][0:HD, bass.ds(g * 2, 2), :], 1.0, None, ALU.mult)
                dve.tensor_scalar(vs_st[:, :, :], keep["vs"][:, :, bass.ds(g * HD, HD)], 1.0, None, ALU.mult)
                dve.tensor_scalar(vw_st[:, :, :], keep["vw"][:, :, bass.ds(g * HD, HD)], 1.0, None, ALU.mult)
                dve.tensor_scalar(sel_st[:, :, :], keep["sel"][:, g, :, :], 1.0, None, ALU.mult)
                dve.tensor_scalar(gate_st[:, :, :, :].rearrange("p i r b -> p i (r b)"), keep["gate"][:, :, bass.ds(g * 12, 12)], 1.0, None, ALU.mult)
                dve.tensor_scalar(o_st[:, :, :, :].rearrange("p i r d -> p i (r d)"), keep["o_tok"][:, :, bass.ds(g * 256, 256)], 1.0, None, ALU.mult).then_inc(st_dve, 1)
                dve.wait_ge(st_dve, g + 1)
                masked_max(g, 0)
                for n in range(1, N):
                    i, r = units[n]
                    masked_max(g, n)
                    if r == 1 and i >= 2:
                        combine(g, i - 2)
                combine(g, NT - 2)
                combine(g, NT - 1)
                assert step[0] == DSTEP
                dve.wait_ge(o_used, g * NT + NT)
                dve.tensor_scalar(keep["o_tok"][:, :, bass.ds(g * 256, 256)], o_st[:, :, :, :].rearrange("p i r d -> p i (r d)"), 1.0, None, ALU.mult).then_inc(out_done, 1)
                dve.wait_ge(out_done, g + 1)


def stage_attention_out(nc, w_out, x, g, b, keep, h_out):
    with ExitStack() as ctx:
        m = Stage(nc, ctx, "ao")
        w = m.sb("w", [P, KC, D])
        oT = m.sb("oT", [P, 2, 4, P])
        y = m.sb("y", [P, 2, D])
        xr = m.sb("xr", [P, 2, D])
        norm = Norm(m, "ln")
        ps_t = m.ps("ps_t", [P, 2, 512])
        ps_y = m.ps("ps_y", [P, 2, D])
        w_in, transposed, t_copied, y_mm, y_ready, dve_step, y_read = (m.sem(n) for n in "w_in transposed t_copied y_mm y_ready dve_step y_read".split())
        x_in = [m.sem(f"x_in{k}") for k in range(2)]
        stored = [m.sem(f"stored{k}") for k in range(2)]
        block = ctx.enter_context(nc.Block())

        @block.sync
        def _(sp):
            sp.dma_start(w[:, :, :], w_out.rearrange("(c p) n -> p c n", p=P)).then_inc(w_in, 16)
            norm.load(sp, g, b)
            for i in range(NT):
                if i >= 2:
                    sp.wait_ge(y_read, i - 1)
                sp.dma_start(xr[:, i % 2, :], x[i * P:(i + 1) * P, :]).then_inc(x_in[i % 2], 16)
                if i:
                    sp.wait_ge(y_ready, i)
                    sp.dma_start(h_out[(i - 1) * P:i * P, :], y[:, (i - 1) % 2, :]).then_inc(stored[(i - 1) % 2], 16)
            sp.wait_ge(y_ready, NT)
            sp.dma_start(h_out[(NT - 1) * P:, :], y[:, (NT - 1) % 2, :]).then_inc(stored[(NT - 1) % 2], 16)
            for k in range(2):
                sp.wait_ge(stored[k], 16 * NT // 2)

        @block.tensor
        def _(pe):
            def transposes(i):
                if i >= 2:
                    pe.wait_ge(t_copied, i - 1)
                for c in range(4):
                    x_ = pe.transpose(ps_t[:, i % 2, c * P:(c + 1) * P], keep["o_tok"][:, i, c * P:(c + 1) * P], keep["ident"][:, :])
                x_.then_inc(transposed, 1)

            transposes(0)
            pe.wait_ge(w_in, 16)
            for i in range(NT):
                if i + 1 < NT:
                    transposes(i + 1)
                if i >= 2:
                    pe.wait_ge(y_read, i - 1)
                pe.wait_ge(t_copied, i + 1)
                for half in range(2):
                    for c in range(KC):
                        lhs = keep["qaT"][:, c, i * P:(i + 1) * P] if c < 4 else oT[:, i % 2, c - 4, :]
                        x_ = pe.matmul(ps_y[:, i % 2, half * 512:(half + 1) * 512], lhs, w[:, c, half * 512:(half + 1) * 512],
                                       start=(c == 0), stop=(c == KC - 1))
                x_.then_inc(y_mm, 1)

        @block.scalar
        def _(act):
            for i in range(NT):
                act.wait_ge(transposed, i + 1)
                if i >= 2:
                    act.wait_ge(y_mm, i - 1)
                act.activation(oT[:, i % 2, :, :], ps_t[:, i % 2, :].rearrange("p (c t) -> p c t", c=4), ACT.Copy).then_inc(t_copied, 1)
                if i:
                    norm.on_act(act, i - 1)
            norm.on_act(act, NT - 1)

        @block.vector
        def _(dve):
            step = [0]

            def then(ins):
                step[0] += 1
                ins.then_inc(dve_step, 1)
                dve.wait_ge(dve_step, step[0])

            for i in range(NT):
                dve.wait_ge(y_mm, i + 1)
                dve.wait_ge(x_in[i % 2], 16 * (i // 2 + 1))
                if i >= 2:
                    dve.wait_ge(stored[i % 2], 16 * (i // 2))
                yy = y[:, i % 2, :]
                dve.scalar_tensor_tensor(out=yy, in0=xr[:, i % 2, :], scalar=ALPHA, in1=ps_y[:, i % 2, :],
                                         op0=ALU.mult, op1=ALU.add).then_inc(y_read, 1)
                dve.wait_ge(y_read, i + 1)
                norm.on_dve(dve, then, yy, i).then_inc(y_ready, 1)


class Moe:

    def __init__(self, nc, ctx, name, y, w_gate, w_up, w_down):
        m = self.m = Stage(nc, ctx, name)
        self.name, self.w_gate, self.w_up, self.w_down = name, w_gate, w_up, w_down
        self.ident = m.sb("ident", [P, P])
        self.acc = m.sb("acc", [P, NT, D])
        self.w = m.sb("w", [P, 4, 3, 2048])
        self.dest = m.sb("dest", [P, NT, TOPK], I32)
        self.gates = m.sb("gates", [P, NT, TOPK])
        self.slot_tok = m.sb("slot_tok", [CAP, NBLK])
        self.spill = m.sb("spill", [1, 1 + NSPILL], I32)
        self.wgu_in = [m.sem(f"wgu_in{s}") for s in range(4)]
        self.wd_in = [m.sem(f"wd_in{s}") for s in range(4)]
        self.tab = nc.dram_tensor(f"{name}_tab", (NBLK * CAP, 1), F32, kind="Internal").ap()
        self.y = y

    def gu(self, s):
        return self.w[:, s, 0:2, :].rearrange("p a b -> p (a b)").rearrange("p (c f) -> p c f", c=KC)

    def down(self, s):
        return self.w[:, s, 2, :].rearrange("p (c n) -> p c n", c=2)

    def load(self, eng, e, s):
        gu = self.gu(s)

        def rows(w):
            v = w[bass.ds(e, 1), :, :]
            return v.rearrange("a (p c) f -> p (a c) f", p=P)

        eng.dma_start(gu[:, :, 0:FH], rows(self.w_gate)).then_inc(self.wgu_in[s], 16)
        eng.dma_start(gu[:, :, FH:2 * FH], rows(self.w_up)).then_inc(self.wgu_in[s], 16)
        eng.dma_start(self.down(s), rows(self.w_down)).then_inc(self.wd_in[s], 16)


def stage_route(nc, M, h, router, bias, sh_gate, sh_up, sh_down, consts):
    with ExitStack() as ctx:
        m = Stage(nc, ctx, M.name + "r")
        spare = M.w[:, 2:4, :, :].rearrange("p s a b -> p (s a b)")
        hT = spare[:, 0:8192].rearrange("p (c t) -> p c t", c=KC)
        hidT = spare[:, 8192:10240].rearrange("p (c t) -> p c t", c=2)
        w_sh = m.sb("w_sh", [P, 2, KC, FH])
        w_shd = m.sb("w_shd", [P, 2, D])
        w_r = m.sb("w_r", [P, KC, NE])
        bias_sb = m.sb("bias", [P, NE])
        tri8 = m.sb("tri8", [P, 8, 8])
        cexp = m.sb("cexp", [P, 3, NE])
        before = m.sb("before", [P, 2, P])
        cspill = m.sb("cspill", [1, NSPILL])
        ctok = m.sb("ctok", [P, NT])
        score = m.sb("score", [P, NT, NE])
        biased = m.sb("biased", [P, NT, NE])
        m8 = m.sb("m8", [P, NT * 8, 8])
        gs = m.sb("gs", [P, 3, NT, 8])
        cmp_ = m.sb("cmp", [P, 2, NT, 8, 8])
        top = m.sb("top", [P, NT, 8])
        tid = m.sb("tid", [P, NT, 8], U32)
        tidf = m.sb("tidf", [P, NT, 8])
        onehot = m.sb("onehot", [P, NT, TOPK, NE])
        prod = m.sb("prod", [P, NT, TOPK, NE])
        mem = m.sb("mem", [P, NT, NE])
        slot = m.sb("slot", [P, NT, NE])
        over = m.sb("over", [P, NT, NE])
        nb = m.sb("nb", [P, 3, NE])
        ones = m.sb("ones", [P, NE])
        gsum = m.sb("gsum", [P, 2, NT])
        destf = m.sb("destf", [P, NT, TOPK])
        sil = m.sb("sil", [P, 2, 512])
        tabT = m.sb("tabT", [NBLK, CAP])
        spillf = m.sb("spillf", [1, 1 + NSPILL])
        ps_t = m.ps("ps_t", [P, 2, 512])
        ps_a = m.ps("ps_a", [P, 4, 512])
        ps_r = m.ps("ps_r", [P, NT, NE])
        ps_p = m.ps("ps_p", [P, NT, NE])
        (h_in, rw_in, sw_in, c_in, tab_zero, transposed, t_act, t_dve, logits_done, score_done, members, pos_done, dest_done,
         hid_mm, sil_done, hid_done, dn_mm, acc_done, dve_step, scattered, tab_in, tab_t, spill_f, cnt_read, cnt_done) = (m.sem(n) for n in
            "h_in rw_in sw_in c_in tab_zero transposed t_act t_dve logits_done score_done members pos_done dest_done hid_mm sil_done hid_done dn_mm acc_done dve_step scattered tab_in tab_t spill_f cnt_read cnt_done".split())
        block = ctx.enter_context(nc.Block())

        @block.sync
        def _(sp):
            sp.dma_start(M.ident[:, :], consts["c_ident"]).then_inc(h_in, 16)
            sp.dma_start(M.acc[:, :, :], h.rearrange("(i p) d -> p i d", p=P)).then_inc(h_in, 16)
            sp.dma_start(w_r[:, :, :], router.rearrange("(p c) e -> p c e", c=KC)).then_inc(rw_in, 16)
            sp.dma_start(M.tab.rearrange("(b s) one -> b (s one)", s=CAP), consts["c_zero"]).then_inc(tab_zero, 16)
            sp.dma_start(bias_sb[:, :], bias.partition_broadcast(P)).then_inc(c_in, 16)
            for dst, n in ((tri8, "c_tri8"), (cexp, "c_exp"), (before, "c_before"), (cspill, "c_spill"), (ctok, "c_tok")):
                sp.dma_start(dst[:], consts[n]).then_inc(c_in, 16)
            for i, w in enumerate((sh_gate, sh_up)):
                sp.dma_start(w_sh[:, i, :, :], w.rearrange("(p c) f -> p c f", c=KC)).then_inc(sw_in, 16)
            sp.dma_start(w_shd[:, :, :], sh_down.rearrange("(p c) n -> p c n", c=2)).then_inc(sw_in, 16)
            for e in range(2):
                M.load(sp, e, e)
            sp.wait_ge(scattered, 16 * NT * TOPK)
            sp.dma_start(tabT[:, :], M.tab.rearrange("(b s) one -> b (s one)", s=CAP)).then_inc(tab_in, 16)

        @block.gpsimd
        def _(pool):
            pool.wait_ge(tab_zero, 16)
            pool.wait_ge(c_in, 96)
            pool.wait_ge(dest_done, 1)
            for i in range(NT):
                for k in range(TOPK):
                    pool.indirect_dma_start(out=M.tab, out_offset=bass.IndirectOffsetOnAxis(ap=M.dest[:, i, k:k + 1], axis=0),
                                            in_=ctok[:, i:i + 1], in_offset=None).then_inc(scattered, 16)

        @block.tensor
        def _(pe):
            pe.wait_ge(h_in, 32)
            for n in range(2 * NT):
                i, c0 = n // 2, 4 * (n % 2)
                if n >= 2:
                    pe.wait_ge((t_act, t_dve)[n % 2], n // 2)
                for c in range(4):
                    x = pe.transpose(ps_t[:, n % 2, c * P:(c + 1) * P],
                                     M.acc[:, i, c0 + c::KC], M.ident[:, :])
                x.then_inc(transposed, 1)
            pe.wait_ge(t_act, NT)
            pe.wait_ge(t_dve, NT)
            pe.wait_ge(rw_in, 16)
            for i in range(NT):
                for c in range(KC):
                    x = pe.matmul(ps_r[:, i, :], hT[:, c, i * P:(i + 1) * P], w_r[:, c, :], start=(c == 0), stop=(c == KC - 1),
                                  skip_group_check=True)
            x.then_inc(logits_done, 1)
            pe.wait_ge(sw_in, 48)
            for u in range(4):
                fc, half = u // 2, u % 2
                if u >= 2:
                    pe.wait_ge(hid_done, u - 1)
                for gu in range(2):
                    for c in range(KC):
                        x = pe.matmul(ps_a[:, 2 * (u % 2) + gu, :], w_sh[:, gu, c, fc::2], hT[:, c, half * 512:(half + 1) * 512],
                                      start=(c == 0), stop=(c == KC - 1))
                x.then_inc(hid_mm, 1)
            pe.wait_ge(c_in, 96)
            pe.wait_ge(members, 1)
            for i in range(NT):
                for j in range(i + 1):
                    x = pe.matmul(ps_p[:, i, :], before[:, 0 if j == i else 1, :], mem[:, j, :], start=(j == 0), stop=(j == i),
                                  skip_group_check=True)
            x.then_inc(pos_done, 1)
            for j in range(NT):
                x = pe.matmul(ps_r[:, 0, :], before[:, 1, :], mem[:, j, :], start=(j == 0), stop=(j == NT - 1), skip_group_check=True)
            x.then_inc(cnt_done, 1)
            for i in range(NT):
                pe.wait_ge(hid_done, 4)
                if i >= 2:
                    pe.wait_ge(acc_done, i - 1)
                for half in range(2):
                    for c in range(2):
                        x = pe.matmul(ps_a[:, 2 * (i % 2) + half, :], hidT[:, c, i * P:(i + 1) * P], w_shd[:, c, half * 512:(half + 1) * 512],
                                      start=(c == 0), stop=(c == 1))
                x.then_inc(dn_mm, 1)
            pe.wait_ge(tab_in, 16)
            pe.transpose(ps_t[0:CAP, 0, 0:NBLK], tabT[:, :], M.ident[0:NBLK, 0:NBLK]).then_inc(tab_t, 1)

        @block.scalar
        def _(act):
            for i in range(NT):
                act.wait_ge(transposed, 2 * i + 1)
                act.activation(hT[:, 0:4, i * P:(i + 1) * P], ps_t[:, 0, :].rearrange("p (c t) -> p c t", c=4), ACT.Copy).then_inc(t_act, 1)
            act.wait_ge(logits_done, 1)
            act.activation(score[:, :, :], ps_r[:, :, :], ACT.Sigmoid).then_inc(score_done, 1)
            for u in range(4):
                act.wait_ge(hid_mm, u + 1)
                if u >= 2:
                    act.wait_ge(hid_done, u - 1)
                act.activation(sil[:, u % 2, :], ps_a[:, 2 * (u % 2), :], ACT.Silu).then_inc(sil_done, 1)

        @block.vector
        def _(dve):
            step = [0]

            def then(ins):
                step[0] += 1
                ins.then_inc(dve_step, 1)
                dve.wait_ge(dve_step, step[0])

            for i in range(NT):
                dve.wait_ge(transposed, 2 * i + 2)
                dve.tensor_copy(hT[:, 4:8, i * P:(i + 1) * P], ps_t[:, 1, :].rearrange("p (c t) -> p c t", c=4)).then_inc(t_dve, 1)

            def hidden(u):
                fc, half = u // 2, u % 2
                dve.wait_ge(sil_done, u + 1)
                dve.tensor_tensor(hidT[:, fc, half * 512:(half + 1) * 512], sil[:, u % 2, :], ps_a[:, 2 * (u % 2) + 1, :], ALU.mult).then_inc(hid_done, 1)

            dve.wait_ge(score_done, 1)
            dve.wait_ge(c_in, 96)
            then(dve.tensor_tensor(biased[:, :, :], score[:, :, :], bias_sb[:, :].unsqueeze(1).to_broadcast([P, NT, NE]), ALU.add))
            bg = biased[:, :, :].rearrange("p i (g e) -> p (i g) e", e=8)
            for n in range(8 * NT):
                x = dve.max(m8[:, n, :], bg[:, n, :])
            then(x)
            pair = m8[:, :, :].rearrange("p (i g) k -> p i g k", g=8)
            then(dve.tensor_tensor(gs[:, 0, :, :], pair[:, :, :, 0], pair[:, :, :, 1], ALU.add))
            other = gs[:, 0, :, :].unsqueeze(2).to_broadcast([P, NT, 8, 8])
            own = gs[:, 0, :, :].unsqueeze(3).to_broadcast([P, NT, 8, 8])
            then(dve.tensor_tensor(cmp_[:, 0, :, :, :], other, own, ALU.is_gt))
            then(dve.tensor_tensor(cmp_[:, 1, :, :, :], other, own, ALU.is_equal))
            then(dve.tensor_tensor(cmp_[:, 1, :, :, :], cmp_[:, 1, :, :, :], tri8[:, :, :].unsqueeze(1).to_broadcast([P, NT, 8, 8]), ALU.mult))
            then(dve.tensor_tensor(cmp_[:, 0, :, :, :], cmp_[:, 0, :, :, :], cmp_[:, 1, :, :, :], ALU.add))
            then(dve.tensor_reduce(gs[:, 1, :, :], cmp_[:, 0, :, :, :], AX, ALU.add))
            then(dve.tensor_scalar(gs[:, 1, :, :], gs[:, 1, :, :], 3.5, None, ALU.is_lt))
            then(dve.tensor_scalar(gs[:, 2, :, :], gs[:, 1, :, :], -NEG, NEG, ALU.mult, ALU.add))
            b4 = biased[:, :, :].rearrange("p i (g e) -> p i g e", e=8)
            then(dve.tensor_tensor(b4, b4, gs[:, 1, :, :].unsqueeze(3).to_broadcast([P, NT, 8, 8]), ALU.mult))
            then(dve.tensor_tensor(b4, b4, gs[:, 2, :, :].unsqueeze(3).to_broadcast([P, NT, 8, 8]), ALU.add))
            for i in range(NT):
                x = dve.max(top[:, i, :], biased[:, i, :])
            then(x)
            for i in range(NT):
                x = dve.max_index(tid[:, i, :], top[:, i, :], biased[:, i, :])
            then(x)
            then(dve.tensor_copy(tidf[:, :, :], tid[:, :, :]))
            then(dve.tensor_tensor(onehot[:, :, :, :], tidf[:, :, 0:TOPK].unsqueeze(3).to_broadcast([P, NT, TOPK, NE]),
                                   cexp[:, 0, :].unsqueeze(1).unsqueeze(1).to_broadcast([P, NT, TOPK, NE]), ALU.is_equal))
            dve.tensor_reduce(mem[:, :, :], onehot[:, :, :, :].rearrange("p i k e -> p i e k"), AX, ALU.add).then_inc(members, 1)
            for u in range(2):
                hidden(u)
            then(dve.tensor_tensor(prod[:, :, :, :], onehot[:, :, :, :], score[:, :, :].unsqueeze(2).to_broadcast([P, NT, TOPK, NE]), ALU.mult))
            then(dve.tensor_reduce(M.gates[:, :, :], prod[:, :, :, :], AX, ALU.add))
            for u in range(2, 4):
                hidden(u)
            then(dve.tensor_reduce(gsum[:, 0, :], M.gates[:, :, :], AX, ALU.add))
            then(dve.reciprocal(gsum[:, 1, :], gsum[:, 0, :]))
            then(dve.tensor_tensor(M.gates[:, :, :], M.gates[:, :, :], gsum[:, 1, :].unsqueeze(2).to_broadcast([P, NT, TOPK]), ALU.mult))
            then(dve.tensor_scalar(M.gates[:, :, :], M.gates[:, :, :], 2.5, None, ALU.mult))
            dve.wait_ge(cnt_done, 1)
            then(dve.memset(ones[:, :], 1.0))
            then(dve.tensor_scalar(nb[:, 0, :], ps_r[:, 0, :], CAP + 0.5, None, ALU.is_gt))
            for k in range(2, S // CAP):
                then(dve.scalar_tensor_tensor(out=nb[:, 0, :], in0=ps_r[:, 0, :], scalar=k * CAP + 0.5, in1=nb[:, 0, :], op0=ALU.is_gt, op1=ALU.add))
            then(dve.tensor_tensor_scan(nb[:, 1, :], ones[:, :], nb[:, 0, :], 0.0, ALU.mult, ALU.add))
            then(dve.tensor_tensor(nb[:, 2, :], nb[:, 1, :], nb[:, 0, :], ALU.subtract))
            then(dve.scalar_tensor_tensor(out=nb[:, 2, :], in0=nb[:, 2, :], scalar=float(CAP), in1=cexp[:, 2, :], op0=ALU.mult, op1=ALU.add))
            dve.wait_ge(pos_done, 1)
            then(dve.tensor_scalar(over[:, :, :], ps_p[:, :, :], CAP - 0.5, None, ALU.is_gt))
            then(dve.tensor_tensor(over[:, :, :], over[:, :, :], nb[:, 2, :].unsqueeze(1).to_broadcast([P, NT, NE]), ALU.mult))
            then(dve.tensor_tensor(slot[:, :, :], ps_p[:, :, :], cexp[:, 1, :].unsqueeze(1).to_broadcast([P, NT, NE]), ALU.add))
            then(dve.tensor_tensor(slot[:, :, :], slot[:, :, :], over[:, :, :], ALU.add))
            then(dve.tensor_tensor(prod[:, :, :, :], onehot[:, :, :, :], slot[:, :, :].unsqueeze(2).to_broadcast([P, NT, TOPK, NE]), ALU.mult))
            then(dve.tensor_reduce(destf[:, :, :], prod[:, :, :, :], AX, ALU.add))
            dve.tensor_copy(M.dest[:, :, :], destf[:, :, :]).then_inc(dest_done, 1)
            sp3 = prod[0:1, :, :, :].rearrange("p i k e -> p (i k) e")
            then(dve.tensor_copy(spillf[:, 0:1], nb[0:1, 1, NE - 1:NE]))
            then(dve.tensor_tensor(sp3, nb[0:1, 1, :].unsqueeze(1).to_broadcast([1, NSPILL, NE]),
                                   cspill[:, :].unsqueeze(2).to_broadcast([1, NSPILL, NE]), ALU.is_le))
            then(dve.tensor_reduce(spillf[:, 1:], sp3, AX, ALU.add))
            then(dve.tensor_scalar(spillf[:, 1:], spillf[:, 1:], float(NE - 1), None, ALU.min))
            then(dve.tensor_copy(M.spill[:, :], spillf[:, :]))
            for i in range(NT):
                dve.wait_ge(dn_mm, i + 1)
                dve.scalar_tensor_tensor(out=M.acc[:, i, :], in0=M.acc[:, i, :], scalar=ALPHA,
                                         in1=ps_a[:, 2 * (i % 2):2 * (i % 2) + 2, :].rearrange("p a b -> p (a b)"),
                                         op0=ALU.mult, op1=ALU.add).then_inc(acc_done, 1)
            dve.wait_ge(tab_t, 1)
            dve.tensor_copy(M.slot_tok[:, :], ps_t[0:CAP, 0, 0:NBLK])


def stage_experts(nc, M, h):
    with ExitStack() as ctx:
        m = Stage(nc, ctx, M.name + "e")
        TURN = 4
        AHEAD = 3
        xg = m.sb("xg", [P, TURN, D])
        xT = m.sb("xT", [P, 2, KC, P])
        idx = m.sb("idx", [P, TURN], I32)
        sil = m.sb("sil", [P, 2, FH])
        a_ = m.sb("a", [P, 2, FH])
        aT = m.sb("aT", [P, 2, 2, P])
        yo = m.sb("yo", [P, 2, D])
        tick = m.sb("tick", [1, 1])
        ps_x = m.ps("ps_x", [P, 2, 512])
        ps_gu = m.ps("ps_gu", [P, 2, 512])
        ps_a = m.ps("ps_a", [P, 512])
        ps_y = m.ps("ps_y", [P, 2, 512])
        (idx_done, xt_mm, x_act, x_dve, gu_done, sil_done, a_done, at_mm, at_done, y_mm, y_act, y_dve) = (m.sem(n) for n in
            "idx_done xt_mm x_act x_dve gu_done sil_done a_done at_mm at_done y_mm y_act y_dve".split())
        ticked = m.sem("ticked")
        gathered = [m.sem(f"gathered{k}") for k in range(TURN)]
        stored = [m.sem(f"stored{k}") for k in range(2)]
        block = ctx.enter_context(nc.Block())

        def turns(eng, steps):
            for s in range(TURN):
                steps(0, s, s)
            with eng.Fori(1, NE // TURN - 1) as t:
                for s in range(TURN):
                    steps(t, s, t * TURN + s)
            for s in range(TURN):
                steps(NE // TURN - 1, s, NE - TURN + s)

        def first(n, count):
            return isinstance(n, int) and n < count

        def last(n, count):
            return isinstance(n, int) and n >= NE - count

        @block.sync
        def _(sp):
            def steps(t, s, n):
                if not first(n, 1):
                    if not last(n, TURN - 1):
                        sp.wait_ge(y_mm, n)
                        M.load(sp, n + (TURN - 1), (s - 1) % TURN)
                    sp.wait_ge(y_act, n)
                    sp.wait_ge(y_dve, n)
                    sp.dma_start(M.y[bass.ds((n - 1) * CAP, CAP), :], yo[:, (s - 1) % 2, :]).then_inc(stored[(s - 1) % 2], 16)

            for s in range(2, TURN):
                M.load(sp, s, s)
            turns(sp, steps)
            sp.wait_ge(y_act, NE)
            sp.wait_ge(y_dve, NE)
            sp.dma_start(M.y[(NE - 1) * CAP:NE * CAP, :], yo[:, (NE - 1) % 2, :]).then_inc(stored[(NE - 1) % 2], 16)
            for k in range(2):
                sp.wait_ge(stored[k], 16 * NE // 2)

        @block.gpsimd
        def _(pool):
            def steps(t, s, n):
                pool.wait_ge(idx_done, n + 1)
                if not first(n, TURN):
                    pool.wait_ge(xt_mm, n - (TURN - 1))
                pool.wait_ge(ticked, n)
                pool.tensor_tensor(tick[:, :], M.slot_tok[0:1, 0:1], M.slot_tok[0:1, 0:1], ALU.add).then_inc(ticked, 1)
                pool.indirect_dma_start(out=xg[:, s, :], out_offset=None, in_=h,
                                        in_offset=bass.IndirectOffsetOnAxis(ap=idx[:, s:s + 1], axis=0)).then_inc(gathered[s], 16)
            turns(pool, steps)

        @block.tensor
        def _(pe):
            def tokens(t, s, n):
                pe.wait_ge(gathered[s], (t + 1) * 16)
                pe.wait_ge(x_act, n)
                pe.wait_ge(x_dve, n)
                for c in range(KC):
                    x = pe.transpose(ps_x[:, c // 4, (c % 4) * P:(c % 4 + 1) * P], xg[:, s, c::KC], M.ident[:, :])
                x.then_inc(xt_mm, 1)

            def gate_up(t, s, n, part):
                if part == 0:
                    pe.wait_ge(M.wgu_in[s], (t + 1) * 32)
                    pe.wait_ge(x_act, n + 1)
                    pe.wait_ge(x_dve, n + 1)
                    if not first(n, 2):
                        pe.wait_ge(a_done, n - 1)
                for c in range(4 * part, 4 * part + 4):
                    x = pe.matmul(ps_gu[:, s % 2, :], xT[:, s % 2, c, :], M.gu(s)[:, c, :], start=(c == 0), stop=(c == KC - 1))
                if part:
                    x.then_inc(gu_done, 1)

            def hidden(s, n):
                pe.wait_ge(a_done, n)
                if not first(n, 2):
                    pe.wait_ge(at_done, n - 1)
                for c in range(2):
                    x = pe.transpose(ps_a[:, c * P:(c + 1) * P], a_[:, (s - 1) % 2, c::2], M.ident[:, :])
                x.then_inc(at_mm, 1)

            def down(wd_count, s, n):
                k = (s - 1) % TURN
                pe.wait_ge(M.wd_in[k], wd_count * 16)
                pe.wait_ge(at_done, n)
                if not first(n, 2):
                    pe.wait_ge(y_act, n - 1)
                    pe.wait_ge(y_dve, n - 1)
                for half in range(2):
                    for c in range(2):
                        x = pe.matmul(ps_y[:, half, :], aT[:, k % 2, c, :], M.down(k)[:, c, half * 512:(half + 1) * 512], start=(c == 0), stop=(c == 1))
                x.then_inc(y_mm, 1)

            def steps(t, s, n):
                if not last(n, 1):
                    tokens(t + (s + 1) // TURN, (s + 1) % TURN, n + 1)
                gate_up(t, s, n, 0)
                if not first(n, 1):
                    hidden(s, n)
                gate_up(t, s, n, 1)
                if not first(n, 1):
                    down(t + 1 if s else t, s, n)

            tokens(0, 0, 0)
            turns(pe, steps)
            hidden(TURN, NE)
            down(NE // TURN, TURN, NE)

        @block.scalar
        def _(act):
            act.preload_act_table(ACT.Silu)

            def tokens(s, n):
                act.wait_ge(xt_mm, n + 1)
                if not first(n, 2):
                    act.wait_ge(gu_done, n - 1)
                act.activation(xT[:, s % 2, 0:4, :], ps_x[:, 0, :].rearrange("p (c t) -> p c t", c=4), ACT.Copy).then_inc(x_act, 1)

            def silu(s, n):
                act.wait_ge(gu_done, n + 1)
                if not first(n, 2):
                    act.wait_ge(a_done, n - 1)
                act.activation(sil[:, s % 2, :], ps_gu[:, s % 2, 0:FH], ACT.Silu).then_inc(sil_done, 1)

            def out(count, s, n):
                act.wait_ge(y_mm, n)
                if not first(n, 3):
                    act.wait_ge(stored[(s - 1) % 2], count * 16)
                act.activation(yo[:, (s - 1) % 2, 0:512], ps_y[:, 0, :], ACT.Copy).then_inc(y_act, 1)

            def steps(t, s, n):
                if not last(n, 1):
                    tokens(s + 1, n + 1)
                silu(s, n)
                if not first(n, 1):
                    out(t * 2 + (s - 1) // 2, s, n)

            tokens(0, 0)
            turns(act, steps)
            out(NE // 2 - 1, TURN, NE)

        @block.vector
        def _(dve):
            def index(t, s, n):
                if not first(n, TURN):
                    dve.wait_ge(gathered[s], t * 16)
                dve.tensor_scalar(idx[:, s:s + 1], M.slot_tok[:, bass.ds(n, 1)], 1.0, None, ALU.mult).then_inc(idx_done, 1)

            def tokens(s, n):
                dve.wait_ge(xt_mm, n + 1)
                if not first(n, 2):
                    dve.wait_ge(gu_done, n - 1)
                dve.tensor_copy(xT[:, s % 2, 4:8, :], ps_x[:, 1, :].rearrange("p (c t) -> p c t", c=4)).then_inc(x_dve, 1)

            def mult(s, n):
                dve.wait_ge(sil_done, n + 1)
                if not first(n, 2):
                    dve.wait_ge(at_mm, n - 1)
                dve.tensor_tensor(a_[:, s % 2, :], sil[:, s % 2, :], ps_gu[:, s % 2, FH:2 * FH], ALU.mult).then_inc(a_done, 1)

            def hidden(s, n):
                dve.wait_ge(at_mm, n)
                if not first(n, 3):
                    dve.wait_ge(y_mm, n - 2)
                dve.tensor_copy(aT[:, (s - 1) % 2, :, :], ps_a[:, 0:2 * P].rearrange("p (c t) -> p c t", c=2)).then_inc(at_done, 1)

            def out(count, s, n):
                dve.wait_ge(y_mm, n)
                if not first(n, 3):
                    dve.wait_ge(stored[(s - 1) % 2], count * 16)
                dve.tensor_copy(yo[:, (s - 1) % 2, 512:1024], ps_y[:, 1, :]).then_inc(y_dve, 1)

            def steps(t, s, n):
                if not last(n, AHEAD):
                    index(t + (s + AHEAD) // TURN, (s + AHEAD) % TURN, n + AHEAD)
                if not last(n, 1):
                    tokens(s + 1, n + 1)
                if not first(n, 1):
                    hidden(s, n)
                mult(s, n)
                if not first(n, 1):
                    out(t * 2 + (s - 1) // 2, s, n)

            for n in range(AHEAD):
                index(0, n, n)
            tokens(0, 0)
            turns(dve, steps)
            hidden(TURN, NE)
            out(NE // 2 - 1, TURN, NE)


def stage_spill(nc, M, h):
    with ExitStack() as ctx:
        m = Stage(nc, ctx, M.name + "s")
        xg = m.sb("xg", [P, D])
        xT = m.sb("xT", [P, KC, P])
        idx = m.sb("idx", [P, 1], I32)
        sil = m.sb("sil", [P, FH])
        a_ = m.sb("a", [P, FH])
        aT = m.sb("aT", [P, 2, P])
        yo = m.sb("yo", [P, D])
        tick = m.sb("tick", [1, 1])
        ps_x = m.ps("ps_x", [P, 2, 512])
        ps_gu = m.ps("ps_gu", [P, 512])
        ps_a = m.ps("ps_a", [P, 512])
        ps_y = m.ps("ps_y", [P, 2, 512])
        (w_in, idx_done, gathered, xt_mm, x_done, gu_done, sil_done, a_done, at_mm, at_done, y_mm, y_done, stored) = (m.sem(n) for n in
            "w_in idx_done gathered xt_mm x_done gu_done sil_done a_done at_mm at_done y_mm y_done stored".split())
        ticked = m.sem("ticked")
        last = m.sb("last", [1, 1])
        gu = M.gu(0)
        block = ctx.enter_context(nc.Block())

        def blocks(eng, body):
            n = eng.value_load(M.spill[0:1, 0:1], min_val=0, max_val=NSPILL)
            with eng.Fori(0, NSPILL) as b:
                with eng.If(b < n):
                    body(b)

        @block.sync
        def _(sp):
            def body(b):
                sp.wait_ge(y_mm, b)
                e = sp.value_load(M.spill[0:1, bass.ds(b + 1, 1)], min_val=0, max_val=NE - 1)
                for dst, w in ((gu[:, :, 0:FH], M.w_gate), (gu[:, :, FH:2 * FH], M.w_up), (M.down(0), M.w_down)):
                    sp.dma_start(dst, w[bass.ds(e, 1), :, :].rearrange("a (p c) f -> p (a c) f", p=P)).then_inc(w_in, 16)
                sp.wait_ge(y_done, b + 1)
                sp.dma_start(M.y[bass.ds(SPILL0 + b * CAP, CAP), :], yo[:, :]).then_inc(stored, 16)
            blocks(sp, body)

        @block.gpsimd
        def _(pool):
            def body(b):
                pool.wait_ge(idx_done, b + 1)
                pool.wait_ge(xt_mm, b)
                pool.wait_ge(ticked, b)
                pool.tensor_tensor(tick[:, :], M.slot_tok[0:1, 0:1], M.slot_tok[0:1, 0:1], ALU.add).then_inc(ticked, 1)
                pool.indirect_dma_start(out=xg[:, :], out_offset=None, in_=h,
                                        in_offset=bass.IndirectOffsetOnAxis(ap=idx[:, 0:1], axis=0)).then_inc(gathered, 16)
            blocks(pool, body)

        @block.tensor
        def _(pe):
            def body(b):
                pe.wait_ge(gathered, (b + 1) * 16)
                for c in range(KC):
                    x = pe.transpose(ps_x[:, c // 4, (c % 4) * P:(c % 4 + 1) * P], xg[:, c::KC], M.ident[:, :])
                x.then_inc(xt_mm, 1)
                pe.wait_ge(x_done, b + 1)
                pe.wait_ge(w_in, (b + 1) * 48)
                for c in range(KC):
                    x = pe.matmul(ps_gu[:, :], xT[:, c, :], gu[:, c, :], start=(c == 0), stop=(c == KC - 1))
                x.then_inc(gu_done, 1)
                pe.wait_ge(a_done, b + 1)
                for c in range(2):
                    x = pe.transpose(ps_a[:, c * P:(c + 1) * P], a_[:, c::2], M.ident[:, :])
                x.then_inc(at_mm, 1)
                pe.wait_ge(at_done, b + 1)
                for half in range(2):
                    for c in range(2):
                        x = pe.matmul(ps_y[:, half, :], aT[:, c, :], M.down(0)[:, c, half * 512:(half + 1) * 512], start=(c == 0), stop=(c == 1))
                x.then_inc(y_mm, 1)
            blocks(pe, body)

        @block.scalar
        def _(act):
            def body(b):
                act.wait_ge(gu_done, b + 1)
                act.activation(sil[:, :], ps_gu[:, 0:FH], ACT.Silu).then_inc(sil_done, 1)
            blocks(act, body)

        @block.vector
        def _(dve):
            def body(b):
                dve.wait_ge(gathered, b * 16)
                dve.tensor_scalar(idx[:, :], M.slot_tok[:, bass.ds(NE + b, 1)], 1.0, None, ALU.mult).then_inc(idx_done, 1)
                dve.wait_ge(xt_mm, b + 1)
                dve.tensor_copy(xT[:, :, :], ps_x[:, :, :].rearrange("p a (c t) -> p (a c) t", c=4)).then_inc(x_done, 1)
                dve.wait_ge(sil_done, b + 1)
                dve.tensor_tensor(a_[:, :], sil[:, :], ps_gu[:, FH:2 * FH], ALU.mult).then_inc(a_done, 1)
                dve.wait_ge(at_mm, b + 1)
                dve.tensor_copy(aT[:, :, :], ps_a[:, 0:2 * P].rearrange("p (c t) -> p c t", c=2)).then_inc(at_done, 1)
                dve.wait_ge(y_mm, b + 1)
                dve.tensor_copy(yo[:, :], ps_y[:, :, :].rearrange("p a b -> p (a b)")).then_inc(y_done, 1)
                dve.wait_ge(stored, (b + 1) * 16)
                dve.memset(last[:, :], 0.0)
            blocks(dve, body)


def stage_combine(nc, M, g, b, h_out):
    with ExitStack() as ctx:
        m = Stage(nc, ctx, M.name + "c")
        rows = m.sb("rows", [P, 2, TOPK, D])
        norm = Norm(m, "ln")
        acc_ready, dve_step, tile_done = (m.sem(n) for n in "acc_ready dve_step tile_done".split())
        rows_in = [m.sem(f"rows_in{k}") for k in range(2)]
        rows_read, stored = m.sem("rows_read"), m.sem("stored")
        block = ctx.enter_context(nc.Block())

        @block.gpsimd
        def _(pool):
            for i in range(NT):
                if i >= 2:
                    pool.wait_ge(rows_read, i - 1)
                for k in range(TOPK):
                    pool.indirect_dma_start(out=rows[:, i % 2, k, :], out_offset=None, in_=M.y,
                                            in_offset=bass.IndirectOffsetOnAxis(ap=M.dest[:, i, k:k + 1], axis=0)).then_inc(rows_in[i % 2], 16)

        @block.sync
        def _(sp):
            norm.load(sp, g, b)
            for i in range(NT):
                sp.wait_ge(tile_done, i + 1)
                sp.dma_start(h_out[i * P:(i + 1) * P, :], M.acc[:, i, :]).then_inc(stored, 16)
            sp.wait_ge(stored, 16 * NT)

        @block.scalar
        def _(act):
            for i in range(NT):
                norm.on_act(act, i)

        @block.vector
        def _(dve):
            step = [0]

            def then(ins):
                step[0] += 1
                ins.then_inc(dve_step, 1)
                dve.wait_ge(dve_step, step[0])

            for i in range(NT):
                y = M.acc[:, i, :]
                dve.wait_ge(rows_in[i % 2], 16 * TOPK * (i // 2 + 1))
                for k in range(TOPK):
                    x = dve.scalar_tensor_tensor(out=y, in0=rows[:, i % 2, k, :], scalar=M.gates[:, i, k:k + 1], in1=y, op0=ALU.mult, op1=ALU.add)
                    if k < TOPK - 1:
                        then(x)
                x.then_inc(rows_read, 1)
                dve.wait_ge(rows_read, i + 1)
                norm.on_dve(dve, then, y, i).then_inc(tile_done, 1)


def moe_layer(nc, name, y, h, weights, ln_g, ln_b, consts, h_out):
    router, bias, w_gate, w_up, w_down, sh_gate, sh_up, sh_down = weights
    with ExitStack() as ctx:
        M = Moe(nc, ctx, name, y, w_gate, w_up, w_down)
        stage_route(nc, M, h, router, bias, sh_gate, sh_up, sh_down, consts)
        stage_experts(nc, M, h)
        stage_spill(nc, M, h)
        stage_combine(nc, M, ln_g, ln_b, h_out)


def stage_ssm_input(nc, h, w_in, lam_re, lam_im, log_dt, b_re, b_im, c_ident, ident, e_y, uT, power, reverse, bbar, into):
    with ExitStack() as ctx:
        m = Stage(nc, ctx, "si")
        ht = m.sb("ht", [P, 2, D])
        hT = m.sb("hT", [P, 2, KC, P])
        w = m.sb("w", [P, KC, D])
        u = e_y[:, :].rearrange("p (g j h) -> p g j h", g=NG, j=L)
        lam = m.sb("lam", [NQ, 3, P])
        ldt = m.sb("ldt", [NQ, 2])
        lp = m.sb("lp", [P, 3, NQ])
        v = m.sb("v", [P, 12, NQ])
        b_ = m.sb("b", [P, 2, NQ, GC])
        g_ = m.sb("g", [P, 2, NQ, L, GC])
        room = into[:, :, :, :].rearrange("p q i s -> p (q i s)")
        tg = room[:, 0:NQ * L * GC].rearrange("p (q j h) -> p q j h", q=NQ, j=L)
        tb = room[:, NQ * L * GC:NQ * L * GC + 4 * NQ * GC].rearrange("p (k q h) -> p k q h", k=4, q=NQ)
        ps_t = m.ps("ps_t", [P, 2, 512])
        ps_u = m.ps("ps_u", [P, 4, 512])
        ps_l = m.ps("ps_l", [P, 3, NQ])
        (c_in, w_in_, transposed, t_copied, u_mm, u_done, g_t, g_act, g_dve) = (m.sem(n) for n in
            "c_in w_in transposed t_copied u_mm u_done g_t g_act g_dve".split())
        (lam_in, ldt_in, b_in, bcast, l_t, l_done, args, acts, into_ready, i_t, i_act, i_dve, dve_step) = (m.sem(n) for n in
            "lam_in ldt_in b_in bcast l_t l_done args acts into_ready i_t i_act i_dve dve_step".split())
        TWO_PI, MAGIC, EDGE = 2 * math.pi, 12582912.0, 3.1415925
        C1 = 6.28125
        C2 = float(np.float32(TWO_PI - C1))
        C3 = TWO_PI - C1 - C2
        h_in = [m.sem(f"h_in{k}") for k in range(2)]
        rows = h.rearrange("(c j) d -> j c d", j=L)
        block = ctx.enter_context(nc.Block())

        @block.sync
        def _(sp):
            sp.dma_start(ident[:, :], c_ident).then_inc(c_in, 16)
            for j in range(2):
                sp.dma_start(ht[:, j, :], rows[j]).then_inc(h_in[j], 16)
            sp.dma_start(lam[:, 0, :], lam_re.rearrange("(q two) p -> q (two p)", two=2)).then_inc(lam_in, 16)
            sp.dma_start(lam[:, 1, :], lam_im.rearrange("(q two) p -> q (two p)", two=2)).then_inc(lam_in, 16)
            sp.dma_start(ldt[:, :], log_dt.rearrange("(q two) -> q two", two=2)).then_inc(ldt_in, 16)
            sp.dma_start(w[:, :, :], w_in.rearrange("(c p) n -> p c n", p=P)).then_inc(w_in_, 16)
            for i, b in enumerate((b_re, b_im)):
                sp.dma_start(b_[:, i, :, :], b.rearrange("(q two) p h -> (two p) q h", two=2)).then_inc(b_in, 16)
            for j in range(2, L):
                sp.wait_ge(transposed, 2 * (j - 1))
                sp.dma_start(ht[:, j % 2, :], rows[j]).then_inc(h_in[j % 2], 16)

        @block.tensor
        def _(pe):
            def transposes(j):
                pe.wait_ge(h_in[j % 2], 16 * (j // 2 + 1))
                for half in range(2):
                    if j:
                        pe.wait_ge(t_copied, 2 * (j - 1) + half + 1)
                    for c in range(4):
                        x = pe.transpose(ps_t[:, half, c * P:(c + 1) * P], ht[:, j % 2, (4 * half + c) * P:(4 * half + c + 1) * P], ident[:, :])
                    x.then_inc(transposed, 1)

            pe.wait_ge(c_in, 16)
            transposes(0)
            pe.wait_ge(lam_in, 32)
            pe.wait_ge(bcast, 1)
            for k in range(3):
                x = pe.transpose(ps_l[:, k, :], lam[:, k, :], ident[0:NQ, 0:NQ])
            x.then_inc(l_t, 1)
            pe.wait_ge(w_in_, 16)
            for j in range(L):
                if j + 1 < L:
                    transposes(j + 1)
                pe.wait_ge(t_copied, 2 * (j + 1))
                if j >= 2:
                    pe.wait_ge(u_done, 2 * (j - 1))
                for half in range(2):
                    for c in range(KC):
                        x = pe.matmul(ps_u[:, 2 * (j % 2) + half, :], hT[:, j % 2, c, :], w[:, c, half * 512:(half + 1) * 512],
                                      start=(c == 0), stop=(c == KC - 1))
                    x.then_inc(u_mm, 1)
            pe.wait_ge(u_done, 2 * L)
            for n in range(NG // 4):
                if n >= 2:
                    pe.wait_ge((g_act, g_dve)[n % 2], n // 2)
                for k in range(4):
                    g = 4 * n + k
                    x = pe.transpose(ps_t[:, n % 2, k * P:(k + 1) * P], u[:, g, :, :].rearrange("p j h -> p (j h)"), ident[:, :])
                x.then_inc(g_t, 1)
            pe.wait_ge(into_ready, 1)
            for n in range(NQ // 2):
                if n >= 2:
                    pe.wait_ge((i_act, i_dve)[n % 2], n // 2)
                else:
                    pe.wait_ge((g_act, g_dve)[n % 2], NG // 8)
                for k in range(4):
                    x = pe.transpose(ps_t[:, n % 2, k * P:(k + 1) * P],
                                     g_[:, k % 2, 2 * n + k // 2, :, :].rearrange("p j h -> p (j h)"), ident[:, :])
                x.then_inc(i_t, 1)

        def u_out(act, n):
            act.wait_ge(u_mm, n + 1)
            j, half = n // 2, n % 2
            act.activation(u[:, half * NQ:(half + 1) * NQ, j, :], ps_u[:, 2 * (j % 2) + half, :].rearrange("p (g h) -> p g h", g=NQ), ACT.Copy).then_inc(u_done, 1)

        @block.scalar
        def _(act):
            act.wait_ge(ldt_in, 16)
            act.activation(lam[:, 2, :].rearrange("q (a p) -> q a p", a=2), ldt[:, :].unsqueeze(2).to_broadcast([NQ, 2, 64]), ACT.Copy).then_inc(bcast, 1)
            for j in range(L):
                for half in range(2):
                    act.wait_ge(transposed, 2 * j + half + 1)
                    if j >= 2:
                        act.wait_ge(u_mm, 2 * (j - 1))
                    act.activation(hT[:, j % 2, 4 * half:4 * half + 4, :], ps_t[:, half, :].rearrange("p (c t) -> p c t", c=4), ACT.Copy).then_inc(t_copied, 1)
                if j == 1:
                    act.wait_ge(l_done, 1)
                    act.activation(v[:, 0, :], lp[:, 2, :], ACT.Exp).then_inc(acts, 1)
                if j == 2:
                    act.wait_ge(args, 1)
                    act.activation(v[:, 3, :], v[:, 1, :], ACT.Exp).then_inc(acts, 1)
                    act.wait_ge(args, 2)
                    act.activation(v[:, 6, :], v[:, 4, :], ACT.Sin).then_inc(acts, 1)
                    act.activation(v[:, 7, :], v[:, 5, :], ACT.Sin).then_inc(acts, 1)
                for n in range(2 * (j - 1) if j else 0, 2 * j):
                    u_out(act, n)
            for n in range(2 * (L - 1), 2 * L):
                u_out(act, n)
            for n in range(0, NG // 4, 2):
                act.wait_ge(g_t, n + 1)
                act.activation(uT[:, 4 * n:4 * n + 4, :], ps_t[:, 0, :].rearrange("p (c t) -> p c t", c=4), ACT.Copy).then_inc(g_act, 1)
            for n in range(0, NQ // 2, 2):
                act.wait_ge(i_t, n + 1)
                act.activation(into[:, 2 * n:2 * n + 2, :, :], ps_t[:, 0, :].rearrange("p (q r s) -> p q r s", q=2, r=2), ACT.Copy).then_inc(i_act, 1)

        @block.vector
        def _(dve):
            step = [0]

            def then(ins):
                step[0] += 1
                ins.then_inc(dve_step, 1)
                dve.wait_ge(dve_step, step[0])

            dve.wait_ge(l_t, 1)
            dve.tensor_copy(lp[:, :, :], ps_l[:, :, :]).then_inc(l_done, 1)
            dve.wait_ge(l_done, 1)
            dve.wait_ge(acts, 1)
            lre, lim, dt = lp[:, 0, :], lp[:, 1, :], v[:, 0, :]
            dve.tensor_tensor(v[:, 1, :], lre, dt, ALU.mult).then_inc(args, 1)
            then(dve.tensor_tensor(v[:, 2, :], lim, dt, ALU.mult))
            for out, turn, shift in ((4, 0.0, 0.0), (5, 0.25, math.pi / 2)):
                k = v[:, 8, :]
                then(dve.tensor_scalar(k, v[:, 2, :], 1 / TWO_PI, turn, ALU.mult, ALU.add))
                then(dve.tensor_scalar(k, k, MAGIC, None, ALU.add))
                then(dve.tensor_scalar(k, k, MAGIC, None, ALU.subtract))
                then(dve.scalar_tensor_tensor(out=v[:, out, :], in0=k, scalar=-C1, in1=v[:, 2, :], op0=ALU.mult, op1=ALU.add))
                then(dve.scalar_tensor_tensor(out=v[:, out, :], in0=k, scalar=-C2, in1=v[:, out, :], op0=ALU.mult, op1=ALU.add))
                then(dve.scalar_tensor_tensor(out=v[:, out, :], in0=k, scalar=-C3, in1=v[:, out, :], op0=ALU.mult, op1=ALU.add))
                then(dve.tensor_scalar(v[:, out, :], v[:, out, :], shift, None, ALU.add))
                then(dve.tensor_scalar(v[:, out, :], v[:, out, :], -EDGE, None, ALU.max))
                x = dve.tensor_scalar(v[:, out, :], v[:, out, :], EDGE, None, ALU.min)
                if out == 4:
                    then(x)
            x.then_inc(args, 1)
            then(dve.memset(power[:, 0, 0, :], 1.0))
            then(dve.memset(power[:, 0, 1, :], 0.0))
            dve.wait_ge(acts, 4)
            ar, ai = power[:, 1, 0, :], power[:, 1, 1, :]
            then(dve.tensor_tensor(ar, v[:, 3, :], v[:, 7, :], ALU.mult))
            then(dve.tensor_tensor(ai, v[:, 3, :], v[:, 6, :], ALU.mult))
            t = [v[:, 4 + i, :] for i in range(4)]
            for n in range(2, L + 1):
                pr, pi = power[:, n - 1, 0, :], power[:, n - 1, 1, :]
                then(dve.tensor_tensor(t[0], pr, ar, ALU.mult))
                then(dve.tensor_tensor(t[1], pi, ai, ALU.mult))
                then(dve.tensor_tensor(t[2], pr, ai, ALU.mult))
                then(dve.tensor_tensor(t[3], pi, ar, ALU.mult))
                then(dve.tensor_tensor(power[:, n, 0, :], t[0], t[1], ALU.subtract))
                then(dve.tensor_tensor(power[:, n, 1, :], t[2], t[3], ALU.add))
            for n in range(L):
                then(dve.tensor_copy(reverse[:, L - 1 - n, :, :], power[:, n, :, :]))
            zr, zi = v[:, 10, :], v[:, 11, :]
            then(dve.tensor_tensor(t[0], lre, lre, ALU.mult))
            then(dve.tensor_tensor(t[1], lim, lim, ALU.mult))
            then(dve.tensor_tensor(t[0], t[0], t[1], ALU.add))
            then(dve.reciprocal(v[:, 8, :], t[0]))
            then(dve.tensor_scalar(v[:, 9, :], ar, -1.0, None, ALU.add))
            then(dve.tensor_tensor(t[0], v[:, 9, :], lre, ALU.mult))
            then(dve.tensor_tensor(t[1], ai, lim, ALU.mult))
            then(dve.tensor_tensor(t[2], ai, lre, ALU.mult))
            then(dve.tensor_tensor(t[3], v[:, 9, :], lim, ALU.mult))
            then(dve.tensor_tensor(zr, t[0], t[1], ALU.add))
            then(dve.tensor_tensor(zi, t[2], t[3], ALU.subtract))
            then(dve.tensor_tensor(zr, zr, v[:, 8, :], ALU.mult))
            then(dve.tensor_tensor(zi, zi, v[:, 8, :], ALU.mult))
            dve.wait_ge(b_in, 32)
            zr_, zi_ = (z.unsqueeze(2).to_broadcast([P, NQ, GC]) for z in (zr, zi))
            then(dve.tensor_tensor(tb[:, 0, :, :], b_[:, 0, :, :], zr_, ALU.mult))
            then(dve.tensor_tensor(tb[:, 1, :, :], b_[:, 1, :, :], zi_, ALU.mult))
            then(dve.tensor_tensor(tb[:, 2, :, :], b_[:, 1, :, :], zr_, ALU.mult))
            then(dve.tensor_tensor(tb[:, 3, :, :], b_[:, 0, :, :], zi_, ALU.mult))
            then(dve.tensor_tensor(bbar[:, 0, :, :], tb[:, 0, :, :], tb[:, 1, :, :], ALU.subtract))
            then(dve.tensor_tensor(bbar[:, 1, :, :], tb[:, 2, :, :], tb[:, 3, :, :], ALU.add))
            wide = [P, NQ, L, GC]
            br, bi = (bbar[:, i, :, :].unsqueeze(2).to_broadcast(wide) for i in range(2))
            rr, ri = (reverse[:, :, i, :].rearrange("p j q -> p q j").unsqueeze(3).to_broadcast(wide) for i in range(2))
            gr, gi = g_[:, 0, :, :, :], g_[:, 1, :, :, :]
            then(dve.tensor_tensor(gr, br, rr, ALU.mult))
            then(dve.tensor_tensor(tg, bi, ri, ALU.mult))
            then(dve.tensor_tensor(gr, gr, tg, ALU.subtract))
            then(dve.tensor_tensor(gi, br, ri, ALU.mult))
            then(dve.tensor_tensor(tg, bi, rr, ALU.mult))
            dve.tensor_tensor(gi, gi, tg, ALU.add).then_inc(into_ready, 1)
            for n in range(1, NG // 4, 2):
                dve.wait_ge(g_t, n + 1)
                dve.tensor_copy(uT[:, 4 * n:4 * n + 4, :], ps_t[:, 1, :].rearrange("p (c t) -> p c t", c=4)).then_inc(g_dve, 1)
            for n in range(1, NQ // 2, 2):
                dve.wait_ge(i_t, n + 1)
                dve.tensor_copy(into[:, 2 * n:2 * n + 2, :, :], ps_t[:, 1, :].rearrange("p (q r s) -> p q r s", q=2, r=2)).then_inc(i_dve, 1)


def stage_ssm_kernel(nc, c_re, c_im, d_skip, diag16, ident, power, bbar, out_of, inside, e_y):
    with ExitStack() as ctx:
        m = Stage(nc, ctx, "sk")
        c_ = m.sb("c", [P, 2, 8, P])
        cT = m.sb("cT", [P, 2, NQ, GC])
        tv = inside[:, :, :, :].rearrange("p q a t -> p (q a t)")[:, 0:NQ * (L + 1) * GC].rearrange("p (q t h) -> p q t h", q=NQ, t=L + 1)
        bpad = m.sb("bpad", [P, 2, NQ, 2, GC])
        taps = e_y[0:2 * GC, :].rearrange("p (q t) -> p q t", q=NQ)
        dT = m.sb("dT", [2 * GC, NQ])
        dg = m.sb("dg", [2 * GC, GC])
        dd = m.sb("dd", [2 * GC, NQ, GC])
        ps_c = m.ps("ps_c", [P, 2, S])
        ps_k = m.ps("ps_k", [2 * GC, 2, 512])
        (c_in, d_in, c_t, c_done, v_done, pad_done, pads, k_mm, k_done, taps_done, moved, dve_step) = (m.sem(n) for n in
            "c_in d_in c_t c_done v_done pad_done pads k_mm k_done taps_done moved dve_step".split())
        block = ctx.enter_context(nc.Block())

        @block.sync
        def _(sp):
            for i, c in enumerate((c_re, c_im)):
                for two in range(2):
                    sp.dma_start(c_[:, i, :, two * 64:(two + 1) * 64],
                                 c.rearrange("(n g) h p -> (g h) n p", n=8)).then_inc(c_in, 16)
            with nc.allow_non_contiguous_dma(reason="1024 elements"):
                sp.dma_start(dT[:, :], d_skip.rearrange("(q two) h -> (two h) q", two=2)).then_inc(d_in, 16)
            sp.dma_start(dg[:, :], diag16).then_inc(d_in, 16)
            sp.wait_ge(taps_done, 1)
            for i in range(L):
                for two in range(2):
                    sp.dma_start(inside[i * GC:(i + 1) * GC, :, two, :],
                                 taps[two * GC:(two + 1) * GC, :, (L - i) * GC:(L - i) * GC + P]).then_inc(moved, 16)
            sp.wait_ge(moved, 16 * 2 * L)

        @block.gpsimd
        def _(pool):
            pool.memset(bpad[:, :, :, :, :], 0.0).then_inc(pads, 1)
            pool.memset(taps[:, :, 0:P], 0.0).then_inc(pads, 1)
            pool.wait_ge(pads, 2)
            for two in range(2):
                h = slice(two * 64, two * 64 + 64)
                x = pool.tensor_copy(bpad[h, :, :, two, :], bbar[h, :, :, :])
            x.then_inc(pad_done, 1)

        @block.tensor
        def _(pe):
            pe.wait_ge(c_in, 16 * 4)
            for i in range(2):
                for n in range(8):
                    x = pe.transpose(ps_c[:, i, n * P:(n + 1) * P], c_[:, i, n, :], ident[:, :])
            x.then_inc(c_t, 1)
            pe.wait_ge(v_done, 1)
            pe.wait_ge(pad_done, 1)
            for n in range(NQ // 4):
                if n >= 2:
                    pe.wait_ge(k_done, n - 1)
                for k in range(4):
                    q = 4 * n + k
                    for i in range(2):
                        x = pe.matmul(ps_k[:, n % 2, k * P:(k + 1) * P], bpad[:, i, q, :, :].rearrange("p a h -> p (a h)"),
                                      out_of[:, i, q, 0:L, :].rearrange("p t h -> p (t h)"), start=(i == 0), stop=(i == 1), skip_group_check=True)
                x.then_inc(k_mm, 1)

        @block.scalar
        def _(act):
            act.wait_ge(c_t, 1)
            for i in range(2):
                for two in range(2):
                    half = slice(two * 64, (two + 1) * 64)
                    x = act.activation(cT[half, i, :, :], ps_c[half, i, :].rearrange("p (q a h) -> p q a h", q=NQ, a=2)[:, :, two, :], ACT.Copy)
            x.then_inc(c_done, 1)
            for n in range(NQ // 4):
                act.wait_ge(k_mm, n + 1)
                act.activation(taps[:, 4 * n:4 * n + 4, P:2 * P], ps_k[:, n % 2, :].rearrange("p (q t) -> p q t", q=4), ACT.Copy).then_inc(k_done, 1)

        @block.vector
        def _(dve):
            step = [0]

            def then(ins):
                step[0] += 1
                ins.then_inc(dve_step, 1)
                dve.wait_ge(dve_step, step[0])

            dve.wait_ge(c_done, 1)
            wide = [P, NQ, L + 1, GC]
            cr, ci = (cT[:, i, :, :].unsqueeze(2).to_broadcast(wide) for i in range(2))
            ar, ai = (power[:, :, i, :].rearrange("p t q -> p q t").unsqueeze(3).to_broadcast(wide) for i in range(2))
            then(dve.tensor_tensor(out_of[:, 0, :, :, :], cr, ar, ALU.mult))
            then(dve.tensor_tensor(tv[:, :, :, :], ci, ai, ALU.mult))
            then(dve.tensor_tensor(out_of[:, 0, :, :, :], out_of[:, 0, :, :, :], tv[:, :, :, :], ALU.subtract))
            then(dve.tensor_tensor(out_of[:, 1, :, :, :], cr, ai, ALU.mult))
            then(dve.tensor_tensor(tv[:, :, :, :], ci, ar, ALU.mult))
            then(dve.scalar_tensor_tensor(out=out_of[:, 1, :, :, :].rearrange("p q t h -> p (q t h)"), in0=out_of[:, 1, :, :, :].rearrange("p q t h -> p (q t h)"),
                                          scalar=-1.0, in1=tv[:, :, :, :].rearrange("p q t h -> p (q t h)"), op0=ALU.mult, op1=ALU.subtract))
            dve.engine_nop().then_inc(v_done, 1)
            dve.wait_ge(d_in, 32)
            then(dve.tensor_tensor(dd[:, :, :], dT[:, :].unsqueeze(2).to_broadcast([2 * GC, NQ, GC]), dg[:, :].unsqueeze(1).to_broadcast([2 * GC, NQ, GC]), ALU.mult))
            dve.wait_ge(k_done, NQ // 4)
            dve.wait_ge(pads, 2)
            dve.tensor_tensor(taps[:, :, P:P + GC], taps[:, :, P:P + GC], dd[:, :, :], ALU.add).then_inc(taps_done, 1)


def complex_product(dve, then, out, x, y, t):
    dve.tensor_tensor(t[0], x[0], y[0], ALU.mult)
    dve.tensor_tensor(t[1], x[1], y[1], ALU.mult)
    dve.tensor_tensor(t[2], x[0], y[1], ALU.mult)
    then(dve.tensor_tensor(t[3], x[1], y[0], ALU.mult))
    dve.tensor_tensor(out[0], t[0], t[1], ALU.subtract)
    then(dve.tensor_tensor(out[1], t[2], t[3], ALU.add))


def stage_ssm_scan(nc, uT, power, powers, into, out_of, inside, e_y):
    with ExitStack() as ctx:
        m = Stage(nc, ctx, "sc")
        K = 16
        B = NC // K
        QG = 8
        st = m.sb("st", [P, NC, 2, NQ])
        mul = m.sb("mul", [P, 2, 2, NQ])
        room = into[:, :, :, :].rearrange("p q i s -> p (q i s)")
        tmp = room[:, 0:2 * B * 2 * NQ].rearrange("p (k b s) -> p k b s", k=2, b=B)
        ends = room[:, 1024:1024 + B * 2 * NQ].rearrange("p (b s) -> p b s", b=B)
        terms = [room[:, 2048 + n * B * (K - 1) * QG:2048 + (n + 1) * B * (K - 1) * QG].rearrange("p (b k q) -> p b k q", b=B, q=QG) for n in range(4)]
        ps_e = m.ps("ps_e", [P, 4, 512])
        ps_y = m.ps("ps_y", [P, 4, 512])
        (e_mm, e_act, e_dve, carried, y_mm, y_done, dve_step, sweep_step) = (m.sem(n) for n in
            "e_mm e_act e_dve carried y_mm y_done dve_step sweep_step".split())
        e = e_y[:, :].rearrange("p (c i q) -> p c i q", i=2, q=NQ)
        y = e_y[:, :].rearrange("p (j d) -> p j d", j=L)
        block = ctx.enter_context(nc.Block())

        @block.tensor
        def _(pe):
            for n in range(NQ // 2):
                if n >= 4:
                    pe.wait_ge((e_act, e_dve)[n % 2], (n - 4) // 2 + 1)
                for k in range(4):
                    q, i = 2 * n + k // 2, k % 2
                    for two in range(2):
                        x = pe.matmul(ps_e[two * 64:(two + 1) * 64, n % 4, k * P:(k + 1) * P], into[:, q, i, two * 64:(two + 1) * 64],
                                      uT[:, 2 * q + two, :], start=True, stop=True, skip_group_check=True)
                x.then_inc(e_mm, 1)
            for n in range(NG // 4):
                two = n % 2
                if n % 4 == 0:
                    pe.wait_ge(carried, n // 4 + 1)
                if n == 0:
                    pe.wait_ge(e_act, NQ // 4)
                half = slice(two * 64, (two + 1) * 64)
                if n >= 4:
                    pe.wait_ge(y_done, n - 3)
                for k in range(4):
                    q = 4 * (n // 2) + k
                    o = ps_y[:, n % 4, k * P:(k + 1) * P]
                    pe.matmul(o, uT[:, 2 * q + two, :], inside[:, q, two, :], start=True, stop=False, skip_group_check=True)
                    for i in range(2):
                        x = pe.matmul(o, st[half, 0:NC, i, q], out_of[half, i, q, 1:L + 1, :].rearrange("p t h -> p (t h)"),
                                      start=False, stop=(i == 1), skip_group_check=True)
                x.then_inc(y_mm, 1)

        def copy_e(eng, n, sem):
            eng.wait_ge(e_mm, n + 1)
            out = e[:, :, :, 2 * n:2 * n + 2].rearrange("p c i q -> p q i c")
            src = ps_e[:, n % 4, :].rearrange("p (q i c) -> p q i c", q=2, i=2)
            (eng.activation(out, src, ACT.Copy) if sem is e_act else eng.tensor_copy(out, src)).then_inc(sem, 1)

        @block.scalar
        def _(act):
            for n in range(0, NQ // 2, 2):
                copy_e(act, n, e_act)
            for n in range(NG // 4):
                act.wait_ge(y_mm, n + 1)
                two = n % 2
                out = y.rearrange("p j (q g) -> p q j g", g=2 * GC)[:, 4 * (n // 2):4 * (n // 2) + 4, :, two * GC:(two + 1) * GC]
                act.activation(out, ps_y[:, n % 4, :].rearrange("p (q j h) -> p q j h", q=4, j=L), ACT.Gelu_apprx_tanh).then_inc(y_done, 1)

        @block.vector
        def _(dve):
            step = [0]

            def then(ins):
                step[0] += 1
                ins.then_inc(dve_step, 1)
                dve.wait_ge(dve_step, step[0])

            dve.memset(st[:, :, :, :].rearrange("p (b k) i q -> p b k (i q)", k=K)[:, :, 0, :], 0.0)
            dve.tensor_copy(mul[:, 0, 0, :], power[:, L, 0, :])
            dve.tensor_copy(mul[:, 0, 1, :], power[:, L, 0, :])
            dve.tensor_copy(mul[:, 1, 0, :], power[:, L, 1, :])
            dve.tensor_scalar(mul[:, 1, 1, :], power[:, L, 1, :], -1.0, None, ALU.mult)
            dve.tensor_copy(powers[:, 0, 0, :], power[:, L, 0, :])
            then(dve.tensor_copy(powers[:, 0, 1, :], power[:, L, 1, :]))
            for n in range(1, NQ // 2, 2):
                copy_e(dve, n, e_dve)
            dve.wait_ge(e_act, NQ // 4)
            dve.wait_ge(e_dve, NQ // 4)
            n = 1
            while n < K:
                wide = [P, n, NQ]
                top = [powers[:, n - 1, i, :].unsqueeze(1).to_broadcast(wide) for i in range(2)]
                t = [room[:, 2048 + k * 512:2048 + k * 512 + n * NQ].rearrange("p (k q) -> p k q", q=NQ) for k in range(4)]
                complex_product(dve, then, [powers[:, n:2 * n, i, :] for i in range(2)], [powers[:, 0:n, i, :] for i in range(2)], top, t)
                n *= 2
            state = st[:, :, :, :].rearrange("p (b k) i q -> p b k (i q)", k=K)
            own = e_y[:, :].rearrange("p (b k s) -> p b k s", b=B, k=K)
            m0, m1 = (mul[:, k, :, :].rearrange("p i q -> p (i q)").unsqueeze(1).to_broadcast([P, B, 2 * NQ]) for k in range(2))
            t0, t1 = tmp[:, 0, :, :], tmp[:, 1, :, :]
            dve.tensor_copy(state[:, :, 1, :], own[:, :, 0, :]).then_inc(sweep_step, 3)

            def advance(k, now, mine, new):
                dve.wait_ge(sweep_step, k * 3)
                dve.tensor_tensor(t0, now, m0, ALU.mult)
                dve.tensor_tensor(t1, now, m1, ALU.mult).then_inc(sweep_step, 1)
                dve.wait_ge(sweep_step, k * 3 + 1)
                dve.tensor_tensor(t0, t0, mine, ALU.add).then_inc(sweep_step, 1)
                dve.wait_ge(sweep_step, k * 3 + 2)
                dve.tensor_tensor(new[:, :, 0:NQ], t0[:, :, 0:NQ], t1[:, :, NQ:2 * NQ], ALU.add)
                dve.tensor_tensor(new[:, :, NQ:2 * NQ], t0[:, :, NQ:2 * NQ], t1[:, :, 0:NQ], ALU.add).then_inc(sweep_step, 1)

            def at(x, k):
                return x[:, :, bass.ds(k, 1), :].rearrange("p b a s -> p b (a s)")

            with dve.Fori(1, K - 1) as k:
                advance(k, at(state, k), at(own, k), at(state, k + 1))
            advance(K - 1, state[:, :, K - 1, :], own[:, :, K - 1, :], ends)
            dve.wait_ge(sweep_step, 3 * K)
            first = st[:, :, :, :].rearrange("p (b k) i q -> p b k i q", k=K)[:, :, 0, :, :]
            end = ends.rearrange("p b (i q) -> p b i q", i=2)
            whole = [powers[:, K - 1, i, :] for i in range(2)]
            then(dve.tensor_copy(first[:, 1, :, :], end[:, 0, :, :]))
            for b in range(1, B - 1):
                cr, ci = first[:, b, 0, :], first[:, b, 1, :]
                t = [room[:, 2048 + k * NQ:2048 + (k + 1) * NQ] for k in range(4)]
                dve.tensor_tensor(t[0], cr, whole[0], ALU.mult)
                dve.tensor_tensor(t[1], ci, whole[1], ALU.mult)
                dve.tensor_tensor(t[2], cr, whole[1], ALU.mult)
                then(dve.tensor_tensor(t[3], ci, whole[0], ALU.mult))
                dve.tensor_tensor(t[0], t[0], t[1], ALU.subtract)
                then(dve.tensor_tensor(t[2], t[2], t[3], ALU.add))
                dve.tensor_tensor(first[:, b + 1, 0, :], end[:, b, 0, :], t[0], ALU.add)
                then(dve.tensor_tensor(first[:, b + 1, 1, :], end[:, b, 1, :], t[2], ALU.add))
            wide = [P, B, K - 1, QG]
            for part in range(NQ // QG):
                qs = slice(part * QG, (part + 1) * QG)
                cr, ci = (first[:, :, i, qs].unsqueeze(2).to_broadcast(wide) for i in range(2))
                pr, pi = (powers[:, 0:K - 1, i, qs].unsqueeze(1).to_broadcast(wide) for i in range(2))
                sr, si = (st[:, :, i, qs].rearrange("p (b k) q -> p b k q", k=K)[:, :, 1:K, :] for i in range(2))
                dve.tensor_tensor(terms[0], cr, pr, ALU.mult)
                dve.tensor_tensor(terms[1], ci, pi, ALU.mult)
                dve.tensor_tensor(terms[2], cr, pi, ALU.mult)
                then(dve.tensor_tensor(terms[3], ci, pr, ALU.mult))
                dve.tensor_tensor(sr, sr, terms[0], ALU.add)
                then(dve.tensor_tensor(si, si, terms[2], ALU.add))
                dve.tensor_tensor(sr, sr, terms[1], ALU.subtract)
                dve.tensor_tensor(si, si, terms[3], ALU.add).then_inc(carried, 1)
                dve.wait_ge(carried, part + 1)


def stage_ssm_out(nc, h, w_glu, w_out, g, b, ident, e_y, h_out):
    with ExitStack() as ctx:
        m = Stage(nc, ctx, "so")
        y = e_y[:, :].rearrange("p (j d) -> p j d", j=L)
        w = m.sb("w", [P, 2, KC, D])
        yT = m.sb("yT", [P, KC, S])
        sg = m.sb("sg", [P, 2, 512])
        o_ = m.sb("o", [P, 2, D])
        z = m.sb("z", [P, KC, 512])
        hr = m.sb("hr", [P, 2, D])
        norm = Norm(m, "ln")
        ps_t = m.ps("ps_t", [P, 2, 512])
        ps_z = m.ps("ps_z", [P, 2, 512])
        ps_o = m.ps("ps_o", [P, 2, D])
        (wg_in, wo_in, transposed, t_act, t_dve, z_mm, sig_done, z_done, o_mm, o_read, o_ready, dve_step) = (m.sem(n) for n in
            "wg_in wo_in transposed t_act t_dve z_mm sig_done z_done o_mm o_read o_ready dve_step".split())
        h_in = [m.sem(f"h_in{k}") for k in range(2)]
        stored = [m.sem(f"stored{k}") for k in range(2)]
        rows = h.rearrange("(c j) d -> j c d", j=L)
        out_rows = h_out.rearrange("(c j) d -> j c d", j=L)
        block = ctx.enter_context(nc.Block())

        @block.sync
        def _(sp):
            sp.dma_start(w[:, 0, :, :], w_glu.rearrange("(c p) n -> p c n", p=P)).then_inc(wg_in, 16)
            sp.dma_start(w[:, 1, :, :], w_out.rearrange("(c p) n -> p c n", p=P)).then_inc(wo_in, 16)
            norm.load(sp, g, b)
            for j in range(L):
                if j >= 2:
                    sp.wait_ge(o_read, j - 1)
                sp.dma_start(hr[:, j % 2, :], rows[j]).then_inc(h_in[j % 2], 16)
                if j:
                    sp.wait_ge(o_ready, j)
                    sp.dma_start(out_rows[j - 1], o_[:, (j - 1) % 2, :]).then_inc(stored[(j - 1) % 2], 16)
            sp.wait_ge(o_ready, L)
            sp.dma_start(out_rows[L - 1], o_[:, (L - 1) % 2, :]).then_inc(stored[(L - 1) % 2], 16)
            for k in range(2):
                sp.wait_ge(stored[k], 16 * L // 2)

        @block.tensor
        def _(pe):
            for n in range(2 * L):
                j, c0 = n // 2, 4 * (n % 2)
                if n >= 2:
                    pe.wait_ge((t_act, t_dve)[n % 2], n // 2)
                for c in range(4):
                    x = pe.transpose(ps_t[:, n % 2, c * P:(c + 1) * P], y[:, j, (c0 + c) * P:(c0 + c + 1) * P], ident[:, :])
                x.then_inc(transposed, 1)
            pe.wait_ge(wg_in, 16)
            pe.wait_ge(t_act, L)
            pe.wait_ge(t_dve, L)
            for half in range(2):
                for f in range(KC):
                    u = half * KC + f
                    if u >= 2:
                        pe.wait_ge(sig_done, u - 1)
                    for c in range(KC):
                        x = pe.matmul(ps_z[:, u % 2, :], w[:, 0, c, f * P:(f + 1) * P], yT[:, c, half * 512:(half + 1) * 512], start=(c == 0), stop=(c == KC - 1))
                    x.then_inc(z_mm, 1)
                pe.wait_ge(z_done, (half + 1) * KC)
                pe.wait_ge(wo_in, 16)
                for jj in range(4):
                    j = half * 4 + jj
                    if j >= 2:
                        pe.wait_ge(o_read, j - 1)
                    for oh in range(2):
                        for c in range(KC):
                            x = pe.matmul(ps_o[:, j % 2, oh * 512:(oh + 1) * 512], z[:, c, jj * P:(jj + 1) * P], w[:, 1, c, oh * 512:(oh + 1) * 512],
                                          start=(c == 0), stop=(c == KC - 1))
                    x.then_inc(o_mm, 1)

        @block.scalar
        def _(act):
            for j in range(L):
                act.wait_ge(transposed, 2 * j + 1)
                act.activation(yT[:, 0:4, j * P:(j + 1) * P], ps_t[:, 0, :].rearrange("p (c t) -> p c t", c=4), ACT.Copy).then_inc(t_act, 1)
            for half in range(2):
                for f in range(KC):
                    u = half * KC + f
                    act.wait_ge(z_mm, u + 1)
                    if u >= 2:
                        act.wait_ge(z_done, u - 1)
                    act.activation(sg[:, u % 2, :], ps_z[:, u % 2, :], ACT.Sigmoid).then_inc(sig_done, 1)
                for jj in range(4):
                    norm.on_act(act, half * 4 + jj)

        @block.vector
        def _(dve):
            step = [0]

            def then(ins):
                step[0] += 1
                ins.then_inc(dve_step, 1)
                dve.wait_ge(dve_step, step[0])

            for j in range(L):
                dve.wait_ge(transposed, 2 * j + 2)
                dve.tensor_copy(yT[:, 4:8, j * P:(j + 1) * P], ps_t[:, 1, :].rearrange("p (c t) -> p c t", c=4)).then_inc(t_dve, 1)
            dve.wait_ge(t_act, L)
            dve.wait_ge(t_dve, L)
            for half in range(2):
                if half:
                    dve.wait_ge(o_mm, 4)
                for f in range(KC):
                    u = half * KC + f
                    dve.wait_ge(sig_done, u + 1)
                    dve.tensor_tensor(z[:, f, :], sg[:, u % 2, :], yT[:, f, half * 512:(half + 1) * 512], ALU.mult).then_inc(z_done, 1)
                for jj in range(4):
                    j = half * 4 + jj
                    dve.wait_ge(o_mm, j + 1)
                    dve.wait_ge(h_in[j % 2], 16 * (j // 2 + 1))
                    if j >= 2:
                        dve.wait_ge(stored[j % 2], 16 * (j // 2))
                    oo = o_[:, j % 2, :]
                    dve.scalar_tensor_tensor(out=oo, in0=hr[:, j % 2, :], scalar=ALPHA, in1=ps_o[:, j % 2, :], op0=ALU.mult, op1=ALU.add).then_inc(o_read, 1)
                    dve.wait_ge(o_read, j + 1)
                    norm.on_dve(dve, then, oo, j).then_inc(o_ready, 1)


def ssm_layer(nc, h, w, ln_g, ln_b, consts, h_out):
    w_in, lam_re, lam_im, b_re, b_im, c_re, c_im, d_skip, log_dt, w_glu, w_out = w
    with ExitStack() as outer:
        m = Stage(nc, outer, "ss")
        ident = m.sb("ident", [P, P])
        e_y = m.sb("e_y", [P, L * D])
        with ExitStack() as ctx:
            k = Stage(nc, ctx, "sb_")
            uT = k.sb("uT", [P, NG, NC])
            power = k.sb("power", [P, L + 1, 2, NQ])
            bbar = k.sb("bbar", [P, 2, NQ, GC])
            into = k.sb("into", [P, NQ, 2, P])
            with ExitStack() as c2:
                reverse = Stage(nc, c2, "sr").sb("reverse", [P, L, 2, NQ])
                stage_ssm_input(nc, h, w_in, lam_re, lam_im, log_dt, b_re, b_im, consts["c_ident"], ident, e_y, uT, power, reverse, bbar, into)
            out_of = k.sb("out_of", [P, 2, NQ, L + 1, GC])
            inside = k.sb("inside", [P, NQ, 2, P])
            stage_ssm_kernel(nc, c_re, c_im, d_skip, consts["c_diag16"], ident, power, bbar, out_of, inside, e_y)
            stage_ssm_scan(nc, uT, power, bbar[:, :, :, :].rearrange("p a q h -> p (a q h)").rearrange("p (k i q) -> p k i q", i=2, q=NQ), into, out_of, inside, e_y)
        stage_ssm_out(nc, h, w_glu, w_out, ln_g, ln_b, ident, e_y, h_out)


def trunk(nc, a, consts, out):
    after = [nc.dram_tensor(f"h{n}", (S, D), F32, kind="Internal").ap() for n in range(3)]
    expert_rows = nc.dram_tensor("expert_rows", (NBLK * CAP, D), F32, kind="Internal").ap()
    x = a["x"].rearrange("b s d -> (b s) d")

    def layer(n, names):
        return [a[f"l{n}_{k}"] for k in names.split()]

    moe_names = "router router_bias w_gate w_up w_down sh_gate sh_up sh_down"
    with ExitStack() as ctx:
        keep = keep_attention(nc, ctx)
        stage_project(nc, x, a["l0_w_in"], consts["c_cos"], consts["c_sin"], consts["c_ident"], keep)
        stage_stick(nc, consts["c_stick"], expert_rows, keep)
        stage_compress(nc, *layer(0, "cmp_pos_k cmp_pos_v cmp_k_w1 cmp_k_w2 cmp_v_w1 cmp_v_w2"), consts["c_cmp"], consts["c_imp"], keep)
        stage_selected(nc, consts["c_win"], keep)
        stage_attention_out(nc, a["l0_w_out"], x, a["l0_ln1_g"], a["l0_ln1_b"], keep, after[0])
    moe_layer(nc, "m0", expert_rows, after[0], layer(0, moe_names), a["l0_ln2_g"], a["l0_ln2_b"], consts, after[1])
    ssm_layer(nc, after[1], layer(1, "w_in lambda_re lambda_im b_re b_im c_re c_im d log_dt w_glu w_out"),
              a["l1_ln1_g"], a["l1_ln1_b"], consts, after[2])
    moe_layer(nc, "m1", expert_rows, after[2], layer(1, moe_names), a["l1_ln2_g"], a["l1_ln2_b"], consts, out)


def kernel(**inputs):
    import concourse.bacc as _bacc
    from concourse.bass_utils import run_bass_kernel_spmd as _run

    nc = _bacc.Bacc("TRN2", target_bir_lowering=False, num_devices=1)
    arrays, tensors, consts = {}, {}, {}
    for name, array in inputs.items():
        array = np.ascontiguousarray(array)
        arrays[f"in_{name}"] = array
        tensors[name] = nc.dram_tensor(f"in_{name}", array.shape, mybir.dt.from_np(array.dtype), kind="ExternalInput").ap()
    for name, array in const_arrays().items():
        arrays[name] = array
        consts[name] = nc.dram_tensor(name, array.shape, F32, kind="ExternalInput").ap()
    out = nc.dram_tensor("out_0", (1, S, D), F32, kind="ExternalOutput").ap()
    trunk(nc, tensors, consts, out.rearrange("b s d -> (b s) d"))
    result = _run(nc, [arrays], core_ids=[0])
    return result.results[0]["out_0"]
```

```python
import math
from contextlib import ExitStack

import numpy as np

import concourse.bass as bass
from concourse import mybir

F32 = mybir.dt.float32
I32 = mybir.dt.int32
U32 = mybir.dt.uint32
ALU = mybir.AluOpType
ACT = mybir.ActivationFunctionType
AX = mybir.AxisListType.X

P = 128
D = 1024
S = 1024
NT = S // P
KC = D // P
HD = 64
N_IN = 2840
NCMP = 63
NSEL = 16
FAR = -3.0e38
L = 8
NC = S // L
NG = 64
NQ = NG // 2
GC = 16
NE = 64
TOPK = 6
CAP = P
NSPILL = S * TOPK // CAP
SPILL0 = NE * CAP
NBLK = NE + NSPILL
FH = 256
ALPHA = 4 ** 0.25
LN_EPS = 1e-5
NEG = -1e30


def const_arrays():
    c = {}
    c["c_ident"] = np.eye(P, dtype=np.float32)
    inv = np.power(np.float32(500000.0), -np.arange(0, 16, 2, dtype=np.float32) / np.float32(16))
    ang = np.arange(S, dtype=np.float32)[:, None] * inv[None, :].astype(np.float32)
    rotated = np.array([1] * 10 + [0, 0] + [1, 1] + [0, 0] + [1, 1] + [0, 0], np.float32)[None, :, None]
    cos, sin = np.cos(ang)[:, None, :], np.sin(ang)[:, None, :]
    c["c_cos"] = (cos * rotated + (1 - rotated)).astype(np.float32)
    c["c_sin"] = (sin * rotated).astype(np.float32)
    k, q = np.arange(P)[:, None], np.arange(P)[None, :]
    c["c_stick"] = np.stack([np.where(k > q, -1.0, 0.0), np.where(k <= q, -1.0, 0.0),
                             np.where(k < q, 1.0, 0.0), np.where(k < q, 0.0, NEG)], 1).astype(np.float32)
    t = np.arange(S)
    seen = (np.arange(NCMP) * 16 + 31)[None, :] <= t[:, None]
    both = np.stack([np.where(seen, 0.0, NEG), np.where(seen, 1.0, 0.0)], 1)
    c["c_cmp"] = np.ascontiguousarray(both.reshape(NT, P, 2, NCMP).transpose(1, 0, 2, 3)).astype(np.float32)
    blk, cur = np.arange(NSEL)[None, :], (t // 64)[:, None]
    valid = blk <= cur
    forced = (blk == 0) | (valid & (blk > cur - 2))
    imp = np.stack([np.where(valid | forced, 1.0, 0.0), np.where(forced, 1e4, np.where(valid, 0.0, NEG))], 1)
    c["c_imp"] = np.ascontiguousarray(imp.reshape(NT, P, 2, NSEL).transpose(1, 0, 2, 3)).astype(np.float32)
    qq, kk = np.arange(P)[:, None], np.arange(P)[None, :]
    win = np.zeros((P, 5 * P))
    win[:, 0:P] = np.where(kk > qq, 0.0, NEG)
    win[:, 4 * P:] = np.where(kk <= qq, 0.0, NEG)
    c["c_win"] = win.astype(np.float32)
    c["c_tri8"] = np.ascontiguousarray(np.broadcast_to(np.tril(np.ones((8, 8), np.float32), -1)[None], (P, 8, 8)))
    e = np.arange(NE)
    c["c_exp"] = np.ascontiguousarray(np.broadcast_to(np.stack([e, e * CAP, SPILL0 - CAP - e * CAP])[None], (P, 3, NE))).astype(np.float32)
    c["c_before"] = np.stack([np.where(k < q, 1.0, 0.0), np.ones((P, P))], 1).astype(np.float32)
    c["c_spill"] = np.arange(NSPILL, dtype=np.float32)[None]
    c["c_tok"] = (np.arange(NT)[None, :] * P + np.arange(P)[:, None]).astype(np.float32)
    c["c_iota"] = np.ascontiguousarray(np.broadcast_to(np.arange(P, dtype=np.float32), (P, P)))
    c["c_diag16"] = np.tile(np.eye(16, dtype=np.float32), (2, 1))
    return c


class Stage:

    def __init__(self, nc, ctx, stage):
        self.nc, self.ctx, self.stage, self.sems = nc, ctx, stage, []
        ctx.callback(self.end)

    def end(self):
        if self.sems:
            self.nc.clear_and_free_semaphores(self.sems)
            self.nc.all_engine_barrier()

    def sb(self, name, shape, dt=F32):
        return self.ctx.enter_context(self.nc.sbuf_tensor(f"{self.stage}_{name}", shape, dt))

    def ps(self, name, shape, dt=F32):
        return self.ctx.enter_context(self.nc.psum_tensor(f"{self.stage}_{name}", shape, dt))

    def sem(self, name):
        self.sems.append(self.nc.alloc_semaphore(f"{self.stage}_{name}"))
        return self.sems[-1]


class Weights:

    PIECES = [(0, slice(0, 4)), (0, slice(4, 8)), (1, slice(0, 8))]

    def __init__(self, m, name):
        self.tile = m.sb(name, [P, KC, D])
        self.here = [m.sem(f"{name}_here{k}") for k in range(len(self.PIECES))]

    def load(self, eng, w):
        view = w.rearrange("(c p) n -> p c n", p=P)
        for (half, cs), here in zip(self.PIECES, self.here):
            cols = slice(half * 512, (half + 1) * 512)
            eng.dma_start(self.tile[:, cs, cols], view[:, cs, cols]).then_inc(here, 16)

    def wait(self, eng, half, c):
        for (h, cs), here in zip(self.PIECES, self.here):
            if h == half and cs.start == c:
                eng.wait_ge(here, 16)


class Norm:

    def __init__(self, m, name):
        self.g = m.sb(f"{name}_g", [P, D])
        self.b = m.sb(f"{name}_b", [P, D])
        self.stats = m.sb(f"{name}_stats", [P, 2, 6])
        self.mv = m.sb(f"{name}_mv", [P, 2])
        self.inv = m.sb(f"{name}_inv", [P, 1])
        self.rstd = m.sb(f"{name}_rstd", [P, 1])
        self.gb_in = m.sem(f"{name}_gb_in")
        self.var_ready = m.sem(f"{name}_var_ready")
        self.rstd_ready = m.sem(f"{name}_rstd_ready")

    def load(self, eng, g, b):
        eng.dma_start(self.g[:, :], g.partition_broadcast(P)).then_inc(self.gb_in, 16)
        eng.dma_start(self.b[:, :], b.partition_broadcast(P)).then_inc(self.gb_in, 16)

    def on_act(self, act, n):
        act.wait_ge(self.var_ready, n + 1)
        act.activation(self.rstd[:, :], self.inv[:, :], ACT.Sqrt).then_inc(self.rstd_ready, 1)

    def on_dve(self, dve, then, y, n):
        if n == 0:
            dve.wait_ge(self.gb_in, 32)
        dve.bn_stats(self.stats[:, 0, :], y[:, 0:512])
        then(dve.bn_stats(self.stats[:, 1, :], y[:, 512:1024]))
        then(dve.bn_aggr(self.mv[:, :], self.stats[:, :, :].rearrange("p a b -> p (a b)")))
        then(dve.tensor_scalar(self.inv[:, :], self.mv[:, 1:2], LN_EPS, None, ALU.add))
        dve.reciprocal(self.inv[:, :], self.inv[:, :]).then_inc(self.var_ready, 1)
        then(dve.scalar_tensor_tensor(out=y, in0=y, scalar=self.mv[:, 0:1], in1=self.g[:, :], op0=ALU.subtract, op1=ALU.mult))
        dve.wait_ge(self.rstd_ready, n + 1)
        return dve.scalar_tensor_tensor(out=y, in0=y, scalar=self.rstd[:, 0:1], in1=self.b[:, :], op0=ALU.mult, op1=ALU.add)


def stage_project(nc, x, w_in, cos, sin, ident, keep):
    with ExitStack() as ctx:
        m = Stage(nc, ctx, "proj")
        x_tile = m.sb("x_tile", [P, 2, D])
        xT = m.sb("xT", [P, KC, S])
        w = m.sb("w", [P, 2, KC, 512])
        tok = m.sb("tok", [P, 2, 512])
        dup = m.sb("dup", [P, 2, 6, 2, HD])
        cs = m.sb("cs", [P, 2, 2, 8, 8])
        r1 = m.sb("r1", [P, 4, 64])

        def x_at(tt):
            return w[:, 1, 2 * (tt - 2):2 * (tt - 1), :].rearrange("p a b -> p (a b)") if 2 <= tt < 6 else x_tile[:, tt % 2, :]

        ps_mm = m.ps("ps_mm", [P, 4, 512])
        ps_t = m.ps("ps_t", [P, 2, 1024])
        const_in = m.sem("const_in")
        x_in = [m.sem(f"x_in{i}") for i in range(8)]
        w_inx = [m.sem(f"w_in{i}") for i in range(2)]
        cs_in = [m.sem(f"cs_in{i}") for i in range(2)]
        x_transposed = m.sem("x_transposed")
        xT_by_act = m.sem("xT_by_act")
        xT_by_dve = m.sem("xT_by_dve")
        mm_done = m.sem("mm_done")
        evicted = m.sem("evicted")
        roped = m.sem("roped")
        dup_done = m.sem("dup_done")
        transposed = m.sem("transposed")
        t_copied = m.sem("t_copied")
        dve_step = m.sem("dve_step")

        w_cols = [(0, 512), (512, 512), (1024, 512), (1536, 512), (2048, 512), (2560, 280)]
        w_view = w_in.rearrange("(c p) n -> p c n", p=P)
        units = [(g, tt) for g in range(6) for tt in range(8)]
        FIRST_ROPE = 24

        def n_rope(g):
            return {3: (0, 8), 4: (8, 8), 5: (16, 4)}[g]

        block = ctx.enter_context(nc.Block())

        @block.sync
        def _(sp):
            sp.dma_start(keep["ident"][:, :], ident).then_inc(const_in, 16)
            for tt in range(8):
                if tt >= 6:
                    sp.wait_ge(x_transposed, tt - 5)
                sp.dma_start(x_at(tt), x[tt * P:(tt + 1) * P, :]).then_inc(x_in[tt], 16)
                if tt == 3:
                    sp.dma_start(w[:, 0, :, 0:w_cols[0][1]], w_view[:, :, 0:w_cols[0][1]]).then_inc(w_inx[0], 16)
            sp.wait_ge(x_transposed, 6)
            for g in range(1, 6):
                c0, n = w_cols[g]
                if g > 1:
                    sp.wait_ge(mm_done, 8 * (g - 1))
                sp.dma_start(w[:, g % 2, :, 0:n], w_view[:, :, c0:c0 + n]).then_inc(w_inx[g % 2], 16)

        @block.gpsimd
        def _(pool):
            for u, (g, tt) in enumerate(units):
                if g < 3:
                    continue
                v = u - FIRST_ROPE
                if v >= 2:
                    pool.wait_ge(roped, v - 1)
                h0, nh = n_rope(g)
                pool.dma_start(cs[:, v % 2, 0, 0:nh, :], cos[tt * P:(tt + 1) * P, h0:h0 + nh, :]).then_inc(cs_in[v % 2], 16)
                pool.dma_start(cs[:, v % 2, 1, 0:nh, :], sin[tt * P:(tt + 1) * P, h0:h0 + nh, :]).then_inc(cs_in[v % 2], 16)

        @block.tensor
        def _(pe):
            pe.wait_ge(const_in, 16)
            for tt in range(8):
                pe.wait_ge(x_in[tt], 16)
                if tt >= 2:
                    pe.wait_ge(xT_by_act, tt - 1)
                    pe.wait_ge(xT_by_dve, tt - 1)
                for c in range(KC):
                    t = pe.transpose(ps_t[:, tt % 2, c * P:(c + 1) * P], x_at(tt)[:, c * P:(c + 1) * P],
                                     keep["ident"][:, :])
                t.then_inc(x_transposed, 1)
            pe.wait_ge(xT_by_act, 8)
            pe.wait_ge(xT_by_dve, 8)

            def transposes(u):
                g, tt = units[u]
                v = u - FIRST_ROPE
                pe.wait_ge(roped, v + 1)
                if g > 3:
                    pe.wait_ge(dup_done, v - 8 + 1)
                if v >= 2:
                    pe.wait_ge(t_copied, v - 1)
                n = {3: 4, 4: 6, 5: 2}[g]
                for k in range(n):
                    src = tok[:, v % 2, k * P:(k + 1) * P] if g == 3 else dup[:, v % 2, k, :, :].rearrange("p a d -> p (a d)")
                    t = pe.transpose(ps_t[:, v % 2, k * P:(k + 1) * P], src, keep["ident"][:, :])
                t.then_inc(transposed, 1)

            for u, (g, tt) in enumerate(units):
                pe.wait_ge(w_inx[g % 2], 16 * (g // 2 + 1))
                if u >= 4:
                    pe.wait_ge(evicted, u - 3)
                n = w_cols[g][1]
                for c in range(KC):
                    if g < 2:
                        fc, half = tt // 2, tt % 2
                        t = pe.matmul(ps_mm[:, u % 4, :], w[:, g % 2, c, fc * P:(fc + 1) * P],
                                      xT[:, c, half * 512:(half + 1) * 512], start=(c == 0), stop=(c == KC - 1))
                    else:
                        t = pe.matmul(ps_mm[:, u % 4, 0:n], xT[:, c, tt * P:(tt + 1) * P],
                                      w[:, g % 2, c, 0:n], start=(c == 0), stop=(c == KC - 1))
                t.then_inc(mm_done, 1)
                if u > FIRST_ROPE:
                    transposes(u - 1)
            transposes(len(units) - 1)

        @block.scalar
        def _(act):
            for tt in range(8):
                act.wait_ge(x_transposed, tt + 1)
                act.activation(xT[:, 0:4, tt * P:(tt + 1) * P],
                               ps_t[:, tt % 2, 0:512].rearrange("p (c t) -> p c t", c=4), ACT.Copy).then_inc(xT_by_act, 1)
            for u, (g, tt) in enumerate(units):
                act.wait_ge(mm_done, u + 1)
                v = u - FIRST_ROPE
                n = w_cols[g][1]
                src = ps_mm[:, u % 4, 0:n]
                if g == 0:
                    act.activation(keep["qaT"][:, tt // 2, (tt % 2) * 512:(tt % 2 + 1) * 512], src, ACT.Copy, scale=0.125).then_inc(evicted, 1)
                elif g == 1:
                    act.activation(keep["kaT"][:, tt // 2, (tt % 2) * 512:(tt % 2 + 1) * 512], src, ACT.Copy).then_inc(evicted, 1)
                elif g == 2:
                    act.activation(keep["va"][:, tt, :], src, ACT.Copy).then_inc(evicted, 1)
                else:
                    if v >= 2:
                        act.wait_ge(transposed, v - 1)
                    act.activation(tok[:, v % 2, 0:n], src, ACT.Copy, scale=0.125 if g == 3 else 1.0).then_inc(evicted, 1)
                    if g > 3:
                        act.wait_ge(roped, v + 1)
                        if g == 4:
                            act.activation(dup[:, v % 2, :, :, :],
                                           tok[:, v % 2, 0:384].rearrange("p (h d) -> p h d", h=6).unsqueeze(2).to_broadcast([P, 6, 2, HD]),
                                           ACT.Copy)
                            act.activation(keep["vs"][:, tt, :], tok[:, v % 2, 384:512], ACT.Copy).then_inc(dup_done, 1)
                        else:
                            act.activation(dup[:, v % 2, 0:2, :, :],
                                           tok[:, v % 2, 0:128].rearrange("p (h d) -> p h d", h=2).unsqueeze(2).to_broadcast([P, 2, 2, HD]),
                                           ACT.Copy)
                            act.activation(keep["gate"][:, tt, :], tok[:, v % 2, 256:280], ACT.Copy)
                            act.activation(keep["vw"][:, tt, :], tok[:, v % 2, 128:256], ACT.Copy).then_inc(dup_done, 1)

        def copy_out(dve, v):
            g, tt = units[v + FIRST_ROPE]
            dve.wait_ge(transposed, v + 1)
            cols = slice(tt * P, (tt + 1) * P)
            if g == 3:
                dve.tensor_copy(keep["qbT"][:, :, cols], ps_t[:, v % 2, 0:512].rearrange("p (c t) -> p c t", c=4)).then_inc(t_copied, 1)
            elif g == 4:
                dve.tensor_copy(keep["kcT"][:, :, cols], ps_t[:, v % 2, 0:256].rearrange("p (c t) -> p c t", c=2))
                dve.tensor_copy(keep["vcT"][:, :, cols], ps_t[:, v % 2, 256:512].rearrange("p (c t) -> p c t", c=2))
                dve.tensor_copy(keep["ksT"][:, :, cols], ps_t[:, v % 2, 512:768].rearrange("p (c t) -> p c t", c=2)).then_inc(t_copied, 1)
            else:
                dve.tensor_copy(keep["kwT"][:, :, cols], ps_t[:, v % 2, 0:256].rearrange("p (c t) -> p c t", c=2)).then_inc(t_copied, 1)

        @block.vector
        def _(dve):
            steps = [0]

            def done(ins):
                steps[0] += 1
                ins.then_inc(dve_step, 1)

            for tt in range(8):
                dve.wait_ge(x_transposed, tt + 1)
                dve.tensor_copy(xT[:, 4:8, tt * P:(tt + 1) * P],
                                ps_t[:, tt % 2, 512:1024].rearrange("p (c t) -> p c t", c=4)).then_inc(xT_by_dve, 1)
            for u, (g, tt) in enumerate(units):
                if g < 3:
                    continue
                v = u - FIRST_ROPE
                h0, nh = n_rope(g)
                dve.wait_ge(evicted, u + 1)
                dve.wait_ge(cs_in[v % 2], 32 * (v // 2 + 1))
                heads = tok[:, v % 2, 0:nh * HD].rearrange("p (h d) -> p h d", h=nh)
                x1, x2 = heads[:, :, 0:8], heads[:, :, 8:16]
                c_, s_ = cs[:, v % 2, 0, 0:nh, :], cs[:, v % 2, 1, 0:nh, :]
                t = [r1[:, i, 0:nh * 8].rearrange("p (h d) -> p h d", h=nh) for i in range(4)]
                if v:
                    dve.wait_ge(dve_step, steps[0])
                done(dve.tensor_tensor(t[0], x1, c_, ALU.mult))
                done(dve.tensor_tensor(t[1], x2, s_, ALU.mult))
                done(dve.tensor_tensor(t[2], x2, c_, ALU.mult))
                done(dve.tensor_tensor(t[3], x1, s_, ALU.mult))
                dve.wait_ge(dve_step, steps[0])
                done(dve.tensor_tensor(x1, t[0], t[1], ALU.subtract))
                dve.wait_ge(dve_step, steps[0])
                steps[0] += 1
                dve.tensor_tensor(x2, t[2], t[3], ALU.add).then_inc(dve_step, 1)
                dve.wait_ge(dve_step, steps[0])
                dve.engine_nop().then_inc(roped, 1)
                if v >= 1:
                    copy_out(dve, v - 1)
            copy_out(dve, len(units) - 1 - FIRST_ROPE)


def keep_attention(nc, ctx):
    m = Stage(nc, ctx, "keep")
    k = {"ident": m.sb("ident", [P, P])}
    for n, shape in (("qaT", [P, 4, S]), ("kaT", [P, 4, S]), ("va", [P, NT, 512]), ("qbT", [P, 4, S]),
                     ("kcT", [P, 2, S]), ("vcT", [P, 2, S]), ("ksT", [P, 2, S]), ("kwT", [P, 2, S]),
                     ("vs", [P, NT, P]), ("vw", [P, NT, P]), ("gate", [P, NT, 24]),
                     ("sel", [P, 2, NT, NSEL]), ("o_tok", [P, NT, 512])):
        k[n] = m.sb(n, shape)
    return k


def stage_stick(nc, stick, expert_rows, keep):
    with ExitStack() as ctx:
        m = Stage(nc, ctx, "sb")
        masks = m.sb("masks", [P, 4, P])
        tri_after, tri_rest, before, not_before = (masks[:, i, :] for i in range(4))
        q_st = m.sb("q_st", [P, S])
        k_st = m.sb("k_st", [P, 2, S])
        v_st = m.sb("v_st", [P, NT, P])
        mag = m.sb("mag", [P, 2, 512])
        ln1 = m.sb("ln1", [P, 2, 512])
        sp_ = m.sb("sp", [P, 4, 512])
        zsp = m.sb("zsp", [P, 4, 512])
        t_ = m.sb("t", [P, 2, 512])
        w_ = m.sb("w", [P, 4, 512])
        zeros = m.sb("zeros", [P, D])
        zeros_ready, cleared, k_zero = m.sem("zeros_ready"), m.sem("cleared"), m.sem("k_zero")
        ps_z = m.ps("ps_z", [P, 2, 512])
        ps_s = m.ps("ps_s", [P, 2, S])
        ps_o = m.ps("ps_o", [P, S])
        const_in, q_staged, k_staged, v_staged, z_done, ln_done, sp_done, tri_done, t_done, w_done, conv_done, pv_done, o_evicted, act_step, dve_step = (
            m.sem(n) for n in "const_in q_staged k_staged v_staged z_done ln_done sp_done tri_done t_done w_done conv_done pv_done o_evicted act_step dve_step".split())

        units = []
        for kt in range(NT - 1, -1, -1):
            pieces = [(kt * P, S)] if kt >= 4 else [(kt * P, 512), (512, S)]
            for a, b in pieces:
                for hh in range(2):
                    units.append((hh, kt, a, b - a))
        N = len(units)
        PAIRS = 4
        DVE_STEPS = sum(1 + 2 * (a == kt * P) for _, kt, a, _ in units)
        block = ctx.enter_context(nc.Block())

        @block.sync
        def _(sp):
            sp.dma_start(masks[:, :, :], stick).then_inc(const_in, 16)
            sp.wait_ge(zeros_ready, 1)
            with sp.Fori(0, NSPILL) as b:
                sp.dma_start(expert_rows[bass.ds(SPILL0 + b * CAP, CAP), :], zeros[:, :]).then_inc(cleared, 16)
            sp.wait_ge(cleared, 16 * NSPILL)

        @block.gpsimd
        def _(pool):
            pool.memset(k_st[HD:P, 0, :], 0.0).then_inc(k_zero, 1)
            pool.wait_ge(k_zero, 1)
            pool.memset(k_st[0:HD, 1, :], 0.0).then_inc(k_zero, 1)
            pool.wait_ge(k_zero, 2)
            pool.memset(zeros[:, :], 0.0).then_inc(zeros_ready, 1)
            with pool.Fori(0, PAIRS) as i:
                pool.wait_ge(pv_done, i * N)
                pool.tensor_copy(v_st[:, :, :], keep["va"][:, :, bass.ds(i * P, P)]).then_inc(v_staged, 1)

        def wait(eng, sem, count):
            if not (isinstance(count, int) and count <= 0):
                eng.wait_ge(sem, count)

        def whose(i, n):
            return (i, n) if n < N else (i + 1, n - N)

        def all_pairs(eng, body):
            body(0)
            with eng.Fori(1, PAIRS - 1) as i:
                body(i)
            body(PAIRS - 1)

        def is_last(i):
            return isinstance(i, int) and i == PAIRS - 1

        @block.tensor
        def _(pe):
            pe.wait_ge(const_in, 16)
            pe.wait_ge(k_zero, 2)

            def scores(i, n):
                hh, kt, a, w = units[n]
                if n == 0:
                    pe.wait_ge(q_staged, i + 1)
                    pe.wait_ge(k_staged, i + 1)
                wait(pe, sp_done, i * N + n - 1)
                pe.matmul(ps_z[:, n % 2, 0:w], k_st[:, hh, kt * P:(kt + 1) * P], q_st[:, a:a + w],
                          start=True, stop=True).then_inc(z_done, 1)

            def is_first(n):
                _, kt, a, _ = units[n]
                return (kt == NT - 1) or (kt == 3 and a < 512)

            def suffix(i, n):
                hh, kt, a, w = units[n]
                pe.wait_ge(sp_done, i * N + n + 1)
                pe.matmul(ps_s[:, hh, a:a + w], tri_after, sp_[:, n % 4, 0:w], start=is_first(n), stop=True,
                          skip_group_check=True).then_inc(tri_done, 1)

            def to_whole(i, n):
                hh, kt, a, w = units[n]
                pe.wait_ge(t_done, i * N + n + 1)
                pe.matmul(ps_s[:, hh, a:a + w], tri_rest, sp_[:, n % 4, 0:w], start=False, stop=True,
                          skip_group_check=True).then_inc(conv_done, 1)

            def values(i, n):
                hh, kt, a, w = units[n]
                pe.wait_ge(w_done, i * N + n + 1)
                if n == 0:
                    pe.wait_ge(v_staged, i + 1)
                    wait(pe, o_evicted, i)
                pe.matmul(ps_o[hh * HD:(hh + 1) * HD, a:a + w], v_st[:, kt, hh * HD:(hh + 1) * HD],
                          w_[:, n % 4, 0:w], start=is_first(n), stop=True, skip_group_check=True).then_inc(pv_done, 1)

            def body(i):
                for n in range(N):
                    suffix(i, n)
                    if n:
                        to_whole(i, n - 1)
                    if n + 3 < N or not is_last(i):
                        scores(*whose(i, n + 3))
                    if n and n % 2 == 0:
                        values(i, n - 2)
                        values(i, n - 1)
                to_whole(i, N - 1)
                values(i, N - 2)
                values(i, N - 1)

            for n in range(3):
                scores(0, n)
            all_pairs(pe, body)

        @block.scalar
        def _(act):
            act.preload_act_table_set("natural_log_exp_and_others")

            def stage_k(i):
                for hh in range(2):
                    h = slice(hh * HD, (hh + 1) * HD)
                    wait(act, z_done, i * N)
                    x = act.activation(k_st[h, hh, :], keep["kaT"][h, i, :], ACT.Copy)
                x.then_inc(k_staged, 1)

            def softplus_part(i, n):
                w = units[n][3]
                z = ps_z[:, n % 2, 0:w]
                done = i * (2 * N) + 2 * n
                act.wait_ge(z_done, i * N + n + 1)
                act.activation(mag[:, n % 2, 0:w], z, ACT.Abs).then_inc(act_step, 1)
                act.wait_ge(act_step, done + 1)
                act.activation(mag[:, n % 2, 0:w], mag[:, n % 2, 0:w], ACT.Exp, scale=-1.0).then_inc(act_step, 1)
                act.wait_ge(act_step, done + 2)
                wait(act, sp_done, i * N + n - 1)
                act.activation(ln1[:, n % 2, 0:w], mag[:, n % 2, 0:w], ACT.Ln, bias=1.0).then_inc(ln_done, 1)

            def weights(i, n):
                w = units[n][3]
                act.wait_ge(t_done, i * N + n + 1)
                wait(act, pv_done, i * N + n - 3)
                act.activation(w_[:, n % 4, 0:w], t_[:, n % 2, 0:w], ACT.Exp).then_inc(w_done, 1)

            def body(i):
                for n in range(N):
                    if n == N - 3 and not is_last(i):
                        stage_k(i + 1)
                    if n + 2 < N or not is_last(i):
                        softplus_part(*whose(i, n + 2))
                    weights(i, n)

            stage_k(0)
            softplus_part(0, 0)
            softplus_part(0, 1)
            all_pairs(act, body)

        @block.vector
        def _(dve):
            step = [0]

            def softplus(i, n, before_it):
                hh, kt, a, w = units[n]
                diagonal = a == kt * P
                z = ps_z[:, n % 2, 0:w]
                s = n % 4

                def then(ins):
                    step[0] += 1
                    ins.then_inc(dve_step, 1)
                    dve.wait_ge(dve_step, before_it + step[0])

                dve.wait_ge(ln_done, i * N + n + 1)
                wait(dve, conv_done, i * N + n - 3)
                then(dve.scalar_tensor_tensor(out=sp_[:, s, 0:w], in0=z, scalar=0.0, in1=ln1[:, n % 2, 0:w],
                                              op0=ALU.max, op1=ALU.add))
                last = dve.tensor_tensor(zsp[:, s, 0:w], z, sp_[:, s, 0:w], ALU.subtract)
                if diagonal:
                    then(last)
                    then(dve.tensor_tensor(sp_[:, s, 0:P], sp_[:, s, 0:P], before, ALU.mult))
                    last = dve.tensor_tensor(zsp[:, s, 0:P], zsp[:, s, 0:P], not_before, ALU.add)
                last.then_inc(sp_done, 1)

            def exponent(i, n):
                hh, kt, a, w = units[n]
                dve.wait_ge(tri_done, i * N + n + 1)
                wait(dve, w_done, i * N + n - 1)
                dve.wait_ge(sp_done, i * N + n + 1)
                dve.tensor_tensor(t_[:, n % 2, 0:w], zsp[:, n % 4, 0:w], ps_s[:, hh, a:a + w], ALU.add).then_inc(t_done, 1)

            def stage_q(i):
                wait(dve, z_done, i * N)
                dve.tensor_scalar(q_st[:, :], keep["qaT"][:, i, :], 1.0, None, ALU.mult).then_inc(q_staged, 1)

            def evict(i):
                dve.wait_ge(pv_done, i * N)
                dve.tensor_scalar(keep["qaT"][:, i - 1, :], ps_o[:, :], 1.0, None, ALU.mult).then_inc(o_evicted, 1)

            def body(i):
                step[0] = ahead
                for n in range(N):
                    exponent(i, n)
                    if n == 0 and not (isinstance(i, int) and i == 0):
                        evict(i)
                    if n == N - 3 and not is_last(i):
                        stage_q(i + 1)
                    if n + 2 < N or not is_last(i):
                        softplus(*whose(i, n + 2), i * DVE_STEPS)

            dve.wait_ge(const_in, 16)
            stage_q(0)
            softplus(0, 0, 0)
            softplus(0, 1, 0)
            ahead = step[0]
            all_pairs(dve, body)
            evict(PAIRS)


def stage_compress(nc, pos_k, pos_v, k_w1, k_w2, v_w1, v_w2, c_cmp, c_imp, keep):
    with ExitStack() as ctx:
        m = Stage(nc, ctx, "cmp")
        w1 = m.sb("w1", [P, 2, 16, 256])
        w2k = m.sb("w2k", [P, 2, 2, HD])
        w2v = m.sb("w2v", [P, 2, HD])
        pos = m.sb("pos", [P, 2, 16])
        mcmp = m.sb("mcmp", [P, NT, 2, NCMP])
        mimp = m.sb("mimp", [P, NT, 2, NSEL])
        kpos = m.sb("kpos", [P, 2, 2, 16, NCMP])
        hid = m.sb("hid", [P, 2, 2, 2 * NCMP])
        kcmp = m.sb("kcmp", [P, 2, NCMP])
        vcmp = m.sb("vcmp", [NCMP, 2, HD])
        s_ = m.sb("s", [P, 2, 8, NCMP])
        e_ = m.sb("e", [P, 2, 8, NCMP])
        p_ = m.sb("p", [P, 2, 8, NCMP])
        st = m.sb("st", [P, 3, 8])
        psum4 = m.sb("psum4", [P, 2, NCMP + 2])
        imp = m.sb("imp", [P, 2, NSEL])
        top = m.sb("top", [P, 2, 8])
        rest = m.sb("rest", [P, 2, NSEL])
        pT = m.sb("pT", [NCMP, 2, 8, P])
        ps_c = m.ps("ps_c", [P, 2, 2, 8, 64])
        ps_t = m.ps("ps_t", [P, 8, P])
        ps_o = m.ps("ps_o", [P, 2, 8, HD])
        w1_in = [m.sem(f"w1_in{k}") for k in range(2)]
        (pos_in, w2_in, c_in, kpos_k, kpos_v, hid_mm, gelu_done, cmp_mm, cmp_copied, sc_done, e_done, gate_done, p_done,
         t_done, t_copied, o_done, o_copied, dve_step, s_read, shifted) = (m.sem(n) for n in
            "pos_in w2_in c_in kpos_k kpos_v hid_mm gelu_done cmp_mm cmp_copied sc_done e_done gate_done p_done t_done t_copied o_done o_copied dve_step s_read shifted".split())
        ps_h = ps_t[:, :, :].rearrange("p a b -> p (a b)")
        block = ctx.enter_context(nc.Block())

        @block.sync
        def _(sp):
            for i, pp in enumerate((pos_k, pos_v)):
                with nc.allow_non_contiguous_dma(reason="2048 elements"):
                    sp.dma_start(pos[:, i, :], pp.rearrange("(i two) d -> (two d) i", two=2)).then_inc(pos_in, 16)
            for i, wa in enumerate((k_w1, v_w1)):
                sp.dma_start(w1[:, i, :, :], wa.rearrange("(i p) f -> p i f", p=P)).then_inc(w1_in[i], 16)
            for a in range(2):
                sp.dma_start(w2k[:, :, a, :], k_w2.rearrange("(c p) d -> p c d", p=P)).then_inc(w2_in, 16)
            sp.dma_start(w2v[:, :, :], v_w2.rearrange("(c p) d -> p c d", p=P)).then_inc(w2_in, 16)
            sp.dma_start(mcmp[:, :, :, :], c_cmp).then_inc(c_in, 16)
            sp.dma_start(mimp[:, :, :, :], c_imp).then_inc(c_in, 16)

        def add_pos(eng, kind, done):
            src = keep["kcT"] if kind == 0 else keep["vcT"]
            for odd in range(2):
                h = slice(odd * HD, (odd + 1) * HD)
                for g in range(2):
                    v = src[h, g, :].rearrange("p (n r) -> p r n", r=16)[:, odd::2, :]
                    for late in range(2):
                        x = eng.tensor_tensor(kpos[h, kind, g, 8 * late:8 * late + 8, :], v[:, :, late:late + NCMP],
                                              pos[h, kind, 8 * late:8 * late + 8].unsqueeze(2).to_broadcast([HD, 8, NCMP]), ALU.add)
            x.then_inc(done, 1)

        @block.gpsimd
        def _(pool):
            pool.wait_ge(pos_in, 32)
            add_pos(pool, 1, kpos_v)

        @block.tensor
        def _(pe):
            for kind in range(2):
                pe.wait_ge(w1_in[kind], 16)
                pe.wait_ge(kpos_k if kind == 0 else kpos_v, 1)
                for fc in range(2):
                    o = (kind * 2 + fc) * 2 * NCMP
                    for l in range(16):
                        x = pe.matmul(ps_h[:, o:o + 2 * NCMP], w1[:, kind, l, fc * P:(fc + 1) * P], kpos[:, kind, :, l, :],
                                      start=(l == 0), stop=(l == 15), skip_group_check=True)
                    x.then_inc(hid_mm, 1)
            pe.wait_ge(gelu_done, 4)
            pe.wait_ge(w2_in, 48)
            for c in range(2):
                x = pe.matmul(ps_c[:, 0, 0, :, :].rearrange("p a b -> p (a b)")[:, 0:2 * NCMP], w2k[:, c, :, :].rearrange("p a d -> p (a d)"),
                              hid[:, 0, c, :], start=(c == 0), stop=(c == 1))
            x.then_inc(cmp_mm, 1)
            for g in range(2):
                for c in range(2):
                    x = pe.matmul(ps_o[0:NCMP, 0, g, :], hid[:, 1, c, g * NCMP:(g + 1) * NCMP], w2v[:, c, :],
                                  start=(c == 0), stop=(c == 1), skip_group_check=True)
            x.then_inc(cmp_mm, 1)
            pe.wait_ge(cmp_copied, 2)

            def scores(i):
                if i >= 2:
                    pe.wait_ge(s_read, i - 1)
                for h in range(8):
                    hp = slice((h % 2) * HD, (h % 2 + 1) * HD)
                    x = pe.matmul(ps_c[:, i % 2, h % 2, h // 2, 0:NCMP], keep["qbT"][hp, h // 2, i * P:(i + 1) * P], kcmp[hp, h // 4, :],
                                  start=True, stop=True, skip_group_check=True)
                x.then_inc(sc_done, 1)

            scores(0)
            scores(1)
            for i in range(NT):
                pe.wait_ge(p_done, i + 1)
                if i:
                    pe.wait_ge(t_copied, i)
                for h in range(8):
                    x = pe.transpose(ps_t[0:NCMP, h, :], p_[:, i % 2, h, :], keep["ident"][:, :])
                x.then_inc(t_done, 1)
                if i + 2 < NT:
                    scores(i + 2)
                pe.wait_ge(t_copied, i + 1)
                if i >= 2:
                    pe.wait_ge(o_copied, i - 1)
                for h in range(8):
                    x = pe.matmul(ps_o[:, i % 2, h, :], pT[:, i % 2, h, :], vcmp[:, h // 4, :], start=True, stop=True,
                                  skip_group_check=True)
                x.then_inc(o_done, 1)

        @block.scalar
        def _(act):
            act.activation(keep["gate"][:, :, :], keep["gate"][:, :, :], ACT.Sigmoid).then_inc(gate_done, 1)
            act.wait_ge(hid_mm, 4)
            for k in range(4):
                act.activation(hid[:, k // 2, k % 2, :], ps_h[:, k * 2 * NCMP:(k + 1) * 2 * NCMP], ACT.Gelu_apprx_tanh).then_inc(gelu_done, 1)
            for i in range(NT):
                act.wait_ge(shifted, i + 1)
                act.activation(e_[:, i % 2, :, :], s_[:, i % 2, :, :], ACT.Exp).then_inc(e_done, 1)
                act.wait_ge(t_done, i + 1)
                if i >= 2:
                    act.wait_ge(o_done, i - 1)
                act.activation(pT[:, i % 2, :, :], ps_t[0:NCMP, :, :], ACT.Copy).then_inc(t_copied, 1)

        @block.vector
        def _(dve):
            step = [0]

            def then(ins):
                step[0] += 1
                ins.then_inc(dve_step, 1)
                dve.wait_ge(dve_step, step[0])

            then(dve.memset(psum4[:, :, :], 0.0))
            dve.wait_ge(pos_in, 32)
            add_pos(dve, 0, kpos_k)
            dve.wait_ge(cmp_mm, 2)
            dve.tensor_copy(kcmp[:, :, :], ps_c[:, 0, 0, :, :].rearrange("p a b -> p (a b)")[:, 0:2 * NCMP].rearrange("p (g n) -> p g n", g=2)).then_inc(cmp_copied, 1)
            dve.tensor_copy(vcmp[:, :, :], ps_o[0:NCMP, 0, 0:2, :]).then_inc(cmp_copied, 1)
            dve.wait_ge(c_in, 32)
            dve.wait_ge(gate_done, 1)

            def wide(x):
                return x.unsqueeze(2).to_broadcast([P, 8, NCMP])

            def shift(i):
                s = s_[:, i % 2, :, :]
                dve.wait_ge(sc_done, i + 1)
                if i >= 2:
                    dve.wait_ge(e_done, i - 1)
                dve.tensor_tensor(s.rearrange("p (b a) n -> p b a n", a=2), ps_c[:, i % 2, :, 0:4, 0:NCMP].rearrange("p a b n -> p b a n"),
                                  mcmp[:, i, 0, :].unsqueeze(1).unsqueeze(1).to_broadcast([P, 4, 2, NCMP]), ALU.add).then_inc(s_read, 1)
                dve.wait_ge(s_read, i + 1)
                then(dve.tensor_reduce(st[:, 0, :], s, AX, ALU.max))
                dve.tensor_tensor(s, s, wide(st[:, 0, :]), ALU.subtract).then_inc(shifted, 1)

            def gated(i):
                dve.wait_ge(o_done, i + 1)
                gate0 = keep["gate"][:, i, :].rearrange("p (h b) -> p h b", b=3)[:, :, 0:1].to_broadcast([P, 8, HD])
                dve.tensor_tensor(keep["o_tok"][:, i, :].rearrange("p (h d) -> p h d", h=8), ps_o[:, i % 2, :, :], gate0, ALU.mult).then_inc(o_copied, 1)

            shift(0)
            for i in range(NT):
                e, p = e_[:, i % 2, :, :], p_[:, i % 2, :, :]
                dve.wait_ge(e_done, i + 1)
                then(dve.tensor_reduce(st[:, 1, :], e, AX, ALU.add))
                then(dve.reciprocal(st[:, 2, :], st[:, 1, :]))
                then(dve.tensor_tensor(e, e, wide(st[:, 2, :]), ALU.mult))
                if i >= 2:
                    dve.wait_ge(t_done, i - 1)
                dve.tensor_tensor(p, e, mcmp[:, i, 1, :].unsqueeze(1).to_broadcast([P, 8, NCMP]), ALU.mult).then_inc(p_done, 1)
                if i + 1 < NT:
                    shift(i + 1)
                dve.wait_ge(p_done, i + 1)
                then(dve.tensor_reduce(psum4[:, :, 1:NCMP + 1], p.rearrange("p (g r) n -> p g n r", g=2), AX, ALU.add))
                base = psum4[:, :, :]
                taps = bass.AP(base.tensor, base.offset, [list(base.ap[0]), [NCMP + 2, 2], [4, NSEL], [1, 5]])
                then(dve.tensor_reduce(imp[:, :, :], taps, AX, ALU.add))
                then(dve.tensor_tensor(imp[:, :, :], imp[:, :, :], mimp[:, i, 0, :].unsqueeze(1).to_broadcast([P, 2, NSEL]), ALU.mult))
                then(dve.tensor_tensor(imp[:, :, :], imp[:, :, :], mimp[:, i, 1, :].unsqueeze(1).to_broadcast([P, 2, NSEL]), ALU.add))
                for g in range(2):
                    then(dve.max(top[:, g, :], imp[:, g, :]))
                for g in range(2):
                    then(dve.match_replace(rest[:, g, :], top[:, g, :], imp[:, g, :], FAR))
                then(dve.tensor_tensor(imp[:, :, :], rest[:, :, :], imp[:, :, :], ALU.is_equal))
                then(dve.tensor_scalar(keep["sel"][:, :, i, :], imp[:, :, :], NEG, None, ALU.mult))
                if i:
                    gated(i - 1)
            gated(NT - 1)


def stage_selected(nc, c_win, keep):
    with ExitStack() as ctx:
        m = Stage(nc, ctx, "sel")
        R = 4
        MOST = 13
        win = m.sb("win", [P, 5 * P])
        q_st = keep["kaT"]
        ks_st, kw_st = keep["kcT"][:, 0, :], keep["kcT"][:, 1, :]
        mask = keep["vcT"]
        spare = keep["va"][:, :, :].rearrange("p a b -> p (a b)")
        pr = spare[:, 0:MOST * P]
        oT = spare[:, MOST * P:MOST * P + 512]
        vs_st = m.sb("vs_st", [P, NT, HD])
        vw_st = m.sb("vw_st", [P, NT, HD])
        sel_st = m.sb("sel_st", [P, NT, NSEL])
        gate_st = m.sb("gate_st", [P, NT, R, 3])
        o_st = m.sb("o_st", [P, NT, R, HD])
        sc = m.sb("sc", [P, MOST * P])
        pT = m.sb("pT", [P, 2 * MOST - 1, R, P])
        scaled = m.sb("scaled", [P, R, 2, HD])
        mx = m.sb("mx", [P, 2, 2])
        nmx = m.sb("nmx", [P, 2, 2])
        nothing = m.sb("nothing", [P, 1])
        sums = m.sb("sums", [P, 3, R, 2])
        cf = m.sb("cf", [P, R, 2])
        ps_s = m.ps("ps_s", [P, S])
        ps_w = m.ps("ps_w", [P, S])
        ps_t = m.ps("ps_t", [P, 2, 512])
        ps_o = m.ps("ps_o", [P, 512])
        ps_b = m.ps("ps_b", [P, R, 2, HD])
        (c_in, st_act, st_dve, zero_done, mask_done, sc_done, sc_read, e_done, t_done, t_copied, o_done, ot_done, back_done,
         o_used, dve_step, out_done) = (m.sem(n) for n in
            "c_in st_act st_dve zero_done mask_done sc_done sc_read e_done t_done t_copied o_done ot_done back_done o_used dve_step out_done".split())
        units = [(i, r) for i in range(NT) for r in range(R)]
        N = len(units)

        def tiles(i):
            return [(0, j) for j in range(i + 1)] + [(1, j) for j in range(max(0, i - 4), i + 1)]

        chunks = [(n, k, len(tiles(i)[k:k + 4])) for n, (i, r) in enumerate(units) for k in range(0, len(tiles(i)), 4)]
        NCH = len(chunks)
        first_chunk = [next(c for c, (u, _, _) in enumerate(chunks) if u == n) for n in range(N)] + [NCH]
        pT_at = lambda i: (i % 2) * (MOST - 1)
        DSTEP = N + 4 * NT
        block = ctx.enter_context(nc.Block())

        @block.sync
        def _(sp):
            sp.dma_start(win[:, :], c_win).then_inc(c_in, 16)

        @block.gpsimd
        def _(pool):
            for r in range(R):
                other = slice((1 - r % 2) * HD, (2 - r % 2) * HD)
                pool.memset(q_st[other, r, :], 0.0).then_inc(zero_done, 1)
                pool.wait_ge(zero_done, r + 1)
            pool.wait_ge(c_in, 16)
            with pool.Fori(0, 2) as g:
                for i in range(NT):
                    if i == 0:
                        pool.wait_ge(st_dve, g + 1)
                    pool.wait_ge(sc_read, g * N + R * max(0, i - 1))
                    w = i * P

                    def blocks(x):
                        return x.rearrange("p (b l) -> p b l", l=64)

                    x = pool.tensor_tensor(blocks(mask[:, i % 2, w:w + P]), sel_st[:, i, w // 64:w // 64 + 2].unsqueeze(2).to_broadcast([P, 2, 64]),
                                           blocks(win[:, 4 * P:5 * P]), ALU.add)
                    if i:
                        x = pool.tensor_copy(blocks(mask[:, i % 2, 0:w]), sel_st[:, i, 0:w // 64].unsqueeze(2).to_broadcast([P, w // 64, 64]))
                    x.then_inc(mask_done, 1)

        @block.tensor
        def _(pe):
            def scores(g, n):
                i, r = units[n]
                pe.wait_ge(sc_read, g * N + n)
                q = q_st[:, r, i * P:(i + 1) * P]
                w = (i + 1) * P
                for a in range(0, w, 512):
                    b = min(a + 512, w)
                    pe.matmul(ps_s[:, a:b], q, ks_st[:, a:b], start=True, stop=True)
                k0 = max(0, i - 4) * P
                ww = w - k0
                for a in range(0, ww, 512):
                    b = min(a + 512, ww)
                    x = pe.matmul(ps_w[:, a:b], q, kw_st[:, k0 + a:k0 + b], start=True, stop=True)
                x.then_inc(sc_done, 1)

            def transposes(g, c):
                n, k, count = chunks[c]
                pe.wait_ge(t_copied, g * NCH + max(0, c - 1))
                for j in range(count):
                    x = pe.transpose(ps_t[:, c % 2, j * P:(j + 1) * P], pr[:, (k + j) * P:(k + j + 1) * P], keep["ident"][:, :])
                x.then_inc(t_done, 1)

            def pairs(i):
                ts = tiles(i)
                s, w = ts[:i + 1], ts[i + 1:]
                return [[(k, s[k])] + ([(i + 1 + k, w[k])] if k < len(w) else []) for k in range(i + 1)]

            def values(g, i, some, last):
                for pair in some:
                    for k, (branch, kt) in pair:
                        v = (vs_st, vw_st)[branch]
                        x = pe.matmul(ps_o[branch * HD:(branch + 1) * HD, :], v[:, kt, :],
                                      pT[:, pT_at(i) + k, :, :].rearrange("p r q -> p (r q)"),
                                      start=(kt == (0, max(0, i - 4))[branch]), stop=(kt == i), skip_group_check=True)
                if last:
                    x.then_inc(o_done, 1)

            def ready(g, i):
                pe.wait_ge(t_copied, g * NCH + first_chunk[R * (i + 1)])
                pe.wait_ge(ot_done, g * NT + i)

            def back(g, i):
                pe.wait_ge(ot_done, g * NT + i + 1)
                pe.wait_ge(o_used, g * NT + i)
                for r in range(R):
                    x = pe.transpose(ps_b[:, r, :, :].rearrange("p a d -> p (a d)"), oT[:, r * P:(r + 1) * P], keep["ident"][:, :])
                x.then_inc(back_done, 1)

            pe.wait_ge(zero_done, R)
            with pe.Fori(0, 2) as g:
                pe.wait_ge(st_act, g + 1)
                pe.wait_ge(st_dve, g + 1)
                scores(g, 0)
                for n in range(N):
                    i, r = units[n]
                    if n + 1 < N:
                        scores(g, n + 1)
                    pe.wait_ge(e_done, g * N + n + 1)
                    todo = pairs(i - 1) if i and r < 3 else []
                    places = 3 * (first_chunk[n + 1] - first_chunk[n])
                    for j, c in enumerate(range(first_chunk[n], first_chunk[n + 1])):
                        transposes(g, c)
                        if todo:
                            if j == 0 and r == 0:
                                ready(g, i - 1)
                            at = r * (places // 3) + j
                            some = todo[len(todo) * at // places:len(todo) * (at + 1) // places]
                            values(g, i - 1, some, at + 1 == places)
                    if i and r == 3:
                        back(g, i - 1)
                ready(g, NT - 1)
                values(g, NT - 1, pairs(NT - 1), True)
                back(g, NT - 1)

        @block.scalar
        def _(act):
            act.preload_act_table_set("exp_and_others")

            def exps(g, n):
                i, r = units[n]
                act.wait_ge(sc_read, g * N + n + 1)
                act.wait_ge(t_done, g * NCH + first_chunk[n])
                act.wait_ge(o_used, g * NT + max(0, i - 2))
                w = (i + 1) * P
                ww = w - max(0, i - 4) * P
                act.activation(pr[:, 0:w], sc[:, 0:w], ACT.Exp, bias=nmx[:, n % 2, 0:1], accum_out=sums[:, i % 3, r, 0:1])
                act.activation(pr[:, w:w + ww], sc[:, w:w + ww], ACT.Exp, bias=nmx[:, n % 2, 1:2],
                               accum_out=sums[:, i % 3, r, 1:2]).then_inc(e_done, 1)

            def copy_out(g, i):
                act.wait_ge(o_done, g * NT + i + 1)
                act.wait_ge(back_done, g * NT + i)
                act.activation(oT[:, :], ps_o[:, :], ACT.Copy).then_inc(ot_done, 1)

            with act.Fori(0, 2) as g:
                act.wait_ge(out_done, g)
                act.activation(ks_st, keep["ksT"][:, g, :], ACT.Copy)
                act.activation(kw_st, keep["kwT"][:, g, :], ACT.Copy)
                act.activation(q_st[HD:P, 1::2, :], keep["qbT"][HD:P, bass.ds(g * 2, 2), :], ACT.Copy).then_inc(st_act, 1)
                exps(g, 0)
                for n in range(N):
                    i, r = units[n]
                    for c in range(first_chunk[n], first_chunk[n + 1]):
                        _, k, count = chunks[c]
                        act.wait_ge(t_done, g * NCH + c + 1)
                        act.wait_ge(o_done, g * NT + max(0, i - 1))
                        act.activation(pT[:, pT_at(i) + k:pT_at(i) + k + count, r, :],
                                       ps_t[:, c % 2, 0:count * P].rearrange("p (k q) -> p k q", q=P), ACT.Copy).then_inc(t_copied, 1)
                        if i and r == 3 and c == first_chunk[n]:
                            copy_out(g, i - 1)
                    if n + 1 < N:
                        exps(g, n + 1)
                copy_out(g, NT - 1)

        @block.vector
        def _(dve):
            step = [0]

            def then(g, ins):
                step[0] += 1
                ins.then_inc(dve_step, 1)
                dve.wait_ge(dve_step, g * DSTEP + step[0])

            def masked_max(g, n):
                i, r = units[n]
                w = (i + 1) * P
                ww = w - max(0, i - 4) * P
                if r == 0:
                    dve.wait_ge(mask_done, g * NT + i + 1)
                dve.wait_ge(sc_done, g * N + n + 1)
                dve.wait_ge(e_done, g * N + n)
                dve.memset(nothing[:, :], 0.0)
                dve.tensor_tensor_reduce(sc[:, 0:w], ps_s[:, 0:w], mask[:, i % 2, 0:w], 1.0, FAR, ALU.add, ALU.max, mx[:, n % 2, 0:1])
                then(g, dve.tensor_tensor_reduce(sc[:, w:w + ww], ps_w[:, 0:ww], win[:, 5 * P - ww:5 * P], 1.0, FAR, ALU.add, ALU.max, mx[:, n % 2, 1:2]))
                dve.tensor_scalar(nmx[:, n % 2, :], mx[:, n % 2, :], -1.0, None, ALU.mult).then_inc(sc_read, 1)

            def combine(g, i):
                dve.wait_ge(e_done, g * N + R * (i + 1))
                then(g, dve.reciprocal(cf[:, :, :], sums[:, i % 3, :, :]))
                then(g, dve.tensor_tensor(cf[:, :, :], cf[:, :, :], gate_st[:, i, :, 1:3], ALU.mult))
                dve.wait_ge(back_done, g * NT + i + 1)
                then(g, dve.tensor_tensor(scaled[:, :, :, :], ps_b[:, :, :, :], cf[:, :, :].unsqueeze(3).to_broadcast([P, R, 2, HD]), ALU.mult))
                o = o_st[:, i, :, :]
                then(g, dve.tensor_tensor(o, o, scaled[:, :, 0, :], ALU.add))
                dve.tensor_tensor(o, o, scaled[:, :, 1, :], ALU.add).then_inc(o_used, 1)

            dve.wait_ge(c_in, 16)
            with dve.Fori(0, 2) as g:
                step[0] = 0
                dve.tensor_scalar(q_st[0:HD, 0::2, :], keep["qbT"][0:HD, bass.ds(g * 2, 2), :], 1.0, None, ALU.mult)
                dve.tensor_scalar(vs_st[:, :, :], keep["vs"][:, :, bass.ds(g * HD, HD)], 1.0, None, ALU.mult)
                dve.tensor_scalar(vw_st[:, :, :], keep["vw"][:, :, bass.ds(g * HD, HD)], 1.0, None, ALU.mult)
                dve.tensor_scalar(sel_st[:, :, :], keep["sel"][:, g, :, :], 1.0, None, ALU.mult)
                dve.tensor_scalar(gate_st[:, :, :, :].rearrange("p i r b -> p i (r b)"), keep["gate"][:, :, bass.ds(g * 12, 12)], 1.0, None, ALU.mult)
                dve.tensor_scalar(o_st[:, :, :, :].rearrange("p i r d -> p i (r d)"), keep["o_tok"][:, :, bass.ds(g * 256, 256)], 1.0, None, ALU.mult).then_inc(st_dve, 1)
                dve.wait_ge(st_dve, g + 1)
                masked_max(g, 0)
                for n in range(1, N):
                    i, r = units[n]
                    masked_max(g, n)
                    if r == 1 and i >= 2:
                        combine(g, i - 2)
                combine(g, NT - 2)
                combine(g, NT - 1)
                assert step[0] == DSTEP
                dve.wait_ge(o_used, g * NT + NT)
                dve.tensor_scalar(keep["o_tok"][:, :, bass.ds(g * 256, 256)], o_st[:, :, :, :].rearrange("p i r d -> p i (r d)"), 1.0, None, ALU.mult).then_inc(out_done, 1)
                dve.wait_ge(out_done, g + 1)


def stage_attention_out(nc, w_out, x, g, b, keep, h_out):
    with ExitStack() as ctx:
        m = Stage(nc, ctx, "ao")
        weights = Weights(m, "w")
        w = weights.tile
        oT = m.sb("oT", [P, 2, 4, P])
        y = m.sb("y", [P, 2, D])
        xr = m.sb("xr", [P, 2, D])
        norm = Norm(m, "ln")
        ps_t = m.ps("ps_t", [P, 2, 512])
        ps_y = m.ps("ps_y", [P, 2, D])
        transposed, t_copied, y_mm, y_ready, dve_step, y_read = (m.sem(n) for n in "transposed t_copied y_mm y_ready dve_step y_read".split())
        x_in = [m.sem(f"x_in{k}") for k in range(2)]
        stored = [m.sem(f"stored{k}") for k in range(2)]
        block = ctx.enter_context(nc.Block())

        @block.sync
        def _(sp):
            weights.load(sp, w_out)
            norm.load(sp, g, b)
            for i in range(NT):
                if i >= 2:
                    sp.wait_ge(y_read, i - 1)
                sp.dma_start(xr[:, i % 2, :], x[i * P:(i + 1) * P, :]).then_inc(x_in[i % 2], 16)
                if i:
                    sp.wait_ge(y_ready, i)
                    sp.dma_start(h_out[(i - 1) * P:i * P, :], y[:, (i - 1) % 2, :]).then_inc(stored[(i - 1) % 2], 16)
            sp.wait_ge(y_ready, NT)
            sp.dma_start(h_out[(NT - 1) * P:, :], y[:, (NT - 1) % 2, :]).then_inc(stored[(NT - 1) % 2], 16)
            for k in range(2):
                sp.wait_ge(stored[k], 16 * NT // 2)

        @block.tensor
        def _(pe):
            def transposes(i):
                if i >= 2:
                    pe.wait_ge(t_copied, i - 1)
                for c in range(4):
                    x_ = pe.transpose(ps_t[:, i % 2, c * P:(c + 1) * P], keep["o_tok"][:, i, c * P:(c + 1) * P], keep["ident"][:, :])
                x_.then_inc(transposed, 1)

            transposes(0)
            for i in range(NT):
                if i + 1 < NT:
                    transposes(i + 1)
                if i >= 2:
                    pe.wait_ge(y_read, i - 1)
                pe.wait_ge(t_copied, i + 1)
                for half in range(2):
                    for c in range(KC):
                        if i == 0:
                            weights.wait(pe, half, c)
                        lhs = keep["qaT"][:, c, i * P:(i + 1) * P] if c < 4 else oT[:, i % 2, c - 4, :]
                        x_ = pe.matmul(ps_y[:, i % 2, half * 512:(half + 1) * 512], lhs, w[:, c, half * 512:(half + 1) * 512],
                                       start=(c == 0), stop=(c == KC - 1))
                x_.then_inc(y_mm, 1)

        @block.scalar
        def _(act):
            for i in range(NT):
                act.wait_ge(transposed, i + 1)
                if i >= 2:
                    act.wait_ge(y_mm, i - 1)
                act.activation(oT[:, i % 2, :, :], ps_t[:, i % 2, :].rearrange("p (c t) -> p c t", c=4), ACT.Copy).then_inc(t_copied, 1)
                if i:
                    norm.on_act(act, i - 1)
            norm.on_act(act, NT - 1)

        @block.vector
        def _(dve):
            step = [0]

            def then(ins):
                step[0] += 1
                ins.then_inc(dve_step, 1)
                dve.wait_ge(dve_step, step[0])

            for i in range(NT):
                dve.wait_ge(y_mm, i + 1)
                dve.wait_ge(x_in[i % 2], 16 * (i // 2 + 1))
                if i >= 2:
                    dve.wait_ge(stored[i % 2], 16 * (i // 2))
                yy = y[:, i % 2, :]
                dve.scalar_tensor_tensor(out=yy, in0=xr[:, i % 2, :], scalar=ALPHA, in1=ps_y[:, i % 2, :],
                                         op0=ALU.mult, op1=ALU.add).then_inc(y_read, 1)
                dve.wait_ge(y_read, i + 1)
                norm.on_dve(dve, then, yy, i).then_inc(y_ready, 1)


TURN = 4
AHEAD = 3


class Moe:

    def __init__(self, nc, ctx, name, y, w_gate, w_up, w_down):
        m = self.m = Stage(nc, ctx, name)
        self.name, self.w_gate, self.w_up, self.w_down = name, w_gate, w_up, w_down
        self.ident = m.sb("ident", [P, P])
        self.acc = m.sb("acc", [P, NT, D])
        self.w = m.sb("w", [P, 4, 3, 2048])
        self.dest = m.sb("dest", [P, NT, TOPK], I32)
        self.gates = m.sb("gates", [P, NT, TOPK])
        self.slot_tok = m.sb("slot_tok", [CAP, NBLK])
        self.spill = m.sb("spill", [1, 1 + NSPILL], I32)
        self.wgu_in = [m.sem(f"wgu_in{s}") for s in range(4)]
        self.wd_in = [m.sem(f"wd_in{s}") for s in range(4)]
        self.work = m.sb("work", [P, NT * TOPK * P])
        self.xg = self.work[:, 0:TURN * D].rearrange("p (s d) -> p s d", s=TURN)
        self.idx = m.sb("idx", [P, TURN], I32)
        self.idx_done = m.sem("idx_done")
        self.gathered = [m.sem(f"gathered{k}") for k in range(TURN)]
        self.y = y

    def index(self, dve, n, s):
        dve.tensor_scalar(self.idx[:, s:s + 1], self.slot_tok[:, bass.ds(n, 1)], 1.0, None, ALU.mult).then_inc(self.idx_done, 1)

    def gather(self, pool, h, s):
        pool.indirect_dma_start(out=self.xg[:, s, :], out_offset=None, in_=h,
                                in_offset=bass.IndirectOffsetOnAxis(ap=self.idx[:, s:s + 1], axis=0)).then_inc(self.gathered[s], 16)

    def gu(self, s, c):
        return self.w[:, s, 0:2, c * FH:(c + 1) * FH]

    def down(self, s):
        return self.w[:, s, 2, :].rearrange("p (c n) -> p c n", c=2)

    def load(self, eng, e, s):
        for k, (w, sem) in enumerate(((self.w_gate, self.wgu_in[s]), (self.w_up, self.wgu_in[s]), (self.w_down, self.wd_in[s]))):
            eng.dma_start(self.w[:, s, k, :], self.rows(w, e)).then_inc(sem, 16)

    def rows(self, w, e):
        return w[bass.ds(e, 1), :, :].rearrange("a (p c) f -> p (a c f)", p=P)


def stage_route(nc, M, h, router, bias, sh_gate, sh_up, sh_down, consts):
    with ExitStack() as ctx:
        m = Stage(nc, ctx, M.name + "r")
        spare = M.w[:, 2:4, :, :].rearrange("p s a b -> p (s a b)")
        hT = spare[:, 0:8192].rearrange("p (c t) -> p c t", c=KC)
        hidT = spare[:, 8192:10240].rearrange("p (c t) -> p c t", c=2)
        w_sh = m.sb("w_sh", [P, 2, KC, FH])
        w_shd = m.sb("w_shd", [P, 2, D])
        w_r = m.sb("w_r", [P, KC, NE])
        bias_sb = m.sb("bias", [P, NE])
        tri8 = m.sb("tri8", [P, 8, 8])
        cexp = m.sb("cexp", [P, 3, NE])
        before = m.sb("before", [P, 2, P])
        cspill = m.sb("cspill", [1, NSPILL])
        ctok = m.sb("ctok", [P, NT])
        score = m.sb("score", [P, NT, NE])
        biased = m.sb("biased", [P, NT, NE])
        m8 = m.sb("m8", [P, NT * 8, 8])
        gs = m.sb("gs", [P, 3, NT, 8])
        cmp_ = m.sb("cmp", [P, 2, NT, 8, 8])
        top = m.sb("top", [P, NT, 8])
        tid = m.sb("tid", [P, NT, 8], U32)
        tidf = m.sb("tidf", [P, NT, 8])
        work = M.work
        onehot = work[:, 0:NT * TOPK * NE].rearrange("p (i k e) -> p i k e", i=NT, k=TOPK)
        prod = work[:, NT * TOPK * NE:].rearrange("p (i k e) -> p i k e", i=NT, k=TOPK)
        place_hot = work[:, :].rearrange("p (i k s) -> p i k s", i=NT, k=TOPK)
        block_tok = M.w[:, 1, :, :].rearrange("p a b -> p (a b)")[:, 0:NT * TOPK * NBLK].rearrange("p (i k b) -> p i k b", i=NT, k=TOPK)
        iota = m.sb("iota", [P, P])
        blockf = m.sb("blockf", [P, 2, NT, TOPK])
        mem = m.sb("mem", [P, NT, NE])
        slot = m.sb("slot", [P, NT, NE])
        over = m.sb("over", [P, NT, NE])
        nb = m.sb("nb", [P, 3, NE])
        ones = m.sb("ones", [P, NE])
        gsum = m.sb("gsum", [P, 2, NT])
        destf = m.sb("destf", [P, NT, TOPK])
        sil = m.sb("sil", [P, 2, 512])
        spillf = m.sb("spillf", [1, 1 + NSPILL])
        ps_t = m.ps("ps_t", [P, 2, 512])
        ps_a = m.ps("ps_a", [P, 4, 512])
        ps_r = m.ps("ps_r", [P, NT, NE])
        ps_p = m.ps("ps_p", [P, NT, NE])
        h_in = [m.sem(f"h_in{i}") for i in range(NT)]
        (ident_in, rw_in, sw_in, c_in, transposed, t_act, t_dve, logits_done, score_done, members, pos_done,
         hid_mm, sil_done, hid_done, dn_mm, acc_done, dve_step, blocks_done, blocks_scaled, places_done, tab_mm, cnt_done) = (m.sem(n) for n in
            "ident_in rw_in sw_in c_in transposed t_act t_dve logits_done score_done members pos_done hid_mm sil_done hid_done dn_mm acc_done dve_step blocks_done blocks_scaled places_done tab_mm cnt_done".split())
        block = ctx.enter_context(nc.Block())

        @block.sync
        def _(sp):
            sp.dma_start(M.ident[:, :], consts["c_ident"]).then_inc(ident_in, 16)
            for i in range(NT):
                sp.dma_start(M.acc[:, i, :], h[i * P:(i + 1) * P, :]).then_inc(h_in[i], 16)
            sp.dma_start(w_r[:, :, :], router.rearrange("(p c) e -> p c e", c=KC)).then_inc(rw_in, 16)
            sp.dma_start(bias_sb[:, :], bias.partition_broadcast(P)).then_inc(c_in, 16)
            for dst, n in ((tri8, "c_tri8"), (cexp, "c_exp"), (before, "c_before"), (cspill, "c_spill"), (ctok, "c_tok"), (iota, "c_iota")):
                sp.dma_start(dst[:], consts[n]).then_inc(c_in, 16)
            for i, w in enumerate((sh_gate, sh_up)):
                sp.dma_start(w_sh[:, i, :, :], w.rearrange("(p c) f -> p c f", c=KC)).then_inc(sw_in, 16)
            sp.dma_start(w_shd[:, :, :], sh_down.rearrange("(p c) n -> p c n", c=2)).then_inc(sw_in, 16)
            M.load(sp, 0, 0)
            sp.wait_ge(tab_mm, 1)
            M.load(sp, 1, 1)

        @block.gpsimd
        def _(pool):
            for n in range(AHEAD):
                pool.wait_ge(M.idx_done, n + 1)
                M.gather(pool, h, n)

        @block.tensor
        def _(pe):
            def hidden(u):
                fc, half = u // 2, u % 2
                if u >= 2:
                    pe.wait_ge(hid_done, u - 1)
                for gu in range(2):
                    for c in range(KC):
                        x = pe.matmul(ps_a[:, 2 * (u % 2) + gu, :], w_sh[:, gu, c, fc::2], hT[:, c, half * 512:(half + 1) * 512],
                                      start=(c == 0), stop=(c == KC - 1))
                x.then_inc(hid_mm, 1)

            pe.wait_ge(ident_in, 16)
            for n in range(2 * NT):
                i, c0 = n // 2, 4 * (n % 2)
                pe.wait_ge(h_in[i], 16)
                if n >= 2:
                    pe.wait_ge((t_act, t_dve)[n % 2], n // 2)
                for c in range(4):
                    x = pe.transpose(ps_t[:, n % 2, c * P:(c + 1) * P],
                                     M.acc[:, i, c0 + c::KC], M.ident[:, :])
                x.then_inc(transposed, 1)
            pe.wait_ge(t_act, NT)
            pe.wait_ge(t_dve, NT)
            pe.wait_ge(rw_in, 16)
            for i in range(NT):
                for c in range(KC):
                    x = pe.matmul(ps_r[:, i, :], hT[:, c, i * P:(i + 1) * P], w_r[:, c, :], start=(c == 0), stop=(c == KC - 1),
                                  skip_group_check=True)
            x.then_inc(logits_done, 1)
            pe.wait_ge(sw_in, 48)
            hidden(0)
            hidden(1)
            pe.wait_ge(c_in, 112)
            pe.wait_ge(members, 1)
            for j in range(NT):
                x = pe.matmul(ps_r[:, 0, :], before[:, 1, :], mem[:, j, :], start=(j == 0), stop=(j == NT - 1), skip_group_check=True)
            x.then_inc(cnt_done, 1)
            for i in range(NT):
                for j in range(i + 1):
                    x = pe.matmul(ps_p[:, i, :], before[:, 0 if j == i else 1, :], mem[:, j, :], start=(j == 0), stop=(j == i),
                                  skip_group_check=True)
            x.then_inc(pos_done, 1)
            hidden(2)
            hidden(3)
            pe.wait_ge(places_done, 1)
            for i in range(NT):
                pe.wait_ge(blocks_scaled, i + 1)
                for k in range(TOPK):
                    x = pe.matmul(ps_t[:, 0, 0:NBLK], place_hot[:, i, k, :], block_tok[:, i, k, :],
                                  start=(i == 0 and k == 0), stop=(i == NT - 1 and k == TOPK - 1))
            x.then_inc(tab_mm, 1)
            for i in range(NT):
                pe.wait_ge(hid_done, 4)
                if i >= 2:
                    pe.wait_ge(acc_done, i - 1)
                for half in range(2):
                    for c in range(2):
                        x = pe.matmul(ps_a[:, 2 * (i % 2) + half, :], hidT[:, c, i * P:(i + 1) * P], w_shd[:, c, half * 512:(half + 1) * 512],
                                      start=(c == 0), stop=(c == 1))
                x.then_inc(dn_mm, 1)

        @block.scalar
        def _(act):
            for i in range(NT):
                act.wait_ge(transposed, 2 * i + 1)
                act.activation(hT[:, 0:4, i * P:(i + 1) * P], ps_t[:, 0, :].rearrange("p (c t) -> p c t", c=4), ACT.Copy).then_inc(t_act, 1)
            act.wait_ge(logits_done, 1)
            act.activation(score[:, :, :], ps_r[:, :, :], ACT.Sigmoid).then_inc(score_done, 1)
            for u in range(4):
                act.wait_ge(hid_mm, u + 1)
                if u >= 2:
                    act.wait_ge(hid_done, u - 1)
                act.activation(sil[:, u % 2, :], ps_a[:, 2 * (u % 2), :], ACT.Silu).then_inc(sil_done, 1)
                if u == 2:
                    act.wait_ge(blocks_done, 1)
                    for i in range(NT):
                        act.activation(block_tok[:, i, :, :], block_tok[:, i, :, :], ACT.Copy, scale=ctok[:, i:i + 1]).then_inc(blocks_scaled, 1)

        @block.vector
        def _(dve):
            step = [0]

            def then(ins):
                step[0] += 1
                ins.then_inc(dve_step, 1)
                dve.wait_ge(dve_step, step[0])

            for i in range(NT):
                dve.wait_ge(transposed, 2 * i + 2)
                dve.tensor_copy(hT[:, 4:8, i * P:(i + 1) * P], ps_t[:, 1, :].rearrange("p (c t) -> p c t", c=4)).then_inc(t_dve, 1)

            def hidden(u):
                fc, half = u // 2, u % 2
                dve.wait_ge(sil_done, u + 1)
                dve.tensor_tensor(hidT[:, fc, half * 512:(half + 1) * 512], sil[:, u % 2, :], ps_a[:, 2 * (u % 2) + 1, :], ALU.mult).then_inc(hid_done, 1)

            dve.wait_ge(score_done, 1)
            dve.wait_ge(c_in, 112)
            then(dve.tensor_tensor(biased[:, :, :], score[:, :, :], bias_sb[:, :].unsqueeze(1).to_broadcast([P, NT, NE]), ALU.add))
            bg = biased[:, :, :].rearrange("p i (g e) -> p (i g) e", e=8)
            for n in range(8 * NT):
                x = dve.max(m8[:, n, :], bg[:, n, :])
            then(x)
            pair = m8[:, :, :].rearrange("p (i g) k -> p i g k", g=8)
            then(dve.tensor_tensor(gs[:, 0, :, :], pair[:, :, :, 0], pair[:, :, :, 1], ALU.add))
            other = gs[:, 0, :, :].unsqueeze(2).to_broadcast([P, NT, 8, 8])
            own = gs[:, 0, :, :].unsqueeze(3).to_broadcast([P, NT, 8, 8])
            then(dve.tensor_tensor(cmp_[:, 0, :, :, :], other, own, ALU.is_gt))
            then(dve.tensor_tensor(cmp_[:, 1, :, :, :], other, own, ALU.is_equal))
            then(dve.tensor_tensor(cmp_[:, 1, :, :, :], cmp_[:, 1, :, :, :], tri8[:, :, :].unsqueeze(1).to_broadcast([P, NT, 8, 8]), ALU.mult))
            then(dve.tensor_tensor(cmp_[:, 0, :, :, :], cmp_[:, 0, :, :, :], cmp_[:, 1, :, :, :], ALU.add))
            then(dve.tensor_reduce(gs[:, 1, :, :], cmp_[:, 0, :, :, :], AX, ALU.add))
            then(dve.tensor_scalar(gs[:, 1, :, :], gs[:, 1, :, :], 3.5, None, ALU.is_lt))
            then(dve.tensor_scalar(gs[:, 2, :, :], gs[:, 1, :, :], -NEG, NEG, ALU.mult, ALU.add))
            b4 = biased[:, :, :].rearrange("p i (g e) -> p i g e", e=8)
            then(dve.tensor_tensor(b4, b4, gs[:, 1, :, :].unsqueeze(3).to_broadcast([P, NT, 8, 8]), ALU.mult))
            then(dve.tensor_tensor(b4, b4, gs[:, 2, :, :].unsqueeze(3).to_broadcast([P, NT, 8, 8]), ALU.add))
            for i in range(NT):
                x = dve.max(top[:, i, :], biased[:, i, :])
            then(x)
            for i in range(NT):
                x = dve.max_index(tid[:, i, :], top[:, i, :], biased[:, i, :])
            then(x)
            then(dve.tensor_copy(tidf[:, :, :], tid[:, :, :]))
            then(dve.tensor_tensor(onehot, tidf[:, :, 0:TOPK].unsqueeze(3).to_broadcast([P, NT, TOPK, NE]),
                                   cexp[:, 0, :].unsqueeze(1).unsqueeze(1).to_broadcast([P, NT, TOPK, NE]), ALU.is_equal))
            dve.tensor_reduce(mem[:, :, :], onehot.rearrange("p i k e -> p i e k"), AX, ALU.add).then_inc(members, 1)
            hidden(0)
            then(dve.tensor_tensor(prod, onehot, score[:, :, :].unsqueeze(2).to_broadcast([P, NT, TOPK, NE]), ALU.mult))
            then(dve.tensor_reduce(M.gates[:, :, :], prod, AX, ALU.add))
            then(dve.tensor_reduce(gsum[:, 0, :], M.gates[:, :, :], AX, ALU.add))
            then(dve.reciprocal(gsum[:, 1, :], gsum[:, 0, :]))
            then(dve.tensor_tensor(M.gates[:, :, :], M.gates[:, :, :], gsum[:, 1, :].unsqueeze(2).to_broadcast([P, NT, TOPK]), ALU.mult))
            then(dve.tensor_scalar(M.gates[:, :, :], M.gates[:, :, :], 2.5, None, ALU.mult))
            hidden(1)
            dve.wait_ge(cnt_done, 1)
            then(dve.memset(ones[:, :], 1.0))
            then(dve.tensor_scalar(nb[:, 0, :], ps_r[:, 0, :], CAP + 0.5, None, ALU.is_gt))
            for k in range(2, S // CAP):
                then(dve.scalar_tensor_tensor(out=nb[:, 0, :], in0=ps_r[:, 0, :], scalar=k * CAP + 0.5, in1=nb[:, 0, :], op0=ALU.is_gt, op1=ALU.add))
            then(dve.tensor_tensor_scan(nb[:, 1, :], ones[:, :], nb[:, 0, :], 0.0, ALU.mult, ALU.add))
            then(dve.tensor_tensor(nb[:, 2, :], nb[:, 1, :], nb[:, 0, :], ALU.subtract))
            then(dve.scalar_tensor_tensor(out=nb[:, 2, :], in0=nb[:, 2, :], scalar=float(CAP), in1=cexp[:, 2, :], op0=ALU.mult, op1=ALU.add))
            dve.wait_ge(pos_done, 1)
            then(dve.tensor_scalar(over[:, :, :], ps_p[:, :, :], CAP - 0.5, None, ALU.is_gt))
            then(dve.tensor_tensor(over[:, :, :], over[:, :, :], nb[:, 2, :].unsqueeze(1).to_broadcast([P, NT, NE]), ALU.mult))
            then(dve.tensor_tensor(slot[:, :, :], ps_p[:, :, :], cexp[:, 1, :].unsqueeze(1).to_broadcast([P, NT, NE]), ALU.add))
            then(dve.tensor_tensor(slot[:, :, :], slot[:, :, :], over[:, :, :], ALU.add))
            then(dve.tensor_tensor(prod, onehot, slot[:, :, :].unsqueeze(2).to_broadcast([P, NT, TOPK, NE]), ALU.mult))
            then(dve.tensor_reduce(destf[:, :, :], prod, AX, ALU.add))
            then(dve.tensor_copy(M.dest[:, :, :], destf[:, :, :]))
            blk, place = blockf[:, 0, :, :], blockf[:, 1, :, :]
            then(dve.tensor_scalar(blk, destf[:, :, :], 1.0 / CAP, -(CAP - 1) / (2.0 * CAP), ALU.mult, ALU.add))
            then(dve.tensor_scalar(blk, blk, 12582912.0, None, ALU.add))
            then(dve.tensor_scalar(blk, blk, 12582912.0, None, ALU.subtract))
            then(dve.scalar_tensor_tensor(out=place, in0=blk, scalar=-float(CAP), in1=destf[:, :, :], op0=ALU.mult, op1=ALU.add))
            dve.tensor_tensor(block_tok, blk.unsqueeze(3).to_broadcast([P, NT, TOPK, NBLK]),
                              iota[:, 0:NBLK].unsqueeze(1).unsqueeze(1).to_broadcast([P, NT, TOPK, NBLK]), ALU.is_equal).then_inc(blocks_done, 1)
            hidden(2)
            dve.tensor_tensor(place_hot, place.unsqueeze(3).to_broadcast([P, NT, TOPK, P]),
                              iota[:, :].unsqueeze(1).unsqueeze(1).to_broadcast([P, NT, TOPK, P]), ALU.is_equal).then_inc(places_done, 1)
            hidden(3)
            dve.wait_ge(tab_mm, 1)
            then(dve.tensor_copy(M.slot_tok[:, :], ps_t[0:CAP, 0, 0:NBLK]))
            for n in range(AHEAD):
                M.index(dve, n, n)
            sp3 = prod[0:1, :, :, :].rearrange("p i k e -> p (i k) e")
            then(dve.tensor_copy(spillf[:, 0:1], nb[0:1, 1, NE - 1:NE]))
            then(dve.tensor_tensor(sp3, nb[0:1, 1, :].unsqueeze(1).to_broadcast([1, NSPILL, NE]),
                                   cspill[:, :].unsqueeze(2).to_broadcast([1, NSPILL, NE]), ALU.is_le))
            then(dve.tensor_reduce(spillf[:, 1:], sp3, AX, ALU.add))
            then(dve.tensor_scalar(spillf[:, 1:], spillf[:, 1:], float(NE - 1), None, ALU.min))
            then(dve.tensor_copy(M.spill[:, :], spillf[:, :]))
            for i in range(NT):
                dve.wait_ge(dn_mm, i + 1)
                dve.scalar_tensor_tensor(out=M.acc[:, i, :], in0=M.acc[:, i, :], scalar=ALPHA,
                                         in1=ps_a[:, 2 * (i % 2):2 * (i % 2) + 2, :].rearrange("p a b -> p (a b)"),
                                         op0=ALU.mult, op1=ALU.add).then_inc(acc_done, 1)


def stage_experts(nc, M, h):
    with ExitStack() as ctx:
        m = Stage(nc, ctx, M.name + "e")
        xg, idx_done, gathered = M.xg, M.idx_done, M.gathered
        xT = m.sb("xT", [P, 2, KC, P])
        sil = m.sb("sil", [P, 2, FH])
        a_ = m.sb("a", [P, 2, FH])
        aT = m.sb("aT", [P, 2, 2, P])
        yo = m.sb("yo", [P, 2, D])
        tick = m.sb("tick", [1, 1])
        ps_x = m.ps("ps_x", [P, 2, 512])
        ps_gu = m.ps("ps_gu", [P, 2, 512])
        ps_a = m.ps("ps_a", [P, 512])
        ps_y = m.ps("ps_y", [P, 2, 512])
        (xt_mm, x_act, x_dve, gu_done, sil_done, a_done, at_mm, at_done, y_mm, y_act, y_dve) = (m.sem(n) for n in
            "xt_mm x_act x_dve gu_done sil_done a_done at_mm at_done y_mm y_act y_dve".split())
        ticked = m.sem("ticked")
        stored = [m.sem(f"stored{k}") for k in range(2)]
        block = ctx.enter_context(nc.Block())

        def turns(eng, steps):
            for s in range(TURN):
                steps(0, s, s)
            with eng.Fori(1, NE // TURN - 1) as t:
                for s in range(TURN):
                    steps(t, s, t * TURN + s)
            for s in range(TURN):
                steps(NE // TURN - 1, s, NE - TURN + s)

        def first(n, count):
            return isinstance(n, int) and n < count

        def last(n, count):
            return isinstance(n, int) and n >= NE - count

        @block.sync
        def _(sp):
            def steps(t, s, n):
                if not first(n, 1):
                    if not last(n, TURN - 1):
                        sp.wait_ge(y_mm, n)
                        M.load(sp, n + (TURN - 1), (s - 1) % TURN)
                    sp.wait_ge(y_act, n)
                    sp.wait_ge(y_dve, n)
                    sp.dma_start(M.y[bass.ds((n - 1) * CAP, CAP), :], yo[:, (s - 1) % 2, :]).then_inc(stored[(s - 1) % 2], 16)

            for s in range(2, TURN):
                M.load(sp, s, s)
            turns(sp, steps)
            sp.wait_ge(y_act, NE)
            sp.wait_ge(y_dve, NE)
            sp.dma_start(M.y[(NE - 1) * CAP:NE * CAP, :], yo[:, (NE - 1) % 2, :]).then_inc(stored[(NE - 1) % 2], 16)
            for k in range(2):
                sp.wait_ge(stored[k], 16 * NE // 2)

        @block.gpsimd
        def _(pool):
            def steps(t, s, n):
                if first(n, AHEAD):
                    return
                pool.wait_ge(idx_done, n + 1)
                if not first(n, TURN):
                    pool.wait_ge(xt_mm, n - (TURN - 1))
                    pool.wait_ge(ticked, n - AHEAD)
                pool.tensor_tensor(tick[:, :], M.slot_tok[0:1, 0:1], M.slot_tok[0:1, 0:1], ALU.add).then_inc(ticked, 1)
                M.gather(pool, h, s)
            turns(pool, steps)

        @block.tensor
        def _(pe):
            def tokens(t, s, n):
                pe.wait_ge(gathered[s], (t + 1) * 16)
                pe.wait_ge(x_act, n)
                pe.wait_ge(x_dve, n)
                for c in range(KC):
                    x = pe.transpose(ps_x[:, c // 4, (c % 4) * P:(c % 4 + 1) * P], xg[:, s, c::KC], M.ident[:, :])
                x.then_inc(xt_mm, 1)

            def gate_up(t, s, n, part):
                if part == 0:
                    pe.wait_ge(M.wgu_in[s], (t + 1) * 32)
                    pe.wait_ge(x_act, n + 1)
                    pe.wait_ge(x_dve, n + 1)
                    if not first(n, 2):
                        pe.wait_ge(a_done, n - 1)
                for c in range(4 * part, 4 * part + 4):
                    x = pe.matmul(ps_gu[:, s % 2, :], xT[:, s % 2, c, :], M.gu(s, c), start=(c == 0), stop=(c == KC - 1))
                if part:
                    x.then_inc(gu_done, 1)

            def hidden(s, n):
                pe.wait_ge(a_done, n)
                if not first(n, 2):
                    pe.wait_ge(at_done, n - 1)
                for c in range(2):
                    x = pe.transpose(ps_a[:, c * P:(c + 1) * P], a_[:, (s - 1) % 2, c::2], M.ident[:, :])
                x.then_inc(at_mm, 1)

            def down(wd_count, s, n):
                k = (s - 1) % TURN
                pe.wait_ge(M.wd_in[k], wd_count * 16)
                pe.wait_ge(at_done, n)
                if not first(n, 2):
                    pe.wait_ge(y_act, n - 1)
                    pe.wait_ge(y_dve, n - 1)
                for half in range(2):
                    for c in range(2):
                        x = pe.matmul(ps_y[:, half, :], aT[:, k % 2, c, :], M.down(k)[:, c, half * 512:(half + 1) * 512], start=(c == 0), stop=(c == 1))
                x.then_inc(y_mm, 1)

            def steps(t, s, n):
                if not last(n, 1):
                    tokens(t + (s + 1) // TURN, (s + 1) % TURN, n + 1)
                gate_up(t, s, n, 0)
                if not first(n, 1):
                    hidden(s, n)
                gate_up(t, s, n, 1)
                if not first(n, 1):
                    down(t + 1 if s else t, s, n)

            tokens(0, 0, 0)
            turns(pe, steps)
            hidden(TURN, NE)
            down(NE // TURN, TURN, NE)

        @block.scalar
        def _(act):
            act.preload_act_table(ACT.Silu)

            def tokens(s, n):
                act.wait_ge(xt_mm, n + 1)
                if not first(n, 2):
                    act.wait_ge(gu_done, n - 1)
                act.activation(xT[:, s % 2, 0:4, :], ps_x[:, 0, :].rearrange("p (c t) -> p c t", c=4), ACT.Copy).then_inc(x_act, 1)

            def silu(s, n):
                act.wait_ge(gu_done, n + 1)
                if not first(n, 2):
                    act.wait_ge(a_done, n - 1)
                act.activation(sil[:, s % 2, :], ps_gu[:, s % 2, 0:FH], ACT.Silu).then_inc(sil_done, 1)

            def out(count, s, n):
                act.wait_ge(y_mm, n)
                if not first(n, 3):
                    act.wait_ge(stored[(s - 1) % 2], count * 16)
                act.activation(yo[:, (s - 1) % 2, 0:512], ps_y[:, 0, :], ACT.Copy).then_inc(y_act, 1)

            def steps(t, s, n):
                if not last(n, 1):
                    tokens(s + 1, n + 1)
                silu(s, n)
                if not first(n, 1):
                    out(t * 2 + (s - 1) // 2, s, n)

            tokens(0, 0)
            turns(act, steps)
            out(NE // 2 - 1, TURN, NE)

        @block.vector
        def _(dve):
            def index(t, s, n):
                if not first(n, TURN):
                    dve.wait_ge(gathered[s], t * 16)
                M.index(dve, n, s)

            def tokens(s, n):
                dve.wait_ge(xt_mm, n + 1)
                if not first(n, 2):
                    dve.wait_ge(gu_done, n - 1)
                dve.tensor_copy(xT[:, s % 2, 4:8, :], ps_x[:, 1, :].rearrange("p (c t) -> p c t", c=4)).then_inc(x_dve, 1)

            def mult(s, n):
                dve.wait_ge(sil_done, n + 1)
                if not first(n, 2):
                    dve.wait_ge(at_mm, n - 1)
                dve.tensor_tensor(a_[:, s % 2, :], sil[:, s % 2, :], ps_gu[:, s % 2, FH:2 * FH], ALU.mult).then_inc(a_done, 1)

            def hidden(s, n):
                dve.wait_ge(at_mm, n)
                if not first(n, 3):
                    dve.wait_ge(y_mm, n - 2)
                dve.tensor_copy(aT[:, (s - 1) % 2, :, :], ps_a[:, 0:2 * P].rearrange("p (c t) -> p c t", c=2)).then_inc(at_done, 1)

            def out(count, s, n):
                dve.wait_ge(y_mm, n)
                if not first(n, 3):
                    dve.wait_ge(stored[(s - 1) % 2], count * 16)
                dve.tensor_copy(yo[:, (s - 1) % 2, 512:1024], ps_y[:, 1, :]).then_inc(y_dve, 1)

            def steps(t, s, n):
                if not last(n, AHEAD):
                    index(t + (s + AHEAD) // TURN, (s + AHEAD) % TURN, n + AHEAD)
                if not last(n, 1):
                    tokens(s + 1, n + 1)
                if not first(n, 1):
                    hidden(s, n)
                mult(s, n)
                if not first(n, 1):
                    out(t * 2 + (s - 1) // 2, s, n)

            tokens(0, 0)
            turns(dve, steps)
            hidden(TURN, NE)
            out(NE // 2 - 1, TURN, NE)


def stage_spill(nc, M, h):
    with ExitStack() as ctx:
        m = Stage(nc, ctx, M.name + "s")
        xg = m.sb("xg", [P, D])
        xT = m.sb("xT", [P, KC, P])
        idx = m.sb("idx", [P, 1], I32)
        sil = m.sb("sil", [P, FH])
        a_ = m.sb("a", [P, FH])
        aT = m.sb("aT", [P, 2, P])
        yo = m.sb("yo", [P, D])
        tick = m.sb("tick", [1, 1])
        ps_x = m.ps("ps_x", [P, 2, 512])
        ps_gu = m.ps("ps_gu", [P, 512])
        ps_a = m.ps("ps_a", [P, 512])
        ps_y = m.ps("ps_y", [P, 2, 512])
        (w_in, idx_done, gathered, xt_mm, x_done, gu_done, sil_done, a_done, at_mm, at_done, y_mm, y_done, stored) = (m.sem(n) for n in
            "w_in idx_done gathered xt_mm x_done gu_done sil_done a_done at_mm at_done y_mm y_done stored".split())
        ticked = m.sem("ticked")
        last = m.sb("last", [1, 1])
        block = ctx.enter_context(nc.Block())

        def blocks(eng, body):
            n = eng.value_load(M.spill[0:1, 0:1], min_val=0, max_val=NSPILL)
            with eng.Fori(0, NSPILL // 6) as six:
                with eng.If(six * 6 < n):
                    with eng.Fori(0, 6) as b:
                        with eng.If(six * 6 + b < n):
                            body(six * 6 + b)

        @block.sync
        def _(sp):
            def body(b):
                sp.wait_ge(y_mm, b)
                e = sp.value_load(M.spill[0:1, bass.ds(b + 1, 1)], min_val=0, max_val=NE - 1)
                for k, w in enumerate((M.w_gate, M.w_up, M.w_down)):
                    sp.dma_start(M.w[:, 0, k, :], M.rows(w, e)).then_inc(w_in, 16)
                sp.wait_ge(y_done, b + 1)
                sp.dma_start(M.y[bass.ds(SPILL0 + b * CAP, CAP), :], yo[:, :]).then_inc(stored, 16)
            blocks(sp, body)

        @block.gpsimd
        def _(pool):
            def body(b):
                pool.wait_ge(idx_done, b + 1)
                pool.wait_ge(xt_mm, b)
                pool.wait_ge(ticked, b)
                pool.tensor_tensor(tick[:, :], M.slot_tok[0:1, 0:1], M.slot_tok[0:1, 0:1], ALU.add).then_inc(ticked, 1)
                pool.indirect_dma_start(out=xg[:, :], out_offset=None, in_=h,
                                        in_offset=bass.IndirectOffsetOnAxis(ap=idx[:, 0:1], axis=0)).then_inc(gathered, 16)
            blocks(pool, body)

        @block.tensor
        def _(pe):
            def body(b):
                pe.wait_ge(gathered, (b + 1) * 16)
                for c in range(KC):
                    x = pe.transpose(ps_x[:, c // 4, (c % 4) * P:(c % 4 + 1) * P], xg[:, c::KC], M.ident[:, :])
                x.then_inc(xt_mm, 1)
                pe.wait_ge(x_done, b + 1)
                pe.wait_ge(w_in, (b + 1) * 48)
                for c in range(KC):
                    x = pe.matmul(ps_gu[:, :], xT[:, c, :], M.gu(0, c), start=(c == 0), stop=(c == KC - 1))
                x.then_inc(gu_done, 1)
                pe.wait_ge(a_done, b + 1)
                for c in range(2):
                    x = pe.transpose(ps_a[:, c * P:(c + 1) * P], a_[:, c::2], M.ident[:, :])
                x.then_inc(at_mm, 1)
                pe.wait_ge(at_done, b + 1)
                for half in range(2):
                    for c in range(2):
                        x = pe.matmul(ps_y[:, half, :], aT[:, c, :], M.down(0)[:, c, half * 512:(half + 1) * 512], start=(c == 0), stop=(c == 1))
                x.then_inc(y_mm, 1)
            blocks(pe, body)

        @block.scalar
        def _(act):
            def body(b):
                act.wait_ge(gu_done, b + 1)
                act.activation(sil[:, :], ps_gu[:, 0:FH], ACT.Silu).then_inc(sil_done, 1)
            blocks(act, body)

        @block.vector
        def _(dve):
            def body(b):
                dve.wait_ge(gathered, b * 16)
                dve.tensor_scalar(idx[:, :], M.slot_tok[:, bass.ds(NE + b, 1)], 1.0, None, ALU.mult).then_inc(idx_done, 1)
                dve.wait_ge(xt_mm, b + 1)
                dve.tensor_copy(xT[:, :, :], ps_x[:, :, :].rearrange("p a (c t) -> p (a c) t", c=4)).then_inc(x_done, 1)
                dve.wait_ge(sil_done, b + 1)
                dve.tensor_tensor(a_[:, :], sil[:, :], ps_gu[:, FH:2 * FH], ALU.mult).then_inc(a_done, 1)
                dve.wait_ge(at_mm, b + 1)
                dve.tensor_copy(aT[:, :, :], ps_a[:, 0:2 * P].rearrange("p (c t) -> p c t", c=2)).then_inc(at_done, 1)
                dve.wait_ge(y_mm, b + 1)
                dve.tensor_copy(yo[:, :], ps_y[:, :, :].rearrange("p a b -> p (a b)")).then_inc(y_done, 1)
                dve.wait_ge(stored, (b + 1) * 16)
                dve.memset(last[:, :], 0.0)
            blocks(dve, body)


def stage_combine(nc, M, g, b, h_out):
    with ExitStack() as ctx:
        m = Stage(nc, ctx, M.name + "c")
        SLOTS = 4
        ON_DVE = 1
        ON_PE = TOPK - ON_DVE
        rows = M.w[:, :, :, :].rearrange("p s a b -> p (s a b)")[:, 0:SLOTS * TOPK * D].rearrange("p (s k d) -> p s k d", s=SLOTS, k=TOPK)
        diag = m.sb("diag", [P, NT, ON_PE, P])
        g_sb, b_sb = m.sb("ln_g", [P, D]), m.sb("ln_b", [P, D])
        stats = m.sb("stats", [P, 2, 2, 6])
        mv = m.sb("mv", [P, 2, 2])
        inv, rstd = (m.sb(n, [P, 2, 1]) for n in ("inv", "rstd"))
        ps = m.ps("sum", [P, 2, D])
        (gb_in, diag_done, rows_read, rows_used, added, var_ready, rstd_ready, tile_done, dve_step, stored) = (m.sem(n) for n in
            "gb_in diag_done rows_read rows_used added var_ready rstd_ready tile_done dve_step stored".split())
        rows_in = [m.sem(f"rows_in{k}") for k in range(SLOTS)]
        block = ctx.enter_context(nc.Block())

        @block.gpsimd
        def _(pool):
            for i in range(NT):
                if i >= SLOTS:
                    pool.wait_ge(rows_read, i - SLOTS + 1)
                    pool.wait_ge(rows_used, i - SLOTS + 1)
                for k in range(TOPK):
                    pool.indirect_dma_start(out=rows[:, i % SLOTS, k, :], out_offset=None, in_=M.y,
                                            in_offset=bass.IndirectOffsetOnAxis(ap=M.dest[:, i, k:k + 1], axis=0)).then_inc(rows_in[i % SLOTS], 16)

        @block.sync
        def _(sp):
            sp.dma_start(g_sb[:, :], g.partition_broadcast(P)).then_inc(gb_in, 16)
            sp.dma_start(b_sb[:, :], b.partition_broadcast(P)).then_inc(gb_in, 16)
            for i in range(NT):
                sp.wait_ge(tile_done, i + 1)
                sp.dma_start(h_out[i * P:(i + 1) * P, :], M.acc[:, i, :]).then_inc(stored, 16)
            sp.wait_ge(stored, 16 * NT)

        @block.tensor
        def _(pe):
            pe.wait_ge(diag_done, 1)
            for i in range(NT):
                pe.wait_ge(rows_in[i % SLOTS], 16 * TOPK * (i // SLOTS + 1))
                if i >= 2:
                    pe.wait_ge(added, i - 1)
                for half in range(2):
                    for k in range(ON_PE):
                        x = pe.matmul(ps[:, i % 2, half * 512:(half + 1) * 512], diag[:, i, k, :],
                                      rows[:, i % SLOTS, ON_DVE + k, half * 512:(half + 1) * 512], start=(k == 0), stop=(k == ON_PE - 1))
                x.then_inc(rows_used, 1)

        @block.scalar
        def _(act):
            for i in range(NT):
                act.wait_ge(var_ready, i + 1)
                act.activation(rstd[:, i % 2, :], inv[:, i % 2, :], ACT.Sqrt).then_inc(rstd_ready, 1)

        @block.vector
        def _(dve):
            step = [0]

            def then(ins):
                step[0] += 1
                ins.then_inc(dve_step, 1)
                dve.wait_ge(dve_step, step[0])

            def total(i):
                y, s = M.acc[:, i, :], i % 2
                dve.wait_ge(rows_in[i % SLOTS], 16 * TOPK * (i // SLOTS + 1))
                for k in range(ON_DVE):
                    x = dve.scalar_tensor_tensor(out=y, in0=rows[:, i % SLOTS, k, :], scalar=M.gates[:, i, k:k + 1], in1=y, op0=ALU.mult, op1=ALU.add)
                    if k < ON_DVE - 1:
                        then(x)
                x.then_inc(rows_read, 1)
                dve.wait_ge(rows_read, i + 1)
                dve.wait_ge(rows_used, i + 1)
                dve.tensor_tensor(y, y, ps[:, s, :], ALU.add).then_inc(added, 1)
                dve.wait_ge(added, i + 1)
                dve.bn_stats(stats[:, s, 0, :], y[:, 0:512])
                then(dve.bn_stats(stats[:, s, 1, :], y[:, 512:1024]))
                then(dve.bn_aggr(mv[:, s, :], stats[:, s, :, :].rearrange("p a b -> p (a b)")))
                then(dve.tensor_scalar(inv[:, s, :], mv[:, s, 1:2], LN_EPS, None, ALU.add))
                dve.reciprocal(inv[:, s, :], inv[:, s, :]).then_inc(var_ready, 1)

            def scale(i):
                y, s = M.acc[:, i, :], i % 2
                then(dve.scalar_tensor_tensor(out=y, in0=y, scalar=mv[:, s, 0:1], in1=g_sb[:, :], op0=ALU.subtract, op1=ALU.mult))
                dve.wait_ge(rstd_ready, i + 1)
                dve.scalar_tensor_tensor(out=y, in0=y, scalar=rstd[:, s, :], in1=b_sb[:, :], op0=ALU.mult, op1=ALU.add).then_inc(tile_done, 1)

            for i in range(NT):
                x = dve.tensor_tensor(diag[:, i, :, :], M.ident[:, :].unsqueeze(1).to_broadcast([P, ON_PE, P]),
                                      M.gates[:, i, ON_DVE:].unsqueeze(2).to_broadcast([P, ON_PE, P]), ALU.mult)
            x.then_inc(diag_done, 1)
            dve.wait_ge(gb_in, 32)
            total(0)
            for i in range(1, NT):
                total(i)
                scale(i - 1)
            scale(NT - 1)


def moe_layer(nc, name, y, h, weights, ln_g, ln_b, consts, h_out):
    router, bias, w_gate, w_up, w_down, sh_gate, sh_up, sh_down = weights
    with ExitStack() as ctx:
        M = Moe(nc, ctx, name, y, w_gate, w_up, w_down)
        stage_route(nc, M, h, router, bias, sh_gate, sh_up, sh_down, consts)
        stage_experts(nc, M, h)
        stage_spill(nc, M, h)
        stage_combine(nc, M, ln_g, ln_b, h_out)


def stage_ssm_input(nc, h, w_in, lam_re, lam_im, log_dt, b_re, b_im, c_re, c_im, c_ident, ident, e_y, uT, power, reverse, bbar, into, out_of):
    with ExitStack() as ctx:
        m = Stage(nc, ctx, "si")
        ht = m.sb("ht", [P, 2, D])
        hT = m.sb("hT", [P, 2, KC, P])
        weights = Weights(m, "w")
        w = weights.tile
        u = e_y[:, :].rearrange("p (g j h) -> p g j h", g=NG, j=L)
        lam = m.sb("lam", [NQ, 3, P])
        ldt = m.sb("ldt", [NQ, 2])
        lp = m.sb("lp", [P, 3, NQ])
        v = m.sb("v", [P, 12, NQ])
        b_ = m.sb("b", [P, 2, NQ, GC])
        g_ = uT[:, :, :].rearrange("p g c -> p (g c)").rearrange("p (i q j h) -> p i q j h", i=2, q=NQ, j=L)
        room = into[:, :, :, :].rearrange("p q i s -> p (q i s)")
        tg = room[:, 0:NQ * L * GC].rearrange("p (q j h) -> p q j h", q=NQ, j=L)
        tb = room[:, NQ * L * GC:NQ * L * GC + 4 * NQ * GC].rearrange("p (k q h) -> p k q h", k=4, q=NQ)
        QV = 8
        tv = room[:, NQ * L * GC:NQ * L * GC + QV * (L + 1) * GC].rearrange("p (q t h) -> p q t h", q=QV, t=L + 1)
        last = room[:, NQ * L * GC + 4 * NQ * GC:]
        c_ = last.rearrange("p (i n s) -> p i n s", i=2, n=8)
        cT = last[:, 0:2 * NQ * GC].rearrange("p (i q h) -> p i q h", i=2, q=NQ)
        ps_c = m.ps("ps_c", [P, 512])
        ps_t = m.ps("ps_t", [P, 2, 512])
        ps_u = m.ps("ps_u", [P, 4, 512])
        ps_l = m.ps("ps_l", [P, 3, NQ])
        (c_in, transposed, t_copied, u_mm, u_done, g_t, g_act, g_dve) = (m.sem(n) for n in
            "c_in transposed t_copied u_mm u_done g_t g_act g_dve".split())
        (lam_in, ldt_in, b_in, bcast, l_t, l_done, args, acts, into_ready, i_t, i_act, i_dve, dve_step) = (m.sem(n) for n in
            "lam_in ldt_in b_in bcast l_t l_done args acts into_ready i_t i_act i_dve dve_step".split())
        cc_in, c_t, c_copied, out_done = (m.sem(n) for n in "cc_in c_t c_copied out_done".split())
        TWO_PI, MAGIC, EDGE = 2 * math.pi, 12582912.0, 3.1415925
        C1 = 6.28125
        C2 = float(np.float32(TWO_PI - C1))
        C3 = TWO_PI - C1 - C2
        h_in = [m.sem(f"h_in{k}") for k in range(2)]
        rows = h.rearrange("(c j) d -> j c d", j=L)
        block = ctx.enter_context(nc.Block())

        @block.sync
        def _(sp):
            sp.dma_start(ident[:, :], c_ident).then_inc(c_in, 16)
            for j in range(2):
                sp.dma_start(ht[:, j, :], rows[j]).then_inc(h_in[j], 16)
            sp.dma_start(lam[:, 0, :], lam_re.rearrange("(q two) p -> q (two p)", two=2)).then_inc(lam_in, 16)
            sp.dma_start(lam[:, 1, :], lam_im.rearrange("(q two) p -> q (two p)", two=2)).then_inc(lam_in, 16)
            sp.dma_start(ldt[:, :], log_dt.rearrange("(q two) -> q two", two=2)).then_inc(ldt_in, 16)
            weights.load(sp, w_in)
            for i, b in enumerate((b_re, b_im)):
                sp.dma_start(b_[:, i, :, :], b.rearrange("(q two) p h -> (two p) q h", two=2)).then_inc(b_in, 16)
            for i, c in enumerate((c_re, c_im)):
                for two in range(2):
                    sp.dma_start(c_[:, i, :, two * 64:(two + 1) * 64],
                                 c.rearrange("(n g) h p -> (g h) n p", n=8)).then_inc(cc_in, 16)
            for j in range(2, L):
                sp.wait_ge(transposed, 2 * (j - 1))
                sp.dma_start(ht[:, j % 2, :], rows[j]).then_inc(h_in[j % 2], 16)

        @block.tensor
        def _(pe):
            def transposes(j):
                pe.wait_ge(h_in[j % 2], 16 * (j // 2 + 1))
                for half in range(2):
                    if j:
                        pe.wait_ge(t_copied, 2 * (j - 1) + half + 1)
                    for c in range(4):
                        x = pe.transpose(ps_t[:, half, c * P:(c + 1) * P], ht[:, j % 2, (4 * half + c) * P:(4 * half + c + 1) * P], ident[:, :])
                    x.then_inc(transposed, 1)

            pe.wait_ge(c_in, 16)
            transposes(0)
            pe.wait_ge(lam_in, 32)
            pe.wait_ge(bcast, 1)
            for k in range(3):
                x = pe.transpose(ps_l[:, k, :], lam[:, k, :], ident[0:NQ, 0:NQ])
            x.then_inc(l_t, 1)
            for j in range(L):
                if j + 1 < L:
                    transposes(j + 1)
                pe.wait_ge(t_copied, 2 * (j + 1))
                if j >= 2:
                    pe.wait_ge(u_done, 2 * (j - 1))
                for half in range(2):
                    for c in range(KC):
                        if j == 0:
                            weights.wait(pe, half, c)
                        x = pe.matmul(ps_u[:, 2 * (j % 2) + half, :], hT[:, j % 2, c, :], w[:, c, half * 512:(half + 1) * 512],
                                      start=(c == 0), stop=(c == KC - 1))
                    x.then_inc(u_mm, 1)
                if 1 <= j <= 4:
                    pe.wait_ge(cc_in, 64)
                    if j > 1:
                        pe.wait_ge(c_copied, j - 1)
                    for n in range(4):
                        x = pe.transpose(ps_c[:, n * P:(n + 1) * P], c_[:, (j - 1) // 2, 4 * ((j - 1) % 2) + n, :], ident[:, :])
                    x.then_inc(c_t, 1)
            pe.wait_ge(into_ready, 1)
            for n in range(NQ // 2):
                if n >= 2:
                    pe.wait_ge((i_act, i_dve)[n % 2], n // 2)
                for k in range(4):
                    x = pe.transpose(ps_t[:, n % 2, k * P:(k + 1) * P],
                                     g_[:, k % 2, 2 * n + k // 2, :, :].rearrange("p j h -> p (j h)"), ident[:, :])
                x.then_inc(i_t, 1)
            pe.wait_ge(u_done, 2 * L)
            for n in range(NG // 4):
                if n >= 2:
                    pe.wait_ge((g_act, g_dve)[n % 2], n // 2)
                else:
                    pe.wait_ge((i_act, i_dve)[n % 2], NQ // 4)
                for k in range(4):
                    g = 4 * n + k
                    x = pe.transpose(ps_t[:, n % 2, k * P:(k + 1) * P], u[:, g, :, :].rearrange("p j h -> p (j h)"), ident[:, :])
                x.then_inc(g_t, 1)

        def u_out(act, n):
            act.wait_ge(u_mm, n + 1)
            j, half = n // 2, n % 2
            act.activation(u[:, half * NQ:(half + 1) * NQ, j, :], ps_u[:, 2 * (j % 2) + half, :].rearrange("p (g h) -> p g h", g=NQ), ACT.Copy).then_inc(u_done, 1)

        @block.scalar
        def _(act):
            act.wait_ge(ldt_in, 16)
            act.activation(lam[:, 2, :].rearrange("q (a p) -> q a p", a=2), ldt[:, :].unsqueeze(2).to_broadcast([NQ, 2, 64]), ACT.Copy).then_inc(bcast, 1)
            for j in range(L):
                for half in range(2):
                    act.wait_ge(transposed, 2 * j + half + 1)
                    if j >= 2:
                        act.wait_ge(u_mm, 2 * (j - 1))
                    act.activation(hT[:, j % 2, 4 * half:4 * half + 4, :], ps_t[:, half, :].rearrange("p (c t) -> p c t", c=4), ACT.Copy).then_inc(t_copied, 1)
                if j == 1:
                    act.wait_ge(l_done, 1)
                    act.activation(v[:, 0, :], lp[:, 2, :], ACT.Exp).then_inc(acts, 1)
                if j == 2:
                    act.wait_ge(args, 1)
                    act.activation(v[:, 3, :], v[:, 1, :], ACT.Exp).then_inc(acts, 1)
                    act.wait_ge(args, 2)
                    act.activation(v[:, 6, :], v[:, 4, :], ACT.Sin).then_inc(acts, 1)
                    act.activation(v[:, 7, :], v[:, 5, :], ACT.Sin).then_inc(acts, 1)
                if 2 <= j <= 5:
                    act.wait_ge(c_t, j - 1)
                    i, late = (j - 2) // 2, (j - 2) % 2
                    for two in range(2):
                        half = slice(two * 64, (two + 1) * 64)
                        x = act.activation(cT[half, i, 16 * late:16 * late + 16, :],
                                           ps_c[half, :].rearrange("p (q a h) -> p q a h", q=16, a=2)[:, :, two, :], ACT.Copy)
                    x.then_inc(c_copied, 1)
                for n in range(2 * (j - 1) if j else 0, 2 * j):
                    u_out(act, n)
            for n in range(2 * (L - 1), 2 * L):
                u_out(act, n)
            act.wait_ge(out_done, 1)
            for n in range(0, NQ // 2, 2):
                act.wait_ge(i_t, n + 1)
                act.activation(into[:, 2 * n:2 * n + 2, :, :], ps_t[:, 0, :].rearrange("p (q r s) -> p q r s", q=2, r=2), ACT.Copy).then_inc(i_act, 1)
            for n in range(0, NG // 4, 2):
                act.wait_ge(g_t, n + 1)
                act.activation(uT[:, 4 * n:4 * n + 4, :], ps_t[:, 0, :].rearrange("p (c t) -> p c t", c=4), ACT.Copy).then_inc(g_act, 1)

        @block.vector
        def _(dve):
            step = [0]

            def then(ins):
                step[0] += 1
                ins.then_inc(dve_step, 1)
                dve.wait_ge(dve_step, step[0])

            dve.wait_ge(l_t, 1)
            dve.tensor_copy(lp[:, :, :], ps_l[:, :, :]).then_inc(l_done, 1)
            dve.wait_ge(l_done, 1)
            dve.wait_ge(acts, 1)
            lre, lim, dt = lp[:, 0, :], lp[:, 1, :], v[:, 0, :]
            dve.tensor_tensor(v[:, 1, :], lre, dt, ALU.mult).then_inc(args, 1)
            then(dve.tensor_tensor(v[:, 2, :], lim, dt, ALU.mult))
            for out, turn, shift in ((4, 0.0, 0.0), (5, 0.25, math.pi / 2)):
                k = v[:, 8, :]
                then(dve.tensor_scalar(k, v[:, 2, :], 1 / TWO_PI, turn, ALU.mult, ALU.add))
                then(dve.tensor_scalar(k, k, MAGIC, None, ALU.add))
                then(dve.tensor_scalar(k, k, MAGIC, None, ALU.subtract))
                then(dve.scalar_tensor_tensor(out=v[:, out, :], in0=k, scalar=-C1, in1=v[:, 2, :], op0=ALU.mult, op1=ALU.add))
                then(dve.scalar_tensor_tensor(out=v[:, out, :], in0=k, scalar=-C2, in1=v[:, out, :], op0=ALU.mult, op1=ALU.add))
                then(dve.scalar_tensor_tensor(out=v[:, out, :], in0=k, scalar=-C3, in1=v[:, out, :], op0=ALU.mult, op1=ALU.add))
                then(dve.tensor_scalar(v[:, out, :], v[:, out, :], shift, None, ALU.add))
                then(dve.tensor_scalar(v[:, out, :], v[:, out, :], -EDGE, None, ALU.max))
                x = dve.tensor_scalar(v[:, out, :], v[:, out, :], EDGE, None, ALU.min)
                if out == 4:
                    then(x)
            x.then_inc(args, 1)
            then(dve.memset(power[:, 0, 0, :], 1.0))
            then(dve.memset(power[:, 0, 1, :], 0.0))
            dve.wait_ge(acts, 4)
            ar, ai = power[:, 1, 0, :], power[:, 1, 1, :]
            then(dve.tensor_tensor(ar, v[:, 3, :], v[:, 7, :], ALU.mult))
            then(dve.tensor_tensor(ai, v[:, 3, :], v[:, 6, :], ALU.mult))
            t = [v[:, 4 + i, :] for i in range(4)]
            for n in range(2, L + 1):
                pr, pi = power[:, n - 1, 0, :], power[:, n - 1, 1, :]
                then(dve.tensor_tensor(t[0], pr, ar, ALU.mult))
                then(dve.tensor_tensor(t[1], pi, ai, ALU.mult))
                then(dve.tensor_tensor(t[2], pr, ai, ALU.mult))
                then(dve.tensor_tensor(t[3], pi, ar, ALU.mult))
                then(dve.tensor_tensor(power[:, n, 0, :], t[0], t[1], ALU.subtract))
                then(dve.tensor_tensor(power[:, n, 1, :], t[2], t[3], ALU.add))
            for n in range(L):
                then(dve.tensor_copy(reverse[:, L - 1 - n, :, :], power[:, n, :, :]))
            zr, zi = v[:, 10, :], v[:, 11, :]
            then(dve.tensor_tensor(t[0], lre, lre, ALU.mult))
            then(dve.tensor_tensor(t[1], lim, lim, ALU.mult))
            then(dve.tensor_tensor(t[0], t[0], t[1], ALU.add))
            then(dve.reciprocal(v[:, 8, :], t[0]))
            then(dve.tensor_scalar(v[:, 9, :], ar, -1.0, None, ALU.add))
            then(dve.tensor_tensor(t[0], v[:, 9, :], lre, ALU.mult))
            then(dve.tensor_tensor(t[1], ai, lim, ALU.mult))
            then(dve.tensor_tensor(t[2], ai, lre, ALU.mult))
            then(dve.tensor_tensor(t[3], v[:, 9, :], lim, ALU.mult))
            then(dve.tensor_tensor(zr, t[0], t[1], ALU.add))
            then(dve.tensor_tensor(zi, t[2], t[3], ALU.subtract))
            then(dve.tensor_tensor(zr, zr, v[:, 8, :], ALU.mult))
            then(dve.tensor_tensor(zi, zi, v[:, 8, :], ALU.mult))
            dve.wait_ge(b_in, 32)
            zr_, zi_ = (z.unsqueeze(2).to_broadcast([P, NQ, GC]) for z in (zr, zi))
            then(dve.tensor_tensor(tb[:, 0, :, :], b_[:, 0, :, :], zr_, ALU.mult))
            then(dve.tensor_tensor(tb[:, 1, :, :], b_[:, 1, :, :], zi_, ALU.mult))
            then(dve.tensor_tensor(tb[:, 2, :, :], b_[:, 1, :, :], zr_, ALU.mult))
            then(dve.tensor_tensor(tb[:, 3, :, :], b_[:, 0, :, :], zi_, ALU.mult))
            then(dve.tensor_tensor(bbar[:, 0, :, :], tb[:, 0, :, :], tb[:, 1, :, :], ALU.subtract))
            then(dve.tensor_tensor(bbar[:, 1, :, :], tb[:, 2, :, :], tb[:, 3, :, :], ALU.add))
            wide = [P, NQ, L, GC]
            br, bi = (bbar[:, i, :, :].unsqueeze(2).to_broadcast(wide) for i in range(2))
            rr, ri = (reverse[:, :, i, :].rearrange("p j q -> p q j").unsqueeze(3).to_broadcast(wide) for i in range(2))
            gr, gi = g_[:, 0, :, :, :], g_[:, 1, :, :, :]
            then(dve.tensor_tensor(gr, br, rr, ALU.mult))
            then(dve.tensor_tensor(tg, bi, ri, ALU.mult))
            then(dve.tensor_tensor(gr, gr, tg, ALU.subtract))
            then(dve.tensor_tensor(gi, br, ri, ALU.mult))
            then(dve.tensor_tensor(tg, bi, rr, ALU.mult))
            dve.tensor_tensor(gi, gi, tg, ALU.add).then_inc(into_ready, 1)
            dve.wait_ge(c_copied, 4)
            wide = [P, QV, L + 1, GC]
            for q0 in range(0, NQ, QV):
                qs = slice(q0, q0 + QV)
                re, im = out_of[:, 0, qs, :, :], out_of[:, 1, qs, :, :]
                cr, ci = (cT[:, i, qs, :].unsqueeze(2).to_broadcast(wide) for i in range(2))
                ar, ai = (power[:, :, i, qs].rearrange("p t q -> p q t").unsqueeze(3).to_broadcast(wide) for i in range(2))
                then(dve.tensor_tensor(re, cr, ar, ALU.mult))
                then(dve.tensor_tensor(tv, ci, ai, ALU.mult))
                then(dve.tensor_tensor(re, re, tv, ALU.subtract))
                then(dve.tensor_tensor(im, cr, ai, ALU.mult))
                then(dve.tensor_tensor(tv, ci, ar, ALU.mult))
                x = dve.scalar_tensor_tensor(out=im.rearrange("p q t h -> p (q t h)"), in0=im.rearrange("p q t h -> p (q t h)"), scalar=-1.0,
                                             in1=tv.rearrange("p q t h -> p (q t h)"), op0=ALU.mult, op1=ALU.subtract)
                if q0 + QV < NQ:
                    then(x)
            x.then_inc(out_done, 1)
            dve.wait_ge(out_done, 1)
            for n in range(1, NQ // 2, 2):
                dve.wait_ge(i_t, n + 1)
                dve.tensor_copy(into[:, 2 * n:2 * n + 2, :, :], ps_t[:, 1, :].rearrange("p (q r s) -> p q r s", q=2, r=2)).then_inc(i_dve, 1)
            for n in range(1, NG // 4, 2):
                dve.wait_ge(g_t, n + 1)
                dve.tensor_copy(uT[:, 4 * n:4 * n + 4, :], ps_t[:, 1, :].rearrange("p (c t) -> p c t", c=4)).then_inc(g_dve, 1)


def stage_ssm_kernel(nc, d_skip, diag16, bbar, out_of, inside, e_y):
    with ExitStack() as ctx:
        m = Stage(nc, ctx, "sk")
        bpad = m.sb("bpad", [P, 2, NQ, 2, GC])
        taps = e_y[0:2 * GC, :].rearrange("p (q t) -> p q t", q=NQ)
        dT = m.sb("dT", [2 * GC, NQ])
        dg = m.sb("dg", [2 * GC, GC])
        dd = m.sb("dd", [2 * GC, NQ, GC])
        ps_k = m.ps("ps_k", [2 * GC, 2, 512])
        (d_in, pad_done, taps_zero, k_mm, k_done, taps_done, moved, dve_step) = (m.sem(n) for n in
            "d_in pad_done taps_zero k_mm k_done taps_done moved dve_step".split())
        block = ctx.enter_context(nc.Block())

        @block.sync
        def _(sp):
            with nc.allow_non_contiguous_dma(reason="1024 elements"):
                sp.dma_start(dT[:, :], d_skip.rearrange("(q two) h -> (two h) q", two=2)).then_inc(d_in, 16)
            sp.dma_start(dg[:, :], diag16).then_inc(d_in, 16)
            sp.wait_ge(taps_done, 1)
            for i in range(L):
                for two in range(2):
                    sp.dma_start(inside[i * GC:(i + 1) * GC, :, two, :],
                                 taps[two * GC:(two + 1) * GC, :, (L - i) * GC:(L - i) * GC + P]).then_inc(moved, 16)
            sp.wait_ge(moved, 16 * 2 * L)

        @block.gpsimd
        def _(pool):
            pool.memset(taps[:, :, 0:P], 0.0).then_inc(taps_zero, 1)

        @block.tensor
        def _(pe):
            pe.wait_ge(pad_done, 1)
            for n in range(NQ // 4):
                if n >= 2:
                    pe.wait_ge(k_done, n - 1)
                for k in range(4):
                    q = 4 * n + k
                    for i in range(2):
                        x = pe.matmul(ps_k[:, n % 2, k * P:(k + 1) * P], bpad[:, i, q, :, :].rearrange("p a h -> p (a h)"),
                                      out_of[:, i, q, 0:L, :].rearrange("p t h -> p (t h)"), start=(i == 0), stop=(i == 1), skip_group_check=True)
                x.then_inc(k_mm, 1)

        @block.scalar
        def _(act):
            for n in range(NQ // 4):
                act.wait_ge(k_mm, n + 1)
                act.activation(taps[:, 4 * n:4 * n + 4, P:2 * P], ps_k[:, n % 2, :].rearrange("p (q t) -> p q t", q=4), ACT.Copy).then_inc(k_done, 1)

        @block.vector
        def _(dve):
            step = [0]

            def then(ins):
                step[0] += 1
                ins.then_inc(dve_step, 1)
                dve.wait_ge(dve_step, step[0])

            then(dve.memset(bpad[:, :, :, :, :], 0.0))
            for two in range(2):
                h = slice(two * 64, two * 64 + 64)
                x = dve.tensor_copy(bpad[h, :, :, two, :], bbar[h, :, :, :])
            x.then_inc(pad_done, 1)
            dve.wait_ge(d_in, 32)
            then(dve.tensor_tensor(dd[:, :, :], dT[:, :].unsqueeze(2).to_broadcast([2 * GC, NQ, GC]), dg[:, :].unsqueeze(1).to_broadcast([2 * GC, NQ, GC]), ALU.mult))
            dve.wait_ge(k_done, NQ // 4)
            dve.wait_ge(taps_zero, 1)
            dve.tensor_tensor(taps[:, :, P:P + GC], taps[:, :, P:P + GC], dd[:, :, :], ALU.add).then_inc(taps_done, 1)


def complex_product(dve, then, out, x, y, t):
    dve.tensor_tensor(t[0], x[0], y[0], ALU.mult)
    dve.tensor_tensor(t[1], x[1], y[1], ALU.mult)
    dve.tensor_tensor(t[2], x[0], y[1], ALU.mult)
    then(dve.tensor_tensor(t[3], x[1], y[0], ALU.mult))
    dve.tensor_tensor(out[0], t[0], t[1], ALU.subtract)
    then(dve.tensor_tensor(out[1], t[2], t[3], ALU.add))


def stage_ssm_scan(nc, uT, power, powers, into, out_of, inside, e_y):
    with ExitStack() as ctx:
        m = Stage(nc, ctx, "sc")
        K = 16
        B = NC // K
        QG = 4
        st = m.sb("st", [P, NC, 2, NQ])
        mul = m.sb("mul", [P, 2, 2, NQ])
        room = into[:, :, :, :].rearrange("p q i s -> p (q i s)")
        tmp = room[:, 0:2 * B * 2 * NQ].rearrange("p (k b s) -> p k b s", k=2, b=B)
        ends = room[:, 1024:1024 + B * 2 * NQ].rearrange("p (b s) -> p b s", b=B)
        terms = [room[:, 2048 + n * B * (K - 1) * QG:2048 + (n + 1) * B * (K - 1) * QG].rearrange("p (b k q) -> p b k q", b=B, q=QG) for n in range(4)]
        AHEAD_Y = 8
        ps_y = m.ps("ps_y", [P, AHEAD_Y, 512])
        ps_e = ps_y
        (e_mm, e_act, e_dve, carried, y_mm, y_done, dve_step, sweep_step) = (m.sem(n) for n in
            "e_mm e_act e_dve carried y_mm y_done dve_step sweep_step".split())
        e = e_y[:, :].rearrange("p (c i q) -> p c i q", i=2, q=NQ)
        y = e_y[:, :].rearrange("p (j d) -> p j d", j=L)
        block = ctx.enter_context(nc.Block())

        @block.tensor
        def _(pe):
            for n in range(NQ // 2):
                if n >= 4:
                    pe.wait_ge((e_act, e_dve)[n % 2], (n - 4) // 2 + 1)
                for k in range(4):
                    q, i = 2 * n + k // 2, k % 2
                    for two in range(2):
                        x = pe.matmul(ps_e[two * 64:(two + 1) * 64, n % 4, k * P:(k + 1) * P], into[:, q, i, two * 64:(two + 1) * 64],
                                      uT[:, 2 * q + two, :], start=True, stop=True, skip_group_check=True)
                x.then_inc(e_mm, 1)

            def within(n):
                for k in range(4):
                    q = 4 * (n // 2) + k
                    pe.matmul(ps_y[:, n % AHEAD_Y, k * P:(k + 1) * P], uT[:, 2 * q + n % 2, :], inside[:, q, n % 2, :],
                              start=(k == 0), stop=False, skip_group_check=True)

            def before(n):
                half = slice(n % 2 * 64, (n % 2 + 1) * 64)
                for k in range(4):
                    q = 4 * (n // 2) + k
                    for i in range(2):
                        x = pe.matmul(ps_y[:, n % AHEAD_Y, k * P:(k + 1) * P], st[half, 0:NC, i, q], out_of[half, i, q, 1:L + 1, :].rearrange("p t h -> p (t h)"),
                                      start=False, stop=(i == 1), skip_group_check=True)
                x.then_inc(y_mm, 1)

            pe.wait_ge(e_act, NQ // 4)
            pe.wait_ge(e_dve, NQ // 4)
            for n in range(AHEAD_Y):
                within(n)
            for n in range(NG // 4):
                if n % 2 == 0:
                    pe.wait_ge(carried, n // 2 + 1)
                if n >= AHEAD_Y:
                    pe.wait_ge(y_done, n - AHEAD_Y + 1)
                    within(n)
                before(n)

        def copy_e(eng, n, sem):
            eng.wait_ge(e_mm, n + 1)
            out = e[:, :, :, 2 * n:2 * n + 2].rearrange("p c i q -> p q i c")
            src = ps_e[:, n % 4, :].rearrange("p (q i c) -> p q i c", q=2, i=2)
            (eng.activation(out, src, ACT.Copy) if sem is e_act else eng.tensor_copy(out, src)).then_inc(sem, 1)

        @block.scalar
        def _(act):
            for n in range(0, NQ // 2, 2):
                copy_e(act, n, e_act)
            for n in range(NG // 4):
                act.wait_ge(y_mm, n + 1)
                two = n % 2
                out = y.rearrange("p j (q g) -> p q j g", g=2 * GC)[:, 4 * (n // 2):4 * (n // 2) + 4, :, two * GC:(two + 1) * GC]
                act.activation(out, ps_y[:, n % AHEAD_Y, :].rearrange("p (q j h) -> p q j h", q=4, j=L), ACT.Gelu_apprx_tanh).then_inc(y_done, 1)

        @block.vector
        def _(dve):
            step = [0]

            def then(ins):
                step[0] += 1
                ins.then_inc(dve_step, 1)
                dve.wait_ge(dve_step, step[0])

            dve.memset(st[:, :, :, :].rearrange("p (b k) i q -> p b k (i q)", k=K)[:, :, 0, :], 0.0)
            dve.tensor_copy(mul[:, 0, 0, :], power[:, L, 0, :])
            dve.tensor_copy(mul[:, 0, 1, :], power[:, L, 0, :])
            dve.tensor_copy(mul[:, 1, 0, :], power[:, L, 1, :])
            dve.tensor_scalar(mul[:, 1, 1, :], power[:, L, 1, :], -1.0, None, ALU.mult)
            dve.tensor_copy(powers[:, 0, 0, :], power[:, L, 0, :])
            then(dve.tensor_copy(powers[:, 0, 1, :], power[:, L, 1, :]))
            for n in range(1, NQ // 2, 2):
                copy_e(dve, n, e_dve)
            dve.wait_ge(e_act, NQ // 4)
            dve.wait_ge(e_dve, NQ // 4)
            n = 1
            while n < K:
                wide = [P, n, NQ]
                top = [powers[:, n - 1, i, :].unsqueeze(1).to_broadcast(wide) for i in range(2)]
                t = [room[:, 2048 + k * 512:2048 + k * 512 + n * NQ].rearrange("p (k q) -> p k q", q=NQ) for k in range(4)]
                complex_product(dve, then, [powers[:, n:2 * n, i, :] for i in range(2)], [powers[:, 0:n, i, :] for i in range(2)], top, t)
                n *= 2
            state = st[:, :, :, :].rearrange("p (b k) i q -> p b k (i q)", k=K)
            own = e_y[:, :].rearrange("p (b k s) -> p b k s", b=B, k=K)
            m0, m1 = (mul[:, k, :, :].rearrange("p i q -> p (i q)").unsqueeze(1).to_broadcast([P, B, 2 * NQ]) for k in range(2))
            t0, t1 = tmp[:, 0, :, :], tmp[:, 1, :, :]
            dve.tensor_copy(state[:, :, 1, :], own[:, :, 0, :]).then_inc(sweep_step, 3)

            def advance(k, now, mine, new):
                dve.wait_ge(sweep_step, k * 3)
                dve.tensor_tensor(t0, now, m0, ALU.mult)
                dve.tensor_tensor(t1, now, m1, ALU.mult).then_inc(sweep_step, 1)
                dve.wait_ge(sweep_step, k * 3 + 1)
                dve.tensor_tensor(t0, t0, mine, ALU.add).then_inc(sweep_step, 1)
                dve.wait_ge(sweep_step, k * 3 + 2)
                dve.tensor_tensor(new[:, :, 0:NQ], t0[:, :, 0:NQ], t1[:, :, NQ:2 * NQ], ALU.add)
                dve.tensor_tensor(new[:, :, NQ:2 * NQ], t0[:, :, NQ:2 * NQ], t1[:, :, 0:NQ], ALU.add).then_inc(sweep_step, 1)

            def at(x, k):
                return x[:, :, bass.ds(k, 1), :].rearrange("p b a s -> p b (a s)")

            with dve.Fori(1, K - 1) as k:
                advance(k, at(state, k), at(own, k), at(state, k + 1))
            advance(K - 1, state[:, :, K - 1, :], own[:, :, K - 1, :], ends)
            dve.wait_ge(sweep_step, 3 * K)
            first = st[:, :, :, :].rearrange("p (b k) i q -> p b k i q", k=K)[:, :, 0, :, :]
            end = ends.rearrange("p b (i q) -> p b i q", i=2)
            whole = [powers[:, K - 1, i, :] for i in range(2)]
            then(dve.tensor_copy(first[:, 1, :, :], end[:, 0, :, :]))
            for b in range(1, B - 1):
                cr, ci = first[:, b, 0, :], first[:, b, 1, :]
                t = [room[:, 2048 + k * NQ:2048 + (k + 1) * NQ] for k in range(4)]
                dve.tensor_tensor(t[0], cr, whole[0], ALU.mult)
                dve.tensor_tensor(t[1], ci, whole[1], ALU.mult)
                dve.tensor_tensor(t[2], cr, whole[1], ALU.mult)
                then(dve.tensor_tensor(t[3], ci, whole[0], ALU.mult))
                dve.tensor_tensor(t[0], t[0], t[1], ALU.subtract)
                then(dve.tensor_tensor(t[2], t[2], t[3], ALU.add))
                dve.tensor_tensor(first[:, b + 1, 0, :], end[:, b, 0, :], t[0], ALU.add)
                then(dve.tensor_tensor(first[:, b + 1, 1, :], end[:, b, 1, :], t[2], ALU.add))
            wide = [P, B, K - 1, QG]
            for part in range(NQ // QG):
                qs = slice(part * QG, (part + 1) * QG)
                cr, ci = (first[:, :, i, qs].unsqueeze(2).to_broadcast(wide) for i in range(2))
                pr, pi = (powers[:, 0:K - 1, i, qs].unsqueeze(1).to_broadcast(wide) for i in range(2))
                sr, si = (st[:, :, i, qs].rearrange("p (b k) q -> p b k q", k=K)[:, :, 1:K, :] for i in range(2))
                dve.tensor_tensor(terms[0], cr, pr, ALU.mult)
                dve.tensor_tensor(terms[1], ci, pi, ALU.mult)
                dve.tensor_tensor(terms[2], cr, pi, ALU.mult)
                then(dve.tensor_tensor(terms[3], ci, pr, ALU.mult))
                dve.tensor_tensor(sr, sr, terms[0], ALU.add)
                then(dve.tensor_tensor(si, si, terms[2], ALU.add))
                dve.tensor_tensor(sr, sr, terms[1], ALU.subtract)
                dve.tensor_tensor(si, si, terms[3], ALU.add).then_inc(carried, 1)
                dve.wait_ge(carried, part + 1)


def stage_ssm_out(nc, h, w_glu, w_out, g, b, ident, e_y, h_out):
    with ExitStack() as ctx:
        m = Stage(nc, ctx, "so")
        y = e_y[:, :].rearrange("p (j d) -> p j d", j=L)
        w = m.sb("w", [P, 2, KC, D])
        yT = m.sb("yT", [P, KC, S])
        sg = m.sb("sg", [P, 2, 512])
        o_ = m.sb("o", [P, 2, D])
        z = m.sb("z", [P, KC, 512])
        hr = m.sb("hr", [P, 2, D])
        norm = Norm(m, "ln")
        ps_t = m.ps("ps_t", [P, 2, 512])
        ps_z = m.ps("ps_z", [P, 2, 512])
        ps_o = m.ps("ps_o", [P, 2, D])
        (wg_in, wo_in, transposed, t_act, t_dve, z_mm, sig_done, z_done, o_mm, o_read, o_ready, dve_step) = (m.sem(n) for n in
            "wg_in wo_in transposed t_act t_dve z_mm sig_done z_done o_mm o_read o_ready dve_step".split())
        h_in = [m.sem(f"h_in{k}") for k in range(2)]
        stored = [m.sem(f"stored{k}") for k in range(2)]
        rows = h.rearrange("(c j) d -> j c d", j=L)
        out_rows = h_out.rearrange("(c j) d -> j c d", j=L)
        block = ctx.enter_context(nc.Block())

        @block.sync
        def _(sp):
            sp.dma_start(w[:, 0, :, :], w_glu.rearrange("(c p) n -> p c n", p=P)).then_inc(wg_in, 16)
            sp.dma_start(w[:, 1, :, :], w_out.rearrange("(c p) n -> p c n", p=P)).then_inc(wo_in, 16)
            norm.load(sp, g, b)
            for j in range(L):
                if j >= 2:
                    sp.wait_ge(o_read, j - 1)
                sp.dma_start(hr[:, j % 2, :], rows[j]).then_inc(h_in[j % 2], 16)
                if j:
                    sp.wait_ge(o_ready, j)
                    sp.dma_start(out_rows[j - 1], o_[:, (j - 1) % 2, :]).then_inc(stored[(j - 1) % 2], 16)
            sp.wait_ge(o_ready, L)
            sp.dma_start(out_rows[L - 1], o_[:, (L - 1) % 2, :]).then_inc(stored[(L - 1) % 2], 16)
            for k in range(2):
                sp.wait_ge(stored[k], 16 * L // 2)

        @block.tensor
        def _(pe):
            for n in range(2 * L):
                j, c0 = n // 2, 4 * (n % 2)
                if n >= 2:
                    pe.wait_ge((t_act, t_dve)[n % 2], n // 2)
                for c in range(4):
                    x = pe.transpose(ps_t[:, n % 2, c * P:(c + 1) * P], y[:, j, (c0 + c) * P:(c0 + c + 1) * P], ident[:, :])
                x.then_inc(transposed, 1)
            pe.wait_ge(wg_in, 16)
            pe.wait_ge(t_act, L)
            pe.wait_ge(t_dve, L)
            for half in range(2):
                for f in range(KC):
                    u = half * KC + f
                    if u >= 2:
                        pe.wait_ge(sig_done, u - 1)
                    for c in range(KC):
                        x = pe.matmul(ps_z[:, u % 2, :], w[:, 0, c, f * P:(f + 1) * P], yT[:, c, half * 512:(half + 1) * 512], start=(c == 0), stop=(c == KC - 1))
                    x.then_inc(z_mm, 1)
                pe.wait_ge(z_done, (half + 1) * KC)
                pe.wait_ge(wo_in, 16)
                for jj in range(4):
                    j = half * 4 + jj
                    if j >= 2:
                        pe.wait_ge(o_read, j - 1)
                    for oh in range(2):
                        for c in range(KC):
                            x = pe.matmul(ps_o[:, j % 2, oh * 512:(oh + 1) * 512], z[:, c, jj * P:(jj + 1) * P], w[:, 1, c, oh * 512:(oh + 1) * 512],
                                          start=(c == 0), stop=(c == KC - 1))
                    x.then_inc(o_mm, 1)

        @block.scalar
        def _(act):
            for j in range(L):
                act.wait_ge(transposed, 2 * j + 1)
                act.activation(yT[:, 0:4, j * P:(j + 1) * P], ps_t[:, 0, :].rearrange("p (c t) -> p c t", c=4), ACT.Copy).then_inc(t_act, 1)
            for half in range(2):
                for f in range(KC):
                    u = half * KC + f
                    act.wait_ge(z_mm, u + 1)
                    if u >= 2:
                        act.wait_ge(z_done, u - 1)
                    act.activation(sg[:, u % 2, :], ps_z[:, u % 2, :], ACT.Sigmoid).then_inc(sig_done, 1)
                for jj in range(4):
                    norm.on_act(act, half * 4 + jj)

        @block.vector
        def _(dve):
            step = [0]

            def then(ins):
                step[0] += 1
                ins.then_inc(dve_step, 1)
                dve.wait_ge(dve_step, step[0])

            for j in range(L):
                dve.wait_ge(transposed, 2 * j + 2)
                dve.tensor_copy(yT[:, 4:8, j * P:(j + 1) * P], ps_t[:, 1, :].rearrange("p (c t) -> p c t", c=4)).then_inc(t_dve, 1)
            dve.wait_ge(t_act, L)
            dve.wait_ge(t_dve, L)
            for half in range(2):
                if half:
                    dve.wait_ge(o_mm, 4)
                for f in range(KC):
                    u = half * KC + f
                    dve.wait_ge(sig_done, u + 1)
                    dve.tensor_tensor(z[:, f, :], sg[:, u % 2, :], yT[:, f, half * 512:(half + 1) * 512], ALU.mult).then_inc(z_done, 1)
                for jj in range(4):
                    j = half * 4 + jj
                    dve.wait_ge(o_mm, j + 1)
                    dve.wait_ge(h_in[j % 2], 16 * (j // 2 + 1))
                    if j >= 2:
                        dve.wait_ge(stored[j % 2], 16 * (j // 2))
                    oo = o_[:, j % 2, :]
                    dve.scalar_tensor_tensor(out=oo, in0=hr[:, j % 2, :], scalar=ALPHA, in1=ps_o[:, j % 2, :], op0=ALU.mult, op1=ALU.add).then_inc(o_read, 1)
                    dve.wait_ge(o_read, j + 1)
                    norm.on_dve(dve, then, oo, j).then_inc(o_ready, 1)


def ssm_layer(nc, h, w, ln_g, ln_b, consts, h_out):
    w_in, lam_re, lam_im, b_re, b_im, c_re, c_im, d_skip, log_dt, w_glu, w_out = w
    with ExitStack() as outer:
        m = Stage(nc, outer, "ss")
        ident = m.sb("ident", [P, P])
        e_y = m.sb("e_y", [P, L * D])
        with ExitStack() as ctx:
            k = Stage(nc, ctx, "sb_")
            uT = k.sb("uT", [P, NG, NC])
            power = k.sb("power", [P, L + 1, 2, NQ])
            bbar = k.sb("bbar", [P, 2, NQ, GC])
            into = k.sb("into", [P, NQ, 2, P])
            out_of = k.sb("out_of", [P, 2, NQ, L + 1, GC])
            with ExitStack() as c2:
                reverse = Stage(nc, c2, "sr").sb("reverse", [P, L, 2, NQ])
                stage_ssm_input(nc, h, w_in, lam_re, lam_im, log_dt, b_re, b_im, c_re, c_im, consts["c_ident"], ident, e_y, uT, power, reverse, bbar, into, out_of)
            inside = k.sb("inside", [P, NQ, 2, P])
            stage_ssm_kernel(nc, d_skip, consts["c_diag16"], bbar, out_of, inside, e_y)
            stage_ssm_scan(nc, uT, power, bbar[:, :, :, :].rearrange("p a q h -> p (a q h)").rearrange("p (k i q) -> p k i q", i=2, q=NQ), into, out_of, inside, e_y)
        stage_ssm_out(nc, h, w_glu, w_out, ln_g, ln_b, ident, e_y, h_out)


def trunk(nc, a, consts, out):
    after = [nc.dram_tensor(f"h{n}", (S, D), F32, kind="Internal").ap() for n in range(3)]
    expert_rows = nc.dram_tensor("expert_rows", (NBLK * CAP, D), F32, kind="Internal").ap()
    x = a["x"].rearrange("b s d -> (b s) d")

    def layer(n, names):
        return [a[f"l{n}_{k}"] for k in names.split()]

    moe_names = "router router_bias w_gate w_up w_down sh_gate sh_up sh_down"
    with ExitStack() as ctx:
        keep = keep_attention(nc, ctx)
        stage_project(nc, x, a["l0_w_in"], consts["c_cos"], consts["c_sin"], consts["c_ident"], keep)
        stage_stick(nc, consts["c_stick"], expert_rows, keep)
        stage_compress(nc, *layer(0, "cmp_pos_k cmp_pos_v cmp_k_w1 cmp_k_w2 cmp_v_w1 cmp_v_w2"), consts["c_cmp"], consts["c_imp"], keep)
        stage_selected(nc, consts["c_win"], keep)
        stage_attention_out(nc, a["l0_w_out"], x, a["l0_ln1_g"], a["l0_ln1_b"], keep, after[0])
    moe_layer(nc, "m0", expert_rows, after[0], layer(0, moe_names), a["l0_ln2_g"], a["l0_ln2_b"], consts, after[1])
    ssm_layer(nc, after[1], layer(1, "w_in lambda_re lambda_im b_re b_im c_re c_im d log_dt w_glu w_out"),
              a["l1_ln1_g"], a["l1_ln1_b"], consts, after[2])
    moe_layer(nc, "m1", expert_rows, after[2], layer(1, moe_names), a["l1_ln2_g"], a["l1_ln2_b"], consts, out)


def kernel(**inputs):
    import concourse.bacc as _bacc
    from concourse.bass_utils import run_bass_kernel_spmd as _run

    nc = _bacc.Bacc("TRN2", target_bir_lowering=False, num_devices=1)
    arrays, tensors, consts = {}, {}, {}
    for name, array in inputs.items():
        array = np.ascontiguousarray(array)
        arrays[f"in_{name}"] = array
        tensors[name] = nc.dram_tensor(f"in_{name}", array.shape, mybir.dt.from_np(array.dtype), kind="ExternalInput").ap()
    for name, array in const_arrays().items():
        arrays[name] = array
        consts[name] = nc.dram_tensor(name, array.shape, F32, kind="ExternalInput").ap()
    out = nc.dram_tensor("out_0", (1, S, D), F32, kind="ExternalOutput").ap()
    trunk(nc, tensors, consts, out.rearrange("b s d -> (b s) d"))
    result = _run(nc, [arrays], core_ids=[0])
    return result.results[0]["out_0"]
```
